# Optimizing a Trainium2 kernel written in Bass

```python
import jax, jax.numpy as jnp
from jax import lax
import numpy as np
import math
import jax
import jax.numpy as jnp

D_MODEL = 1024
BATCH = 1
SEQ = 512
DEPTH = 1

HEAD_DIM = 64
N_RWKV_HEADS = 8
RWKV_WIDTH = N_RWKV_HEADS * HEAD_DIM
DECAY_LORA = 64
AAA_LORA = 64
GATE_LORA = 128
GN_EPS = 64e-5
N_Q_HEADS = 8
N_KV_HEADS = 2
Q_PER_KV = N_Q_HEADS // N_KV_HEADS
ATTN_WIDTH = N_Q_HEADS * HEAD_DIM
KV_WIDTH = N_KV_HEADS * HEAD_DIM
WINDOW = 128
BLOCK = 128
RWKV_COLS = 3 * RWKV_WIDTH + DECAY_LORA + AAA_LORA + GATE_LORA
ATTN_COLS = ATTN_WIDTH + 2 * KV_WIDTH
IN_COLS = RWKV_COLS + ATTN_COLS
MIX_WIDTH = RWKV_WIDTH + ATTN_WIDTH
D_FF = 2816
NORM_EPS = 1e-5


def rms_norm(x, g):
    xf = x.astype(jnp.float32)
    y = xf * lax.rsqrt(jnp.mean(xf * xf, axis=-1, keepdims=True) + NORM_EPS)
    return (y * g.astype(jnp.float32)).astype(x.dtype)

def swiglu(x, w_gate, w_up, w_down):
    return (jax.nn.silu(x @ w_gate) * (x @ w_up)) @ w_down

def rwkv7_time_mix(p, shift_mix, w0, w2, a0, a2, g2, k_k, k_a, r_k, ln_w, ln_b):
    f32 = jnp.float32
    B, S, _ = p.shape
    H, N = N_RWKV_HEADS, HEAD_DIM
    p = p.astype(f32)
    p_prev = jnp.pad(p, ((0, 0), (1, 0), (0, 0)))[:, :-1]
    p = p + (p_prev - p) * shift_mix.astype(f32)
    cuts = [RWKV_WIDTH, 2 * RWKV_WIDTH, 3 * RWKV_WIDTH,
            3 * RWKV_WIDTH + DECAY_LORA, 3 * RWKV_WIDTH + DECAY_LORA + AAA_LORA]
    r, k, v, w_lo, a_lo, g_lo = jnp.split(p, cuts, axis=-1)
    w = -jax.nn.softplus(-(w0.astype(f32) + jnp.tanh(w_lo) @ w2.astype(f32))) - 0.5
    a = jax.nn.sigmoid(a0.astype(f32) + a_lo @ a2.astype(f32))
    g = jax.nn.sigmoid(g_lo) @ g2.astype(f32)
    kk = (k * k_k.astype(f32)).reshape(B, S, H, N)
    kk = kk / jnp.maximum(jnp.sqrt(jnp.sum(kk * kk, axis=-1, keepdims=True)), 1e-12)
    k = k * (1.0 + (a - 1.0) * k_a.astype(f32))
    rh, kh, vh, ah = [t.reshape(B, S, H, N) for t in (r, k, v, a)]
    decay = jnp.exp(-jnp.exp(w)).reshape(B, S, H, N)
    bh = kk * ah

    def step(state, inp):
        r_t, w_t, k_t, v_t, kk_t, b_t = inp
        sa = jnp.einsum('bhvk,bhk->bhv', state, -kk_t)
        state = (state * w_t[:, :, None, :] + sa[..., None] * b_t[:, :, None, :]
                 + v_t[..., None] * k_t[:, :, None, :])
        return state, jnp.einsum('bhvk,bhk->bhv', state, r_t)

    seq_first = lambda t: jnp.moveaxis(t, 1, 0)
    s0 = jnp.zeros((B, H, N, N), f32)
    _, o = lax.scan(step, s0, tuple(seq_first(t) for t in (rh, decay, kh, vh, kk, bh)))
    o = jnp.moveaxis(o, 0, 1)
    mu = jnp.mean(o, axis=-1, keepdims=True)
    var = jnp.mean(jnp.square(o - mu), axis=-1, keepdims=True)
    o = ((o - mu) * lax.rsqrt(var + GN_EPS)).reshape(B, S, RWKV_WIDTH)
    o = o * ln_w.astype(f32) + ln_b.astype(f32)
    bonus = jnp.sum(rh * kh * r_k.astype(f32), axis=-1, keepdims=True) * vh
    return (o + bonus.reshape(B, S, RWKV_WIDTH)) * g

def sliding_window_sink_attention(q, k, v, sinks):
    f32 = jnp.float32
    B, S, _ = q.shape
    nb = S // BLOCK
    qb = q.astype(f32).reshape(B, nb, BLOCK, N_KV_HEADS, Q_PER_KV, HEAD_DIM)
    kb = k.astype(f32).reshape(B, nb, BLOCK, N_KV_HEADS, HEAD_DIM)
    vb = v.astype(f32).reshape(B, nb, BLOCK, N_KV_HEADS, HEAD_DIM)

    def with_prev_block(t):
        prev = jnp.pad(t, ((0, 0), (1, 0), (0, 0), (0, 0), (0, 0)))[:, :-1]
        return jnp.concatenate([prev, t], axis=2)

    kb, vb = with_prev_block(kb), with_prev_block(vb)
    scores = jnp.einsum('bnqhgd,bnkhd->bnhgqk', qb, kb) * (HEAD_DIM ** -0.5)
    qi = jnp.arange(BLOCK)[:, None]
    kj = jnp.arange(2 * BLOCK)[None, :]
    dist = qi + BLOCK - kj
    band = (dist >= 0) & (dist < WINDOW)
    valid = band[None] & ((jnp.arange(nb)[:, None, None] > 0) | (kj[None] >= BLOCK))
    scores = jnp.where(valid[None, :, None, None], scores, -jnp.inf)
    sink = jnp.broadcast_to(sinks.astype(f32).reshape(N_KV_HEADS, Q_PER_KV, 1, 1),
                            scores.shape[:-1] + (1,))
    probs = jax.nn.softmax(jnp.concatenate([scores, sink], axis=-1), axis=-1)[..., :-1]
    out = jnp.einsum('bnhgqk,bnkhd->bnqhgd', probs, vb)
    return out.reshape(B, S, ATTN_WIDTH)

def first_inputs(seed: int = 0) -> dict:
    key = jax.random.key(seed)
    ks = jax.random.split(key, 26)
    L, D, F, R = DEPTH, D_MODEL, D_FF, RWKV_WIDTH
    nrm = lambda i, shape, scale: scale * jax.random.normal(ks[i], shape, jnp.float32)
    chan = jnp.arange(R, dtype=jnp.float32) / (R - 1)
    w0_base = -5.5 + 5.0 * chan ** 0.85
    return {
        'x': nrm(0, (BATCH, SEQ, D), 1.0),
        'norm_ffn1': 1.0 + nrm(1, (L, D), 0.01),
        'ffn1_gate': nrm(2, (L, D, F), D ** -0.5),
        'ffn1_up': nrm(3, (L, D, F), D ** -0.5),
        'ffn1_down': nrm(4, (L, F, D), F ** -0.5),
        'norm_mix': 1.0 + nrm(5, (L, D), 0.01),
        'w_in': nrm(6, (L, D, IN_COLS), D ** -0.5),
        'b_in_attn': nrm(7, (L, ATTN_COLS), 0.01),
        'rwkv_shift_mix': jax.random.uniform(ks[8], (L, RWKV_COLS), jnp.float32),
        'rwkv_w0': w0_base[None, :] + nrm(9, (L, R), 0.1),
        'rwkv_w2': nrm(10, (L, DECAY_LORA, R), 0.1 * DECAY_LORA ** -0.5),
        'rwkv_a0': nrm(11, (L, R), 0.1),
        'rwkv_a2': nrm(12, (L, AAA_LORA, R), AAA_LORA ** -0.5),
        'rwkv_g2': nrm(13, (L, GATE_LORA, R), GATE_LORA ** -0.5),
        'rwkv_k_k': 0.85 + nrm(14, (L, R), 0.05),
        'rwkv_k_a': 1.0 + nrm(15, (L, R), 0.05),
        'rwkv_r_k': nrm(16, (L, N_RWKV_HEADS, HEAD_DIM), 0.1),
        'rwkv_ln_w': 1.0 + nrm(17, (L, R), 0.01),
        'rwkv_ln_b': nrm(18, (L, R), 0.01),
        'attn_sinks': nrm(19, (L, N_Q_HEADS), 1.0),
        'w_out': nrm(20, (L, MIX_WIDTH, D), 0.5 * MIX_WIDTH ** -0.5),
        'norm_ffn2': 1.0 + nrm(21, (L, D), 0.01),
        'ffn2_gate': nrm(22, (L, D, F), D ** -0.5),
        'ffn2_up': nrm(23, (L, D, F), D ** -0.5),
        'ffn2_down': nrm(24, (L, F, D), F ** -0.5),
        'norm_final': 1.0 + nrm(25, (D,), 0.01),
    }

def first_block(x, norm_ffn1, ffn1_gate, ffn1_up, ffn1_down, norm_mix, w_in, b_in_attn,
              rwkv_shift_mix, rwkv_w0, rwkv_w2, rwkv_a0, rwkv_a2, rwkv_g2, rwkv_k_k, rwkv_k_a,
              rwkv_r_k, rwkv_ln_w, rwkv_ln_b, attn_sinks, w_out, norm_ffn2, ffn2_gate, ffn2_up,
              ffn2_down, norm_final):
    for l in range(DEPTH):
        h = rms_norm(x, norm_ffn1[l])
        x = x + 0.5 * swiglu(h, ffn1_gate[l], ffn1_up[l], ffn1_down[l])
        h = rms_norm(x, norm_mix[l])
        p = h @ w_in[l]
        p_rwkv = p[..., :RWKV_COLS]
        p_attn = p[..., RWKV_COLS:] + b_in_attn[l]
        q, k, v = jnp.split(p_attn, [ATTN_WIDTH, ATTN_WIDTH + KV_WIDTH], axis=-1)
        o_rwkv = rwkv7_time_mix(p_rwkv, rwkv_shift_mix[l], rwkv_w0[l], rwkv_w2[l], rwkv_a0[l],
                                rwkv_a2[l], rwkv_g2[l], rwkv_k_k[l], rwkv_k_a[l], rwkv_r_k[l],
                                rwkv_ln_w[l], rwkv_ln_b[l])
        o_attn = sliding_window_sink_attention(q, k, v, attn_sinks[l])
        mixed = jnp.concatenate([o_rwkv.astype(x.dtype), o_attn.astype(x.dtype)], axis=-1)
        x = x + mixed @ w_out[l]
        h = rms_norm(x, norm_ffn2[l])
        x = x + 0.5 * swiglu(h, ffn2_gate[l], ffn2_up[l], ffn2_down[l])
    return rms_norm(x, norm_final)


_first_inputs = first_inputs


def first_inputs(seed=0):
    import zlib

    import numpy as np

    out = dict(_first_inputs(seed))
    spreads = {}
    factors = {'norm_ffn1': 8.0,
     'norm_mix': 8.0,
     'b_in_attn': 200.0,
     'rwkv_w2': 64.0,
     'rwkv_a0': 6.991,
     'rwkv_k_k': 200.0,
     'rwkv_k_a': 5.552,
     'rwkv_ln_w': 200.0,
     'rwkv_ln_b': 200.0,
     'attn_sinks': 200.0,
     'norm_ffn2': 200.0,
     'norm_final': 175.966,
     'rwkv_w0': 7.499}
    for name, (base, spread) in spreads.items():
        noise = np.random.default_rng([zlib.crc32(name.encode()), seed]).standard_normal(out[name].shape)
        drawn = base * np.exp(spread * noise) if base else spread * noise
        out[name] = __import__('jax').numpy.asarray(drawn.astype(out[name].dtype))
    for name, factor in factors.items():
        out[name] = (out[name] * factor).astype(out[name].dtype)
    return out


_narrow_inputs = first_inputs


def first_inputs(seed=0):

    out = dict(_narrow_inputs(seed))
    wider = {'b_in_attn': 4.36,
     'rwkv_ln_w': 12.0,
     'rwkv_ln_b': 12.0,
     'attn_sinks': 4.54,
     'norm_ffn2': 4.39,
     'norm_final': 6.31}
    for name, times in wider.items():
        mean = out[name].mean()
        out[name] = (mean + times * (out[name] - mean)).astype(out[name].dtype)
    return out


CHUNK = 64
D_RNN = 1280
RNN_HEADS = 20
RNN_HEAD_DIM = D_RNN // RNN_HEADS
CONV_WIDTH = 4
LRU_C = 8.0
D_SGU = 1024
SGU_GROUPS = 8
SGU_GROUP_DIM = D_SGU // SGU_GROUPS
SGU_BLOCK = 128
N_BRANCH = 2
D_FF_2 = 4 * D_MODEL
D_IN = 2 * D_RNN + 2 * D_SGU + N_BRANCH * D_MODEL
EPS = 1e-6


def rmsnorm(x, g):
    xf = x.astype(jnp.float32)
    y = xf * lax.rsqrt(jnp.mean(xf * xf, axis=-1, keepdims=True) + EPS)
    return (y * g.astype(jnp.float32)).astype(x.dtype)

def layernorm(x, g, b):
    xf = x.astype(jnp.float32)
    mu = jnp.mean(xf, axis=-1, keepdims=True)
    xc = xf - mu
    y = xc * lax.rsqrt(jnp.mean(xc * xc, axis=-1, keepdims=True) + EPS)
    return (y * g.astype(jnp.float32) + b.astype(jnp.float32)).astype(x.dtype)

def causal_depthwise_conv(x, w, b):
    s = x.shape[1]
    xp = jnp.pad(x, ((0, 0), (CONV_WIDTH - 1, 0), (0, 0)))
    y = b
    for k in range(CONV_WIDTH):
        y = y + xp[:, k:k + s, :] * w[k]
    return y

def rg_lru(x, w_a, b_a, w_x, b_x, lam):
    bsz, s, _ = x.shape
    xh = x.reshape(bsz, s, RNN_HEADS, RNN_HEAD_DIM)
    r = jax.nn.sigmoid(jnp.einsum('bshi,hij->bshj', xh, w_a) + b_a).reshape(bsz, s, D_RNN)
    i = jax.nn.sigmoid(jnp.einsum('bshi,hij->bshj', xh, w_x) + b_x).reshape(bsz, s, D_RNN)
    log_a = (-LRU_C * r.astype(jnp.float32)) * jax.nn.softplus(-lam.astype(jnp.float32))
    a = jnp.exp(log_a)
    norm = jnp.sqrt(-jnp.expm1(2.0 * log_a))
    u = norm * (i * x).astype(jnp.float32)

    def combine(left, right):
        a_l, b_l = left
        a_r, b_r = right
        return a_l * a_r, a_r * b_l + b_r

    _, h = lax.associative_scan(combine, (a, u), axis=1)
    return h.astype(x.dtype)

def spatial_gating(u, v, w_s, b_s, ln_g, ln_b):
    bsz, s, _ = u.shape
    nblk = s // SGU_BLOCK
    v = layernorm(v, ln_g, ln_b)
    vb = v.reshape(bsz, nblk, SGU_BLOCK, SGU_GROUPS, SGU_GROUP_DIM)
    chunk_id = jnp.arange(SGU_BLOCK) // CHUNK
    mask = (chunk_id[:, None] >= chunk_id[None, :]).astype(w_s.dtype)
    mixed = jnp.einsum('gts,bnsgc->bntgc', w_s * mask, vb)
    mixed = mixed + jnp.transpose(b_s)[None, None, :, :, None]
    return u * mixed.reshape(bsz, s, D_SGU)

def hybrid_layer(x, norm_mix_g, w_in, conv_w, conv_b, lru_w_a, lru_b_a, lru_w_x, lru_b_x,
                 lru_lambda, sgu_ln_g, sgu_ln_b, sgu_w_s, sgu_b_s, w_branch_a, w_branch_b,
                 w_out, norm_ffn_g, w_up, w_down):
    h = rmsnorm(x, norm_mix_g)
    proj = jnp.einsum('bsd,de->bse', h, w_in)
    cuts = np.cumsum([D_RNN, D_RNN, D_SGU, D_SGU, D_MODEL])
    x_rnn, g_rnn, u, v, gate_a, gate_b = jnp.split(proj, cuts, axis=-1)

    xr = causal_depthwise_conv(x_rnn, conv_w, conv_b)
    ya = rg_lru(xr, lru_w_a, lru_b_a, lru_w_x, lru_b_x, lru_lambda) * jax.nn.gelu(g_rnn)
    ya = jnp.einsum('bsr,rd->bsd', ya, w_branch_a)

    yb = spatial_gating(jax.nn.gelu(u), jax.nn.gelu(v), sgu_w_s, sgu_b_s, sgu_ln_g, sgu_ln_b)
    yb = jnp.einsum('bsc,cd->bsd', yb, w_branch_b)

    merged = jax.nn.sigmoid(gate_a) * ya + jax.nn.sigmoid(gate_b) * yb
    x = x + jnp.einsum('bsd,de->bse', merged, w_out)

    h2 = rmsnorm(x, norm_ffn_g)
    f = jnp.square(jax.nn.relu(jnp.einsum('bsd,df->bsf', h2, w_up)))
    return x + jnp.einsum('bsf,fd->bsd', f, w_down)

def second_inputs(seed: int = 0) -> dict:
    key = jax.random.key(seed)
    ks = jax.random.split(key, 24)
    f32 = jnp.float32

    def nrm(k, shape, scale):
        return jax.random.normal(k, shape, f32) * scale

    a_c = jax.random.uniform(ks[7], (DEPTH, D_RNN), f32, 0.9, 0.999)
    a0 = a_c ** (1.0 / LRU_C)
    lru_lambda = jnp.log(a0) - jnp.log1p(-a0)

    return {
        "x": nrm(ks[0], (BATCH, SEQ, D_MODEL), 1.0),
        "norm_mix_g": 1.0 + nrm(ks[1], (DEPTH, D_MODEL), 0.02),
        "w_in": nrm(ks[2], (DEPTH, D_MODEL, D_IN), D_MODEL ** -0.5),
        "conv_w": nrm(ks[3], (DEPTH, CONV_WIDTH, D_RNN), CONV_WIDTH ** -0.5),
        "conv_b": nrm(ks[4], (DEPTH, D_RNN), 0.02),
        "lru_w_a": nrm(ks[5], (DEPTH, RNN_HEADS, RNN_HEAD_DIM, RNN_HEAD_DIM), RNN_HEAD_DIM ** -0.5),
        "lru_b_a": nrm(ks[6], (DEPTH, RNN_HEADS, RNN_HEAD_DIM), 0.02),
        "lru_w_x": nrm(ks[8], (DEPTH, RNN_HEADS, RNN_HEAD_DIM, RNN_HEAD_DIM), RNN_HEAD_DIM ** -0.5),
        "lru_b_x": nrm(ks[9], (DEPTH, RNN_HEADS, RNN_HEAD_DIM), 0.02),
        "lru_lambda": lru_lambda,
        "sgu_ln_g": 1.0 + nrm(ks[10], (DEPTH, D_SGU), 0.02),
        "sgu_ln_b": nrm(ks[11], (DEPTH, D_SGU), 0.02),
        "sgu_w_s": nrm(ks[12], (DEPTH, SGU_GROUPS, SGU_BLOCK, SGU_BLOCK), SGU_BLOCK ** -0.5),
        "sgu_b_s": 1.0 + nrm(ks[13], (DEPTH, SGU_GROUPS, SGU_BLOCK), 0.02),
        "w_branch_a": nrm(ks[14], (DEPTH, D_RNN, D_MODEL), D_RNN ** -0.5),
        "w_branch_b": nrm(ks[15], (DEPTH, D_SGU, D_MODEL), D_SGU ** -0.5),
        "w_out": nrm(ks[16], (DEPTH, D_MODEL, D_MODEL), D_MODEL ** -0.5),
        "norm_ffn_g": 1.0 + nrm(ks[17], (DEPTH, D_MODEL), 0.02),
        "w_up": nrm(ks[18], (DEPTH, D_MODEL, D_FF_2), D_MODEL ** -0.5),
        "w_down": nrm(ks[19], (DEPTH, D_FF_2, D_MODEL), D_FF_2 ** -0.5),
        "final_norm_g": 1.0 + nrm(ks[20], (D_MODEL,), 0.02),
    }

def second_block(x, norm_mix_g, w_in, conv_w, conv_b, lru_w_a, lru_b_a, lru_w_x, lru_b_x,
              lru_lambda, sgu_ln_g, sgu_ln_b, sgu_w_s, sgu_b_s, w_branch_a, w_branch_b,
              w_out, norm_ffn_g, w_up, w_down, final_norm_g):
    for l in range(DEPTH):
        x = hybrid_layer(x, norm_mix_g[l], w_in[l], conv_w[l], conv_b[l], lru_w_a[l], lru_b_a[l],
                         lru_w_x[l], lru_b_x[l], lru_lambda[l], sgu_ln_g[l], sgu_ln_b[l],
                         sgu_w_s[l], sgu_b_s[l], w_branch_a[l], w_branch_b[l], w_out[l],
                         norm_ffn_g[l], w_up[l], w_down[l])
    return rmsnorm(x, final_norm_g)


_first_inputs_2 = second_inputs


def second_inputs(seed=0):
    import zlib

    import numpy as np

    out = dict(_first_inputs_2(seed))
    spreads = {}
    factors = {'norm_mix_g': 3.885,
     'lru_b_a': 60.502,
     'lru_b_x': 51.103,
     'sgu_ln_g': 36.175,
     'sgu_ln_b': 33.39,
     'sgu_b_s': 29.128,
     'norm_ffn_g': 14.147,
     'final_norm_g': 8.813,
     'conv_b': 7.129}
    for name, (base, spread) in spreads.items():
        noise = np.random.default_rng([zlib.crc32(name.encode()), seed]).standard_normal(out[name].shape)
        drawn = base * np.exp(spread * noise) if base else spread * noise
        out[name] = __import__('jax').numpy.asarray(drawn.astype(out[name].dtype))
    for name, factor in factors.items():
        out[name] = (out[name] * factor).astype(out[name].dtype)
    return out


_narrow_inputs_2 = second_inputs


def second_inputs(seed=0):

    out = dict(_narrow_inputs_2(seed))
    wider = {'conv_b': 3.97,
     'lru_b_a': 4.02,
     'lru_b_x': 4.13,
     'sgu_ln_g': 4.03,
     'sgu_ln_b': 4.03,
     'sgu_b_s': 4.01,
     'final_norm_g': 3.35}
    for name, times in wider.items():
        mean = out[name].mean()
        out[name] = (mean + times * (out[name] - mean)).astype(out[name].dtype)
    return out


DEPTH_3 = 2

EXPAND = 2
D_INNER = EXPAND * D_MODEL
CHUNK_3 = 128
NORM_EPS_3 = 1e-6
S5_WIDTH = D_INNER // 2
S5_GROUP = 16
S5_GROUPS = S5_WIDTH // S5_GROUP
S5_STATE = 64
SSD_WIDTH = D_INNER - S5_WIDTH
SSD_HEAD_DIM = 64
SSD_HEADS = SSD_WIDTH // SSD_HEAD_DIM
SSD_GROUPS = 2
SSD_REP = SSD_HEADS // SSD_GROUPS
SSD_STATE = 128
SSD_CONV = 4
SSD_CONV_DIM = SSD_WIDTH + 2 * SSD_GROUPS * SSD_STATE
AB_PROJ = D_INNER + S5_WIDTH + SSD_CONV_DIM + SSD_HEADS
RET_HEADS = 4
RET_QK_DIM = D_MODEL // RET_HEADS
RET_V_DIM = D_INNER // RET_HEADS
RET_PROJ = 2 * RET_HEADS * RET_QK_DIM + 2 * D_INNER
ROPE_BASE = 10000.0
N_EVEN = (DEPTH_3 + 1) // 2
N_ODD = DEPTH_3 // 2


F32 = jnp.float32

def rmsnorm_3(x, w, n_groups=1):
    xf = x.astype(F32)
    xg = xf.reshape(*x.shape[:-1], n_groups, x.shape[-1] // n_groups)
    xg = xg * lax.rsqrt(jnp.mean(xg * xg, axis=-1, keepdims=True) + NORM_EPS_3)
    return (xg.reshape(x.shape) * w.astype(F32)).astype(x.dtype)

def _complex_affine_combine(left, right):
    a1r, a1i, b1r, b1i = left
    a2r, a2i, b2r, b2i = right
    return (a2r * a1r - a2i * a1i,
            a2r * a1i + a2i * a1r,
            a2r * b1r - a2i * b1i + b2r,
            a2r * b1i + a2i * b1r + b2i)

def s5_mixer(u, lam_re, lam_im, log_dt, b_re, b_im, c_re, c_im, d_skip, glu_w, glu_b):
    bsz, seqlen, _ = u.shape
    n_chunks = seqlen // CHUNK_3
    uf = u.astype(F32)
    dt = jnp.exp(log_dt.astype(F32))[:, None]
    lr = jnp.minimum(lam_re.astype(F32), -1e-4)
    li = lam_im.astype(F32)
    mag = jnp.exp(lr * dt)
    ab_re = mag * jnp.cos(li * dt)
    ab_im = mag * jnp.sin(li * dt)
    den = lr * lr + li * li
    nr = ab_re - 1.0
    coef_re = (nr * lr + ab_im * li) / den
    coef_im = (ab_im * lr - nr * li) / den
    br = b_re.astype(F32)
    bi = b_im.astype(F32)
    bb_re = coef_re[..., None] * br - coef_im[..., None] * bi
    bb_im = coef_re[..., None] * bi + coef_im[..., None] * br
    cr = c_re.astype(F32)
    ci = c_im.astype(F32)
    st_shape = (bsz, CHUNK_3, S5_GROUPS, S5_STATE)
    a_re = jnp.broadcast_to(ab_re, st_shape)
    a_im = jnp.broadcast_to(ab_im, st_shape)
    u_chunks = uf.reshape(bsz, n_chunks, CHUNK_3, S5_GROUPS, S5_GROUP).transpose(1, 0, 2, 3, 4)

    def step(carry, u_c):
        h_re, h_im = carry
        bu_re = jnp.einsum('btgh,gph->btgp', u_c, bb_re)
        bu_im = jnp.einsum('btgh,gph->btgp', u_c, bb_im)
        acum_re, acum_im, x_re, x_im = lax.associative_scan(
            _complex_affine_combine, (a_re, a_im, bu_re, bu_im), axis=1)
        x_re = x_re + acum_re * h_re[:, None] - acum_im * h_im[:, None]
        x_im = x_im + acum_re * h_im[:, None] + acum_im * h_re[:, None]
        y = jnp.einsum('btgp,ghp->btgh', x_re, cr) - jnp.einsum('btgp,ghp->btgh', x_im, ci)
        return (x_re[:, -1], x_im[:, -1]), y

    zero = jnp.zeros((bsz, S5_GROUPS, S5_STATE), F32)
    _, ys = lax.scan(step, (zero, zero), u_chunks)
    y = ys.transpose(1, 0, 2, 3, 4).reshape(bsz, seqlen, S5_WIDTH)
    y = jax.nn.gelu(y + d_skip.astype(F32) * uf)
    return y * jax.nn.sigmoid(y @ glu_w.astype(F32) + glu_b.astype(F32))

def causal_depthwise_conv_3(x, w, b):
    k = w.shape[0]
    y = lax.conv_general_dilated(x, w[:, None, :], window_strides=(1,), padding=[(k - 1, 0)],
                                 dimension_numbers=('NWC', 'WIO', 'NWC'),
                                 feature_group_count=x.shape[-1])
    return y + b

def ssd_mixer(xbc, dt_raw, conv_w, conv_b, dt_bias, a_log, d_skip):
    bsz, seqlen, _ = xbc.shape
    nc = seqlen // CHUNK_3
    xbc = jax.nn.silu(causal_depthwise_conv_3(xbc.astype(F32), conv_w.astype(F32), conv_b.astype(F32)))
    gn = SSD_GROUPS * SSD_STATE
    xs = xbc[..., :SSD_WIDTH].reshape(bsz, nc, CHUNK_3, SSD_GROUPS, SSD_REP, SSD_HEAD_DIM)
    bm = xbc[..., SSD_WIDTH:SSD_WIDTH + gn].reshape(bsz, nc, CHUNK_3, SSD_GROUPS, SSD_STATE)
    cm = xbc[..., SSD_WIDTH + gn:].reshape(bsz, nc, CHUNK_3, SSD_GROUPS, SSD_STATE)
    dt = jax.nn.softplus(dt_raw.astype(F32) + dt_bias.astype(F32))
    a = -jnp.exp(a_log.astype(F32))
    xdt = xs * dt.reshape(bsz, nc, CHUNK_3, SSD_GROUPS, SSD_REP)[..., None]
    da = (dt * a).reshape(bsz, nc, CHUNK_3, SSD_HEADS).transpose(0, 3, 1, 2)
    a_cs = jnp.cumsum(da, axis=-1)
    causal = jnp.tril(jnp.ones((CHUNK_3, CHUNK_3), dtype=bool))
    seg = a_cs[..., :, None] - a_cs[..., None, :]
    decay_mat = jnp.exp(jnp.where(causal, seg, -jnp.inf)).reshape(
        bsz, SSD_GROUPS, SSD_REP, nc, CHUNK_3, CHUNK_3)
    cb = jnp.einsum('bclgn,bcsgn->bgcls', cm, bm)
    y_diag = jnp.einsum('bgrcls,bcsgrp->bclgrp', cb[:, :, None] * decay_mat, xdt)

    def to_bclgr(t):
        return t.reshape(bsz, SSD_GROUPS, SSD_REP, nc, CHUNK_3).transpose(0, 3, 4, 1, 2)

    decay_states = to_bclgr(jnp.exp(a_cs[..., -1:] - a_cs))
    states = jnp.einsum('bclgn,bclgrp->bcgrpn', bm, xdt * decay_states[..., None])
    chunk_decay = jnp.exp(a_cs[..., -1]).reshape(bsz, SSD_GROUPS, SSD_REP, nc).transpose(3, 0, 1, 2)

    def step(h, inp):
        dec, st = inp
        return h * dec[..., None, None] + st, h

    init = jnp.zeros((bsz, SSD_GROUPS, SSD_REP, SSD_HEAD_DIM, SSD_STATE), F32)
    _, prev = lax.scan(step, init, (chunk_decay, states.transpose(1, 0, 2, 3, 4, 5)))
    prev = prev.transpose(1, 0, 2, 3, 4, 5)
    y_off = jnp.einsum('bclgn,bcgrpn->bclgrp', cm, prev) * to_bclgr(jnp.exp(a_cs))[..., None]
    y = y_diag + y_off + xs * d_skip.astype(F32).reshape(SSD_GROUPS, SSD_REP)[:, :, None]
    return y.reshape(bsz, seqlen, SSD_WIDTH)

def s5_ssd_layer(h, w_in, lam_re, lam_im, log_dt, b_re, b_im, c_re, c_im, s5_d, glu_w, glu_b,
                 conv_w, conv_b, dt_bias, a_log, ssd_d, ssd_norm_w, w_out):
    p = h @ w_in
    o1 = D_INNER
    o2 = o1 + S5_WIDTH
    o3 = o2 + SSD_CONV_DIM
    z = p[..., :o1].astype(F32)
    y_a = s5_mixer(p[..., o1:o2], lam_re, lam_im, log_dt, b_re, b_im, c_re, c_im, s5_d, glu_w, glu_b)
    y_a = y_a * jax.nn.silu(z[..., :S5_WIDTH])
    y_b = ssd_mixer(p[..., o2:o3], p[..., o3:], conv_w, conv_b, dt_bias, a_log, ssd_d)
    y_b = rmsnorm_3(y_b * jax.nn.silu(z[..., S5_WIDTH:]), ssd_norm_w, SSD_GROUPS)
    y = jnp.concatenate([y_a, y_b], axis=-1)
    return y.astype(w_out.dtype) @ w_out

def rotary(x, cos, sin):
    x1 = x[..., ::2]
    x2 = x[..., 1::2]
    rot = jnp.stack([-x2, x1], axis=-1).reshape(x.shape)
    return x * cos[:, None] + rot * sin[:, None]

def chunkwise_retention(q, k, v):
    bsz, seqlen = q.shape[0], q.shape[1]
    nc = seqlen // CHUNK_3
    log_gamma = jnp.log(1.0 - 2.0 ** (-5.0 - jnp.arange(RET_HEADS, dtype=F32)))
    pos = jnp.arange(CHUNK_3, dtype=F32)
    rel = pos[:, None] - pos[None, :]
    intra = jnp.where(rel >= 0, jnp.exp(log_gamma[:, None, None] * jnp.maximum(rel, 0.0)), 0.0)
    qc = q.reshape(bsz, nc, CHUNK_3, RET_HEADS, RET_QK_DIM)
    kc = k.reshape(bsz, nc, CHUNK_3, RET_HEADS, RET_QK_DIM)
    vc = v.reshape(bsz, nc, CHUNK_3, RET_HEADS, RET_V_DIM)
    scores = jnp.einsum('bclhd,bcshd->bchls', qc, kc) * intra
    inner = jnp.einsum('bchls,bcshv->bclhv', scores, vc)
    q_decay = jnp.exp(log_gamma[None, :] * (pos[:, None] + 1.0))
    k_decay = jnp.exp(log_gamma[None, :] * (CHUNK_3 - 1.0 - pos)[:, None])
    chunk_decay = jnp.exp(log_gamma * CHUNK_3)
    qd = (qc * q_decay[..., None]).transpose(1, 0, 2, 3, 4)
    kd = (kc * k_decay[..., None]).transpose(1, 0, 2, 3, 4)
    vt = vc.transpose(1, 0, 2, 3, 4)

    def step(state, inp):
        q_t, k_t, v_t = inp
        cross = jnp.einsum('blhd,bhdv->blhv', q_t, state)
        state = state * chunk_decay[:, None, None] + jnp.einsum('blhd,blhv->bhdv', k_t, v_t)
        return state, cross

    init = jnp.zeros((bsz, RET_HEADS, RET_QK_DIM, RET_V_DIM), F32)
    _, cross = lax.scan(step, init, (qd, kd, vt))
    o = inner + cross.transpose(1, 0, 2, 3, 4)
    return o.reshape(bsz, seqlen, RET_HEADS, RET_V_DIM)

def retention_layer(h, w_in, gn_w, gn_b, w_out):
    bsz, seqlen, _ = h.shape
    p = (h @ w_in).astype(F32)
    qk_w = RET_HEADS * RET_QK_DIM
    q = p[..., :qk_w].reshape(bsz, seqlen, RET_HEADS, RET_QK_DIM)
    k = p[..., qk_w:2 * qk_w].reshape(bsz, seqlen, RET_HEADS, RET_QK_DIM)
    v = p[..., 2 * qk_w:2 * qk_w + D_INNER].reshape(bsz, seqlen, RET_HEADS, RET_V_DIM)
    g = p[..., 2 * qk_w + D_INNER:]
    pos = jnp.arange(seqlen, dtype=F32)
    angle = jnp.repeat(1.0 / (ROPE_BASE ** jnp.linspace(0.0, 1.0, RET_QK_DIM // 2, dtype=F32)), 2)
    theta = pos[:, None] * angle[None, :]
    cos = jnp.cos(theta)
    sin = jnp.sin(theta)
    q = rotary(q, cos, sin)
    k = rotary(k, cos, sin) * (RET_QK_DIM ** -0.5)
    o = chunkwise_retention(q, k, v)
    mu = jnp.mean(o, axis=-1, keepdims=True)
    var = jnp.mean(jnp.square(o - mu), axis=-1, keepdims=True)
    o = ((o - mu) * lax.rsqrt(var + NORM_EPS_3)).reshape(bsz, seqlen, D_INNER)
    o = o * gn_w.astype(F32) + gn_b.astype(F32)
    y = jax.nn.silu(g) * o
    return y.astype(w_out.dtype) @ w_out

def third_inputs(seed: int = 0) -> dict:
    key = jax.random.key(seed)
    ks = jax.random.split(key, 25)

    def nrm(k, shape, s):
        return jax.random.normal(k, shape, F32) * s

    dt_ssd = jnp.exp(jax.random.uniform(ks[15], (N_EVEN, SSD_HEADS), F32,
                                        minval=math.log(1e-3), maxval=math.log(1e-1)))
    return {
        'x': nrm(ks[0], (BATCH, SEQ, D_MODEL), 1.0),
        'layer_norm_w': 1.0 + nrm(ks[1], (DEPTH_3, D_MODEL), 0.01),
        'ab_w_in': nrm(ks[2], (N_EVEN, D_MODEL, AB_PROJ), D_MODEL ** -0.5),
        's5_lam_re': -0.5 + nrm(ks[3], (N_EVEN, S5_GROUPS, S5_STATE), 0.01),
        's5_lam_im': math.pi * jnp.arange(S5_STATE, dtype=F32) + nrm(ks[4], (N_EVEN, S5_GROUPS, S5_STATE), 0.01),
        's5_log_dt': jax.random.uniform(ks[5], (N_EVEN, S5_GROUPS), F32,
                                        minval=math.log(1e-3), maxval=math.log(1e-1)),
        's5_b_re': nrm(ks[6], (N_EVEN, S5_GROUPS, S5_STATE, S5_GROUP), (2 * S5_GROUP) ** -0.5),
        's5_b_im': nrm(ks[7], (N_EVEN, S5_GROUPS, S5_STATE, S5_GROUP), (2 * S5_GROUP) ** -0.5),
        's5_c_re': nrm(ks[8], (N_EVEN, S5_GROUPS, S5_GROUP, S5_STATE), S5_STATE ** -0.5),
        's5_c_im': nrm(ks[9], (N_EVEN, S5_GROUPS, S5_GROUP, S5_STATE), S5_STATE ** -0.5),
        's5_d': nrm(ks[10], (N_EVEN, S5_WIDTH), 1.0),
        's5_glu_w': nrm(ks[11], (N_EVEN, S5_WIDTH, S5_WIDTH), S5_WIDTH ** -0.5),
        's5_glu_b': nrm(ks[12], (N_EVEN, S5_WIDTH), 0.01),
        'ssd_conv_w': nrm(ks[13], (N_EVEN, SSD_CONV, SSD_CONV_DIM), SSD_CONV ** -0.5),
        'ssd_conv_b': nrm(ks[14], (N_EVEN, SSD_CONV_DIM), 0.01),
        'ssd_dt_bias': dt_ssd + jnp.log(-jnp.expm1(-dt_ssd)),
        'ssd_a_log': jnp.log(jax.random.uniform(ks[16], (N_EVEN, SSD_HEADS), F32, minval=1.0, maxval=16.0)),
        'ssd_d': 1.0 + nrm(ks[17], (N_EVEN, SSD_HEADS), 0.1),
        'ssd_norm_w': 1.0 + nrm(ks[18], (N_EVEN, SSD_WIDTH), 0.01),
        'ab_w_out': nrm(ks[19], (N_EVEN, D_INNER, D_MODEL), D_INNER ** -0.5),
        'ret_w_in': nrm(ks[20], (N_ODD, D_MODEL, RET_PROJ), D_MODEL ** -0.5),
        'ret_gn_w': 1.0 + nrm(ks[21], (N_ODD, D_INNER), 0.01),
        'ret_gn_b': nrm(ks[22], (N_ODD, D_INNER), 0.01),
        'ret_w_out': nrm(ks[23], (N_ODD, D_INNER, D_MODEL), D_INNER ** -0.5),
        'final_norm_w': 1.0 + nrm(ks[24], (D_MODEL,), 0.01),
    }

def third_block(x, layer_norm_w, ab_w_in, s5_lam_re, s5_lam_im, s5_log_dt, s5_b_re, s5_b_im,
              s5_c_re, s5_c_im, s5_d, s5_glu_w, s5_glu_b, ssd_conv_w, ssd_conv_b, ssd_dt_bias,
              ssd_a_log, ssd_d, ssd_norm_w, ab_w_out, ret_w_in, ret_gn_w, ret_gn_b, ret_w_out,
              final_norm_w):
    h = x
    for i in range(DEPTH_3):
        hn = rmsnorm_3(h, layer_norm_w[i])
        j = i // 2
        if i % 2 == 0:
            y = s5_ssd_layer(hn, ab_w_in[j], s5_lam_re[j], s5_lam_im[j], s5_log_dt[j],
                             s5_b_re[j], s5_b_im[j], s5_c_re[j], s5_c_im[j], s5_d[j],
                             s5_glu_w[j], s5_glu_b[j], ssd_conv_w[j], ssd_conv_b[j],
                             ssd_dt_bias[j], ssd_a_log[j], ssd_d[j], ssd_norm_w[j], ab_w_out[j])
        else:
            y = retention_layer(hn, ret_w_in[j], ret_gn_w[j], ret_gn_b[j], ret_w_out[j])
        h = h + y.astype(h.dtype)
    return rmsnorm_3(h, final_norm_w)


_first_inputs_3 = third_inputs


def third_inputs(seed=0):
    import zlib

    import numpy as np

    out = dict(_first_inputs_3(seed))
    spreads = {}
    factors = {'layer_norm_w': 3.87,
     's5_lam_re': 64.0,
     's5_lam_im': 33.312,
     's5_log_dt': 200.0,
     's5_b_re': 47.488,
     's5_b_im': 48.376,
     's5_c_re': 47.128,
     's5_c_im': 200.0,
     's5_glu_b': 77.041,
     'ssd_conv_b': 5.525,
     'ssd_norm_w': 76.581,
     'ret_gn_w': 200.0,
     'ret_gn_b': 200.0,
     'final_norm_w': 185.045,
     'ssd_d': 50.629}
    for name, (base, spread) in spreads.items():
        noise = np.random.default_rng([zlib.crc32(name.encode()), seed]).standard_normal(out[name].shape)
        drawn = base * np.exp(spread * noise) if base else spread * noise
        out[name] = jnp.asarray(drawn.astype(out[name].dtype))
    for name, factor in factors.items():
        out[name] = (out[name] * factor).astype(out[name].dtype)
    return out


_narrow_inputs_3 = third_inputs


def third_inputs(seed=0):

    out = dict(_narrow_inputs_3(seed))
    wider = {'s5_glu_b': 3.33,
     'ssd_norm_w': 3.22,
     'ret_gn_w': 6.3,
     'ret_gn_b': 6.33,
     'final_norm_w': 6.41}
    for name, times in wider.items():
        mean = out[name].mean()
        out[name] = (mean + times * (out[name] - mean)).astype(out[name].dtype)
    return out


def setup_inputs(seed=0):
    out = dict(first_inputs(seed))
    for name, value in second_inputs(seed + 1).items():
        if name != "x":
            out[name + "_2"] = value
    for name, value in third_inputs(seed + 2).items():
        if name != "x":
            out[name + "_3"] = value
    return out


def reference(
    x, norm_ffn1, ffn1_gate, ffn1_up, ffn1_down, norm_mix, w_in, b_in_attn, rwkv_shift_mix,
    rwkv_w0, rwkv_w2, rwkv_a0, rwkv_a2, rwkv_g2, rwkv_k_k, rwkv_k_a, rwkv_r_k, rwkv_ln_w,
    rwkv_ln_b, attn_sinks, w_out, norm_ffn2, ffn2_gate, ffn2_up, ffn2_down, norm_final,
    norm_mix_g_2, w_in_2, conv_w_2, conv_b_2, lru_w_a_2, lru_b_a_2, lru_w_x_2, lru_b_x_2,
    lru_lambda_2, sgu_ln_g_2, sgu_ln_b_2, sgu_w_s_2, sgu_b_s_2, w_branch_a_2, w_branch_b_2,
    w_out_2, norm_ffn_g_2, w_up_2, w_down_2, final_norm_g_2, layer_norm_w_3, ab_w_in_3,
    s5_lam_re_3, s5_lam_im_3, s5_log_dt_3, s5_b_re_3, s5_b_im_3, s5_c_re_3, s5_c_im_3, s5_d_3,
    s5_glu_w_3, s5_glu_b_3, ssd_conv_w_3, ssd_conv_b_3, ssd_dt_bias_3, ssd_a_log_3, ssd_d_3,
    ssd_norm_w_3, ab_w_out_3, ret_w_in_3, ret_gn_w_3, ret_gn_b_3, ret_w_out_3, final_norm_w_3,
):
    x = first_block(
        x, norm_ffn1, ffn1_gate, ffn1_up, ffn1_down, norm_mix, w_in, b_in_attn, rwkv_shift_mix,
        rwkv_w0, rwkv_w2, rwkv_a0, rwkv_a2, rwkv_g2, rwkv_k_k, rwkv_k_a, rwkv_r_k, rwkv_ln_w,
        rwkv_ln_b, attn_sinks, w_out, norm_ffn2, ffn2_gate, ffn2_up, ffn2_down, norm_final,
    )
    x = second_block(
        x, norm_mix_g_2, w_in_2, conv_w_2, conv_b_2, lru_w_a_2, lru_b_a_2, lru_w_x_2, lru_b_x_2,
        lru_lambda_2, sgu_ln_g_2, sgu_ln_b_2, sgu_w_s_2, sgu_b_s_2, w_branch_a_2, w_branch_b_2,
        w_out_2, norm_ffn_g_2, w_up_2, w_down_2, final_norm_g_2,
    )
    return third_block(
        x, layer_norm_w_3, ab_w_in_3, s5_lam_re_3, s5_lam_im_3, s5_log_dt_3, s5_b_re_3,
        s5_b_im_3, s5_c_re_3, s5_c_im_3, s5_d_3, s5_glu_w_3, s5_glu_b_3, ssd_conv_w_3,
        ssd_conv_b_3, ssd_dt_bias_3, ssd_a_log_3, ssd_d_3, ssd_norm_w_3, ab_w_out_3, ret_w_in_3,
        ret_gn_w_3, ret_gn_b_3, ret_w_out_3, final_norm_w_3,
    )


_drawn_inputs = setup_inputs


def setup_inputs(seed=0):
    import zlib

    import numpy as np

    out = dict(_drawn_inputs(seed))
    spreads = {}
    factors = {}
    for name, (base, spread) in spreads.items():
        noise = np.random.default_rng([zlib.crc32(name.encode()), seed]).standard_normal(out[name].shape)
        drawn = base * np.exp(spread * noise) if base else spread * noise
        out[name] = jnp.asarray(drawn.astype(out[name].dtype))
    for name, factor in factors.items():
        out[name] = (out[name] * factor).astype(out[name].dtype)
    return out
```

```python
from contextlib import ExitStack

import numpy as np

import concourse.bass as bass
from concourse import mybir

F32 = mybir.dt.float32
ALU = mybir.AluOpType
ACT = mybir.ActivationFunctionType
AX = mybir.AxisListType

P = 128
T = 512
D = 1024
DC = D // P
SLOT = 2048
RING = 4
BANKS = 8

FF = 2816
FFC = FF // P
HEAD = 64
RW_HEADS = 8
PAIRS = RW_HEADS // 2
LC = 64
NLC = T // LC
LORA_W, LORA_G = 12, 13
ATT_Q, ATT_K, ATT_V = 14, 18, 19
AB = 128
NAB = T // AB
Q_HEADS = 8
MASKED = -1.0e30
DECAY_RATE = float(np.exp(-0.5))
RNNC = 1280 // P
CONV = 4
SGU_G = 8
S5_G, S5_IN, S5_P = 64, 16, 64
S5_L = P // S5_IN
S5_N = T // S5_L
SSD_H, SSD_REP = 16, 8
CH = 128
NCH = T // CH
RET_H, RET_QK, RET_V = 4, 256, 512


class Gemm:

    def __init__(self, first, blocks, q, kc, cols):
        self.first, self.blocks, self.q, self.kc, self.cols = first, blocks, q, kc, cols
        self.n = blocks * q
        self.width = kc * cols


STREAM = [
    ("ffn1_up", FF // P, 1, DC, 2 * P), ("ffn1_down", DC, 2, FFC // 2, P),
    ("mix_in", 10, 1, DC, 2 * P), ("mix_out", 4, 1, DC, 2 * P),
    ("ffn2_up", FF // P, 1, DC, 2 * P), ("ffn2_down", DC, 2, FFC // 2, P),
    ("b2_in", 26, 1, DC, 2 * P), ("branch_a", 4, 2, RNNC // 2, 2 * P), ("branch_b", 4, 1, DC, 2 * P),
    ("b2_out", 4, 1, DC, 2 * P), ("mlp_up", 16, 1, DC, 2 * P), ("mlp_down", 4, 4, DC, 2 * P),
    ("ab_in", 18, 1, DC, 2 * P), ("s5_glu", 4, 1, DC, 2 * P), ("ab_out", 4, 2, DC, 2 * P),
    ("ret_qk", 8, 1, DC, 2 * P), ("ret_v", 8, 1, DC, 2 * P), ("ret_g", 8, 1, DC, 2 * P), ("ret_out", 4, 2, DC, 2 * P),
]


def lay_stream(which):
    gemms, at = {}, 0
    for name, blocks, q, kc, cols in STREAM:
        if which is None or name in which:
            gemms[name] = Gemm(at, blocks, q, kc, cols)
            at += blocks * q
    return gemms, at


VECTORS = [
    ("norm_ffn1", 8), ("norm_mix", 8), ("b_in_attn", 6), ("shift_mix", 14), ("w0", 4), ("a0", 4),
    ("k_k", 4), ("k_a", 4), ("r_k", 4), ("ln_w", 4), ("ln_b", 4), ("norm_ffn2", 8), ("norm_final", 8),
    ("norm_mix_g", 8), ("conv_w", 40), ("conv_b", 10), ("lru_b_a", 10), ("lru_b_x", 10), ("lru_lambda", 10),
    ("sgu_ln_g", 8), ("sgu_ln_b", 8), ("norm_ffn_g", 8), ("final_norm_g", 8),
    ("layer_norm", 16), ("s5_d", 8), ("s5_glu_b", 8), ("ssd_conv_w", 48), ("ssd_conv_b", 12),
    ("ssd_norm_w", 8), ("ret_gn_w", 16), ("ret_gn_b", 16), ("final_norm_w", 8),
]
VEC_AT = {}
_n = 0
for _name, _k in VECTORS:
    VEC_AT[_name] = _n
    _n += _k
N_VEC = _n


def pair_masks():
    i = np.arange(P)
    same = (i[:, None] // LC) == (i[None, :] // LC)
    r, c = i[:, None] % LC, i[None, :] % LC
    f = lambda m: (m & same).astype(np.float32)
    out = {"strict": f(r < c), "upto": f(r <= c)}
    for n in (1, 2, 4, 8, 16, 32):
        m = (r // (2 * n) == c // (2 * n)) & (r // n % 2 == 0) & (c // n % 2 == 1)
        out[f"level{n}"] = f(m)
    m = (c // 2 == r // 2) & (c % 2 == 0) & (r % 2 == 1)
    out["level1_ts"] = f(m)
    return out


def block1_consts():
    i = np.arange(P)
    m = pair_masks()
    parts = [("head_ones", ((i[:, None] // HEAD) == (i[None, :] // HEAD)).astype(np.float32)),
             ("stacked_eye", np.concatenate([np.eye(HEAD), np.eye(HEAD)]).astype(np.float32)),
             ("resets", np.tile((np.arange(T) % LC != 0).astype(np.float32), (P, 1)))]
    parts += list(m.items())
    qi, kj = np.arange(AB)[:, None], np.arange(2 * AB)[None, :]
    dist = qi + AB - kj
    band = (dist >= 0) & (dist < AB)
    for n in range(NAB):
        ok = band if n else band & (kj >= AB)
        parts.append((f"band{n}", np.where(ok, 0.0, MASKED).astype(np.float32)))
    for g in range(2):
        dup = np.zeros((P, P), np.float32)
        for j in range(2):
            dup[g * HEAD + np.arange(HEAD), j * HEAD + np.arange(HEAD)] = 1
        parts.append((f"dup{g}", dup))
    return parts


def block2_consts():
    chunk = np.arange(P) // 64
    return [("sgu_mask", (chunk[None, :] >= chunk[:, None]).astype(np.float32))]


def s5_swap():
    swap = np.zeros((P, P), np.float32)
    p = np.arange(S5_P)
    swap[S5_P + p, p] = -1.0
    swap[p, S5_P + p] = 1.0
    return swap


def block3_consts():
    i = np.arange(P)
    sign = np.where(i < S5_P, 1.0, -1.0).astype(np.float32)[:, None]
    sel = np.zeros((P, SSD_H, P), np.float32)
    for h in range(SSD_H):
        sel[h, h, :] = 1.0
    last = np.zeros((P, P), np.float32)
    last[P - 1, :] = 1.0
    return [("swap", s5_swap()), ("sign", sign), ("causal", np.where(i[:, None] <= i[None, :], 0.0, MASKED).astype(np.float32)),
            ("last_row", last), ("head_rows", sel.reshape(P, -1)),
            ("dt_resets", np.tile((np.arange(T) % CH != 0).astype(np.float32), (P, 1)))]


def block4_consts():
    f = np.float32
    i = np.arange(P)
    rot = np.zeros((P, P), f)
    rot[np.arange(1, P, 2), np.arange(0, P, 2)] = -1.0
    rot[np.arange(0, P, 2), np.arange(1, P, 2)] = 1.0
    angle = np.repeat(f(1.0) / (f(10000.0) ** np.linspace(0.0, 1.0, RET_QK // 2, dtype=f)), 2).astype(f)
    theta = angle[:, None] * np.arange(T, dtype=f)[None, :]
    cos, sin = np.cos(theta).astype(f), np.sin(theta).astype(f)
    parts = [("rotate", rot)]
    for h in range(2):
        parts += [(f"cos{h}", cos[h * P:(h + 1) * P]), (f"sin{h}", sin[h * P:(h + 1) * P])]
    lg = np.log(1.0 - 2.0 ** (-5.0 - np.arange(RET_H)))
    rel = i[None, :] - i[:, None]
    for h in range(RET_H):
        parts.append((f"intra{h}", np.where(rel >= 0, np.exp(lg[h] * np.maximum(rel, 0)), 0.0).astype(f)))
    for h in range(RET_H):
        parts.append((f"q_decay{h}", np.tile(np.exp(lg[h] * (i + 1.0)), (P, 1)).astype(f)))
    parts.append(("k_decay", np.exp(lg[None, :] * (CH - 1.0 - i)[:, None]).astype(f)))
    parts.append(("chunk_decay", np.tile(np.exp(lg * CH)[None, :], (P, 1)).astype(f)))
    return parts


CONSTS = {1: block1_consts, 2: block2_consts, 3: block3_consts, 4: block4_consts}


def const_columns(which):
    at, out = 0, {}
    for name, a in CONSTS[which]():
        out[name] = (at, a.shape[1])
        at += a.shape[1]
    return out, at


class Steps:

    def __init__(self, eng, sem):
        self.eng, self.sem, self.base, self.n, self.i, self.per = eng, sem, 0, 0, None, 0

    def loop(self, i, per):
        self.base, self.i, self.per, self.n = self.base + self.n, i, per, 0

    def end(self, times):
        assert self.n == self.per, (self.n, self.per)
        self.base, self.i, self.n = self.base + times * self.per, None, 0

    def value(self):
        return self.base + self.n + (0 if self.i is None else self.i * self.per)

    def then(self, ins):
        ins.then_inc(self.sem, 1)
        self.n += 1
        self.eng.wait_ge(self.sem, self.value())


class Core:

    def __init__(self, nc, ctx, dram, which):
        self.nc, self.ctx, self.dram = nc, ctx, dram
        self.block_sems = []
        self.gemms, self.n_slots = lay_stream(which)
        sb = lambda name, shape: ctx.enter_context(nc.sbuf_tensor(name, shape, F32))
        self.x = sb("x", [P, DC, T])
        self.h = sb("h", [P, DC, T])
        self.p = sb("p", [P, 52, T])
        self.weight_ring = sb("weight_ring", [P, RING, SLOT])
        self.vec = sb("vec", [P, N_VEC])
        self.cst = sb("cst", [P, 4352])
        self.eye = sb("eye", [P, P])
        self.ones = sb("ones", [P, P])
        self.rstd = sb("rstd", [P, T])
        self.scr = sb("scr", [P, 8, T])
        self.small = sb("small", [P, 640])
        self.acc = ctx.enter_context(nc.psum_tensor("acc", [P, BANKS, T], F32))
        self.slot_loaded = [self.sem(f"slot{r}_loaded") for r in range(RING)]
        self.products_done = self.sem("products_done")
        self.acc_free = self.sem("acc_free")
        self.blocks_read = 0
        self.norm = {n: self.sem(f"norm_{n}") for n in ("squared", "summed", "var", "inv", "rstd", "consts")}
        self.const_loads = 0
        self.norms = 0
        self.block_sems = []

    def sem(self, name):
        s = self.nc.alloc_semaphore(name)
        self.block_sems.append(s)
        return s

    def clear_sems(self):
        self.nc.clear_and_free_semaphores(self.block_sems)
        self.nc.all_engine_barrier()
        self.block_sems = []

    def vcol(self, name, c):
        return self.vec[:, bass.ds(VEC_AT[name] + c, 1)]

    def const(self, which, name, part=slice(None)):
        at, n = const_columns(which)[0][name]
        return self.cst[part, at:at + n]

    def const_load(self, eng, which, signal):
        n = const_columns(which)[1]
        eng.dma_start(self.cst[:, 0:n], self.dram[f"consts{which}"]).then_inc(signal, 16)

    def width_of(self, s):
        for g in self.gemms.values():
            if g.first <= s < g.first + g.n:
                return g.width
        raise ValueError(s)

    def one_load(self, sp, s, r, width, wait):
        if wait is not None:
            sp.wait_ge(self.products_done, wait)
        sp.dma_start(self.weight_ring[:, r, 0:width], self.dram["weights"][s, :, 0:width])\
            .then_inc(self.slot_loaded[r], 16)

    def first_loads(self, sp):
        for s in range(min(RING, self.n_slots)):
            self.one_load(sp, s, s % RING, self.width_of(s), None)

    def stream(self, sp, g):
        lo, hi = g.first + RING, g.first + g.n
        rounds = max(0, hi - lo) // RING
        if rounds > 0:
            with sp.Fori(0, rounds) as i:
                for j in range(RING):
                    self.one_load(sp, lo + i * RING + j, (lo + j) % RING, g.width, g.first + 1 + i * RING + j)
        for s in range(lo + rounds * RING, min(hi + RING, self.n_slots)):
            self.one_load(sp, s, s % RING, self.width_of(s), s - RING + 1)

    def product(self, pe, g, rhs, by_token=False):
        mb = g.cols // P
        body = RING if g.q < RING else 2 * RING
        sets = min(body // g.q, BANKS // mb)

        def round_of(i, at, n):
            for j in range(n):
                s, b, sub = at + j, (at + j) // g.q if i is None else None, j % g.q
                local = j // g.q
                r = (g.first + s) % RING
                turn = 16 * ((g.first + s) // RING + 1)
                pe.wait_ge(self.slot_loaded[r], turn if i is None else turn + i * (16 * body // RING))
                if sub == 0 and (i is not None or b >= sets):
                    freed = self.blocks_read + s // g.q - sets + 1
                    pe.wait_ge(self.acc_free, freed if i is None else freed + i * (body // g.q))
                if by_token:
                    for n in range(T // P):
                        at_bank = n * g.cols
                        out = self.acc[:, (local % sets) * mb + at_bank // T, at_bank % T:at_bank % T + g.cols]
                        for k in range(g.kc):
                            mm = pe.matmul(out, rhs(k)[:, n * P:(n + 1) * P], self.weight_ring[:, r, k * g.cols:(k + 1) * g.cols],
                                           start=(k == 0), stop=(k == g.kc - 1))
                for m in range(0 if by_token else mb):
                    bank = (local % sets) * mb + m
                    for k in range(g.kc):
                        at_w = k * g.cols + m * P
                        mm = pe.matmul(self.acc[:, bank, :], self.weight_ring[:, r, at_w:at_w + P],
                                       rhs(sub * g.kc + k), start=(sub == 0 and k == 0),
                                       stop=(sub == g.q - 1 and k == g.kc - 1))
                mm.then_inc(self.products_done, 1)

        rounds = g.n // body
        round_of(None, 0, min(body, g.n))
        if rounds > 1:
            with pe.Fori(0, rounds - 1) as i:
                round_of(i, body, body)
        if g.n > body and g.n % body:
            round_of(None, rounds * body, g.n % body)

    def drain(self, eng, g, read):
        mb = g.cols // P
        body = RING if g.q < RING else 2 * RING
        per = body // g.q
        sets = min(per, BANKS // mb)

        def round_of(i, at, n):
            for l in range(n):
                b = at + l if i is None else at + l + i * per
                eng.wait_ge(self.products_done, g.first + (b + 1) * g.q)
                set_ = l % sets
                read(b, [self.acc[:, set_ * mb + m, :] for m in range(mb)], set_)

        rounds = g.blocks // per
        if rounds > 0:
            with eng.Fori(0, rounds) as i:
                round_of(i, 0, per)
        if g.blocks % per:
            round_of(None, rounds * per, g.blocks % per)


def start_stage(core, block0):
    nc = core.nc
    loaded, eye_zero = core.sem("inputs_loaded"), core.sem("eye_zeroed")
    with nc.Block(no_gpsimd_drain=True) as block:
        @block.sync
        def _(sp):
            sp.dma_start(core.x[:, :, :], core.dram["x"]).then_inc(loaded, 16)
            sp.dma_start(core.vec[:, :], core.dram["vectors"]).then_inc(loaded, 16)
            core.first_loads(sp)
            core.const_load(sp, block0, loaded)
            sp.wait_ge(loaded, 48)

        @block.gpsimd
        def _(pool):
            nc.gpsimd.memset(core.ones[:, :], 1.0)
            nc.gpsimd.memset(core.eye[:, :], 0.0).then_inc(eye_zero, 1)
            pool.wait_ge(eye_zero, 1)
            nc.gpsimd.affine_select(out=core.eye[:, :], in_=core.eye[:, :], compare_op=ALU.not_equal, fill=1.0,
                                    base=0, pattern=[[-1, P]], channel_multiplier=1).then_inc(eye_zero, 1)
            pool.wait_ge(eye_zero, 2)


def norm_stage(core, gain, eps, dst=None, load_consts=None):
    nc = core.nc
    squared, summed, var_ready, inv_ready, rstd_ready, consts_in = core.norm.values()
    nth = core.norms
    core.norms += 1
    dst = core.h if dst is None else dst
    with nc.Block(no_gpsimd_drain=True) as block:
        @block.sync
        def _(sp):
            if load_consts:
                core.const_load(sp, load_consts, consts_in)
                core.const_loads += 16
                sp.wait_ge(consts_in, core.const_loads)

        @block.scalar
        def _(act):
            for c in range(DC):
                nc.scalar.activation(core.p[:, c, :], core.x[:, c, :], ACT.Square).then_inc(squared, 1)
            act.wait_ge(inv_ready, nth + 1)
            nc.scalar.activation(core.rstd[:, :], core.rstd[:, :], ACT.Sqrt).then_inc(rstd_ready, 1)

        @block.tensor
        def _(pe):
            for c in range(DC):
                pe.wait_ge(squared, DC * nth + c + 1)
                mm = pe.matmul(core.acc[:, 0, :], core.ones[:, :], core.p[:, c, :], start=(c == 0), stop=(c == DC - 1))
            mm.then_inc(summed, 1)

        @block.vector
        def _(dve):
            dve.wait_ge(summed, nth + 1)
            nc.vector.tensor_scalar(core.rstd[:, :], core.acc[:, 0, :], 1.0 / D, eps, ALU.mult, ALU.add).then_inc(var_ready, 1)
            dve.wait_ge(var_ready, nth + 1)
            nc.vector.reciprocal(core.rstd[:, :], core.rstd[:, :]).then_inc(inv_ready, 1)
            dve.wait_ge(rstd_ready, nth + 1)
            for c in range(DC):
                nc.vector.scalar_tensor_tensor(out=dst[:, c, :], in0=core.x[:, c, :], scalar=core.vcol(gain[0], gain[1] + c),
                                               in1=core.rstd[:, :], op0=ALU.mult, op1=ALU.mult)


def swiglu_up_stage(core, name):
    nc, g = core.nc, core.gemms[name]
    acc_free, silu_ready = core.acc_free, core.sem(f"{name}_silu")
    with nc.Block(no_gpsimd_drain=True) as block:
        @block.sync
        def _(sp):
            core.stream(sp, g)

        @block.tensor
        def _(pe):
            core.product(pe, g, lambda k: core.h[:, k, :])

        @block.scalar
        def _(act):
            def read(b, banks, s):
                nc.scalar.activation(core.scr[:, s, :], banks[0], ACT.Silu).then_inc(silu_ready, 1)
            core.drain(act, g, read)

        @block.vector
        def _(dve):
            def read(b, banks, s):
                dve.wait_ge(silu_ready, b + 1)
                nc.vector.tensor_tensor(core.p[:, b, :], core.scr[:, s, :], banks[1], ALU.mult).then_inc(acc_free, 1)
            core.drain(dve, g, read)
    core.blocks_read += g.blocks


def residual_stage(core, name, scale, rhs):
    nc, g = core.nc, core.gemms[name]
    acc_free = core.acc_free
    mb = g.cols // P
    with nc.Block(no_gpsimd_drain=True) as block:
        @block.sync
        def _(sp):
            core.stream(sp, g)

        @block.tensor
        def _(pe):
            core.product(pe, g, rhs)

        @block.vector
        def _(dve):
            def read(b, banks, s):
                for m in range(mb):
                    xc = core.x[:, b * mb + m, :]
                    ins = nc.vector.scalar_tensor_tensor(out=xc, in0=banks[m], scalar=scale, in1=xc, op0=ALU.mult, op1=ALU.add)
                ins.then_inc(acc_free, 1)
            core.drain(dve, g, read)
    core.blocks_read += g.blocks


def project_stage(core, name, at=0, func=ACT.Copy, by_token=False):
    nc, g = core.nc, core.gemms[name]
    mb = g.cols // P
    with nc.Block(no_gpsimd_drain=True) as block:
        @block.sync
        def _(sp):
            core.stream(sp, g)

        @block.tensor
        def _(pe):
            core.product(pe, g, lambda k: core.h[:, k, :], by_token)

        @block.scalar
        def _(act):
            def read(b, banks, s):
                for m in range(mb):
                    ins = nc.scalar.activation(core.p[:, at + b * mb + m, :], banks[m], func)
                ins.then_inc(core.acc_free, 1)
            core.drain(act, g, read)
    core.blocks_read += g.blocks


def rwkv_lora_stage(core):
    nc, p, scr, h, acc = core.nc, core.p, core.scr, core.h, core.acc
    step, act_in, done, read, lora_loaded, zeroed = (core.sem(f"rw_{s}") for s in (
        "shift_step", "lora_act", "lora_mm", "lora_read", "lora_loaded", "zeroed"))
    lora = p[:, 20:23, :]
    bd_zero = p[:, 23:33, :]
    diff = scr[:, 4, :]
    with nc.Block(no_gpsimd_drain=True) as block:
        @block.sync
        def _(sp):
            sp.dma_start(lora, core.dram["lora"]).then_inc(lora_loaded, 16)

        @block.gpsimd
        def _(pool):
            nc.gpsimd.memset(bd_zero, 0.0).then_inc(zeroed, 1)
            pool.wait_ge(zeroed, 1)

        @block.vector
        def _(dve):
            mine = Steps(dve, step)
            with dve.Fori(0, 14) as c:
                mine.loop(c, 2)
                nc.vector.tensor_scalar(diff[:, 0:1], p[:, c, 0:1], -1.0, None, ALU.mult)
                mine.then(nc.vector.tensor_tensor(diff[:, 1:T], p[:, c, 0:T - 1], p[:, c, 1:T], ALU.subtract))
                ins = nc.vector.scalar_tensor_tensor(out=p[:, c, :], in0=diff, scalar=core.vcol("shift_mix", c),
                                                     in1=p[:, c, :], op0=ALU.mult, op1=ALU.add)
                mine.then(ins)
            mine.end(14)

        @block.scalar
        def _(act):
            act.wait_ge(step, 2 * 14)
            nc.scalar.activation(scr[:, 6, :], p[:, LORA_W, :], ACT.Tanh)
            nc.scalar.activation(scr[:, 7, :], p[:, LORA_G, :], ACT.Sigmoid).then_inc(act_in, 1)
            act.wait_ge(done, 1)
            for c in range(PAIRS):
                nc.scalar.activation(scr[:, c, :], acc[:, c, :], ACT.Sigmoid, bias=core.vcol("w0", c)).then_inc(read, 1)
            for c in range(PAIRS):
                nc.scalar.activation(h[:, 4 + c, :], acc[:, 4 + c, :], ACT.Sigmoid, bias=core.vcol("a0", c))
            act.wait_ge(done, 2)
            for c in range(PAIRS):
                nc.scalar.activation(h[:, c, :], acc[:, c, :], ACT.Copy)

        @block.tensor
        def _(pe):
            pe.wait_ge(lora_loaded, 16)
            pe.wait_ge(act_in, 1)
            for c in range(PAIRS):
                pe.matmul(acc[:, c, :], lora[:, 0, c * P:(c + 1) * P], scr[:, 6, :], start=True, stop=True)
            for c in range(PAIRS):
                mm = pe.matmul(acc[:, 4 + c, :], lora[:, 1, c * P:(c + 1) * P], p[:, LORA_W, :], start=True, stop=True)
            mm.then_inc(done, 1)
            for c in range(PAIRS):
                pe.wait_ge(read, c + 1)
                mm = pe.matmul(acc[:, c, :], lora[:, 2, c * P:(c + 1) * P], scr[:, 7, :], start=True, stop=True)
            mm.then_inc(done, 1)


def rwkv_stage(core):
    nc, p, scr, h, acc = core.nc, core.p, core.scr, core.h, core.acc
    names = ("step", "cs", "exps", "sq", "sqsum", "inv", "root", "bd", "bonus_in", "bonus_sum", "unit1", "unit2",
             "a_read", "u1_read", "u2_read", "atn", "y", "y_read", "z", "z_read", "gt_read",
             "w", "w_neg", "sa", "sa_read", "vst", "vst_read", "s_new", "o", "var", "std", "obd", "ot")
    q = {s: core.sem(f"rw_{s}") for s in names}
    C = lambda n: core.const(1, n)
    two = lambda a: p[:, a:a + 2, :].rearrange("p a (b c) -> p (a b) c", c=P)
    bdb, bdkk, bdk, bdr, bdv = (two(23 + 2 * n) for n in range(5))
    et, gt, ft, at = two(33), two(35), two(37), two(39)
    tm, tt, ym, atn = two(41), two(43), two(45), two(47)
    btok, ktok = two(49), two(20)
    vst = p[:, 51, :].rearrange("p (c v) -> p c v", v=HEAD)
    e1, e2, e3 = p[:, 45, :], p[:, 46, :], p[:, 47, :]
    t4, t5, t6, t7 = (scr[:, n, :] for n in range(4, 8))
    t8, t9 = p[:, 22, :], p[:, 48, :]
    chunks = lambda a: a.rearrange("p (c t) -> p c t", t=LC)
    small = core.small
    pend, state, wneg, sas = small[:, 0:8], small[:, 64:128], small[:, 128:192], small[:, 192:256]
    s1, s2 = small[:, 16:24], small[:, 24:32]
    bank2 = lambda b: acc[:, b:b + 2, :].rearrange("p a (b c) -> p (a b) c", c=P)
    half = lambda m, k: m[:, 4 * k:4 * k + 4, :]
    rep = lambda m: m.unsqueeze(1).to_broadcast([P, 4, P])
    LEVELS = (2, 4, 8, 16, 32)
    NL = len(LEVELS)
    eye = core.eye[:, :]

    with nc.Block(no_gpsimd_drain=True) as block:
        @block.vector
        def _(dve):
            v = nc.vector
            mine = Steps(dve, q["step"])
            with dve.Fori(0, PAIRS) as i:
                mine.loop(i, 18)
                r, k, val, a, sig = p[:, i, :], p[:, 4 + i, :], p[:, 8 + i, :], h[:, 4 + i, :], scr[:, i, :]
                mine.then(v.tensor_tensor_scan(t4, C("resets"), sig, 0.0, ALU.mult, ALU.add))
                v.tensor_tensor(t5, t4, sig, ALU.subtract).then_inc(q["cs"], 1)
                v.tensor_scalar(t6, k, core.vcol("k_k", i), None, ALU.mult).then_inc(q["sq"], 1)
                mine.then(v.tensor_scalar(t8, a, -1.0, core.vcol("k_a", i), ALU.add, ALU.mult))
                mine.then(v.scalar_tensor_tensor(out=t8, in0=t8, scalar=1.0, in1=k, op0=ALU.add, op1=ALU.mult))
                mine.then(v.tensor_scalar(t9, r, core.vcol("r_k", i), None, ALU.mult))
                v.tensor_tensor(t9, t9, t8, ALU.mult).then_inc(q["bonus_in"], 1)
                dve.wait_ge(q["sqsum"], i + 1)
                mine.then(v.tensor_scalar(t7, acc[:, 6, :], 1e-24, None, ALU.max))
                v.reciprocal(t7, t7).then_inc(q["inv"], 1)
                dve.wait_ge(q["root"], i + 1)
                dve.wait_ge(q["exps"], i + 1)
                mine.then(v.tensor_tensor(t6, t6, t7, ALU.mult))
                mine.then(v.tensor_tensor(t5, t6, a, ALU.mult))
                v.tensor_copy(pend, chunks(e1)[:, :, LC - 1:LC].rearrange("p c o -> p (c o)"))
                v.memset(state, 0.0)
                for j in range(2):
                    rows = slice(j * HEAD, (j + 1) * HEAD)
                    for m, a0, a1 in ((bdkk, t6, e3), (bdb, t5, e2), (bdk, t8, e2), (bdr, r, e1)):
                        v.tensor_tensor(m[rows, :, j * LC:(j + 1) * LC], chunks(a0)[rows], chunks(a1)[rows], ALU.mult)
                    ins = v.tensor_copy(bdv[rows, :, j * LC:(j + 1) * LC], chunks(val)[rows])
                ins.then_inc(q["bd"], 1)
                dve.wait_ge(q["bonus_sum"], i + 1)
                mine.then(v.tensor_tensor(t7, acc[:, 7, :], val, ALU.mult))
                dve.wait_ge(q["unit1"], i + 1)
                for k2 in range(2):
                    v.tensor_copy(half(at, k2), half(bank2(0), k2))
                    v.scalar_tensor_tensor(out=half(tm, k2), in0=half(bank2(2), k2), scalar=-1.0, in1=rep(C("level1_ts")), op0=ALU.mult, op1=ALU.mult)
                    ins = v.tensor_tensor(half(et, k2), half(bank2(4), k2), rep(C("upto")), ALU.mult)
                ins.then_inc(q["u1_read"], 1)
                dve.wait_ge(q["u1_read"], 2 * i + 1)
                for k2 in range(2):
                    v.scalar_tensor_tensor(out=half(tt, k2), in0=half(at, k2), scalar=-1.0, in1=rep(C("level1")), op0=ALU.mult, op1=ALU.mult)
                    ins = v.tensor_tensor(half(tm, k2), half(tm, k2), rep(eye), ALU.add)
                mine.then(ins)
                for k2 in range(2):
                    ins = v.tensor_tensor(half(tt, k2), half(tt, k2), rep(eye), ALU.add)
                ins.then_inc(q["u1_read"], 1)
                dve.wait_ge(q["unit2"], i + 1)
                for k2 in range(2):
                    v.tensor_tensor(half(gt, k2), half(bank2(6), k2), rep(C("strict")), ALU.mult)
                    ins = v.tensor_tensor(half(ft, k2), half(bank2(0), k2), rep(C("upto")), ALU.mult)
                ins.then_inc(q["gt_read"], 1)
                for n in range(NL):
                    for k2 in range(2):
                        dve.wait_ge(q["z"], i * (2 * NL) + 2 * n + k2 + 1)
                        v.tensor_tensor(half(tm, k2), half(tm, k2), half(bank2(2), k2), ALU.subtract)
                        ins = v.tensor_tensor(half(tt, k2), half(tt, k2), half(bank2(4), k2), ALU.subtract)
                        ins.then_inc(q["z_read"], 1)
                for c in range(NLC):
                    dve.wait_ge(q["w"], i * NLC + c + 1)
                    v.tensor_scalar(wneg, acc[:, 2, 0:HEAD], -1.0, None, ALU.mult).then_inc(q["w_neg"], 1)
                    dve.wait_ge(q["sa"], i * NLC + c + 1)
                    v.tensor_copy(sas, acc[:, 3, 0:HEAD]).then_inc(q["sa_read"], 1)
                    dve.wait_ge(q["o"], i * NLC + c + 1)
                    v.tensor_scalar(state, acc[:, 4, 0:HEAD], pend[:, c:c + 1], None, ALU.mult).then_inc(q["s_new"], 1)
                ob = chunks(acc[:, 5, :])
                col = lambda x: x.unsqueeze(2).to_broadcast([P, NLC, HEAD])
                mine.then(v.tensor_reduce(s1, ob, AX.X, ALU.add))
                mine.then(v.tensor_scalar(s1, s1, 1.0 / HEAD, None, ALU.mult))
                mine.then(v.tensor_tensor(chunks(t5), ob, col(s1), ALU.subtract))
                mine.then(v.tensor_tensor(t6, t5, t5, ALU.mult))
                mine.then(v.tensor_reduce(s2, chunks(t6), AX.X, ALU.add))
                mine.then(v.tensor_scalar(s2, s2, 1.0 / HEAD, 64e-5, ALU.mult, ALU.add))
                v.reciprocal(s2, s2).then_inc(q["var"], 1)
                dve.wait_ge(q["std"], i + 1)
                for j in range(2):
                    rows = slice(j * HEAD, (j + 1) * HEAD)
                    ins = v.tensor_tensor(bdv[rows, :, j * LC:(j + 1) * LC], chunks(t5)[rows], col(s2)[rows], ALU.mult)
                ins.then_inc(q["obd"], 1)
                dve.wait_ge(q["ot"], i + 1)
                mine.then(v.tensor_scalar(t4, acc[:, 6, :], core.vcol("ln_w", i), core.vcol("ln_b", i), ALU.mult, ALU.add))
                mine.then(v.tensor_tensor(t4, t4, t7, ALU.add))
                mine.then(v.tensor_tensor(h[:, i, :], t4, h[:, i, :], ALU.mult))
            mine.end(PAIRS)

        @block.scalar
        def _(act):
            s = nc.scalar
            with act.Fori(0, PAIRS) as i:
                act.wait_ge(q["cs"], i + 1)
                s.activation(e1, t4, ACT.Exp, scale=-DECAY_RATE)
                s.activation(e2, t4, ACT.Exp, scale=DECAY_RATE)
                s.activation(e3, t5, ACT.Exp, scale=-DECAY_RATE).then_inc(q["exps"], 1)
                act.wait_ge(q["sq"], i + 1)
                s.activation(t7, t6, ACT.Square).then_inc(q["a_read"], 1)
                act.wait_ge(q["inv"], i + 1)
                s.activation(t7, t7, ACT.Sqrt).then_inc(q["root"], 1)
                act.wait_ge(q["unit2"], i + 1)
                for k2 in range(2):
                    s.activation(half(btok, k2), half(bank2(2), k2), ACT.Copy)
                    s.activation(half(ktok, k2), half(bank2(4), k2), ACT.Copy).then_inc(q["u2_read"], 1)
                act.wait_ge(q["vst"], i + 1)
                s.activation(vst, acc[:, 7, :].rearrange("p (c v) -> p c v", v=HEAD), ACT.Copy).then_inc(q["vst_read"], 1)
                for n in range(NL):
                    for k2 in range(2):
                        act.wait_ge(q["y"], i * (2 * NL) + 2 * n + k2 + 1)
                        s.activation(half(ym, k2), half(bank2(0), k2), ACT.Copy).then_inc(q["y_read"], 1)
                act.wait_ge(q["var"], i + 1)
                s.activation(s2, s2, ACT.Sqrt).then_inc(q["std"], 1)

        @block.gpsimd
        def _(pool):
            with pool.Fori(0, PAIRS) as i:
                pool.wait_ge(q["u1_read"], 2 * i + 1)
                for n, level in enumerate(LEVELS):
                    for k2 in range(2):
                        if n:
                            pool.wait_ge(q["y"], i * (2 * NL) + 2 * (n - 1) + k2 + 1)
                        nc.gpsimd.tensor_tensor(half(atn, k2), half(at, k2), rep(C(f"level{level}")), ALU.mult).then_inc(q["atn"], 1)

        @block.tensor
        def _(pe):
            mm = pe.matmul
            with pe.Fori(0, PAIRS) as i:
                pe.wait_ge(q["a_read"], i + 1)
                mm(acc[:, 6, :], C("head_ones"), t7, start=True, stop=True).then_inc(q["sqsum"], 1)
                pe.wait_ge(q["bonus_in"], i + 1)
                mm(acc[:, 7, :], C("head_ones"), t9, start=True, stop=True).then_inc(q["bonus_sum"], 1)
                pe.wait_ge(q["bd"], i + 1)
                for c in range(NLC):
                    mm(bank2(0)[:, c, :], bdb[:, c, :], bdkk[:, c, :], start=True, stop=True)
                    mm(bank2(2)[:, c, :], bdkk[:, c, :], bdb[:, c, :], start=True, stop=True)
                    ins = mm(bank2(4)[:, c, :], bdb[:, c, :], bdr[:, c, :], start=True, stop=True)
                ins.then_inc(q["unit1"], 1)
                pe.wait_ge(q["u1_read"], 2 * i + 2)
                for c in range(NLC):
                    mm(bank2(6)[:, c, :], bdk[:, c, :], bdkk[:, c, :], start=True, stop=True)
                    mm(bank2(0)[:, c, :], bdk[:, c, :], bdr[:, c, :], start=True, stop=True)
                    pe.transpose(bank2(2)[:, c, :], bdb[:, c, :], eye)
                    ins = pe.transpose(bank2(4)[:, c, :], bdk[:, c, :], eye)
                ins.then_inc(q["unit2"], 1)
                pe.wait_ge(q["gt_read"], i + 1)
                pe.wait_ge(q["u2_read"], 2 * i + 2)
                for c in range(NLC):
                    ins = mm(acc[:, 7, c * HEAD:(c + 1) * HEAD], bdv[:, c, :], C("stacked_eye"), start=True, stop=True)
                ins.then_inc(q["vst"], 1)
                for n in range(NL):
                    for k2 in range(2):
                        at_ = i * (2 * NL) + 2 * n + k2
                        pe.wait_ge(q["atn"], at_ + 1)
                        if n:
                            pe.wait_ge(q["z_read"], i * (2 * NL) + 2 * (n - 1) + k2 + 1)
                        for c in range(4 * k2, 4 * k2 + 4):
                            ins = mm(bank2(0)[:, c, :], atn[:, c, :], tm[:, c, :], start=True, stop=True)
                        ins.then_inc(q["y"], 1)
                    for k2 in range(2):
                        pe.wait_ge(q["y_read"], i * (2 * NL) + 2 * n + k2 + 1)
                        for c in range(4 * k2, 4 * k2 + 4):
                            mm(bank2(2)[:, c, :], tt[:, c, :], ym[:, c, :], start=True, stop=True)
                            ins = mm(bank2(4)[:, c, :], ym[:, c, :], tt[:, c, :], start=True, stop=True)
                        ins.then_inc(q["z"], 1)
                pe.wait_ge(q["z_read"], i * (2 * NL) + 2 * NL)
                pe.wait_ge(q["vst_read"], i + 1)
                for c in range(NLC):
                    if c:
                        pe.wait_ge(q["s_new"], i * NLC + c)
                    mm(acc[:, 2, 0:HEAD], bdkk[:, c, :], state, start=True, stop=False)
                    mm(acc[:, 2, 0:HEAD], gt[:, c, :], vst[:, c, :], start=False, stop=True).then_inc(q["w"], 1)
                    pe.wait_ge(q["w_neg"], i * NLC + c + 1)
                    mm(acc[:, 3, 0:HEAD], tt[:, c, :], wneg, start=True, stop=True).then_inc(q["sa"], 1)
                    pe.wait_ge(q["sa_read"], i * NLC + c + 1)
                    mm(acc[:, 4, 0:HEAD], eye, state, start=True, stop=False)
                    mm(acc[:, 4, 0:HEAD], btok[:, c, :], sas, start=False, stop=False)
                    mm(acc[:, 4, 0:HEAD], ktok[:, c, :], vst[:, c, :], start=False, stop=True)
                    o = acc[:, 5, c * HEAD:(c + 1) * HEAD]
                    mm(o, bdr[:, c, :], state, start=True, stop=False)
                    mm(o, et[:, c, :], sas, start=False, stop=False)
                    mm(o, ft[:, c, :], vst[:, c, :], start=False, stop=True).then_inc(q["o"], 1)
                pe.wait_ge(q["obd"], i + 1)
                for c in range(NLC):
                    ins = mm(acc[:, 6, c * LC:(c + 1) * LC], bdv[:, c, :], C("stacked_eye"), start=True, stop=True)
                ins.then_inc(q["ot"], 1)


def attention_stage(core):
    nc, p, scr, h, acc, small = core.nc, core.p, core.scr, core.h, core.acc, core.small
    names = ("step", "biased", "mm0", "kd_read", "q_ready", "scores", "masked", "max", "exp", "sink", "pt", "pt_read", "o",
             "o_ready", "ot", "ot_read")
    q = {s: core.sem(f"at_{s}") for s in names}
    C = lambda n: core.const(1, n)
    kdup = p[:, 20:23, :].rearrange("p a t -> p (a t)")[:, 0:2 * (AB + T)].rearrange("p (g t) -> p g t", g=2)
    vtok = p[:, 23:25, :].rearrange("p a t -> p (a t)")[:, 0:5 * AB].rearrange("p (n d) -> p n d", d=AB)
    qz = p[:, 26:28, :].rearrange("p a (h t) -> p (a h) t", t=AB)
    sc = p[:, 28:32, :].rearrange("p a (h t) -> p (a h) t", t=2 * AB)
    pt = p[:, 32:36, :].rearrange("p a (h t) -> p (a h) t", t=AB)
    otok = p[:, 36, :]
    sinks, mx, nmx, rs, es = (small[:, 8 * n:8 * n + 8] for n in range(5))
    pairs2 = lambda b: acc[:, b, :].rearrange("p (h t) -> p h t", t=2 * AB)
    with nc.Block(no_gpsimd_drain=True) as block:
        sinks_in = core.sem("at_sinks")

        @block.sync
        def _(sp):
            sp.dma_start(sinks, core.dram["sinks"].partition_broadcast(P)).then_inc(sinks_in, 16)
            sp.wait_ge(sinks_in, 16)

        @block.gpsimd
        def _(pool):
            nc.gpsimd.memset(kdup[:, :, 0:AB], 0.0)
            nc.gpsimd.memset(vtok[:, 0, :], 0.0)
            nc.gpsimd.memset(qz, 0.0).then_inc(q["biased"], 1)

        @block.vector
        def _(dve):
            v = nc.vector
            mine = Steps(dve, q["step"])
            for c in range(4):
                v.tensor_scalar(p[:, ATT_Q + c, :], p[:, ATT_Q + c, :], core.vcol("b_in_attn", c), HEAD ** -0.5, ALU.add, ALU.mult)
            for c in (4, 5):
                ins = v.tensor_scalar(p[:, ATT_Q + c, :], p[:, ATT_Q + c, :], core.vcol("b_in_attn", c), None, ALU.add)
            mine.then(ins)
            dve.wait_ge(q["mm0"], 1)
            for g in range(2):
                v.tensor_copy(kdup[:, g, AB:AB + T], acc[:, g, :])
            v.tensor_copy(vtok[:, 1:5, :], acc[:, 2, :].rearrange("p (n d) -> p n d", d=AB)).then_inc(q["kd_read"], 1)
            dve.wait_ge(q["biased"], 1)
            dve.wait_ge(sinks_in, 16)
            with dve.Fori(0, NAB) as n:
                mine.loop(n, 7)
                for hd in range(Q_HEADS):
                    rows = slice(hd % 2 * HEAD, hd % 2 * HEAD + HEAD)
                    ins = v.tensor_copy(qz[rows, hd, :], p[rows, ATT_Q + hd // 2, bass.ds(n * AB, AB)])
                ins.then_inc(q["q_ready"], 1)
                dve.wait_ge(q["scores"], n + 1)
                band = core.cst[:, bass.ds(BAND0 + n * (2 * AB), 2 * AB)].unsqueeze(1).to_broadcast([P, 2, 2 * AB])
                for b in range(4):
                    ins = v.tensor_tensor(sc[:, 2 * b:2 * b + 2, :], pairs2(b), band, ALU.add)
                mine.then(ins)
                mine.then(v.tensor_reduce(mx, sc, AX.X, ALU.max))
                mine.then(v.tensor_tensor(mx, mx, sinks, ALU.max))
                mine.then(v.tensor_tensor(es, sinks, mx, ALU.subtract))
                v.tensor_scalar(nmx, mx, -1.0, None, ALU.mult).then_inc(q["max"], 1)
                dve.wait_ge(q["exp"], n + 1)
                mine.then(v.tensor_tensor(rs, rs, es, ALU.add))
                mine.then(v.reciprocal(rs, rs))
                dve.wait_ge(q["pt"], n + 1)
                for b in range(4):
                    ins = v.tensor_copy(pt[:, 4 * b:4 * b + 4, :], acc[:, 4 + b, :].rearrange("p (a t) -> p a t", t=AB))
                ins.then_inc(q["pt_read"], 1)
                dve.wait_ge(q["o"], n + 1)
                v.tensor_tensor(otok.rearrange("p (a d) -> p a d", d=HEAD), acc[:, 0, :].rearrange("p (a d) -> p a d", d=HEAD),
                                rs.unsqueeze(2).to_broadcast([P, Q_HEADS, HEAD]), ALU.mult).then_inc(q["o_ready"], 1)
                dve.wait_ge(q["ot"], n + 1)
                mine.then(v.tensor_copy(h[:, 4:8, bass.ds(n * AB, AB)], acc[:, 1, :].rearrange("p (c t) -> p c t", t=AB)))
            mine.end(NAB)

        @block.scalar
        def _(act):
            with act.Fori(0, NAB) as n:
                act.wait_ge(q["max"], n + 1)
                for hd in range(Q_HEADS):
                    nc.scalar.activation(sc[:, hd, :], sc[:, hd, :], ACT.Exp, bias=nmx[:, hd:hd + 1], accum_out=rs[:, hd:hd + 1])
                nc.scalar.activation(es, es, ACT.Exp).then_inc(q["exp"], 1)

        @block.tensor
        def _(pe):
            pe.wait_ge(q["step"], 1)
            for g in range(2):
                pe.matmul(acc[:, g, :], C(f"dup{g}"), p[:, ATT_K, :], start=True, stop=True)
            for n in range(NAB):
                ins = pe.transpose(acc[:, 2, n * AB:(n + 1) * AB], p[:, ATT_V, n * AB:(n + 1) * AB], core.eye[:, :])
            ins.then_inc(q["mm0"], 1)
            pe.wait_ge(q["kd_read"], 1)
            with pe.Fori(0, NAB) as n:
                pe.wait_ge(q["q_ready"], n + 1)
                for hd in range(Q_HEADS):
                    keys = kdup[:, hd // 4, bass.ds(n * AB, 2 * AB)]
                    ins = pe.matmul(pairs2(hd // 2)[:, hd % 2, :], qz[:, hd, :], keys, start=True, stop=True)
                ins.then_inc(q["scores"], 1)
                pe.wait_ge(q["exp"], n + 1)
                for hd in range(Q_HEADS):
                    for k in range(2):
                        m = 2 * hd + k
                        ins = pe.transpose(acc[:, 4 + m // 4, m % 4 * AB:(m % 4 + 1) * AB], sc[:, hd, k * AB:(k + 1) * AB], core.eye[:, :])
                ins.then_inc(q["pt"], 1)
                pe.wait_ge(q["pt_read"], n + 1)
                for hd in range(Q_HEADS):
                    g = hd // 4
                    for k in range(2):
                        ins = pe.matmul(acc[:, 0, hd * HEAD:(hd + 1) * HEAD], pt[:, 2 * hd + k, :],
                                        vtok[:, n + k, g * HEAD:(g + 1) * HEAD], start=(k == 0), stop=(k == 1))
                ins.then_inc(q["o"], 1)
                pe.wait_ge(q["o_ready"], n + 1)
                for c in range(4):
                    ins = pe.transpose(acc[:, 1, c * AB:(c + 1) * AB], otok[:, c * AB:(c + 1) * AB], core.eye[:, :])
                ins.then_inc(q["ot"], 1)


BAND0 = const_columns(1)[0]["band0"][0]


def block1(core):
    norm_stage(core, ("norm_ffn1", 0), 1e-5)
    swiglu_up_stage(core, "ffn1_up")
    residual_stage(core, "ffn1_down", 0.5, lambda k: core.p[:, k, :])
    norm_stage(core, ("norm_mix", 0), 1e-5)
    project_stage(core, "mix_in")
    rwkv_lora_stage(core)
    rwkv_stage(core)
    attention_stage(core)
    residual_stage(core, "mix_out", 1.0, lambda k: core.h[:, k, :])
    norm_stage(core, ("norm_ffn2", 0), 1e-5)
    swiglu_up_stage(core, "ffn2_up")
    residual_stage(core, "ffn2_down", 0.5, lambda k: core.p[:, k, :])


def softplus_steps(nc, mine, x, m, e, t, d, act_wait, act_signal, n):
    v = nc.vector
    mine.then(v.tensor_scalar(m, x, 0.0, None, ALU.max))
    mine.then(v.tensor_scalar(e, x, 0.0, None, ALU.min))
    ins = v.tensor_tensor(e, e, m, ALU.subtract)
    ins.then_inc(act_signal, 1)
    mine.eng.wait_ge(act_wait, 2 * n + 1)
    mine.then(v.tensor_scalar(t, e, 1.0, None, ALU.add))
    v.tensor_scalar(d, t, -1.0, None, ALU.add).then_inc(act_signal, 1)
    mine.eng.wait_ge(act_wait, 2 * n + 2)
    mine.then(v.scalar_tensor_tensor(out=t, in0=d, scalar=0.0, in1=t, op0=ALU.is_equal, op1=ALU.add))
    mine.then(v.scalar_tensor_tensor(out=d, in0=d, scalar=0.0, in1=d, op0=ALU.is_equal, op1=ALU.add))
    mine.then(v.reciprocal(d, d))
    mine.then(v.tensor_tensor(t, t, d, ALU.mult))
    mine.then(v.tensor_tensor(t, t, e, ALU.mult))
    mine.then(v.tensor_tensor(m, m, t, ALU.add))


SOFTPLUS_STEPS = 9


def softplus_act(nc, act, e, t, from_dve, to_dve, n):
    act.wait_ge(from_dve, 2 * n + 1)
    nc.scalar.activation(e, e, ACT.Exp).then_inc(to_dve, 1)
    act.wait_ge(from_dve, 2 * n + 2)
    nc.scalar.activation(t, t, ACT.Ln).then_inc(to_dve, 1)


HC = RNNC // 2


def rnn_stage(core):
    nc, p, scr, h, acc, small = core.nc, core.p, core.scr, core.h, core.acc, core.small
    names = ("step", "sp_dve", "sp_act", "weights", "conv", "gates", "r", "i", "exped", "decay", "half", "root", "gelu")
    q = {s: core.sem(f"rnn_{s}") for s in names}
    lruw = core.cst[:, 128:128 + 2 * RNNC * P].rearrange("p (c g j) -> p c g j", g=2, j=P)
    x0 = small[:, 0:10]
    m, e, t, d = (small[:, 16 * n:16 * n + RNNC] for n in range(1, 5))
    coef = m
    ncoef = small[:, 80:90]
    xr = lambda c: h[:, c, :]
    ix = lambda c: scr[:, c, :]
    decays = [h[:, 5, :], h[:, 6, :], h[:, 7, :], scr[:, 5, :], scr[:, 6, :]]
    with nc.Block(no_gpsimd_drain=True) as block:
        @block.sync
        def _(sp):
            sp.dma_start(core.cst[:, 128:128 + 2 * RNNC * P], core.dram["lru_w"]).then_inc(q["weights"], 16)
            sp.wait_ge(q["weights"], 16)

        @block.vector
        def _(dve):
            v = nc.vector
            mine = Steps(dve, q["step"])
            mine.then(v.tensor_scalar(x0, core.vec[:, VEC_AT["lru_lambda"]:VEC_AT["lru_lambda"] + RNNC], -1.0, None, ALU.mult))
            softplus_steps(nc, mine, x0, m, e, t, d, q["sp_act"], q["sp_dve"], 0)
            v.tensor_scalar(ncoef, m, 8.0, None, ALU.mult)
            mine.then(v.tensor_scalar(coef, m, -8.0, None, ALU.mult))
            with dve.Fori(0, 2) as i:
                mine.loop(i, 3 * HC + 7)
                wcol = lambda k, c: core.vcol("conv_w", k * RNNC + i * HC + c)
                for c in range(HC):
                    ins = v.tensor_scalar(xr(c), p[:, i * HC + c, :], wcol(CONV - 1, c), core.vcol("conv_b", i * HC + c), ALU.mult, ALU.add)
                mine.then(ins)
                for k in range(CONV - 2, -1, -1):
                    back = CONV - 1 - k
                    for c in range(HC):
                        ins = v.scalar_tensor_tensor(out=xr(c)[:, back:T], in0=p[:, i * HC + c, 0:T - back], scalar=wcol(k, c),
                                                     in1=xr(c)[:, back:T], op0=ALU.mult, op1=ALU.add)
                    if k:
                        mine.then(ins)
                ins.then_inc(q["conv"], 1)
                dve.wait_ge(q["conv"], i + 1)
                for c in range(HC):
                    dve.wait_ge(q["i"], i * HC + c + 1)
                    mine.then(v.tensor_tensor(ix(c), ix(c), xr(c), ALU.mult))
                dve.wait_ge(q["decay"], i + 1)
                tanh5 = p[:, bass.ds(i * HC, HC), :]
                den5 = h[:, 0:HC, :]
                mine.then(v.tensor_scalar(den5, tanh5, 1.0, None, ALU.add))
                for c in range(HC):
                    ins = v.reciprocal(den5[:, c, :], den5[:, c, :])
                mine.then(ins)
                mine.then(v.tensor_tensor(den5, den5, tanh5, ALU.mult))
                v.tensor_scalar(den5, den5, 1e-34, None, ALU.max).then_inc(q["half"], 1)
                dve.wait_ge(q["root"], i + 1)
                for c in range(HC):
                    ins = v.tensor_tensor(ix(c), ix(c), den5[:, c, :], ALU.mult)
                mine.then(ins)
                for c in range(HC):
                    mine.then(v.tensor_tensor_scan(ix(c), decays[c], ix(c), 0.0, ALU.mult, ALU.add))
                dve.wait_ge(q["gelu"], 1)
                for c in range(HC):
                    mine.then(v.tensor_tensor(p[:, i * HC + c, :], ix(c), p[:, i * HC + (RNNC + c), :], ALU.mult))
            mine.end(2)

        @block.scalar
        def _(act):
            s = nc.scalar
            softplus_act(nc, act, e, t, q["sp_dve"], q["sp_act"], 0)
            s.activation(p[:, 10:36, :], p[:, 10:36, :], ACT.Gelu_apprx_tanh).then_inc(q["gelu"], 1)
            s.activation(p[:, 36:52, :], p[:, 36:52, :], ACT.Sigmoid)
            act.wait_ge(q["step"], SOFTPLUS_STEPS + 2)
            with act.Fori(0, 2) as i:
                for c in range(HC):
                    act.wait_ge(q["gates"], i * HC + c + 1)
                    s.activation(p[:, i * HC + c, :], acc[:, 2 * c % 8, :], ACT.Sigmoid, bias=core.vcol("lru_b_a", i * HC + c)).then_inc(q["r"], 1)
                    s.activation(ix(c), acc[:, (2 * c + 1) % 8, :], ACT.Sigmoid, bias=core.vcol("lru_b_x", i * HC + c)).then_inc(q["i"], 1)
                act.wait_ge(q["r"], i * HC + HC)
                for c in range(HC):
                    ins = s.activation(decays[c], p[:, i * HC + c, :], ACT.Exp, scale=coef_at(core, 16, i * HC + c))
                ins.then_inc(q["exped"], 1)
                act.wait_ge(q["exped"], i + 1)
                for c in range(HC):
                    ins = s.activation(p[:, i * HC + c, :], p[:, i * HC + c, :], ACT.Tanh, scale=coef_at(core, 80, i * HC + c))
                ins.then_inc(q["decay"], 1)
                act.wait_ge(q["half"], i + 1)
                s.activation(h[:, 0:HC, :], h[:, 0:HC, :], ACT.Sqrt, scale=2.0).then_inc(q["root"], 1)

        @block.tensor
        def _(pe):
            pe.wait_ge(q["weights"], 16)
            for i in range(2):
                pe.wait_ge(q["conv"], i + 1)
                for c in range(HC):
                    w = lruw[:, i * HC + c]
                    if c == HC - 1:
                        pe.wait_ge(q["i"], i * HC + 1)
                    pe.matmul(acc[:, 2 * c % 8, :], w[:, 0, :], xr(c), start=True, stop=True)
                    pe.matmul(acc[:, (2 * c + 1) % 8, :], w[:, 1, :], xr(c), start=True, stop=True).then_inc(q["gates"], 1)


def coef_at(core, at, c):
    return core.small[:, bass.ds(at + c, 1)]


def sgu_stage(core):
    nc, p, scr, h, acc = core.nc, core.p, core.scr, core.h, core.acc
    names = ("step", "loaded", "sum", "sq", "sum2", "inv", "rstd", "gained", "normed", "turned", "turned_read", "mixed", "mixed_read", "masked")
    q = {s: core.sem(f"sgu_{s}") for s in names}
    V, U = 28, 20
    wt = core.cst[:, 2688:2688 + SGU_G * P].rearrange("p (g t) -> p g t", t=P)
    bias = scr[:, 0:2, :].rearrange("p a (g t) -> p (a g) t", t=P)
    mean = scr[:, 2, :]
    vt = h[:, :, :].rearrange("p (n a) t -> p n (a t)", n=4)
    blocks = lambda a: a.rearrange("p (n t) -> p n t", t=P)
    with nc.Block(no_gpsimd_drain=True) as block:
        @block.sync
        def _(sp):
            sp.dma_start(wt, core.dram["sgu_w"]).then_inc(q["loaded"], 16)
            sp.dma_start(scr[:, 0:2, :].rearrange("p a t -> p (a t)"), core.dram["sgu_b"].partition_broadcast(P)).then_inc(q["loaded"], 16)

        @block.gpsimd
        def _(pool):
            pool.wait_ge(q["loaded"], 32)
            nc.gpsimd.tensor_tensor(wt, wt, core.const(2, "sgu_mask").unsqueeze(1).to_broadcast([P, SGU_G, P]), ALU.mult).then_inc(q["masked"], 1)

        @block.vector
        def _(dve):
            v = nc.vector
            mine = Steps(dve, q["step"])
            dve.wait_ge(q["sum"], 1)
            mine.then(v.tensor_scalar(mean, acc[:, 0, :], 1.0 / D, None, ALU.mult))
            for c in range(DC):
                v.tensor_tensor(p[:, V + c, :], p[:, V + c, :], mean, ALU.subtract).then_inc(q["gained"], 1)
            dve.wait_ge(q["sum2"], 1)
            mine.then(v.tensor_scalar(core.rstd[:, :], acc[:, 1, :], 1.0 / D, 1e-6, ALU.mult, ALU.add))
            v.reciprocal(core.rstd[:, :], core.rstd[:, :]).then_inc(q["inv"], 1)
            dve.wait_ge(q["rstd"], 1)
            for c in range(DC):
                v.scalar_tensor_tensor(out=p[:, V + c, :], in0=p[:, V + c, :], scalar=core.vcol("sgu_ln_g", c),
                                       in1=core.rstd[:, :], op0=ALU.mult, op1=ALU.mult).then_inc(q["gained"], 1)
            for g in range(SGU_G):
                dve.wait_ge(q["mixed"], g + 1)
                if g >= 2:
                    dve.wait_ge(q["step"], mine.base + mine.n)
                t = scr[:, 3 + g % 2, :]
                mine.then(v.tensor_tensor(blocks(t), blocks(acc[:, 4 + g % 4, :]), bias[:, g, :].unsqueeze(1).to_broadcast([P, 4, P]), ALU.add))
                v.tensor_tensor(p[:, U + g, :], p[:, U + g, :], t, ALU.mult).then_inc(q["mixed_read"], 1)

        @block.scalar
        def _(act):
            s = nc.scalar
            for c in range(DC):
                act.wait_ge(q["gained"], c + 1)
                s.activation(h[:, c, :], p[:, V + c, :], ACT.Square).then_inc(q["sq"], 1)
            act.wait_ge(q["inv"], 1)
            s.activation(core.rstd[:, :], core.rstd[:, :], ACT.Sqrt).then_inc(q["rstd"], 1)
            for c in range(DC):
                act.wait_ge(q["gained"], DC + c + 1)
                s.activation(p[:, V + c, :], p[:, V + c, :], ACT.Identity, bias=core.vcol("sgu_ln_b", c)).then_inc(q["normed"], 1)
            for g in range(SGU_G):
                act.wait_ge(q["turned"], g + 1)
                s.activation(vt[:, :, g * P:(g + 1) * P], blocks(acc[:, g % 4, :]), ACT.Copy).then_inc(q["turned_read"], 1)

        @block.tensor
        def _(pe):
            for c in range(DC):
                ins = pe.matmul(acc[:, 0, :], core.ones[:, :], p[:, V + c, :], start=(c == 0), stop=(c == DC - 1))
            ins.then_inc(q["sum"], 1)
            for c in range(DC):
                pe.wait_ge(q["sq"], c + 1)
                ins = pe.matmul(acc[:, 1, :], core.ones[:, :], h[:, c, :], start=(c == 0), stop=(c == DC - 1))
            ins.then_inc(q["sum2"], 1)
            for g in range(SGU_G):
                pe.wait_ge(q["normed"], g + 1)
                if g >= 4:
                    pe.wait_ge(q["turned_read"], g - 3)
                for n in range(4):
                    ins = pe.transpose(acc[:, g % 4, n * P:(n + 1) * P], p[:, V + g, n * P:(n + 1) * P], core.eye[:, :])
                ins.then_inc(q["turned"], 1)
            pe.wait_ge(q["masked"], 1)
            for g in range(SGU_G):
                pe.wait_ge(q["turned_read"], g + 1)
                if g >= 4:
                    pe.wait_ge(q["mixed_read"], g - 3)
                for n in range(4):
                    ins = pe.matmul(acc[:, 4 + g % 4, n * P:(n + 1) * P], vt[:, n, g * P:(g + 1) * P], wt[:, g, :], start=True, stop=True)
                ins.then_inc(q["mixed"], 1)


def gated_stage(core, name, first, gate, rhs):
    nc, g, p, scr = core.nc, core.gemms[name], core.p, core.scr
    mb = g.cols // P
    step = None if first else core.sem(f"{name}_step")
    with nc.Block(no_gpsimd_drain=True) as block:
        @block.sync
        def _(sp):
            core.stream(sp, g)

        @block.tensor
        def _(pe):
            core.product(pe, g, rhs)

        @block.vector
        def _(dve):
            mine = None if first else Steps(dve, step)

            def read(b, banks, s):
                for m in range(mb):
                    c = b * mb + m
                    if first:
                        ins = nc.vector.tensor_tensor(p[:, 36 + c, :], banks[m], p[:, gate + c, :], ALU.mult)
                    else:
                        t = scr[:, s * mb + m, :]
                        ins = nc.vector.tensor_tensor(t, banks[m], p[:, gate + c, :], ALU.mult)
                ins.then_inc(core.acc_free, 1)
                if not first:
                    dve.wait_ge(core.acc_free, core.blocks_read + b + 1)
                    for m in range(mb):
                        c = b * mb + m
                        nc.vector.tensor_tensor(p[:, 36 + c, :], p[:, 36 + c, :], scr[:, s * mb + m, :], ALU.add)
            core.drain(dve, g, read)
    core.blocks_read += g.blocks


def relu2_stage(core, name):
    nc, g, p, scr = core.nc, core.gemms[name], core.p, core.scr
    mb = g.cols // P
    relu = core.sem(f"{name}_relu")
    with nc.Block(no_gpsimd_drain=True) as block:
        @block.sync
        def _(sp):
            core.stream(sp, g)

        @block.tensor
        def _(pe):
            core.product(pe, g, lambda k: core.h[:, k, :])

        @block.scalar
        def _(act):
            def read(b, banks, s):
                for m in range(mb):
                    ins = nc.scalar.activation(scr[:, s * mb + m, :], banks[m], ACT.Relu)
                ins.then_inc(relu, 1)
            core.drain(act, g, read)

        @block.vector
        def _(dve):
            def read(b, banks, s):
                dve.wait_ge(relu, b + 1)
                t = scr[:, s * mb:s * mb + mb, :]
                nc.vector.tensor_tensor(p[:, bass.ds(b * mb, mb), :], t, t, ALU.mult).then_inc(core.acc_free, 1)
            core.drain(dve, g, read)
    core.blocks_read += g.blocks


def block2(core):
    norm_stage(core, ("norm_mix_g", 0), 1e-6, load_consts=2)
    project_stage(core, "b2_in")
    rnn_stage(core)
    sgu_stage(core)
    gated_stage(core, "branch_a", True, 36, lambda k: core.p[:, k, :])
    gated_stage(core, "branch_b", False, 44, lambda k: core.p[:, 20 + k, :])
    residual_stage(core, "b2_out", 1.0, lambda k: core.p[:, 36 + k, :])
    norm_stage(core, ("norm_ffn_g", 0), 1e-6)
    relu2_stage(core, "mlp_up")
    residual_stage(core, "mlp_down", 1.0, lambda k: core.p[:, k, :])


C3_DT = const_columns(3)[1]
C3_HEADS = C3_DT + DC * P
C3_SKIP = C3_HEADS + 2
C3_END = C3_SKIP + DC
Z, S5U, XS, SB, SC = 0, 16, 24, 32, 34


def ab_in_stage(core):
    nc, g, p, acc = core.nc, core.gemms["ab_in"], core.p, core.acc
    loaded, dt_done = core.sem("dt_loaded"), core.sem("dt_done")
    wdt = core.cst[:, C3_DT:C3_DT + DC * P].rearrange("p (k m) -> p k m", m=P)
    mb = g.cols // P
    with nc.Block(no_gpsimd_drain=True) as block:
        @block.sync
        def _(sp):
            sp.dma_start(core.cst[:, C3_DT:C3_DT + DC * P], core.dram["w_dt"]).then_inc(loaded, 16)
            sp.dma_start(core.cst[:, C3_HEADS:C3_END], core.dram["ssd_small"]).then_inc(loaded, 16)
            core.stream(sp, g)

        @block.tensor
        def _(pe):
            core.product(pe, g, lambda k: core.h[:, k, :])
            pe.wait_ge(loaded, 32)
            pe.wait_ge(core.acc_free, core.blocks_read + g.blocks)
            for k in range(DC):
                ins = pe.matmul(acc[:, 0, :], wdt[:, k, :], core.h[:, k, :], start=(k == 0), stop=(k == DC - 1))
            ins.then_inc(dt_done, 1)

        @block.scalar
        def _(act):
            def read(b, banks, s):
                for m in range(mb):
                    ins = nc.scalar.activation(p[:, b * mb + m, :], banks[m], ACT.Copy)
                ins.then_inc(core.acc_free, 1)
            core.drain(act, g, read)
            act.wait_ge(dt_done, 1)
            nc.scalar.activation(core.scr[:, 0, :], acc[:, 0, :], ACT.Copy)
    core.blocks_read += g.blocks


def ssd_prepare_stage(core):
    nc, p, scr, h, acc, small = core.nc, core.p, core.scr, core.h, core.acc, core.small
    names = ("step", "conv", "silu", "sp_dve", "sp_act", "a", "turned", "sums", "last", "exps", "zeroed")
    q = {s: core.sem(f"sd_{s}") for s in names}
    R = slice(0, SSD_H)
    dt_raw, acs, tok = scr[:, 0, :], scr[:, 1, :], scr[:, 2, :]
    m, e, t, d = (scr[R, 3 + n, :] for n in range(4))
    dtf = scr[:, 3, :]
    heads = lambda n: core.cst[R, C3_HEADS + n:C3_HEADS + n + 1]
    a_col = small[R, 0:1]
    conv = lambda c: h[:, c % 4, :]
    NX = 12
    col = lambda n: tok[:, 64 * n:64 * n + 64]
    with nc.Block(no_gpsimd_drain=True) as block:
        @block.gpsimd
        def _(pool):
            nc.gpsimd.memset(scr[:, 1, :], 0.0)
            nc.gpsimd.memset(scr[:, 3, :], 0.0).then_inc(q["zeroed"], 1)

        @block.vector
        def _(dve):
            v = nc.vector
            mine = Steps(dve, q["step"])
            dve.wait_ge(q["zeroed"], 1)
            mine.then(v.tensor_scalar(dt_raw[R], dt_raw[R], heads(0), None, ALU.add))
            softplus_steps(nc, mine, dt_raw[R], m, e, t, d, q["sp_act"], q["sp_dve"], 0)
            dve.wait_ge(q["a"], 1)
            mine.then(v.tensor_scalar(t, m, a_col, -1.0, ALU.mult, ALU.mult))
            v.tensor_tensor_scan(acs[R], core.const(3, "dt_resets", R), t, 0.0, ALU.mult, ALU.add).then_inc(q["sums"], 1)
            wcol = lambda k, c: core.vcol("ssd_conv_w", k * NX + c)
            for c0 in range(0, NX, 4):
                group = range(c0, c0 + 4)
                if c0:
                    dve.wait_ge(q["silu"], c0)
                for c in group:
                    ins = v.tensor_scalar(conv(c), p[:, XS + c, :], wcol(SSD_K - 1, c), None, ALU.mult)
                mine.then(ins)
                for k in range(SSD_K - 2, -1, -1):
                    back = SSD_K - 1 - k
                    for c in group:
                        ins = v.scalar_tensor_tensor(out=conv(c)[:, back:T], in0=p[:, XS + c, 0:T - back], scalar=wcol(k, c),
                                                     in1=conv(c)[:, back:T], op0=ALU.mult, op1=ALU.add)
                    if k:
                        mine.then(ins)
                ins.then_inc(q["conv"], 1)
            dve.wait_ge(q["turned"], 1)
            for n in range(NCH):
                v.tensor_copy(col(0)[:, n * SSD_H:(n + 1) * SSD_H], acc[:, 0, n * P:n * P + SSD_H])
                ins = v.tensor_copy(col(1)[:, n * SSD_H:(n + 1) * SSD_H], acc[:, 1, n * P:n * P + SSD_H])
            mine.then(ins)
            dve.wait_ge(q["last"], 1)
            mine.then(v.tensor_tensor(col(2), acc[:, 2, 0:64], col(1), ALU.subtract))

        @block.scalar
        def _(act):
            s = nc.scalar
            s.activation(a_col, heads(1), ACT.Exp).then_inc(q["a"], 1)
            softplus_act(nc, act, e, t, q["sp_dve"], q["sp_act"], 0)
            for c in range(NX):
                act.wait_ge(q["conv"], c // 4 + 1)
                s.activation(p[:, XS + c, :], conv(c), ACT.Silu, bias=core.vcol("ssd_conv_b", c)).then_inc(q["silu"], 1)
            act.wait_ge(q["step"], SSD_PREP_STEPS)
            s.activation(col(2), col(2), ACT.Exp)
            s.activation(col(3), col(1), ACT.Exp)
            s.activation(col(4), acc[:, 2, 0:64], ACT.Exp)

        @block.tensor
        def _(pe):
            pe.wait_ge(q["sums"], 1)
            for n in range(NCH):
                pe.transpose(acc[:, 0, n * P:(n + 1) * P], dtf[:, n * P:(n + 1) * P], core.eye[:, :])
                ins = pe.transpose(acc[:, 1, n * P:(n + 1) * P], acs[:, n * P:(n + 1) * P], core.eye[:, :])
            ins.then_inc(q["turned"], 1)
            pe.wait_ge(q["step"], SSD_PREP_STEPS - 1)
            pe.matmul(acc[:, 2, 0:64], core.const(3, "last_row"), col(1), start=True, stop=True).then_inc(q["last"], 1)


SSD_K = 4
SSD_PREP_STEPS = 1 + SOFTPLUS_STEPS + 1 + 3 * 3 + 2


def ssd_stage(core):
    nc, p, scr, h, acc, small = core.nc, core.p, core.scr, core.h, core.acc, core.small
    names = ("step", "staged", "xs_t", "xdt", "b_read", "cb", "cb_read", "bc", "seg", "exp", "m", "yd", "off", "y", "state", "yt", "st", "xds", "zero")
    q = {s: core.sem(f"ssd_{s}") for s in names}
    tok, acs = scr[:, 2, :], scr[:, 1, :]
    col = lambda k, n: tok[:, bass.ds(64 * k + n * SSD_H, SSD_H)]
    free = p[:, 36:52, :]
    stg = p[:, 36:39, :].rearrange("p a t -> p (a t)").rearrange("p (c t) -> p c t", t=P)
    xdt = p[:, 39:41, :].rearrange("p a (h d) -> p (a h) d", d=64)
    xds = p[:, 41:43, :].rearrange("p a (h d) -> p (a h) d", d=64)
    mt = p[:, 43:47, :].rearrange("p a (h l) -> p (a h) l", l=P)
    prev = p[:, 47:49, :]
    y = p[:, 49:51, :]
    btok = p[:, 51, 0:2 * P].rearrange("p (g n) -> p g n", n=P)
    cbs = p[:, 51, 2 * P:4 * P].rearrange("p (g n) -> p g n", n=P)
    h4 = lambda a: a.rearrange("p (h l) -> p h l", l=P)
    h8 = lambda a: a.rearrange("p (h d) -> p h d", d=64)
    b8 = lambda c, g: c[:, 8 * g:8 * g + 8].unsqueeze(2).to_broadcast([P, 8, 64])
    causal = core.const(3, "causal").unsqueeze(1).to_broadcast([P, 4, P])
    rows = core.const(3, "head_rows").rearrange("p (h l) -> p h l", l=P)
    with nc.Block(no_gpsimd_drain=True) as block:
        @block.gpsimd
        def _(pool):
            nc.gpsimd.memset(prev, 0.0).then_inc(q["zero"], 1)
            with pool.Fori(0, NCH) as n:
                pool.wait_ge(q["zero"], 1)
                with_n = bass.ds(n * CH, CH)
                pool.wait_ge(q["step"], n * SSD_STEPS + 1)
                nc.gpsimd.tensor_copy(stg[:, 0:12, :], p[:, XS:XS + 12, with_n]).then_inc(q["staged"], 1)

        @block.vector
        def _(dve):
            v = nc.vector
            mine = Steps(dve, q["step"])
            dve.wait_ge(q["zero"], 1)
            with dve.Fori(0, NCH) as n:
                mine.loop(n, SSD_STEPS)
                ce = small[:, 32:48]
                mine.then(v.tensor_copy(ce, col(3, n)))
                cs, cdt, cds, cdec = col(1, n), col(0, n), col(2, n), col(4, n)
                v.tensor_copy(small[:, 48:64], cdec)
                v.tensor_copy(small[:, 64:80], cdt)
                v.tensor_copy(small[:, 80:96], cds)
                mine.then(v.tensor_copy(small[:, 96:112], cs))
                ldec, ldt, lds, lcs = (small[:, 48 + 16 * k:64 + 16 * k] for k in range(4))
                dve.wait_ge(q["xs_t"], n + 1)
                for g in range(2):
                    v.tensor_tensor(xdt[:, 8 * g:8 * g + 8, :], h8(acc[:, g, :]), b8(ldt, g), ALU.mult)
                v.tensor_copy(btok, acc[:, 2, 0:2 * P].rearrange("p (g n) -> p g n", n=P))
                v.tensor_copy(cbs, acc[:, 2, 2 * P:4 * P].rearrange("p (g n) -> p g n", n=P)).then_inc(q["xdt"], 1)
                dve.wait_ge(q["xdt"], 2 * n + 1)
                for g in range(2):
                    ins = v.tensor_tensor(xds[:, 8 * g:8 * g + 8, :], xdt[:, 8 * g:8 * g + 8, :], b8(lds, g), ALU.mult)
                ins.then_inc(q["xdt"], 1)
                dve.wait_ge(q["bc"], n + 1)
                for b in range(4):
                    ins = v.tensor_tensor(mt[:, 4 * b:4 * b + 4, :], h4(acc[:, 4 + b, :]),
                                          lcs[:, 4 * b:4 * b + 4].unsqueeze(2).to_broadcast([P, 4, P]), ALU.subtract)
                mine.then(ins)
                for b in range(4):
                    v.tensor_tensor(mt[:, 4 * b:4 * b + 4, :], mt[:, 4 * b:4 * b + 4, :], causal, ALU.add).then_inc(q["seg"], 1)
                for b in range(4):
                    dve.wait_ge(q["exp"], 4 * n + b + 1)
                    v.tensor_tensor(mt[:, 4 * b:4 * b + 4, :], mt[:, 4 * b:4 * b + 4, :],
                                    cbs[:, b // 2, :].unsqueeze(1).to_broadcast([P, 4, P]), ALU.mult).then_inc(q["m"], 1)
                dve.wait_ge(q["off"], n + 1)
                for g in range(2):
                    ins = v.tensor_tensor(h8(y[:, g, :]), h8(acc[:, 4 + g, :]), b8(ce, g), ALU.mult)
                mine.then(ins)
                dve.wait_ge(q["yd"], n + 1)
                for g in range(2):
                    ins = v.tensor_tensor(y[:, g, :], y[:, g, :], acc[:, g, :], ALU.add)
                ins.then_inc(q["y"], 1)
                for g in range(2):
                    ins = v.tensor_tensor(h8(prev[:, g, :]), h8(prev[:, g, :]), b8(ldec, g), ALU.mult)
                mine.then(ins)
                for g in range(2):
                    ins = v.tensor_tensor(prev[:, g, :], prev[:, g, :], acc[:, 6 + g, :], ALU.add)
                mine.then(ins)
                dve.wait_ge(q["yt"], n + 1)
                for c in range(8):
                    xs = p[:, XS + c, bass.ds(n * CH, CH)]
                    ins = v.scalar_tensor_tensor(out=xs, in0=xs, scalar=core.cst[:, C3_SKIP + c:C3_SKIP + c + 1],
                                                 in1=h4(acc[:, 2 + c // 4, :])[:, c % 4, :], op0=ALU.mult, op1=ALU.add)
                mine.then(ins)
            mine.end(NCH)

        @block.scalar
        def _(act):
            with act.Fori(0, NCH) as n:
                for b in range(4):
                    act.wait_ge(q["seg"], 4 * n + b + 1)
                    nc.scalar.activation(mt[:, 4 * b:4 * b + 4, :], mt[:, 4 * b:4 * b + 4, :], ACT.Exp).then_inc(q["exp"], 1)

        @block.tensor
        def _(pe):
            mm = pe.matmul
            pe.wait_ge(q["zero"], 1)
            with pe.Fori(0, NCH) as n:
                pe.wait_ge(q["staged"], n + 1)
                for c in range(8):
                    pe.transpose(acc[:, c // 4, (c % 4) * P:(c % 4 + 1) * P], stg[:, c, :], core.eye[:, :])
                for g in range(2):
                    pe.transpose(acc[:, 2, g * P:(g + 1) * P], stg[:, 8 + g, :], core.eye[:, :])
                for g in range(2):
                    ins = mm(acc[:, 2, (2 + g) * P:(3 + g) * P], stg[:, 8 + g, :], stg[:, 10 + g, :], start=True, stop=True)
                ins.then_inc(q["xs_t"], 1)
                for hd in range(SSD_H):
                    ins = mm(acc[:, 4 + hd // 4, (hd % 4) * P:(hd % 4 + 1) * P], rows[:, hd, :], acs[:, bass.ds(n * CH, CH)], start=True, stop=True)
                ins.then_inc(q["bc"], 1)
                pe.wait_ge(q["seg"], 4 * n + 4)
                for g in range(2):
                    ins = mm(acc[:, 4 + g, :], stg[:, 10 + g, :], prev[:, g, :], start=True, stop=True)
                ins.then_inc(q["off"], 1)
                pe.wait_ge(q["xdt"], 2 * n + 2)
                for g in range(2):
                    mm(acc[:, 6 + g, :], btok[:, g, :], xds[:, 8 * g:8 * g + 8, :], start=True, stop=True)
                for hd in range(SSD_H):
                    if hd % 4 == 0:
                        pe.wait_ge(q["m"], 4 * n + hd // 4 + 1)
                    ins = mm(acc[:, hd // 8, (hd % 8) * 64:(hd % 8 + 1) * 64], mt[:, hd, :], xdt[:, hd, :], start=True, stop=True)
                ins.then_inc(q["yd"], 1)
                pe.wait_ge(q["y"], n + 1)
                for c in range(8):
                    ins = pe.transpose(acc[:, 2 + c // 4, (c % 4) * P:(c % 4 + 1) * P], y[:, c // 4, (c % 4) * P:(c % 4 + 1) * P], core.eye[:, :])
                ins.then_inc(q["yt"], 1)


SSD_STEPS = 7


def ssd_gate_stage(core):
    nc, p, scr, h, acc = core.nc, core.p, core.scr, core.h, core.acc
    names = ("step", "gate", "sq", "sum", "inv", "rstd")
    q = {s: core.sem(f"sg_{s}") for s in names}
    rs = scr[:, 0:2, :]
    with nc.Block(no_gpsimd_drain=True) as block:
        @block.scalar
        def _(act):
            s = nc.scalar
            for c in range(8):
                s.activation(h[:, c, :], p[:, Z + 8 + c, :], ACT.Silu).then_inc(q["gate"], 1)
            for c in range(8):
                act.wait_ge(q["step"], c + 1)
                s.activation(h[:, c, :], p[:, XS + c, :], ACT.Square).then_inc(q["sq"], 1)
            act.wait_ge(q["inv"], 1)
            s.activation(rs, rs, ACT.Sqrt).then_inc(q["rstd"], 1)

        @block.tensor
        def _(pe):
            for c in range(8):
                pe.wait_ge(q["sq"], c + 1)
                ins = pe.matmul(acc[:, c // 4, :], core.ones[:, :], h[:, c, :], start=(c % 4 == 0), stop=(c % 4 == 3))
            ins.then_inc(q["sum"], 1)

        @block.vector
        def _(dve):
            v = nc.vector
            mine = Steps(dve, q["step"])
            for c in range(8):
                dve.wait_ge(q["gate"], c + 1)
                mine.then(v.tensor_tensor(p[:, XS + c, :], p[:, XS + c, :], h[:, c, :], ALU.mult))
            dve.wait_ge(q["sum"], 1)
            mine.then(v.tensor_scalar(rs, acc[:, 0:2, :], 2.0 / D, 1e-6, ALU.mult, ALU.add))
            v.reciprocal(rs, rs).then_inc(q["inv"], 1)
            dve.wait_ge(q["rstd"], 1)
            for c in range(8):
                v.scalar_tensor_tensor(out=p[:, XS + c, :], in0=p[:, XS + c, :], scalar=core.vcol("ssd_norm_w", c), in1=rs[:, c // 4, :],
                                       op0=ALU.mult, op1=ALU.mult)


S5_TAB = const_columns(3)[0]["head_rows"][0]
S5_REV = S5_TAB + 2 * 9 * S5_G
S5_COEF = S5_REV + 2 * 8 * S5_G
TWO_PI_1 = 6.28125
TWO_PI_2 = float(np.float32(np.round((2 * np.pi - TWO_PI_1) * 2 ** 22) / 2 ** 22))
TWO_PI_3 = float(np.float32(2 * np.pi - TWO_PI_1 - TWO_PI_2))
TO_INT = 1.5 * 2.0 ** 23
PI_BELOW = 3.1415925


def s5_discretize_stage(core):
    nc, p, scr, cst = core.nc, core.p, core.scr, core.cst
    names = ("loaded", "step", "exp", "half", "tanh", "angle", "sin", "lifted", "stored", "back")
    q = {s: core.sem(f"s5_{s}") for s in names}
    tile = lambda n: scr[:, 6 + n // 8, (n % 8) * 64:(n % 8 + 1) * 64]
    lre, li, dt, th, em, ang, kf, r, sn, hs, cm, cos, rec, t0 = (tile(n) for n in range(14))
    tab = cst[:, S5_TAB:S5_REV].rearrange("p (r m g) -> p r m g", r=2, g=S5_G)
    rev = cst[:, S5_REV:S5_COEF].rearrange("p (r m g) -> p r m g", r=2, g=S5_G)
    y1, y2 = p[:, 32:34, :], p[:, 34:36, :]
    b_, b2 = scr[:, 0:2, :], scr[:, 2:4, :]
    g3 = lambda a: a.rearrange("p a (g i) -> p (a g) i", i=S5_IN)
    bc = lambda c: c.unsqueeze(2).to_broadcast([P, S5_G, S5_IN])
    spread = p[:, 44:52, :]
    big = g3(scr[:, 4:6, :])
    with nc.Block(no_gpsimd_drain=True) as block:
        @block.sync
        def _(sp):
            sp.dma_start(lre, core.dram["lam_re"]).then_inc(q["loaded"], 16)
            sp.dma_start(li, core.dram["lam_im"]).then_inc(q["loaded"], 16)
            sp.dma_start(dt, core.dram["log_dt"].partition_broadcast(P)).then_inc(q["loaded"], 16)
            sp.dma_start(p[:, 32:36, :], core.dram["s5_b"]).then_inc(q["loaded"], 16)
            sp.wait_ge(q["lifted"], DC)
            sp.dma_start(core.dram["lift"].rearrange("(c p) t -> p c t", p=P), spread).then_inc(q["stored"], 16)
            sp.wait_ge(q["stored"], 16)
            by_place = core.dram["lift"].rearrange("(g i) (l n) -> l i g n", i=S5_IN, l=S5_L)
            for l in range(S5_L):
                sp.dma_start(p[l * S5_IN:(l + 1) * S5_IN, 36:44, :].rearrange("p a (g n) -> p (a g) n", n=S5_N), by_place[l]).then_inc(q["back"], 16)
            sp.wait_ge(q["back"], 16 * S5_L)

        @block.gpsimd
        def _(pool):
            for c in range(DC):
                nc.gpsimd.tensor_copy(spread[:, c, :].rearrange("p (l n) -> p l n", l=S5_L),
                                      p[:, S5U + c, :].rearrange("p (n l) -> p l n", l=S5_L)).then_inc(q["lifted"], 1)

        @block.scalar
        def _(act):
            s = nc.scalar
            act.wait_ge(q["loaded"], 64)
            s.activation(dt, dt, ACT.Exp).then_inc(q["exp"], 1)
            act.wait_ge(q["half"], 1)
            s.activation(th, th, ACT.Tanh).then_inc(q["tanh"], 1)
            act.wait_ge(q["angle"], 1)
            s.activation(sn, r, ACT.Sin)
            s.activation(hs, r, ACT.Sin, scale=0.5).then_inc(q["sin"], 1)

        @block.vector
        def _(dve):
            v = nc.vector
            mine = Steps(dve, q["step"])
            then = mine.then
            mul = lambda o, a, b: v.tensor_tensor(o, a, b, ALU.mult)
            dve.wait_ge(q["exp"], 1)
            then(v.tensor_scalar(lre, lre, -1e-4, None, ALU.min))
            v.scalar_tensor_tensor(out=th, in0=lre, scalar=0.5, in1=dt, op0=ALU.mult, op1=ALU.mult).then_inc(q["half"], 1)
            then(mul(ang, li, dt))
            then(v.tensor_scalar(kf, ang, 1 / (2 * np.pi), TO_INT, ALU.mult, ALU.add))
            then(v.tensor_scalar(kf, kf, -TO_INT, None, ALU.add))
            for src, part in ((ang, TWO_PI_1), (r, TWO_PI_2), (r, TWO_PI_3)):
                then(v.scalar_tensor_tensor(out=r, in0=kf, scalar=-part, in1=src, op0=ALU.mult, op1=ALU.add))
            v.tensor_scalar(r, r, PI_BELOW, -PI_BELOW, ALU.min, ALU.max).then_inc(q["angle"], 1)
            dve.wait_ge(q["tanh"], 1)
            then(v.tensor_scalar(em, th, -1.0, 1.0, ALU.mult, ALU.add))
            then(v.reciprocal(em, em))
            then(v.scalar_tensor_tensor(out=em, in0=th, scalar=2.0, in1=em, op0=ALU.mult, op1=ALU.mult))
            then(v.tensor_scalar(t0, em, 1.0, None, ALU.add))
            dve.wait_ge(q["sin"], 1)
            then(v.scalar_tensor_tensor(out=cm, in0=hs, scalar=-2.0, in1=hs, op0=ALU.mult, op1=ALU.mult))
            then(v.tensor_scalar(cos, cm, 1.0, None, ALU.add))
            are, aim = tab[:, 0, 1, :], tab[:, 1, 1, :]
            mul(are, t0, cos)
            then(mul(aim, t0, sn))
            nr = em
            then(mul(nr, em, cos))
            then(v.tensor_tensor(nr, nr, cm, ALU.add))
            mul(rec, lre, lre)
            then(mul(t0, li, li))
            then(v.tensor_tensor(rec, rec, t0, ALU.add))
            then(v.reciprocal(rec, rec))
            mul(ang, nr, lre)
            mul(kf, aim, li)
            mul(r, aim, lre)
            then(mul(t0, nr, li))
            cre, cim = ang, r
            v.tensor_tensor(cre, ang, kf, ALU.add)
            then(v.tensor_tensor(cim, r, t0, ALU.subtract))
            mul(cre, cre, rec)
            then(mul(cim, cim, rec))
            then(v.tensor_scalar(y2, y2, core.const(3, "sign"), -1.0, ALU.mult, ALU.mult))
            mul(g3(b_), g3(y1), bc(cre))
            mul(g3(b2), g3(y2), bc(cre))
            then(mul(big, g3(y2), bc(cim)))
            then(v.tensor_tensor(g3(b_), g3(b_), big, ALU.add))
            then(mul(big, g3(y1), bc(cim)))
            then(v.tensor_tensor(g3(b2), g3(b2), big, ALU.subtract))
            v.memset(tab[:, 0, 0, :], 1.0)
            then(v.memset(tab[:, 1, 0, :], 0.0))
            for m in range(2, S5_L + 1):
                xr, xi = tab[:, 0, m - 1, :], tab[:, 1, m - 1, :]
                mul(th, xr, are)
                mul(em, xi, aim)
                mul(kf, xr, aim)
                then(mul(t0, xi, are))
                v.tensor_tensor(tab[:, 0, m, :], th, em, ALU.subtract)
                then(v.tensor_tensor(tab[:, 1, m, :], kf, t0, ALU.add))
            for s_ in range(S5_L):
                v.tensor_copy(rev[:, :, s_, :], tab[:, :, S5_L - 1 - s_, :])


def s5_state_stage(core):
    nc, p, scr, h, acc, cst = core.nc, core.p, core.scr, core.h, core.acc, core.cst
    names = ("step", "r", "rt", "rt_read", "v", "v_read", "swap", "h")
    q = {s: core.sem(f"sh_{s}") for s in names}
    rev = cst[:, S5_REV:S5_COEF].rearrange("p (r m g) -> p r g m", r=2, g=S5_G)
    tab = cst[:, S5_TAB:S5_REV].rearrange("p (r m g) -> p r m g", r=2, g=S5_G)
    g3 = lambda a: a.rearrange("p a (g i) -> p (a g) i", i=S5_IN)
    b_, b2 = g3(scr[:, 0:2, :]), g3(scr[:, 2:4, :])
    NB = 8
    rows = lambda a: a.rearrange("p a (g s i) -> p (a g) s i", g=4, i=S5_IN)
    cols = lambda a: a.rearrange("p a (g c) -> p (a g) c", g=4)
    r, rt, tmp = p[:, 44:46, :], p[:, 46:48, :], p[:, 48:50, :]
    ul = p[:, 36:44, :].rearrange("p a (g n) -> p (a g) n", n=S5_N)
    hp = h[:, :, :].rearrange("p a (n g) -> p (a n) g", g=S5_G)
    m1, m2 = core.small[:, 0:64], core.small[:, 64:128]
    with nc.Block(no_gpsimd_drain=True) as block:
        @block.vector
        def _(dve):
            v = nc.vector
            mine = Steps(dve, q["step"])
            v.memset(hp[:, 0, :], 0.0)
            with dve.Fori(0, S5_G // NB) as c:
                mine.loop(c, 1)
                gs = bass.ds(c * NB, NB)
                wide = lambda a: a[:, gs, :].unsqueeze(2).to_broadcast([P, NB, S5_L, S5_IN])
                power = lambda k: rev[:, k, gs, :].unsqueeze(3).to_broadcast([P, NB, S5_L, S5_IN])
                v.tensor_tensor(rows(r), wide(b_), power(0), ALU.mult)
                mine.then(v.tensor_tensor(rows(tmp), wide(b2), power(1), ALU.mult))
                v.tensor_tensor(r, r, tmp, ALU.add).then_inc(q["r"], 1)
                dve.wait_ge(q["v"], c + 1)
                v.tensor_copy(hp[:, 1:S5_N, gs].rearrange("p n g -> p g n"),
                              acc[:, 2, :].rearrange("p (g n) -> p g n", n=S5_N)[:, :, 0:S5_N - 1]).then_inc(q["v_read"], 1)
            mine.end(S5_G // NB)
            dve.wait_ge(q["v_read"], S5_G // NB)
            with dve.Fori(0, S5_N - 1) as n:
                mine.loop(n, 2)
                now, nxt = hp[:, n, :], hp[:, n + 1, :]
                mine.then(v.tensor_tensor(m1, tab[:, 0, S5_L, :], now, ALU.mult))
                mine.then(v.tensor_tensor(nxt, nxt, m1, ALU.add))
                dve.wait_ge(q["swap"], n + 1)
                v.tensor_tensor(m2, tab[:, 1, S5_L, :], acc[:, 3, 0:S5_G], ALU.mult).then_inc(q["h"], 1)
                dve.wait_ge(q["h"], 2 * n + 1)
                v.tensor_tensor(nxt, nxt, m2, ALU.add).then_inc(q["h"], 1)
                dve.wait_ge(q["h"], 2 * n + 2)
            mine.end(S5_N - 1)

        @block.scalar
        def _(act):
            with act.Fori(0, S5_G // NB) as c:
                act.wait_ge(q["rt"], c + 1)
                nc.scalar.activation(cols(rt), acc[:, 0:2, :].rearrange("p a (g c) -> p (a g) c", g=4), ACT.Copy).then_inc(q["rt_read"], 1)

        @block.tensor
        def _(pe):
            with pe.Fori(0, S5_G // NB) as c:
                pe.wait_ge(q["r"], c + 1)
                for g in range(NB):
                    ins = pe.transpose(acc[:, g // 4, (g % 4) * P:(g % 4 + 1) * P], cols(r)[:, g, :], core.eye[:, :])
                ins.then_inc(q["rt"], 1)
                pe.wait_ge(q["rt_read"], c + 1)
                for g in range(NB):
                    ins = pe.matmul(acc[:, 2, g * S5_N:(g + 1) * S5_N], cols(rt)[:, g, :], ul[:, c * NB + g, :], start=True, stop=True)
                ins.then_inc(q["v"], 1)
            pe.wait_ge(q["v_read"], S5_G // NB)
            pe.matmul(acc[:, 3, 0:S5_G], core.const(3, "swap"), hp[:, 0, :], start=True, stop=True).then_inc(q["swap"], 1)
            with pe.Fori(1, S5_N - 1) as n:
                pe.wait_ge(q["h"], 2 * n)
                pe.matmul(acc[:, 3, 0:S5_G], core.const(3, "swap"), hp[:, n, :], start=True, stop=True).then_inc(q["swap"], 1)


def s5_output_stage(core):
    nc, p, scr, h, acc, cst = core.nc, core.p, core.scr, core.h, core.acc, core.cst
    names = ("step", "loaded", "zeroed", "pads", "k", "k_read", "y", "y_read", "back")
    q = {s: core.sem(f"so_{s}") for s in names}
    q["stored"] = [core.sem(f"so_stored{b}") for b in range(2)]
    tab = cst[:, S5_TAB:S5_REV].rearrange("p (r m g) -> p r g m", r=2, g=S5_G)
    NB = 8
    ZB = (S5_L - 1) * S5_IN
    g3 = lambda a: a.rearrange("p a (g i) -> p (a g) i", i=S5_IN)
    b_ = g3(scr[:, 0:2, :])
    x1, x2 = g3(p[:, 32:34, :]), g3(p[:, 34:36, :])
    cpad = scr[:, 4:8, :].rearrange("p a (g c) -> p (a g) c", c=256)
    bpad = p[:, 44:48, :].rearrange("p a (g c) -> p (a g) c", c=256)
    kt = p[:, 48:50, :].rearrange("p a (g c) -> p (a g) c", c=P)
    tmp = scr[:, 2:4, :].rearrange("p a (g m o) -> p (a g) m o", g=4, o=S5_IN)
    yl = [p[:, 50 + b, :].rearrange("p (g n) -> p g n", n=S5_N) for b in range(2)]
    ul = p[:, 36:44, :].rearrange("p a (g n) -> p (a g) n", n=S5_N)
    hp = h[:, :, :].rearrange("p a (n g) -> p (a n) g", g=S5_G)
    cdata = lambda m0, m1: cpad[:, :, ZB + m0 * S5_IN:ZB + m1 * S5_IN].rearrange("p g (m o) -> p g m o", o=S5_IN)
    last = core.small[:, 0:NB * S5_IN].rearrange("p (g o) -> p g o", o=S5_IN)
    lift = core.dram["lift"].rearrange("(g o) (l n) -> l o g n", o=S5_IN, l=S5_L)
    with nc.Block(no_gpsimd_drain=True) as block:
        @block.sync
        def _(sp):
            sp.dma_start(p[:, 32:36, :], core.dram["s5_c"]).then_inc(q["loaded"], 16)
            with sp.Fori(0, S5_G // NB // 2) as i:
                for b in range(2):
                    sp.wait_ge(q["y_read"], 2 * i + b + 1)
                    for l in range(S5_L):
                        sp.dma_start(lift[l][:, bass.ds(i * (2 * NB) + b * NB, NB), :], yl[b][l * S5_IN:(l + 1) * S5_IN]).then_inc(q["stored"][b], 16)
            for b in range(2):
                sp.wait_ge(q["stored"][b], 16 * S5_L * (S5_G // NB // 2))
            sp.dma_start(p[:, 36:44, :], core.dram["lift"].rearrange("(c p) t -> p c t", p=P)).then_inc(q["back"], 16)
            sp.wait_ge(q["back"], 16)

        @block.gpsimd
        def _(pool):
            nc.gpsimd.memset(cpad, 0.0)
            nc.gpsimd.memset(bpad, 0.0).then_inc(q["zeroed"], 1)

        @block.vector
        def _(dve):
            v = nc.vector
            mine = Steps(dve, q["step"])
            dve.wait_ge(q["loaded"], 16)
            dve.wait_ge(q["zeroed"], 1)
            v.tensor_scalar(p[:, 32:34, :], p[:, 32:34, :], core.const(3, "sign"), None, ALU.mult)
            mine.then(v.tensor_scalar(p[:, 34:36, :], p[:, 34:36, :], -1.0, None, ALU.mult))
            with dve.Fori(0, S5_G // NB) as c:
                mine.loop(c, 2)
                gs = bass.ds(c * NB, NB)
                wide = lambda a, m: a[:, gs, :].unsqueeze(2).to_broadcast([P, NB, m, S5_IN])
                power = lambda k, m0, m1: tab[:, k, gs, m0:m1].unsqueeze(3).to_broadcast([P, NB, m1 - m0, S5_IN])
                v.tensor_tensor(tmp, wide(x2, 8), power(1, 0, 8), ALU.mult)
                mine.then(v.tensor_tensor(last.unsqueeze(2), wide(x2, 1), power(1, 8, 9), ALU.mult))
                v.tensor_tensor(cdata(0, 8), wide(x1, 8), power(0, 0, 8), ALU.mult)
                v.tensor_copy(bpad[:, :, ZB:ZB + S5_IN], b_[:, gs, :])
                mine.then(v.tensor_tensor(cdata(8, 9), wide(x1, 1), power(0, 8, 9), ALU.mult))
                v.tensor_tensor(cdata(0, 8), cdata(0, 8), tmp, ALU.add)
                v.tensor_tensor(cdata(8, 9), cdata(8, 9), last.unsqueeze(2), ALU.add).then_inc(q["pads"], 1)
                dve.wait_ge(q["y"], c + 1)
            mine.end(S5_G // NB)

        @block.scalar
        def _(act):
            def rounds(i, first):
                for b in range(2):
                    act.wait_ge(q["k"], 2 * i + b + 1)
                    nc.scalar.activation(kt, acc[:, 0:2, :].rearrange("p a (g c) -> p (a g) c", g=4), ACT.Copy).then_inc(q["k_read"], 1)
                    act.wait_ge(q["y"], 2 * i + b + 1)
                    if not first:
                        act.wait_ge(q["stored"][b], i * (16 * S5_L))
                    nc.scalar.activation(yl[b], acc[:, 2, :].rearrange("p (g n) -> p g n", n=S5_N), ACT.Copy).then_inc(q["y_read"], 1)

            rounds(0, True)
            with act.Fori(1, S5_G // NB // 2) as i:
                rounds(i, False)

        @block.tensor
        def _(pe):
            with pe.Fori(0, S5_G // NB) as c:
                pe.wait_ge(q["pads"], c + 1)
                for g in range(NB):
                    out = acc[:, g // 4, (g % 4) * P:(g % 4 + 1) * P]
                    for s in range(S5_L):
                        ins = pe.matmul(out[:, s * S5_IN:P], bpad[:, g, ZB - s * S5_IN:ZB - s * S5_IN + P],
                                        cpad[:, g, ZB:ZB + P - s * S5_IN], start=(s == 0), stop=(s == S5_L - 1), skip_group_check=True)
                ins.then_inc(q["k"], 1)
                pe.wait_ge(q["k_read"], c + 1)
                for g in range(NB):
                    out = acc[:, 2, g * S5_N:(g + 1) * S5_N]
                    pe.matmul(out, kt[:, g, :], ul[:, c * NB + g, :], start=True, stop=False)
                    ins = pe.matmul(out, cpad[:, g, ZB + S5_IN:ZB + S5_IN + P], hp[:, :, c * NB + g], start=False, stop=True)
                ins.then_inc(q["y"], 1)


def s5_skip_stage(core):
    nc, p = core.nc, core.p
    step = core.sem("s5_skipped")
    with nc.Block(no_gpsimd_drain=True) as block:
        @block.vector
        def _(dve):
            for c in range(DC):
                by_token = lambda a: a.rearrange("p (n l) -> p n l", l=S5_L)
                u = by_token(p[:, S5U + c, :])
                nc.vector.scalar_tensor_tensor(out=u, in0=u, scalar=core.vcol("s5_d", c), in1=p[:, 36 + c, :].rearrange("p (l n) -> p n l", l=S5_L),
                                               op0=ALU.mult, op1=ALU.add).then_inc(step, 1)

        @block.scalar
        def _(act):
            nc.scalar.activation(p[:, Z:Z + DC, :], p[:, Z:Z + DC, :], ACT.Silu)
            for c in range(DC):
                act.wait_ge(step, c + 1)
                nc.scalar.activation(p[:, S5U + c, :], p[:, S5U + c, :], ACT.Gelu_apprx_tanh)


def s5_glu_stage(core):
    nc, g, p, scr = core.nc, core.gemms["s5_glu"], core.p, core.scr
    gate, step = core.sem("glu_gate"), core.sem("glu_step")
    mb = g.cols // P
    with nc.Block(no_gpsimd_drain=True) as block:
        @block.sync
        def _(sp):
            core.stream(sp, g)

        @block.tensor
        def _(pe):
            core.product(pe, g, lambda k: p[:, S5U + k, :])

        @block.scalar
        def _(act):
            def read(b, banks, s):
                for m in range(mb):
                    ins = nc.scalar.activation(scr[:, s * mb + m, :], banks[m], ACT.Sigmoid, bias=core.vcol("s5_glu_b", b * mb + m))
                ins.then_inc(gate, 1)
            core.drain(act, g, read)

        @block.vector
        def _(dve):
            def read(b, banks, s):
                dve.wait_ge(gate, b + 1)
                t = scr[:, s * mb:s * mb + mb, :]
                nc.vector.tensor_tensor(t, t, p[:, bass.ds(S5U + b * mb, mb), :], ALU.mult).then_inc(step, 1)
                dve.wait_ge(step, b + 1)
                nc.vector.tensor_tensor(p[:, bass.ds(36 + b * mb, mb), :], t, p[:, bass.ds(Z + b * mb, mb), :], ALU.mult).then_inc(core.acc_free, 1)
            core.drain(dve, g, read)
    core.blocks_read += g.blocks


def block3_first(core):
    norm_stage(core, ("layer_norm", 0), 1e-6, load_consts=3)
    ab_in_stage(core)
    ssd_prepare_stage(core)
    ssd_stage(core)
    ssd_gate_stage(core)
    s5_discretize_stage(core)
    s5_state_stage(core)
    s5_output_stage(core)
    s5_skip_stage(core)
    s5_glu_stage(core)
    residual_stage(core, "ab_out", 1.0, lambda k: core.p[:, 36 + k, :] if k < DC else core.p[:, XS + k - DC, :])


RQ, RK, RV, RG, RO = 0, DC, 2 * DC, 4 * DC, 6 * DC
RET_C = RET_V // P


def ret_rotate_stage(core):
    nc, p, scr, acc = core.nc, core.p, core.scr, core.acc
    names = ("rot", "sin", "cos", "turned")
    q = {s: core.sem(f"rr_{s}") for s in names}
    table = lambda name, c: core.const(4, f"{name}{c % 2}")
    with nc.Block(no_gpsimd_drain=True) as block:
        @block.tensor
        def _(pe):
            for c in range(2 * DC):
                if c >= BANKS:
                    pe.wait_ge(q["sin"], c - BANKS + 1)
                pe.matmul(acc[:, c % BANKS, :], core.const(4, "rotate"), p[:, RQ + c, :], start=True, stop=True).then_inc(q["rot"], 1)

        @block.gpsimd
        def _(pool):
            for c in range(2 * DC):
                pool.wait_ge(q["rot"], c + 1)
                nc.gpsimd.tensor_tensor(p[:, RQ + c, :], p[:, RQ + c, :], table("cos", c), ALU.mult).then_inc(q["cos"], 1)

        @block.vector
        def _(dve):
            for c in range(2 * DC):
                t = scr[:, c % 8, :]
                dve.wait_ge(q["rot"], c + 1)
                if c >= 8:
                    dve.wait_ge(q["turned"], c - 7)
                nc.vector.tensor_tensor(t, acc[:, c % BANKS, :], table("sin", c), ALU.mult).then_inc(q["sin"], 1)
                dve.wait_ge(q["sin"], c + 1)
                dve.wait_ge(q["cos"], c + 1)
                nc.vector.tensor_tensor(p[:, RQ + c, :], p[:, RQ + c, :], t, ALU.add).then_inc(q["turned"], 1)


def retention_stage(core):
    nc, p, scr, h, acc, small = core.nc, core.p, core.scr, core.h, core.acc, core.small
    names = ("step", "staged", "qd", "scores", "st", "kd", "o", "su", "state", "var", "std", "normed", "ot", "gained", "gated")
    q = {s: core.sem(f"rt_{s}") for s in names}
    wide = lambda a, b: scr[:, a:b, :].rearrange("p a (c t) -> p (a c) t", t=CH)
    k_now, q_now, s_t, k_dec = wide(0, 2), wide(2, 4), wide(4, 5), wide(5, 7)
    gains = [scr[:, 7, :], core.rstd[:, :]]
    o_n = p[:, RO:RO + RET_H, :]
    state = lambda hd: h[:, 2 * hd:2 * hd + 2, :]
    value = lambda hd, n: p[:, RV + 4 * hd:RV + 4 * hd + 4, :].rearrange("p (j a) t -> p j (a t)", j=2)[:, :, bass.ds(n * 256, 256)]
    stats, mv, rs = small[:, 0:24], small[:, 24:32], small[:, 32:36]
    tables = lambda name: core.cst[:, const_columns(4)[0][name + "0"][0]:][:, 0:RET_H * P].rearrange("p (h t) -> p h t", t=P)
    with nc.Block(no_gpsimd_drain=True) as block:
        @block.gpsimd
        def _(pool):

            def chunk(n, first=False, last=False):
                if not first:
                    pool.wait_ge(q["o"], n * RET_H)
                nc.gpsimd.tensor_tensor(q_now.rearrange("p (h c) t -> p h c t", c=2),
                                        p[:, RQ:RQ + DC, bass.ds(n * CH, CH)].rearrange("p (h c) t -> p h c t", c=2),
                                        tables("q_decay").unsqueeze(2).to_broadcast([P, RET_H, 2, CH]), ALU.mult).then_inc(q["qd"], 1)

            chunk(0, first=True)
            with pool.Fori(1, NCH - 1) as n:
                chunk(n)
            chunk(NCH - 1, last=True)

        @block.scalar
        def _(act):
            s = nc.scalar

            def chunk(n, first=False, last=False):
                if not first:
                    act.wait_ge(q["scores"], n)
                s.activation(k_now, p[:, RK:RK + DC, bass.ds(n * CH, CH)], ACT.Copy, scale=float(RET_QK ** -0.5)).then_inc(q["staged"], 1)
                act.wait_ge(q["scores"], n + 1)
                if not first:
                    act.wait_ge(q["su"], n * RET_H)
                for hd in range(0 if last else RET_H):
                    ins = s.activation(k_dec[:, 2 * hd:2 * hd + 2, :], acc[:, 1 + hd // 2, (hd % 2) * 256:(hd % 2 + 1) * 256].rearrange("p (c t) -> p c t", t=P),
                                       ACT.Copy, scale=core.const(4, "k_decay")[:, hd:hd + 1])
                if not last:
                    ins.then_inc(q["kd"], 1)
                act.wait_ge(q["var"], n + 1)
                s.activation(rs, rs, ACT.Sqrt).then_inc(q["std"], 1)
                for hd in range(RET_H):
                    act.wait_ge(q["ot"], n * RET_H + hd + 1)
                    if hd >= 2 or not first:
                        act.wait_ge(q["gated"], n * RET_H + hd - 1)
                    for j in range(RET_C):
                        c = RET_C * hd + j
                        ins = s.activation(gains[hd % 2][:, j * P:(j + 1) * P], acc[:, 4 + hd, j * P:(j + 1) * P], ACT.Identity,
                                           scale=core.vcol("ret_gn_w", c), bias=core.vcol("ret_gn_b", c))
                    ins.then_inc(q["gained"], 1)

            chunk(0, first=True)
            with act.Fori(1, NCH - 1) as n:
                chunk(n)
            chunk(NCH - 1, last=True)

        @block.vector
        def _(dve):
            v = nc.vector
            mine = Steps(dve, q["step"])

            def chunk(n, first=False, last=False):
                if not (first or last):
                    mine.loop(n - 1, 3)
                dve.wait_ge(q["scores"], n + 1)
                v.tensor_tensor(s_t, acc[:, 0, :].rearrange("p (h t) -> p h t", t=P), tables("intra"), ALU.mult).then_inc(q["st"], 1)
                for hd in range(RET_H):
                    if hd == RET_H - 1:
                        dve.wait_ge(q["o"], n * RET_H + RET_H)
                        for o in range(RET_H):
                            ins = v.bn_stats(stats[:, 6 * o:6 * o + 6], acc[:, 4 + o, :])
                        mine.then(ins)
                    if last:
                        continue
                    dve.wait_ge(q["su"], n * RET_H + hd + 1)
                    added = acc[:, 2 * (hd % 2):2 * (hd % 2) + 2, :]
                    if first:
                        v.tensor_copy(state(hd), added).then_inc(q["state"], 1)
                    else:
                        v.scalar_tensor_tensor(out=state(hd), in0=state(hd), scalar=core.const(4, "chunk_decay")[:, hd:hd + 1], in1=added,
                                               op0=ALU.mult, op1=ALU.add).then_inc(q["state"], 1)
                for hd in range(RET_H):
                    ins = v.bn_aggr(mv[:, 2 * hd:2 * hd + 2], stats[:, 6 * hd:6 * hd + 6])
                mine.then(ins)
                mine.then(v.tensor_scalar(rs, mv.rearrange("p (h k) -> p h k", k=2)[:, :, 1:2].rearrange("p h k -> p (h k)"), 1e-6, None, ALU.add))
                v.reciprocal(rs, rs).then_inc(q["var"], 1)
                dve.wait_ge(q["std"], n + 1)
                if not first:
                    dve.wait_ge(q["ot"], n * RET_H)
                for hd in range(RET_H):
                    v.tensor_scalar(o_n[:, hd, :], acc[:, 4 + hd, :], mv[:, 2 * hd:2 * hd + 1], rs[:, hd:hd + 1], ALU.subtract, ALU.mult).then_inc(q["normed"], 1)
                for hd in range(RET_H):
                    dve.wait_ge(q["gained"], n * RET_H + hd + 1)
                    y = p[:, RG + 4 * hd:RG + 4 * hd + 4, bass.ds(n * CH, CH)]
                    v.tensor_tensor(y, y, gains[hd % 2].rearrange("p (c t) -> p c t", t=P), ALU.mult).then_inc(q["gated"], 1)

            chunk(0, first=True)
            with dve.Fori(1, NCH - 1) as n:
                chunk(n)
            mine.end(NCH - 2)
            chunk(NCH - 1, last=True)

        @block.tensor
        def _(pe):
            mm = pe.matmul

            def chunk(n, first=False, last=False):
                pe.wait_ge(q["staged"], n + 1)
                if not first:
                    pe.wait_ge(q["state"], n * RET_H)
                for hd in range(RET_H):
                    for j in range(2):
                        ins = mm(acc[:, 0, hd * P:(hd + 1) * P], k_now[:, 2 * hd + j, :], p[:, RQ + 2 * hd + j, bass.ds(n * CH, CH)], start=(j == 0), stop=(j == 1))
                for c in range(0 if last else 2 * RET_H):
                    ins = pe.transpose(acc[:, 1 + c // 4, (c % 4) * P:(c % 4 + 1) * P], k_now[:, c, :], core.eye[:, :])
                ins.then_inc(q["scores"], 1)
                pe.wait_ge(q["qd"], n + 1)
                if not first:
                    pe.wait_ge(q["gained"], n * RET_H)
                pe.wait_ge(q["st"], n + 1)
                if not last:
                    pe.wait_ge(q["kd"], n + 1)
                for pair in range(0, RET_H, 2):
                    for hd in (pair, pair + 1):
                        for j in range(0 if first else 2):
                            mm(acc[:, 4 + hd, :], q_now[:, 2 * hd + j, :], state(hd)[:, j, :], start=(j == 0), stop=False)
                        mm(acc[:, 4 + hd, :], s_t[:, hd, :], value(hd, n), start=first, stop=True).then_inc(q["o"], 1)
                    if last:
                        continue
                    if pair:
                        pe.wait_ge(q["state"], n * RET_H + 2)
                    for hd in (pair, pair + 1):
                        for j in range(2):
                            ins = mm(acc[:, 2 * (hd % 2) + j, :], k_dec[:, 2 * hd + j, :], value(hd, n), start=True, stop=True)
                        ins.then_inc(q["su"], 1)
                for hd in range(RET_H):
                    pe.wait_ge(q["normed"], n * RET_H + hd + 1)
                    for j in range(RET_C):
                        ins = pe.transpose(acc[:, 4 + hd, j * P:(j + 1) * P], o_n[:, hd, j * P:(j + 1) * P], core.eye[:, :])
                    ins.then_inc(q["ot"], 1)

            chunk(0, first=True)
            with pe.Fori(1, NCH - 1) as n:
                chunk(n)
            chunk(NCH - 1, last=True)


def block3_second(core):
    norm_stage(core, ("layer_norm", DC), 1e-6, load_consts=4)
    project_stage(core, "ret_qk")
    project_stage(core, "ret_v", at=RV, by_token=True)
    project_stage(core, "ret_g", at=RG, func=ACT.Silu)
    ret_rotate_stage(core)
    retention_stage(core)
    residual_stage(core, "ret_out", 1.0, lambda k: core.p[:, RG + k, :])


def lay_weights(which, inputs):
    gemms, n = lay_stream(which)
    out = np.zeros((n, P, SLOT), np.float32)

    def fill(name, *mats):
        g = gemms.get(name)
        if g is None:
            return
        cols = g.cols // len(mats)
        for b in range(g.blocks):
            for sub in range(g.q):
                slot = out[g.first + b * g.q + sub, :, 0:g.width].reshape(P, g.kc, g.cols)
                for j, w in enumerate(mats):
                    part = w[sub * g.kc * P:(sub + 1) * g.kc * P, b * cols:(b + 1) * cols]
                    slot[:, :, j * cols:(j + 1) * cols] = part.reshape(g.kc, P, cols).transpose(1, 0, 2)

    a = {k: np.asarray(v) for k, v in inputs.items()}
    for f in ("ffn1", "ffn2"):
        fill(f"{f}_up", a[f"{f}_gate"][0], a[f"{f}_up"][0])
        fill(f"{f}_down", a[f"{f}_down"][0])
    fill("mix_in", a["w_in"][0])
    fill("mix_out", a["w_out"][0])
    fill("b2_in", a["w_in_2"][0])
    fill("branch_a", a["w_branch_a_2"][0])
    fill("branch_b", a["w_branch_b_2"][0])
    fill("b2_out", a["w_out_2"][0])
    fill("mlp_up", a["w_up_2"][0])
    fill("mlp_down", a["w_down_2"][0])
    fill("ab_in", a["ab_w_in_3"][0][:, 0:18 * 2 * P])
    fill("s5_glu", a["s5_glu_w_3"][0])
    fill("ab_out", a["ab_w_out_3"][0])
    qk = 2 * RET_H * RET_QK
    fill("ret_qk", a["ret_w_in_3"][0][:, 0:qk])
    fill("ret_v", a["ret_w_in_3"][0][:, qk:qk + RET_H * RET_V])
    fill("ret_g", a["ret_w_in_3"][0][:, qk + RET_H * RET_V:])
    fill("ret_out", a["ret_w_out_3"][0])
    return out


def lay_vectors(inputs):
    a = {k: np.asarray(v) for k, v in inputs.items()}
    src = {"norm_ffn1": "norm_ffn1", "norm_mix": "norm_mix", "b_in_attn": "b_in_attn", "shift_mix": "rwkv_shift_mix",
           "w0": "rwkv_w0", "a0": "rwkv_a0", "k_k": "rwkv_k_k", "k_a": "rwkv_k_a", "r_k": "rwkv_r_k", "ln_w": "rwkv_ln_w",
           "ln_b": "rwkv_ln_b", "norm_ffn2": "norm_ffn2", "norm_final": "norm_final", "norm_mix_g": "norm_mix_g_2",
           "conv_w": "conv_w_2", "conv_b": "conv_b_2", "lru_b_a": "lru_b_a_2", "lru_b_x": "lru_b_x_2",
           "lru_lambda": "lru_lambda_2", "sgu_ln_g": "sgu_ln_g_2", "sgu_ln_b": "sgu_ln_b_2", "norm_ffn_g": "norm_ffn_g_2",
           "final_norm_g": "final_norm_g_2", "layer_norm": "layer_norm_w_3", "s5_d": "s5_d_3", "s5_glu_b": "s5_glu_b_3",
           "ssd_conv_w": "ssd_conv_w_3", "ssd_conv_b": "ssd_conv_b_3", "ssd_norm_w": "ssd_norm_w_3", "ret_gn_w": "ret_gn_w_3", "ret_gn_b": "ret_gn_b_3",
           "final_norm_w": "final_norm_w_3"}
    cols = [a[src[name]].reshape(k, P) for name, k in VECTORS]
    return np.ascontiguousarray(np.concatenate(cols, 0).T)


def lay_small(inputs):
    a = {k: np.asarray(v) for k, v in inputs.items()}
    out = {}
    lora = np.zeros((P, 3, T), np.float32)
    lora[0:64, 0], lora[64:128, 1], lora[:, 2] = a["rwkv_w2"][0], a["rwkv_a2"][0], a["rwkv_g2"][0]
    out["lora"] = lora
    out["sinks"] = a["attn_sinks"].reshape(Q_HEADS)
    bd = np.zeros((P, RNNC, 2, P), np.float32)
    for g, w in enumerate((a["lru_w_a_2"][0], a["lru_w_x_2"][0])):
        for c in range(RNNC):
            for j in range(2):
                bd[j * 64:j * 64 + 64, c, g, j * 64:j * 64 + 64] = w[2 * c + j]
    out["lru_w"] = bd.reshape(P, -1)
    out["sgu_w"] = np.ascontiguousarray(a["sgu_w_s_2"][0].transpose(2, 0, 1))
    out["sgu_b"] = a["sgu_b_s_2"].reshape(-1)
    wdt = np.zeros((DC, P, P), np.float32)
    wdt[:, :, 0:SSD_H] = a["ab_w_in_3"][0][:, 18 * 2 * P:].reshape(DC, P, SSD_H)
    out["w_dt"] = np.ascontiguousarray(wdt.transpose(1, 0, 2)).reshape(P, -1)
    heads = np.zeros((P, 2 + DC), np.float32)
    heads[0:SSD_H, 0], heads[0:SSD_H, 1] = a["ssd_dt_bias_3"][0], a["ssd_a_log_3"][0]
    heads[:, 2:] = np.repeat(a["ssd_d_3"][0], 64).reshape(DC, P).T
    out["ssd_small"] = heads
    twice = lambda m: np.ascontiguousarray(np.concatenate([m, m], 0))
    out["lam_re"], out["lam_im"] = twice(a["s5_lam_re_3"][0].T), twice(a["s5_lam_im_3"][0].T)
    out["log_dt"] = a["s5_log_dt_3"].reshape(-1)
    by_state = lambda re, im: np.concatenate([re, im], 0).reshape(P, -1)
    br, bi = (a[f"s5_b_{k}_3"][0].transpose(1, 0, 2) for k in ("re", "im"))
    cr, ci = (a[f"s5_c_{k}_3"][0].transpose(2, 0, 1) for k in ("re", "im"))
    out["s5_b"] = np.concatenate([by_state(br, bi), by_state(bi, br)], 1).reshape(P, 4, T)
    out["s5_c"] = np.concatenate([by_state(cr, ci), by_state(ci, cr)], 1).reshape(P, 4, T)
    return out


def lay_out(which, inputs):
    x = np.asarray(inputs["x"])[0]
    arrays = {"x": np.ascontiguousarray(x.reshape(T, DC, P).transpose(2, 1, 0)), "weights": lay_weights(which, inputs),
              "vectors": lay_vectors(inputs)}
    arrays.update(lay_small(inputs))
    for n, make in CONSTS.items():
        arrays[f"consts{n}"] = np.concatenate([part for _, part in make()], axis=1)
    return arrays


def build(nc, dram, out, run, which=None):
    dram = dict(dram, lift=nc.dram_tensor("lift", (D, T), F32, kind="Internal").ap())
    with ExitStack() as ctx:
        core = Core(nc, ctx, dram, which)
        run(core, out)


def whole(core, out):
    start_stage(core, 1)
    block1(core)
    norm_stage(core, ("norm_final", 0), 1e-5, dst=core.x)
    core.clear_sems()
    block2(core)
    norm_stage(core, ("final_norm_g", 0), 1e-6, dst=core.x)
    core.clear_sems()
    block3_first(core)
    block3_second(core)
    norm_stage(core, ("final_norm_w", 0), 1e-6, dst=core.x)
    finish_stage(core, out)


def finish_stage(core, out):
    nc = core.nc
    stored = core.sem("stored")
    with nc.Block(no_gpsimd_drain=True) as block:
        @block.sync
        def _(sp):
            sp.dma_start(out, core.x[:, :, :]).then_inc(stored, 16)
            sp.wait_ge(stored, 16)


def kernel(**inputs):
    import concourse.bacc as bacc
    from concourse.bass_utils import run_bass_kernel_spmd

    nc = bacc.Bacc("TRN2", target_bir_lowering=False, num_devices=1)
    arrays = lay_out(None, inputs)
    dram = {n: nc.dram_tensor(f"in_{n}", a.shape, F32, kind="ExternalInput").ap() for n, a in arrays.items()}
    out = nc.dram_tensor("out", (P, DC, T), F32, kind="ExternalOutput").ap()
    build(nc, dram, out, whole)
    r = run_bass_kernel_spmd(nc, [{f"in_{n}": a for n, a in arrays.items()}], core_ids=[0])
    got = r.results[0]["out"]
    return np.ascontiguousarray(got.transpose(2, 1, 0)).reshape(1, T, D)
```

```python
from contextlib import ExitStack

import numpy as np

import concourse.bass as bass
from concourse import mybir

F32 = mybir.dt.float32
F32R = mybir.dt.float32r
ALU = mybir.AluOpType
ACT = mybir.ActivationFunctionType
AX = mybir.AxisListType

P = 128
T = 512
D = 1024
DC = D // P
SLOT = 1408
RING = 4
AHEAD = 2
BANKS = 8

FF = 2816
FFC = FF // P
HEAD = 64
RW_HEADS = 8
PAIRS = RW_HEADS // 2
LC = 64
NLC = T // LC
LORA_W, LORA_G = 12, 13
ATT_Q, ATT_K, ATT_V = 14, 18, 19
AB = 128
NAB = T // AB
Q_HEADS = 8
MASKED = -1.0e30
DECAY_RATE = float(np.exp(-0.5))
RNNC = 1280 // P
CONV = 4
SGU_G = 8
S5_G, S5_IN, S5_P = 64, 16, 64
S5_L = P // S5_IN
S5_N = T // S5_L
SSD_H, SSD_REP = 16, 8
CH = 128
NCH = T // CH
RET_H, RET_QK, RET_V = 4, 256, 512


class Gemm:

    def __init__(self, first, blocks, q, kc, cols, by_token):
        self.by_token = by_token
        self.first, self.blocks, self.q, self.kc, self.cols = first, blocks, q, kc, cols
        self.n = blocks * q
        self.width = kc * cols
        self.body = max(8, 2 * q)
        self.per = self.body // q
        self.mb = T // P if by_token else cols // P
        self.sets = min(self.per, BANKS // self.mb)


class Operand:

    def __init__(self, core, n, x, hi, lo=None):
        self.n = n
        self.x = lambda k: x(core, k)
        self.hi = lambda k: hi(core.r, k)
        self.lo = lambda k: (lo or x)(core.r, k)


class Rounded:
    pass


class Chunks:

    def __init__(self, chunks):
        self.chunks = chunks

    def __getitem__(self, at):
        partitions, chunk, tokens = at
        return self.chunks[chunk][partitions, tokens]


STREAM = [
    ("ffn1_up", FF // P, 2, 4, 2 * P), ("ffn1_down", DC, 2, FFC // 2, P),
    ("mix_in", 10, 2, 4, 2 * P), ("mix_out", 4, 2, 4, 2 * P),
    ("ffn2_up", FF // P, 2, 4, 2 * P), ("ffn2_down", DC, 2, FFC // 2, P),
    ("b2_in", 26, 2, 4, 2 * P), ("branch_a", 4, 2, RNNC // 2, 2 * P), ("branch_b", 4, 2, 4, 2 * P),
    ("b2_out", 4, 2, 4, 2 * P), ("mlp_up", 16, 2, 4, 2 * P), ("mlp_down", 4, 8, 4, 2 * P),
    ("ab_in", 18, 2, 4, 2 * P), ("s5_glu", 4, 2, 4, 2 * P), ("ab_out", 4, 4, 4, 2 * P),
    ("ret_qk", 8, 2, 4, 2 * P), ("ret_v", 8, 2, 4, 2 * P), ("ret_g", 8, 2, 4, 2 * P), ("ret_out", 4, 4, 4, 2 * P),
]
BY_TOKEN = ("ret_v",)


def lay_stream(which):
    gemms, at = {}, 0
    for name, blocks, q, kc, cols in STREAM:
        if which is None or name in which:
            gemms[name] = Gemm(at, blocks, q, kc, cols, name in BY_TOKEN)
            at += blocks * q
    return gemms, at


VECTORS = [
    ("norm_ffn1", 8), ("norm_mix", 8), ("b_in_attn", 6), ("shift_mix", 14), ("w0", 4), ("a0", 4),
    ("k_k", 4), ("k_a", 4), ("r_k", 4), ("ln_w", 4), ("ln_b", 4), ("norm_ffn2", 8), ("norm_final", 8),
    ("norm_mix_g", 8), ("conv_w", 40), ("conv_b", 10), ("lru_b_a", 10), ("lru_b_x", 10), ("lru_lambda", 10),
    ("sgu_ln_g", 8), ("sgu_ln_b", 8), ("norm_ffn_g", 8), ("final_norm_g", 8),
    ("layer_norm", 16), ("s5_d", 8), ("s5_glu_b", 8), ("ssd_conv_w", 48), ("ssd_conv_b", 12),
    ("ssd_norm_w", 8), ("ret_gn_w", 16), ("ret_gn_b", 16), ("final_norm_w", 8),
]
VEC_AT = {}
_n = 0
for _name, _k in VECTORS:
    VEC_AT[_name] = _n
    _n += _k
N_VEC = _n


def pair_masks():
    i = np.arange(P)
    same = (i[:, None] // LC) == (i[None, :] // LC)
    r, c = i[:, None] % LC, i[None, :] % LC
    f = lambda m: (m & same).astype(np.float32)
    out = {"strict": f(r < c), "upto": f(r <= c)}
    for n in (1, 2, 4, 8, 16, 32):
        m = (r // (2 * n) == c // (2 * n)) & (r // n % 2 == 0) & (c // n % 2 == 1)
        out[f"level{n}"] = f(m)
    m = (c // 2 == r // 2) & (c % 2 == 0) & (r % 2 == 1)
    out["level1_ts"] = f(m)
    return out


def block1_consts():
    i = np.arange(P)
    m = pair_masks()
    parts = [("head_ones", ((i[:, None] // HEAD) == (i[None, :] // HEAD)).astype(np.float32)),
             ("stacked_eye", np.concatenate([np.eye(HEAD), np.eye(HEAD)]).astype(np.float32)),
             ("resets", np.tile((np.arange(T) % LC != 0).astype(np.float32), (P, 1)))]
    parts += list(m.items())
    qi, kj = np.arange(AB)[:, None], np.arange(2 * AB)[None, :]
    dist = qi + AB - kj
    band = (dist >= 0) & (dist < AB)
    for n in range(NAB):
        ok = band if n else band & (kj >= AB)
        parts.append((f"band{n}", np.where(ok, 0.0, MASKED).astype(np.float32)))
    for g in range(2):
        dup = np.zeros((P, P), np.float32)
        for j in range(2):
            dup[g * HEAD + np.arange(HEAD), j * HEAD + np.arange(HEAD)] = 1
        parts.append((f"dup{g}", dup))
    return parts


def block2_consts():
    chunk = np.arange(P) // 64
    return [("sgu_mask", (chunk[None, :] >= chunk[:, None]).astype(np.float32))]


def s5_swap():
    swap = np.zeros((P, P), np.float32)
    p = np.arange(S5_P)
    swap[S5_P + p, p] = -1.0
    swap[p, S5_P + p] = 1.0
    return swap


def block3_consts():
    i = np.arange(P)
    sign = np.where(i < S5_P, 1.0, -1.0).astype(np.float32)[:, None]
    sel = np.zeros((P, SSD_H, P), np.float32)
    for h in range(SSD_H):
        sel[h, h, :] = 1.0
    last = np.zeros((P, P), np.float32)
    last[P - 1, :] = 1.0
    return [("swap", s5_swap()), ("sign", sign), ("causal", np.where(i[:, None] <= i[None, :], 0.0, MASKED).astype(np.float32)),
            ("last_row", last), ("head_rows", sel.reshape(P, -1)),
            ("dt_resets", np.tile((np.arange(T) % CH != 0).astype(np.float32), (P, 1)))]


def block4_consts():
    f = np.float32
    i = np.arange(P)
    rot = np.zeros((P, P), f)
    rot[np.arange(1, P, 2), np.arange(0, P, 2)] = -1.0
    rot[np.arange(0, P, 2), np.arange(1, P, 2)] = 1.0
    angle = np.repeat(f(1.0) / (f(10000.0) ** np.linspace(0.0, 1.0, RET_QK // 2, dtype=f)), 2).astype(f)
    theta = angle[:, None] * np.arange(T, dtype=f)[None, :]
    cos, sin = np.cos(theta).astype(f), np.sin(theta).astype(f)
    parts = [("rotate", rot)]
    for h in range(2):
        parts += [(f"cos{h}", cos[h * P:(h + 1) * P]), (f"sin{h}", sin[h * P:(h + 1) * P])]
    lg = np.log(1.0 - 2.0 ** (-5.0 - np.arange(RET_H)))
    rel = i[None, :] - i[:, None]
    for h in range(RET_H):
        parts.append((f"intra{h}", np.where(rel >= 0, np.exp(lg[h] * np.maximum(rel, 0)), 0.0).astype(f)))
    for h in range(RET_H):
        parts.append((f"q_decay{h}", np.tile(np.exp(lg[h] * (i + 1.0)), (P, 1)).astype(f)))
    parts.append(("k_decay", np.exp(lg[None, :] * (CH - 1.0 - i)[:, None]).astype(f)))
    parts.append(("chunk_decay", np.tile(np.exp(lg * CH)[None, :], (P, 1)).astype(f)))
    return parts


CONSTS = {1: block1_consts, 2: block2_consts, 3: block3_consts, 4: block4_consts}


def const_columns(which):
    at, out = 0, {}
    for name, a in CONSTS[which]():
        out[name] = (at, a.shape[1])
        at += a.shape[1]
    return out, at


class Steps:

    def __init__(self, eng, sem):
        self.eng, self.sem, self.base, self.n, self.i, self.per = eng, sem, 0, 0, None, 0

    def loop(self, i, per):
        self.base, self.i, self.per, self.n = self.base + self.n, i, per, 0

    def end(self, times):
        assert self.n == self.per, (self.n, self.per)
        self.base, self.i, self.n = self.base + times * self.per, None, 0

    def value(self):
        return self.base + self.n + (0 if self.i is None else self.i * self.per)

    def then(self, ins):
        ins.then_inc(self.sem, 1)
        self.n += 1
        self.eng.wait_ge(self.sem, self.value())


class Core:

    def __init__(self, nc, ctx, dram, which):
        self.nc, self.ctx, self.dram = nc, ctx, dram
        self.block_sems = []
        self.gemms, self.n_slots = lay_stream(which)
        shapes = dict(
            x=[P, DC, T],
            h=[P, DC, T],
            p=[P, 52, T],
            weight_ring=[P, RING, SLOT],
            weight_hi=[P, AHEAD, SLOT],
            vec=[P, N_VEC],
            cst=[P, 3980],
            eye=[P, P], ones=[P, P], rstd=[P, T], scr=[P, 8, T], small=[P, 256])
        self.r, at = Rounded(), -(-nc.sbuf_base // 32) * 32
        place, alias = {}, {}
        for name, shape in shapes.items():
            place[name] = nc.alloc_sbuf_tensor_at(name, shape, F32, offset=at)
            if name in ("weight_ring", "weight_hi", "cst"):
                alias[name] = nc.alloc_sbuf_tensor_at(f"{name}_r", shape, F32R, offset=at)
            elif name in ("h", "p", "scr"):
                alias[name] = Chunks([nc.alloc_sbuf_tensor_at(f"{name}_r{c}", [P, T], F32R, offset=at + 4 * T * c) for c in range(shape[1])])
            at += -(-4 * int(np.prod(shape[1:])) // 32) * 32
        self.x, self.h, self.p, self.weight_ring, self.weight_hi, self.vec, self.cst, self.eye, self.ones, self.rstd, self.scr, self.small = place.values()
        self.r.h, self.r.p, self.r.weight_ring, self.r.weight_hi, self.r.cst, self.r.scr = (
            alias[n] for n in ("h", "p", "weight_ring", "weight_hi", "cst", "scr"))
        self.acc = ctx.enter_context(nc.psum_tensor("acc", [P, BANKS, T], F32))
        self.slot_loaded = [self.sem(f"slot{r}_loaded") for r in range(RING)]
        self.weights_rounded, self.weights_split = self.sem("weights_rounded"), self.sem("weights_split")
        self.input_rounded, self.input_split = self.sem("input_rounded"), self.sem("input_split")
        self.inputs = 0
        self.products_done = self.sem("products_done")
        self.acc_free = self.sem("acc_free")
        self.blocks_read = 0
        self.norm = {n: self.sem(f"norm_{n}") for n in ("squared", "summed", "var", "inv", "rstd", "consts")}
        self.const_loads = 0
        self.norms = 0
        self.block_sems = []

    def sem(self, name):
        s = self.nc.alloc_semaphore(name)
        self.block_sems.append(s)
        return s

    def clear_sems(self):
        self.nc.clear_and_free_semaphores(self.block_sems)
        self.nc.all_engine_barrier()
        self.block_sems = []

    def vcol(self, name, c):
        return self.vec[:, bass.ds(VEC_AT[name] + c, 1)]

    def const(self, which, name, part=slice(None)):
        at, n = const_columns(which)[0][name]
        return self.cst[part, at:at + n]

    def const_load(self, eng, which, signal):
        n = const_columns(which)[1]
        eng.dma_start(self.cst[:, 0:n], self.dram[f"consts{which}"]).then_inc(signal, 16)

    def width_of(self, s):
        for g in self.gemms.values():
            if g.first <= s < g.first + g.n:
                return g.width
        raise ValueError(s)

    def one_load(self, sp, s, r, width, wait):
        if wait is not None:
            sp.wait_ge(self.products_done, wait)
        sp.dma_start(self.weight_ring[:, r, 0:width], self.dram["weights"][s, :, 0:width])\
            .then_inc(self.slot_loaded[r], 16)

    def first_loads(self, sp):
        for s in range(min(RING, self.n_slots)):
            self.one_load(sp, s, s % RING, self.width_of(s), None)

    def stream(self, sp, g):
        lo, hi = g.first + RING, g.first + g.n
        rounds = max(0, hi - lo) // RING
        if rounds > 0:
            with sp.Fori(0, rounds) as i:
                for j in range(RING):
                    self.one_load(sp, lo + i * RING + j, (lo + j) % RING, g.width, g.first + 1 + i * RING + j)
        for s in range(lo + rounds * RING, min(hi + RING, self.n_slots)):
            self.one_load(sp, s, s % RING, self.width_of(s), s - RING + 1)

    def round_slot(self, act, s, r, ahead, width, turn, used=None):
        act.wait_ge(self.slot_loaded[r], turn)
        if used is not None:
            act.wait_ge(self.products_done, used)
        self.nc.scalar.activation(self.r.weight_hi[:, ahead, 0:width], self.weight_ring[:, r, 0:width], ACT.Copy)\
            .then_inc(self.weights_rounded, 1)

    def rest_slot(self, pool, s, r, ahead, width):
        raw, rest, hi = (m[:, n, 0:width] for m, n in ((self.weight_ring, r), (self.r.weight_ring, r), (self.r.weight_hi, ahead)))
        pool.wait_ge(self.weights_rounded, s + 1)
        self.nc.gpsimd.tensor_tensor(rest, raw, hi, ALU.subtract).then_inc(self.weights_split, 1)

    def round_parts(self, act, g, op, read=None):
        mb, per, sets, body = g.mb, g.per, g.sets, g.body
        turn = lambda s: 16 * (s // RING + 1)

        def inputs(sub):
            for k in range(sub * g.kc, (sub + 1) * g.kc):
                self.nc.scalar.activation(op.hi(k), op.x(k), ACT.Copy).then_inc(self.input_rounded, 1)

        def round_of(i, at, n):
            for b in range(n):
                for sub in range(g.q):
                    done = g.first + (at + b) * g.q + sub + 1
                    s = done + 1
                    if i is None and s < min(g.first + g.n + 1, self.n_slots):
                        self.round_slot(act, s, s % RING, s % AHEAD, self.width_of(s), turn(s), done)
                    elif i is not None:
                        self.round_slot(act, s + i * body, s % RING, s % AHEAD, g.width, turn(s) + i * (16 * body // RING), done + i * body)
                    if op is not None and i is None and at + b == 0 and sub + 2 < g.q:
                        inputs(sub + 2)
                if read is not None:
                    block_ = at + b if i is None else at + b + i * per
                    act.wait_ge(self.products_done, g.first + (block_ + 1) * g.q)
                    set_ = b % sets
                    read(block_, [self.acc[:, set_ * mb + m, :] for m in range(mb)], set_)

        if op is not None:
            inputs(0)
        second = g.first + 1
        self.round_slot(act, second, second % RING, second % AHEAD, g.width, turn(second), second - 1 if second > 1 else None)
        if op is not None:
            inputs(1)
        rounds = -(-g.blocks // per)
        round_of(None, 0, min(per, g.blocks))
        if rounds > 2:
            with act.Fori(0, rounds - 2) as i:
                round_of(i, per, per)
        if rounds > 1:
            round_of(None, (rounds - 1) * per, g.blocks - (rounds - 1) * per)

    def rest_weights(self, pool, g):
        lo, hi = g.first + 1, g.first + g.n
        rounds = (hi - lo) // RING
        if rounds > 0:
            with pool.Fori(0, rounds) as i:
                for s in range(lo, lo + RING):
                    self.rest_slot(pool, i * RING + s, s % RING, s % AHEAD, g.width)
        for s in range(lo + rounds * RING, min(hi + 1, self.n_slots)):
            self.rest_slot(pool, s, s % RING, s % AHEAD, self.width_of(s))

    def rest_input(self, dve, op):
        for k in range(op.n):
            dve.wait_ge(self.input_rounded, self.inputs + k + 1)
            self.nc.vector.tensor_tensor(op.lo(k), op.x(k), op.hi(k), ALU.subtract).then_inc(self.input_split, 1)

    def end_product(self, g, op, fresh=True):
        self.blocks_read += g.blocks
        self.inputs += op.n if fresh else 0

    def product(self, pe, g, op, fresh=True):
        mb, body, sets, by_token = g.mb, g.body, g.sets, g.by_token

        def parts(out, w, x, start, stop):
            for n, (wp, xp) in enumerate(((w[0], x[0]), (w[0], x[1]), (w[1], x[0]))):
                a, b = (xp, wp) if by_token else (wp, xp)
                mm = pe.matmul(out, a, b, start=start and n == 0, stop=stop and n == 2)
            return mm

        def round_of(i, at, n):
            for j in range(n):
                s, b, sub = at + j, (at + j) // g.q if i is None else None, j % g.q
                local = j // g.q
                r, ahead = (g.first + s) % RING, (g.first + s) % AHEAD
                ready = g.first + s + 1
                pe.wait_ge(self.weights_split, ready if i is None else ready + i * body)
                if sub == 0 and (i is not None or b >= sets):
                    freed = self.blocks_read + s // g.q - sets + 1
                    pe.wait_ge(self.acc_free, freed if i is None else freed + i * g.per)
                bank0 = (local % sets) * mb
                for m in range(mb):
                    for k in range(g.kc):
                        kx = sub * g.kc + k
                        if fresh and b == 0 and m == 0:
                            pe.wait_ge(self.input_split, self.inputs + kx + 1)
                        first, last = kx == 0, sub == g.q - 1 and k == g.kc - 1
                        if by_token:
                            w_at, x_at = slice(k * g.cols, (k + 1) * g.cols), slice(m * P, (m + 1) * P)
                        else:
                            w_at, x_at = slice(k * g.cols + m * P, k * g.cols + m * P + P), slice(0, T)
                        out = self.acc[:, bank0 + m, 0:g.cols if by_token else T]
                        mm = parts(out, (self.r.weight_hi[:, ahead, w_at], self.r.weight_ring[:, r, w_at]),
                                   (op.hi(kx)[:, x_at], op.lo(kx)[:, x_at]), first, last)
                mm.then_inc(self.products_done, 1)

        rounds = g.n // body
        round_of(None, 0, min(body, g.n))
        if rounds > 1:
            with pe.Fori(0, rounds - 1) as i:
                round_of(i, body, body)
        if g.n > body and g.n % body:
            round_of(None, rounds * body, g.n % body)

    def drain(self, eng, g, read):
        mb, per, sets = g.mb, g.per, g.sets

        def round_of(i, at, n):
            for l in range(n):
                b = at + l if i is None else at + l + i * per
                eng.wait_ge(self.products_done, g.first + (b + 1) * g.q)
                set_ = l % sets
                read(b, [self.acc[:, set_ * mb + m, :] for m in range(mb)], set_)

        rounds = g.blocks // per
        if rounds > 0:
            with eng.Fori(0, rounds) as i:
                round_of(i, 0, per)
        if g.blocks % per:
            round_of(None, rounds * per, g.blocks % per)


def start_stage(core, block0):
    nc = core.nc
    loaded, eye_zero = core.sem("inputs_loaded"), core.sem("eye_zeroed")
    with nc.Block(no_gpsimd_drain=True) as block:
        @block.sync
        def _(sp):
            sp.dma_start(core.x[:, :, :], core.dram["x"]).then_inc(loaded, 16)
            sp.dma_start(core.vec[:, :], core.dram["vectors"]).then_inc(loaded, 16)
            core.first_loads(sp)
            core.const_load(sp, block0, loaded)
            sp.wait_ge(loaded, 48)

        @block.gpsimd
        def _(pool):
            nc.gpsimd.memset(core.ones[:, :], 1.0)
            nc.gpsimd.memset(core.eye[:, :], 0.0).then_inc(eye_zero, 1)
            pool.wait_ge(eye_zero, 1)
            nc.gpsimd.affine_select(out=core.eye[:, :], in_=core.eye[:, :], compare_op=ALU.not_equal, fill=1.0,
                                    base=0, pattern=[[-1, P]], channel_multiplier=1).then_inc(eye_zero, 1)
            core.rest_slot(pool, 0, 0, 0, core.width_of(0))
            pool.wait_ge(eye_zero, 2)

        @block.scalar
        def _(act):
            core.round_slot(act, 0, 0, 0, core.width_of(0), 16)


def norm_stage(core, gain, eps, dst=None, load_consts=None):
    nc = core.nc
    squared, summed, var_ready, inv_ready, rstd_ready, consts_in = core.norm.values()
    nth = core.norms
    core.norms += 1
    dst = core.h if dst is None else dst
    with nc.Block(no_gpsimd_drain=True) as block:
        @block.sync
        def _(sp):
            if load_consts:
                core.const_load(sp, load_consts, consts_in)
                core.const_loads += 16
                sp.wait_ge(consts_in, core.const_loads)

        @block.scalar
        def _(act):
            for c in range(DC):
                nc.scalar.activation(core.p[:, c, :], core.x[:, c, :], ACT.Square).then_inc(squared, 1)
            act.wait_ge(inv_ready, nth + 1)
            nc.scalar.activation(core.rstd[:, :], core.rstd[:, :], ACT.Sqrt).then_inc(rstd_ready, 1)

        @block.tensor
        def _(pe):
            for c in range(DC):
                pe.wait_ge(squared, DC * nth + c + 1)
                mm = pe.matmul(core.acc[:, 0, :], core.ones[:, :], core.p[:, c, :], start=(c == 0), stop=(c == DC - 1))
            mm.then_inc(summed, 1)

        @block.vector
        def _(dve):
            dve.wait_ge(summed, nth + 1)
            nc.vector.tensor_scalar(core.rstd[:, :], core.acc[:, 0, :], 1.0 / D, eps, ALU.mult, ALU.add).then_inc(var_ready, 1)
            dve.wait_ge(var_ready, nth + 1)
            nc.vector.reciprocal(core.rstd[:, :], core.rstd[:, :]).then_inc(inv_ready, 1)
            dve.wait_ge(rstd_ready, nth + 1)
            for c in range(DC):
                nc.vector.scalar_tensor_tensor(out=dst[:, c, :], in0=core.x[:, c, :], scalar=core.vcol(gain[0], gain[1] + c),
                                               in1=core.rstd[:, :], op0=ALU.mult, op1=ALU.mult)


def swiglu_up_stage(core, name):
    nc, g = core.nc, core.gemms[name]
    op = Operand(core, DC, lambda m, k: m.h[:, k, :], lambda m, k: m.p[:, 44 + k, :])
    silu_ready = core.sem(f"{name}_silu")
    with nc.Block(no_gpsimd_drain=True) as block:
        @block.sync
        def _(sp):
            core.stream(sp, g)

        @block.gpsimd
        def _(pool):
            core.rest_weights(pool, g)

        @block.tensor
        def _(pe):
            core.product(pe, g, op)

        @block.scalar
        def _(act):
            def read(b, banks, s):
                nc.scalar.activation(core.scr[:, s, :], banks[0], ACT.Silu).then_inc(silu_ready, 1)
            core.round_parts(act, g, op, read)

        @block.vector
        def _(dve):
            core.rest_input(dve, op)

            def read(b, banks, s):
                dve.wait_ge(silu_ready, b + 1)
                nc.vector.tensor_tensor(core.p[:, b, :], core.scr[:, s, :], banks[1], ALU.mult).then_inc(core.acc_free, 1)
            core.drain(dve, g, read)
    core.end_product(g, op)


def residual_stage(core, name, scale, op):
    nc, g = core.nc, core.gemms[name]
    mb = g.cols // P
    with nc.Block(no_gpsimd_drain=True) as block:
        @block.sync
        def _(sp):
            core.stream(sp, g)

        @block.gpsimd
        def _(pool):
            core.rest_weights(pool, g)

        @block.tensor
        def _(pe):
            core.product(pe, g, op)

        @block.scalar
        def _(act):
            core.round_parts(act, g, op)

        @block.vector
        def _(dve):
            core.rest_input(dve, op)

            def read(b, banks, s):
                for m in range(mb):
                    xc = core.x[:, b * mb + m, :]
                    ins = nc.vector.scalar_tensor_tensor(out=xc, in0=banks[m], scalar=scale, in1=xc, op0=ALU.mult, op1=ALU.add)
                ins.then_inc(core.acc_free, 1)
            core.drain(dve, g, read)
    core.end_product(g, op)


def project_stage(core, name, at=0, func=ACT.Copy, fresh=True):
    nc, g = core.nc, core.gemms[name]
    op = Operand(core, DC, lambda m, k: m.h[:, k, :], lambda m, k: m.scr[:, k, :])
    mb = g.cols // P
    with nc.Block(no_gpsimd_drain=True) as block:
        @block.sync
        def _(sp):
            core.stream(sp, g)

        @block.gpsimd
        def _(pool):
            core.rest_weights(pool, g)

        @block.tensor
        def _(pe):
            core.product(pe, g, op, fresh)

        @block.vector
        def _(dve):
            if fresh:
                core.rest_input(dve, op)

        @block.scalar
        def _(act):
            def read(b, banks, s):
                if g.by_token:
                    to = core.p[:, bass.ds(at + b * mb, mb), :].rearrange("p a (n c) -> p (a n) c", c=g.cols)
                    nc.scalar.activation(to, core.acc[:, s * g.mb:(s + 1) * g.mb, 0:g.cols], func).then_inc(core.acc_free, 1)
                    return
                for m in range(mb):
                    ins = nc.scalar.activation(core.p[:, at + b * mb + m, :], banks[m], func)
                ins.then_inc(core.acc_free, 1)
            core.round_parts(act, g, op if fresh else None, read)
    core.end_product(g, op, fresh)


def rwkv_lora_stage(core):
    nc, p, scr, h, acc = core.nc, core.p, core.scr, core.h, core.acc
    step, act_in, done, read, lora_loaded, zeroed = (core.sem(f"rw_{s}") for s in (
        "shift_step", "lora_act", "lora_mm", "lora_read", "lora_loaded", "zeroed"))
    lora = p[:, 20:23, :]
    bd_zero = p[:, 23:33, :]
    diff = scr[:, 4, :]
    with nc.Block(no_gpsimd_drain=True) as block:
        @block.sync
        def _(sp):
            sp.dma_start(lora, core.dram["lora"]).then_inc(lora_loaded, 16)

        @block.gpsimd
        def _(pool):
            nc.gpsimd.memset(bd_zero, 0.0).then_inc(zeroed, 1)
            pool.wait_ge(zeroed, 1)

        @block.vector
        def _(dve):
            mine = Steps(dve, step)
            with dve.Fori(0, 14) as c:
                mine.loop(c, 2)
                nc.vector.tensor_scalar(diff[:, 0:1], p[:, c, 0:1], -1.0, None, ALU.mult)
                mine.then(nc.vector.tensor_tensor(diff[:, 1:T], p[:, c, 0:T - 1], p[:, c, 1:T], ALU.subtract))
                ins = nc.vector.scalar_tensor_tensor(out=p[:, c, :], in0=diff, scalar=core.vcol("shift_mix", c),
                                                     in1=p[:, c, :], op0=ALU.mult, op1=ALU.add)
                mine.then(ins)
            mine.end(14)

        @block.scalar
        def _(act):
            act.wait_ge(step, 2 * 14)
            nc.scalar.activation(scr[:, 6, :], p[:, LORA_W, :], ACT.Tanh)
            nc.scalar.activation(scr[:, 7, :], p[:, LORA_G, :], ACT.Sigmoid).then_inc(act_in, 1)
            act.wait_ge(done, 1)
            for c in range(PAIRS):
                nc.scalar.activation(scr[:, c, :], acc[:, c, :], ACT.Sigmoid, bias=core.vcol("w0", c)).then_inc(read, 1)
            for c in range(PAIRS):
                nc.scalar.activation(h[:, 4 + c, :], acc[:, 4 + c, :], ACT.Sigmoid, bias=core.vcol("a0", c))
            act.wait_ge(done, 2)
            for c in range(PAIRS):
                nc.scalar.activation(h[:, c, :], acc[:, c, :], ACT.Copy)

        @block.tensor
        def _(pe):
            pe.wait_ge(lora_loaded, 16)
            pe.wait_ge(act_in, 1)
            for c in range(PAIRS):
                pe.matmul(acc[:, c, :], lora[:, 0, c * P:(c + 1) * P], scr[:, 6, :], start=True, stop=True)
            for c in range(PAIRS):
                mm = pe.matmul(acc[:, 4 + c, :], lora[:, 1, c * P:(c + 1) * P], p[:, LORA_W, :], start=True, stop=True)
            mm.then_inc(done, 1)
            for c in range(PAIRS):
                pe.wait_ge(read, c + 1)
                mm = pe.matmul(acc[:, c, :], lora[:, 2, c * P:(c + 1) * P], scr[:, 7, :], start=True, stop=True)
            mm.then_inc(done, 1)


def rwkv_stage(core):
    nc, p, scr, h, acc = core.nc, core.p, core.scr, core.h, core.acc
    names = ("step", "cs", "exps", "sq", "sqsum", "inv", "root", "bd", "bonus_in", "bonus_sum", "unit1", "unit2",
             "a_read", "u1_read", "u2_read", "atn", "y", "y_read", "z", "z_read", "gt_read",
             "w", "w_neg", "sa", "sa_read", "s", "vst", "vst_read", "s_new", "o", "var", "std", "obd", "ot")
    q = {s: core.sem(f"rw_{s}") for s in names}
    C = lambda n: core.const(1, n)
    two = lambda a: p[:, a:a + 2, :].rearrange("p a (b c) -> p (a b) c", c=P)
    bdb, bdkk, bdk, bdr, bdv = (two(23 + 2 * n) for n in range(5))
    et, gt, ft, at = two(33), two(35), two(37), two(39)
    tm, tt, ym, atn = two(41), two(43), two(45), two(47)
    btok, ktok = two(49), two(20)
    vst = p[:, 51, :].rearrange("p (c v) -> p c v", v=HEAD)
    e1, e2, e3 = p[:, 45, :], p[:, 46, :], p[:, 47, :]
    t4, t5, t6, t7 = (scr[:, n, :] for n in range(4, 8))
    t8, t9 = p[:, 22, :], p[:, 48, :]
    chunks = lambda a: a.rearrange("p (c t) -> p c t", t=LC)
    small = core.small
    pend, wneg, sas = small[:, 0:8], small[:, 128:192], small[:, 192:256]
    state = small[:, 64:128], core.rstd[:, 0:HEAD]
    s1, s2 = small[:, 16:24], small[:, 24:32]
    bank2 = lambda b: acc[:, b:b + 2, :].rearrange("p a (b c) -> p (a b) c", c=P)
    half = lambda m, k: m[:, 4 * k:4 * k + 4, :]
    rep = lambda m: m.unsqueeze(1).to_broadcast([P, 4, P])
    LEVELS = (2, 4, 8, 16, 32)
    NL = len(LEVELS)
    eye = core.eye[:, :]

    with nc.Block(no_gpsimd_drain=True) as block:
        @block.vector
        def _(dve):
            v = nc.vector
            mine = Steps(dve, q["step"])
            with dve.Fori(0, PAIRS) as i:
                mine.loop(i, 18)
                r, k, val, a, sig = p[:, i, :], p[:, 4 + i, :], p[:, 8 + i, :], h[:, 4 + i, :], scr[:, i, :]
                mine.then(v.tensor_tensor_scan(t4, C("resets"), sig, 0.0, ALU.mult, ALU.add))
                v.tensor_tensor(t5, t4, sig, ALU.subtract).then_inc(q["cs"], 1)
                v.tensor_scalar(t6, k, core.vcol("k_k", i), None, ALU.mult).then_inc(q["sq"], 1)
                mine.then(v.tensor_scalar(t8, a, -1.0, core.vcol("k_a", i), ALU.add, ALU.mult))
                mine.then(v.scalar_tensor_tensor(out=t8, in0=t8, scalar=1.0, in1=k, op0=ALU.add, op1=ALU.mult))
                mine.then(v.tensor_scalar(t9, r, core.vcol("r_k", i), None, ALU.mult))
                v.tensor_tensor(t9, t9, t8, ALU.mult).then_inc(q["bonus_in"], 1)
                dve.wait_ge(q["sqsum"], i + 1)
                mine.then(v.tensor_scalar(t7, acc[:, 6, :], 1e-24, None, ALU.max))
                v.reciprocal(t7, t7).then_inc(q["inv"], 1)
                dve.wait_ge(q["root"], i + 1)
                dve.wait_ge(q["exps"], i + 1)
                mine.then(v.tensor_tensor(t6, t6, t7, ALU.mult))
                mine.then(v.tensor_tensor(t5, t6, a, ALU.mult))
                v.tensor_copy(pend, chunks(e1)[:, :, LC - 1:LC].rearrange("p c o -> p (c o)"))
                for j in range(2):
                    rows = slice(j * HEAD, (j + 1) * HEAD)
                    for m, a0, a1 in ((bdkk, t6, e3), (bdb, t5, e2), (bdk, t8, e2), (bdr, r, e1)):
                        v.tensor_tensor(m[rows, :, j * LC:(j + 1) * LC], chunks(a0)[rows], chunks(a1)[rows], ALU.mult)
                    ins = v.tensor_copy(bdv[rows, :, j * LC:(j + 1) * LC], chunks(val)[rows])
                ins.then_inc(q["bd"], 1)
                dve.wait_ge(q["bonus_sum"], i + 1)
                mine.then(v.tensor_tensor(t7, acc[:, 7, :], val, ALU.mult))
                dve.wait_ge(q["unit1"], i + 1)
                for k2 in range(2):
                    v.tensor_copy(half(at, k2), half(bank2(0), k2))
                    v.scalar_tensor_tensor(out=half(tm, k2), in0=half(bank2(2), k2), scalar=-1.0, in1=rep(C("level1_ts")), op0=ALU.mult, op1=ALU.mult)
                    ins = v.tensor_tensor(half(et, k2), half(bank2(4), k2), rep(C("upto")), ALU.mult)
                ins.then_inc(q["u1_read"], 1)
                dve.wait_ge(q["u1_read"], 2 * i + 1)
                for k2 in range(2):
                    v.scalar_tensor_tensor(out=half(tt, k2), in0=half(at, k2), scalar=-1.0, in1=rep(C("level1")), op0=ALU.mult, op1=ALU.mult)
                    ins = v.tensor_tensor(half(tm, k2), half(tm, k2), rep(eye), ALU.add)
                mine.then(ins)
                for k2 in range(2):
                    ins = v.tensor_tensor(half(tt, k2), half(tt, k2), rep(eye), ALU.add)
                ins.then_inc(q["u1_read"], 1)
                dve.wait_ge(q["unit2"], i + 1)
                for k2 in range(2):
                    v.tensor_tensor(half(gt, k2), half(bank2(6), k2), rep(C("strict")), ALU.mult)
                    ins = v.tensor_tensor(half(ft, k2), half(bank2(0), k2), rep(C("upto")), ALU.mult)
                ins.then_inc(q["gt_read"], 1)
                for n in range(NL):
                    for k2 in range(2):
                        dve.wait_ge(q["z"], i * (2 * NL) + 2 * n + k2 + 1)
                        v.tensor_tensor(half(tm, k2), half(tm, k2), half(bank2(2), k2), ALU.subtract)
                        ins = v.tensor_tensor(half(tt, k2), half(tt, k2), half(bank2(4), k2), ALU.subtract)
                        ins.then_inc(q["z_read"], 1)
                for c in range(NLC):
                    dve.wait_ge(q["w"], i * NLC + c + 1)
                    v.tensor_scalar(wneg, acc[:, 2, 0:HEAD], -1.0, None, ALU.mult).then_inc(q["w_neg"], 1)
                    dve.wait_ge(q["sa"], i * NLC + c + 1)
                    v.tensor_copy(sas, acc[:, 3, 0:HEAD]).then_inc(q["sa_read"], 1)
                    if c < NLC - 1:
                        dve.wait_ge(q["s"], i * (NLC - 1) + c + 1)
                        v.tensor_scalar(state[(c + 1) % 2], acc[:, 4, 0:HEAD], pend[:, c:c + 1], None, ALU.mult).then_inc(q["s_new"], 1)
                dve.wait_ge(q["o"], i + 1)
                ob = chunks(acc[:, 5, :])
                col = lambda x: x.unsqueeze(2).to_broadcast([P, NLC, HEAD])
                mine.then(v.tensor_reduce(s1, ob, AX.X, ALU.add))
                mine.then(v.tensor_scalar(s1, s1, 1.0 / HEAD, None, ALU.mult))
                mine.then(v.tensor_tensor(chunks(t5), ob, col(s1), ALU.subtract))
                mine.then(v.tensor_tensor(t6, t5, t5, ALU.mult))
                mine.then(v.tensor_reduce(s2, chunks(t6), AX.X, ALU.add))
                mine.then(v.tensor_scalar(s2, s2, 1.0 / HEAD, 64e-5, ALU.mult, ALU.add))
                v.reciprocal(s2, s2).then_inc(q["var"], 1)
                dve.wait_ge(q["std"], i + 1)
                for j in range(2):
                    rows = slice(j * HEAD, (j + 1) * HEAD)
                    ins = v.tensor_tensor(bdv[rows, :, j * LC:(j + 1) * LC], chunks(t5)[rows], col(s2)[rows], ALU.mult)
                ins.then_inc(q["obd"], 1)
                dve.wait_ge(q["ot"], i + 1)
                mine.then(v.tensor_scalar(t4, acc[:, 6, :], core.vcol("ln_w", i), core.vcol("ln_b", i), ALU.mult, ALU.add))
                mine.then(v.tensor_tensor(t4, t4, t7, ALU.add))
                mine.then(v.tensor_tensor(h[:, i, :], t4, h[:, i, :], ALU.mult))
            mine.end(PAIRS)

        @block.scalar
        def _(act):
            s = nc.scalar
            with act.Fori(0, PAIRS) as i:
                act.wait_ge(q["cs"], i + 1)
                s.activation(e1, t4, ACT.Exp, scale=-DECAY_RATE)
                s.activation(e2, t4, ACT.Exp, scale=DECAY_RATE)
                s.activation(e3, t5, ACT.Exp, scale=-DECAY_RATE).then_inc(q["exps"], 1)
                act.wait_ge(q["sq"], i + 1)
                s.activation(t7, t6, ACT.Square).then_inc(q["a_read"], 1)
                act.wait_ge(q["inv"], i + 1)
                s.activation(t7, t7, ACT.Sqrt).then_inc(q["root"], 1)
                act.wait_ge(q["unit2"], i + 1)
                for k2 in range(2):
                    s.activation(half(btok, k2), half(bank2(2), k2), ACT.Copy)
                    s.activation(half(ktok, k2), half(bank2(4), k2), ACT.Copy).then_inc(q["u2_read"], 1)
                act.wait_ge(q["vst"], i + 1)
                s.activation(vst, acc[:, 7, :].rearrange("p (c v) -> p c v", v=HEAD), ACT.Copy).then_inc(q["vst_read"], 1)
                for n in range(NL):
                    for k2 in range(2):
                        act.wait_ge(q["y"], i * (2 * NL) + 2 * n + k2 + 1)
                        s.activation(half(ym, k2), half(bank2(0), k2), ACT.Copy).then_inc(q["y_read"], 1)
                act.wait_ge(q["var"], i + 1)
                s.activation(s2, s2, ACT.Sqrt).then_inc(q["std"], 1)

        @block.gpsimd
        def _(pool):
            with pool.Fori(0, PAIRS) as i:
                pool.wait_ge(q["u1_read"], 2 * i + 1)
                for n, level in enumerate(LEVELS):
                    for k2 in range(2):
                        if n:
                            pool.wait_ge(q["y"], i * (2 * NL) + 2 * (n - 1) + k2 + 1)
                        nc.gpsimd.tensor_tensor(half(atn, k2), half(at, k2), rep(C(f"level{level}")), ALU.mult).then_inc(q["atn"], 1)

        @block.tensor
        def _(pe):
            mm = pe.matmul
            with pe.Fori(0, PAIRS) as i:
                pe.wait_ge(q["a_read"], i + 1)
                mm(acc[:, 6, :], C("head_ones"), t7, start=True, stop=True).then_inc(q["sqsum"], 1)
                pe.wait_ge(q["bonus_in"], i + 1)
                mm(acc[:, 7, :], C("head_ones"), t9, start=True, stop=True).then_inc(q["bonus_sum"], 1)
                pe.wait_ge(q["bd"], i + 1)
                for c in range(NLC):
                    mm(bank2(0)[:, c, :], bdb[:, c, :], bdkk[:, c, :], start=True, stop=True)
                    mm(bank2(2)[:, c, :], bdkk[:, c, :], bdb[:, c, :], start=True, stop=True)
                    ins = mm(bank2(4)[:, c, :], bdb[:, c, :], bdr[:, c, :], start=True, stop=True)
                ins.then_inc(q["unit1"], 1)
                pe.wait_ge(q["u1_read"], 2 * i + 2)
                for c in range(NLC):
                    mm(bank2(6)[:, c, :], bdk[:, c, :], bdkk[:, c, :], start=True, stop=True)
                    mm(bank2(0)[:, c, :], bdk[:, c, :], bdr[:, c, :], start=True, stop=True)
                    pe.transpose(bank2(2)[:, c, :], bdb[:, c, :], eye)
                    ins = pe.transpose(bank2(4)[:, c, :], bdk[:, c, :], eye)
                ins.then_inc(q["unit2"], 1)
                pe.wait_ge(q["gt_read"], i + 1)
                pe.wait_ge(q["u2_read"], 2 * i + 2)
                for c in range(NLC):
                    ins = mm(acc[:, 7, c * HEAD:(c + 1) * HEAD], bdv[:, c, :], C("stacked_eye"), start=True, stop=True)
                ins.then_inc(q["vst"], 1)
                for n in range(NL):
                    for k2 in range(2):
                        at_ = i * (2 * NL) + 2 * n + k2
                        pe.wait_ge(q["atn"], at_ + 1)
                        if n:
                            pe.wait_ge(q["z_read"], i * (2 * NL) + 2 * (n - 1) + k2 + 1)
                        for c in range(4 * k2, 4 * k2 + 4):
                            ins = mm(bank2(0)[:, c, :], atn[:, c, :], tm[:, c, :], start=True, stop=True)
                        ins.then_inc(q["y"], 1)
                    for k2 in range(2):
                        pe.wait_ge(q["y_read"], i * (2 * NL) + 2 * n + k2 + 1)
                        for c in range(4 * k2, 4 * k2 + 4):
                            mm(bank2(2)[:, c, :], tt[:, c, :], ym[:, c, :], start=True, stop=True)
                            ins = mm(bank2(4)[:, c, :], ym[:, c, :], tt[:, c, :], start=True, stop=True)
                        ins.then_inc(q["z"], 1)
                pe.wait_ge(q["z_read"], i * (2 * NL) + 2 * NL)
                pe.wait_ge(q["vst_read"], i + 1)
                mm(acc[:, 2, 0:HEAD], gt[:, 0, :], vst[:, 0, :], start=True, stop=True).then_inc(q["w"], 1)
                for c in range(NLC):
                    s_now, o = state[c % 2], acc[:, 5, c * HEAD:(c + 1) * HEAD]
                    if c:
                        pe.wait_ge(q["s_new"], i * (NLC - 1) + c)
                        mm(acc[:, 2, 0:HEAD], bdkk[:, c, :], s_now, start=False, stop=True).then_inc(q["w"], 1)
                        mm(o, bdr[:, c, :], s_now, start=True, stop=False)
                    mm(o, ft[:, c, :], vst[:, c, :], start=(c == 0), stop=False)
                    if c < NLC - 1:
                        if c:
                            mm(acc[:, 4, 0:HEAD], eye, s_now, start=True, stop=False)
                        mm(acc[:, 4, 0:HEAD], ktok[:, c, :], vst[:, c, :], start=(c == 0), stop=False)
                    pe.wait_ge(q["w_neg"], i * NLC + c + 1)
                    mm(acc[:, 3, 0:HEAD], tt[:, c, :], wneg, start=True, stop=True).then_inc(q["sa"], 1)
                    if c < NLC - 1:
                        mm(acc[:, 2, 0:HEAD], gt[:, c + 1, :], vst[:, c + 1, :], start=True, stop=False)
                    pe.wait_ge(q["sa_read"], i * NLC + c + 1)
                    if c < NLC - 1:
                        mm(acc[:, 4, 0:HEAD], btok[:, c, :], sas, start=False, stop=True).then_inc(q["s"], 1)
                    ins = mm(o, et[:, c, :], sas, start=False, stop=True)
                ins.then_inc(q["o"], 1)
                pe.wait_ge(q["obd"], i + 1)
                for c in range(NLC):
                    ins = mm(acc[:, 6, c * LC:(c + 1) * LC], bdv[:, c, :], C("stacked_eye"), start=True, stop=True)
                ins.then_inc(q["ot"], 1)


def attention_stage(core):
    nc, p, scr, h, acc, small = core.nc, core.p, core.scr, core.h, core.acc, core.small
    names = ("step", "biased", "mm0", "kd_read", "q_ready", "scores", "masked", "max", "exp", "sink", "pt", "pt_read", "o",
             "o_ready", "ot", "ot_read")
    q = {s: core.sem(f"at_{s}") for s in names}
    C = lambda n: core.const(1, n)
    kdup = p[:, 20:23, :].rearrange("p a t -> p (a t)")[:, 0:2 * (AB + T)].rearrange("p (g t) -> p g t", g=2)
    vtok = p[:, 23:25, :].rearrange("p a t -> p (a t)")[:, 0:5 * AB].rearrange("p (n d) -> p n d", d=AB)
    qz = p[:, 26:28, :].rearrange("p a (h t) -> p (a h) t", t=AB)
    sc = p[:, 28:32, :].rearrange("p a (h t) -> p (a h) t", t=2 * AB)
    pt = p[:, 32:36, :].rearrange("p a (h t) -> p (a h) t", t=AB)
    otok = p[:, 36, :]
    sinks, mx, nmx, rs, es = (small[:, 8 * n:8 * n + 8] for n in range(5))
    pairs2 = lambda b: acc[:, b, :].rearrange("p (h t) -> p h t", t=2 * AB)
    with nc.Block(no_gpsimd_drain=True) as block:
        sinks_in = core.sem("at_sinks")

        @block.sync
        def _(sp):
            sp.dma_start(sinks, core.dram["sinks"].partition_broadcast(P)).then_inc(sinks_in, 16)
            sp.wait_ge(sinks_in, 16)

        @block.gpsimd
        def _(pool):
            nc.gpsimd.memset(kdup[:, :, 0:AB], 0.0)
            nc.gpsimd.memset(vtok[:, 0, :], 0.0)
            nc.gpsimd.memset(qz, 0.0).then_inc(q["biased"], 1)

        @block.vector
        def _(dve):
            v = nc.vector
            mine = Steps(dve, q["step"])
            for c in range(4):
                v.tensor_scalar(p[:, ATT_Q + c, :], p[:, ATT_Q + c, :], core.vcol("b_in_attn", c), HEAD ** -0.5, ALU.add, ALU.mult)
            for c in (4, 5):
                ins = v.tensor_scalar(p[:, ATT_Q + c, :], p[:, ATT_Q + c, :], core.vcol("b_in_attn", c), None, ALU.add)
            mine.then(ins)
            dve.wait_ge(q["mm0"], 1)
            for g in range(2):
                v.tensor_copy(kdup[:, g, AB:AB + T], acc[:, g, :])
            v.tensor_copy(vtok[:, 1:5, :], acc[:, 2, :].rearrange("p (n d) -> p n d", d=AB)).then_inc(q["kd_read"], 1)
            dve.wait_ge(q["biased"], 1)
            dve.wait_ge(sinks_in, 16)
            with dve.Fori(0, NAB) as n:
                mine.loop(n, 7)
                for hd in range(Q_HEADS):
                    rows = slice(hd % 2 * HEAD, hd % 2 * HEAD + HEAD)
                    ins = v.tensor_copy(qz[rows, hd, :], p[rows, ATT_Q + hd // 2, bass.ds(n * AB, AB)])
                ins.then_inc(q["q_ready"], 1)
                dve.wait_ge(q["scores"], n + 1)
                band = core.cst[:, bass.ds(BAND0 + n * (2 * AB), 2 * AB)].unsqueeze(1).to_broadcast([P, 2, 2 * AB])
                for b in range(4):
                    ins = v.tensor_tensor(sc[:, 2 * b:2 * b + 2, :], pairs2(b), band, ALU.add)
                mine.then(ins)
                mine.then(v.tensor_reduce(mx, sc, AX.X, ALU.max))
                mine.then(v.tensor_tensor(mx, mx, sinks, ALU.max))
                mine.then(v.tensor_tensor(es, sinks, mx, ALU.subtract))
                v.tensor_scalar(nmx, mx, -1.0, None, ALU.mult).then_inc(q["max"], 1)
                dve.wait_ge(q["exp"], n + 1)
                mine.then(v.tensor_tensor(rs, rs, es, ALU.add))
                mine.then(v.reciprocal(rs, rs))
                dve.wait_ge(q["pt"], n + 1)
                for b in range(4):
                    ins = v.tensor_copy(pt[:, 4 * b:4 * b + 4, :], acc[:, 4 + b, :].rearrange("p (a t) -> p a t", t=AB))
                ins.then_inc(q["pt_read"], 1)
                dve.wait_ge(q["o"], n + 1)
                v.tensor_tensor(otok.rearrange("p (a d) -> p a d", d=HEAD), acc[:, 0, :].rearrange("p (a d) -> p a d", d=HEAD),
                                rs.unsqueeze(2).to_broadcast([P, Q_HEADS, HEAD]), ALU.mult).then_inc(q["o_ready"], 1)
                dve.wait_ge(q["ot"], n + 1)
                mine.then(v.tensor_copy(h[:, 4:8, bass.ds(n * AB, AB)], acc[:, 1, :].rearrange("p (c t) -> p c t", t=AB)))
            mine.end(NAB)

        @block.scalar
        def _(act):
            with act.Fori(0, NAB) as n:
                act.wait_ge(q["max"], n + 1)
                for hd in range(Q_HEADS):
                    nc.scalar.activation(sc[:, hd, :], sc[:, hd, :], ACT.Exp, bias=nmx[:, hd:hd + 1], accum_out=rs[:, hd:hd + 1])
                nc.scalar.activation(es, es, ACT.Exp).then_inc(q["exp"], 1)

        @block.tensor
        def _(pe):
            pe.wait_ge(q["step"], 1)
            for g in range(2):
                pe.matmul(acc[:, g, :], C(f"dup{g}"), p[:, ATT_K, :], start=True, stop=True)
            for n in range(NAB):
                ins = pe.transpose(acc[:, 2, n * AB:(n + 1) * AB], p[:, ATT_V, n * AB:(n + 1) * AB], core.eye[:, :])
            ins.then_inc(q["mm0"], 1)
            pe.wait_ge(q["kd_read"], 1)
            with pe.Fori(0, NAB) as n:
                pe.wait_ge(q["q_ready"], n + 1)
                for hd in range(Q_HEADS):
                    keys = kdup[:, hd // 4, bass.ds(n * AB, 2 * AB)]
                    ins = pe.matmul(pairs2(hd // 2)[:, hd % 2, :], qz[:, hd, :], keys, start=True, stop=True)
                ins.then_inc(q["scores"], 1)
                pe.wait_ge(q["exp"], n + 1)
                for hd in range(Q_HEADS):
                    for k in range(2):
                        m = 2 * hd + k
                        ins = pe.transpose(acc[:, 4 + m // 4, m % 4 * AB:(m % 4 + 1) * AB], sc[:, hd, k * AB:(k + 1) * AB], core.eye[:, :])
                ins.then_inc(q["pt"], 1)
                pe.wait_ge(q["pt_read"], n + 1)
                for hd in range(Q_HEADS):
                    g = hd // 4
                    for k in range(2):
                        ins = pe.matmul(acc[:, 0, hd * HEAD:(hd + 1) * HEAD], pt[:, 2 * hd + k, :],
                                        vtok[:, n + k, g * HEAD:(g + 1) * HEAD], start=(k == 0), stop=(k == 1))
                ins.then_inc(q["o"], 1)
                pe.wait_ge(q["o_ready"], n + 1)
                for c in range(4):
                    ins = pe.transpose(acc[:, 1, c * AB:(c + 1) * AB], otok[:, c * AB:(c + 1) * AB], core.eye[:, :])
                ins.then_inc(q["ot"], 1)


BAND0 = const_columns(1)[0]["band0"][0]


def block1(core):
    norm_stage(core, ("norm_ffn1", 0), 1e-5)
    swiglu_up_stage(core, "ffn1_up")
    residual_stage(core, "ffn1_down", 0.5, Operand(core, FFC, lambda m, k: m.p[:, k, :], lambda m, k: m.p[:, FFC + k, :]))
    norm_stage(core, ("norm_mix", 0), 1e-5)
    project_stage(core, "mix_in")
    rwkv_lora_stage(core)
    rwkv_stage(core)
    attention_stage(core)
    residual_stage(core, "mix_out", 1.0, Operand(core, DC, lambda m, k: m.h[:, k, :], lambda m, k: m.scr[:, k, :]))
    norm_stage(core, ("norm_ffn2", 0), 1e-5)
    swiglu_up_stage(core, "ffn2_up")
    residual_stage(core, "ffn2_down", 0.5, Operand(core, FFC, lambda m, k: m.p[:, k, :], lambda m, k: m.p[:, FFC + k, :]))


def softplus_steps(nc, mine, x, m, e, t, d, act_wait, act_signal, n):
    v = nc.vector
    mine.then(v.tensor_scalar(m, x, 0.0, None, ALU.max))
    mine.then(v.tensor_scalar(e, x, 0.0, None, ALU.min))
    ins = v.tensor_tensor(e, e, m, ALU.subtract)
    ins.then_inc(act_signal, 1)
    mine.eng.wait_ge(act_wait, 2 * n + 1)
    mine.then(v.tensor_scalar(t, e, 1.0, None, ALU.add))
    v.tensor_scalar(d, t, -1.0, None, ALU.add).then_inc(act_signal, 1)
    mine.eng.wait_ge(act_wait, 2 * n + 2)
    mine.then(v.scalar_tensor_tensor(out=t, in0=d, scalar=0.0, in1=t, op0=ALU.is_equal, op1=ALU.add))
    mine.then(v.scalar_tensor_tensor(out=d, in0=d, scalar=0.0, in1=d, op0=ALU.is_equal, op1=ALU.add))
    mine.then(v.reciprocal(d, d))
    mine.then(v.tensor_tensor(t, t, d, ALU.mult))
    mine.then(v.tensor_tensor(t, t, e, ALU.mult))
    mine.then(v.tensor_tensor(m, m, t, ALU.add))


SOFTPLUS_STEPS = 9


def softplus_act(nc, act, e, t, from_dve, to_dve, n):
    act.wait_ge(from_dve, 2 * n + 1)
    nc.scalar.activation(e, e, ACT.Exp).then_inc(to_dve, 1)
    act.wait_ge(from_dve, 2 * n + 2)
    nc.scalar.activation(t, t, ACT.Ln).then_inc(to_dve, 1)


HC = RNNC // 2


def rnn_stage(core):
    nc, p, scr, h, acc, small = core.nc, core.p, core.scr, core.h, core.acc, core.small
    names = ("step", "sp_dve", "sp_act", "weights", "conv", "gates", "r", "i", "exped", "decay", "half", "root", "gelu")
    q = {s: core.sem(f"rnn_{s}") for s in names}
    lruw = core.cst[:, 128:128 + 2 * RNNC * P].rearrange("p (c g j) -> p c g j", g=2, j=P)
    x0 = small[:, 0:10]
    m, e, t, d = (small[:, 16 * n:16 * n + RNNC] for n in range(1, 5))
    coef = m
    ncoef = small[:, 80:90]
    xr = lambda c: h[:, c, :]
    ix = lambda c: scr[:, c, :]
    decays = [h[:, 5, :], h[:, 6, :], h[:, 7, :], scr[:, 5, :], scr[:, 6, :]]
    with nc.Block(no_gpsimd_drain=True) as block:
        @block.sync
        def _(sp):
            sp.dma_start(core.cst[:, 128:128 + 2 * RNNC * P], core.dram["lru_w"]).then_inc(q["weights"], 16)
            sp.wait_ge(q["weights"], 16)

        @block.vector
        def _(dve):
            v = nc.vector
            mine = Steps(dve, q["step"])
            mine.then(v.tensor_scalar(x0, core.vec[:, VEC_AT["lru_lambda"]:VEC_AT["lru_lambda"] + RNNC], -1.0, None, ALU.mult))
            softplus_steps(nc, mine, x0, m, e, t, d, q["sp_act"], q["sp_dve"], 0)
            v.tensor_scalar(ncoef, m, 8.0, None, ALU.mult)
            mine.then(v.tensor_scalar(coef, m, -8.0, None, ALU.mult))
            with dve.Fori(0, 2) as i:
                mine.loop(i, 3 * HC + 7)
                wcol = lambda k, c: core.vcol("conv_w", k * RNNC + i * HC + c)
                for c in range(HC):
                    ins = v.tensor_scalar(xr(c), p[:, i * HC + c, :], wcol(CONV - 1, c), core.vcol("conv_b", i * HC + c), ALU.mult, ALU.add)
                mine.then(ins)
                for k in range(CONV - 2, -1, -1):
                    back = CONV - 1 - k
                    for c in range(HC):
                        ins = v.scalar_tensor_tensor(out=xr(c)[:, back:T], in0=p[:, i * HC + c, 0:T - back], scalar=wcol(k, c),
                                                     in1=xr(c)[:, back:T], op0=ALU.mult, op1=ALU.add)
                    if k:
                        mine.then(ins)
                ins.then_inc(q["conv"], 1)
                dve.wait_ge(q["conv"], i + 1)
                for c in range(HC):
                    dve.wait_ge(q["i"], i * HC + c + 1)
                    mine.then(v.tensor_tensor(ix(c), ix(c), xr(c), ALU.mult))
                dve.wait_ge(q["decay"], i + 1)
                tanh5 = p[:, bass.ds(i * HC, HC), :]
                den5 = h[:, 0:HC, :]
                mine.then(v.tensor_scalar(den5, tanh5, 1.0, None, ALU.add))
                for c in range(HC):
                    ins = v.reciprocal(den5[:, c, :], den5[:, c, :])
                mine.then(ins)
                mine.then(v.tensor_tensor(den5, den5, tanh5, ALU.mult))
                v.tensor_scalar(den5, den5, 1e-34, None, ALU.max).then_inc(q["half"], 1)
                dve.wait_ge(q["root"], i + 1)
                for c in range(HC):
                    ins = v.tensor_tensor(ix(c), ix(c), den5[:, c, :], ALU.mult)
                mine.then(ins)
                for c in range(HC):
                    mine.then(v.tensor_tensor_scan(ix(c), decays[c], ix(c), 0.0, ALU.mult, ALU.add))
                dve.wait_ge(q["gelu"], 1)
                for c in range(HC):
                    mine.then(v.tensor_tensor(p[:, i * HC + c, :], ix(c), p[:, i * HC + (RNNC + c), :], ALU.mult))
            mine.end(2)

        @block.scalar
        def _(act):
            s = nc.scalar
            softplus_act(nc, act, e, t, q["sp_dve"], q["sp_act"], 0)
            s.activation(p[:, 10:36, :], p[:, 10:36, :], ACT.Gelu_apprx_tanh).then_inc(q["gelu"], 1)
            s.activation(p[:, 36:52, :], p[:, 36:52, :], ACT.Sigmoid)
            act.wait_ge(q["step"], SOFTPLUS_STEPS + 2)
            with act.Fori(0, 2) as i:
                for c in range(HC):
                    act.wait_ge(q["gates"], i * HC + c + 1)
                    s.activation(p[:, i * HC + c, :], acc[:, 2 * c % 8, :], ACT.Sigmoid, bias=core.vcol("lru_b_a", i * HC + c)).then_inc(q["r"], 1)
                    s.activation(ix(c), acc[:, (2 * c + 1) % 8, :], ACT.Sigmoid, bias=core.vcol("lru_b_x", i * HC + c)).then_inc(q["i"], 1)
                act.wait_ge(q["r"], i * HC + HC)
                for c in range(HC):
                    ins = s.activation(decays[c], p[:, i * HC + c, :], ACT.Exp, scale=coef_at(core, 16, i * HC + c))
                ins.then_inc(q["exped"], 1)
                act.wait_ge(q["exped"], i + 1)
                for c in range(HC):
                    ins = s.activation(p[:, i * HC + c, :], p[:, i * HC + c, :], ACT.Tanh, scale=coef_at(core, 80, i * HC + c))
                ins.then_inc(q["decay"], 1)
                act.wait_ge(q["half"], i + 1)
                s.activation(h[:, 0:HC, :], h[:, 0:HC, :], ACT.Sqrt, scale=2.0).then_inc(q["root"], 1)

        @block.tensor
        def _(pe):
            pe.wait_ge(q["weights"], 16)
            for i in range(2):
                pe.wait_ge(q["conv"], i + 1)
                for c in range(HC):
                    w = lruw[:, i * HC + c]
                    if c == HC - 1:
                        pe.wait_ge(q["i"], i * HC + 1)
                    pe.matmul(acc[:, 2 * c % 8, :], w[:, 0, :], xr(c), start=True, stop=True)
                    pe.matmul(acc[:, (2 * c + 1) % 8, :], w[:, 1, :], xr(c), start=True, stop=True).then_inc(q["gates"], 1)


def coef_at(core, at, c):
    return core.small[:, bass.ds(at + c, 1)]


def sgu_stage(core):
    nc, p, scr, h, acc = core.nc, core.p, core.scr, core.h, core.acc
    names = ("step", "loaded", "sum", "sq", "sum2", "inv", "rstd", "gained", "normed", "turned", "turned_read", "mixed", "mixed_read", "masked")
    q = {s: core.sem(f"sgu_{s}") for s in names}
    V, U = 28, 20
    wt = core.cst[:, 2688:2688 + SGU_G * P].rearrange("p (g t) -> p g t", t=P)
    bias = scr[:, 0:2, :].rearrange("p a (g t) -> p (a g) t", t=P)
    mean = scr[:, 2, :]
    vt = h[:, :, :].rearrange("p (n a) t -> p n (a t)", n=4)
    blocks = lambda a: a.rearrange("p (n t) -> p n t", t=P)
    with nc.Block(no_gpsimd_drain=True) as block:
        @block.sync
        def _(sp):
            sp.dma_start(wt, core.dram["sgu_w"]).then_inc(q["loaded"], 16)
            sp.dma_start(scr[:, 0:2, :].rearrange("p a t -> p (a t)"), core.dram["sgu_b"].partition_broadcast(P)).then_inc(q["loaded"], 16)

        @block.gpsimd
        def _(pool):
            pool.wait_ge(q["loaded"], 32)
            nc.gpsimd.tensor_tensor(wt, wt, core.const(2, "sgu_mask").unsqueeze(1).to_broadcast([P, SGU_G, P]), ALU.mult).then_inc(q["masked"], 1)

        @block.vector
        def _(dve):
            v = nc.vector
            mine = Steps(dve, q["step"])
            dve.wait_ge(q["sum"], 1)
            mine.then(v.tensor_scalar(mean, acc[:, 0, :], 1.0 / D, None, ALU.mult))
            for c in range(DC):
                v.tensor_tensor(p[:, V + c, :], p[:, V + c, :], mean, ALU.subtract).then_inc(q["gained"], 1)
            dve.wait_ge(q["sum2"], 1)
            mine.then(v.tensor_scalar(core.rstd[:, :], acc[:, 1, :], 1.0 / D, 1e-6, ALU.mult, ALU.add))
            v.reciprocal(core.rstd[:, :], core.rstd[:, :]).then_inc(q["inv"], 1)
            dve.wait_ge(q["rstd"], 1)
            for c in range(DC):
                v.scalar_tensor_tensor(out=p[:, V + c, :], in0=p[:, V + c, :], scalar=core.vcol("sgu_ln_g", c),
                                       in1=core.rstd[:, :], op0=ALU.mult, op1=ALU.mult).then_inc(q["gained"], 1)
            for g in range(SGU_G):
                dve.wait_ge(q["mixed"], g + 1)
                if g >= 2:
                    dve.wait_ge(q["step"], mine.base + mine.n)
                t = scr[:, 3 + g % 2, :]
                mine.then(v.tensor_tensor(blocks(t), blocks(acc[:, 4 + g % 4, :]), bias[:, g, :].unsqueeze(1).to_broadcast([P, 4, P]), ALU.add))
                v.tensor_tensor(p[:, U + g, :], p[:, U + g, :], t, ALU.mult).then_inc(q["mixed_read"], 1)

        @block.scalar
        def _(act):
            s = nc.scalar
            for c in range(DC):
                act.wait_ge(q["gained"], c + 1)
                s.activation(h[:, c, :], p[:, V + c, :], ACT.Square).then_inc(q["sq"], 1)
            act.wait_ge(q["inv"], 1)
            s.activation(core.rstd[:, :], core.rstd[:, :], ACT.Sqrt).then_inc(q["rstd"], 1)
            for c in range(DC):
                act.wait_ge(q["gained"], DC + c + 1)
                s.activation(p[:, V + c, :], p[:, V + c, :], ACT.Identity, bias=core.vcol("sgu_ln_b", c)).then_inc(q["normed"], 1)
            for g in range(SGU_G):
                act.wait_ge(q["turned"], g + 1)
                s.activation(vt[:, :, g * P:(g + 1) * P], blocks(acc[:, g % 4, :]), ACT.Copy).then_inc(q["turned_read"], 1)

        @block.tensor
        def _(pe):
            for c in range(DC):
                ins = pe.matmul(acc[:, 0, :], core.ones[:, :], p[:, V + c, :], start=(c == 0), stop=(c == DC - 1))
            ins.then_inc(q["sum"], 1)
            for c in range(DC):
                pe.wait_ge(q["sq"], c + 1)
                ins = pe.matmul(acc[:, 1, :], core.ones[:, :], h[:, c, :], start=(c == 0), stop=(c == DC - 1))
            ins.then_inc(q["sum2"], 1)
            for g in range(SGU_G):
                pe.wait_ge(q["normed"], g + 1)
                if g >= 4:
                    pe.wait_ge(q["turned_read"], g - 3)
                for n in range(4):
                    ins = pe.transpose(acc[:, g % 4, n * P:(n + 1) * P], p[:, V + g, n * P:(n + 1) * P], core.eye[:, :])
                ins.then_inc(q["turned"], 1)
            pe.wait_ge(q["masked"], 1)
            for g in range(SGU_G):
                pe.wait_ge(q["turned_read"], g + 1)
                if g >= 4:
                    pe.wait_ge(q["mixed_read"], g - 3)
                for n in range(4):
                    ins = pe.matmul(acc[:, 4 + g % 4, n * P:(n + 1) * P], vt[:, n, g * P:(g + 1) * P], wt[:, g, :], start=True, stop=True)
                ins.then_inc(q["mixed"], 1)


def gated_stage(core, name, first, gate, op):
    nc, g, p, scr = core.nc, core.gemms[name], core.p, core.scr
    mb = g.cols // P
    step = None if first else core.sem(f"{name}_step")
    with nc.Block(no_gpsimd_drain=True) as block:
        @block.sync
        def _(sp):
            core.stream(sp, g)

        @block.gpsimd
        def _(pool):
            core.rest_weights(pool, g)

        @block.tensor
        def _(pe):
            core.product(pe, g, op)

        @block.scalar
        def _(act):
            core.round_parts(act, g, op)

        @block.vector
        def _(dve):
            core.rest_input(dve, op)
            mine = None if first else Steps(dve, step)

            def read(b, banks, s):
                for m in range(mb):
                    c = b * mb + m
                    if first:
                        ins = nc.vector.tensor_tensor(p[:, 36 + c, :], banks[m], p[:, gate + c, :], ALU.mult)
                    else:
                        t = scr[:, s * mb + m, :]
                        ins = nc.vector.tensor_tensor(t, banks[m], p[:, gate + c, :], ALU.mult)
                ins.then_inc(core.acc_free, 1)
                if not first:
                    dve.wait_ge(core.acc_free, core.blocks_read + b + 1)
                    for m in range(mb):
                        c = b * mb + m
                        nc.vector.tensor_tensor(p[:, 36 + c, :], p[:, 36 + c, :], scr[:, s * mb + m, :], ALU.add)
            core.drain(dve, g, read)
    core.end_product(g, op)


def relu2_stage(core, name):
    nc, g, p, scr = core.nc, core.gemms[name], core.p, core.scr
    mb = g.cols // P
    op = Operand(core, DC, lambda m, k: m.h[:, k, :], lambda m, k: m.p[:, 44 + k, :])
    relu = core.sem(f"{name}_relu")
    with nc.Block(no_gpsimd_drain=True) as block:
        @block.sync
        def _(sp):
            core.stream(sp, g)

        @block.gpsimd
        def _(pool):
            core.rest_weights(pool, g)

        @block.tensor
        def _(pe):
            core.product(pe, g, op)

        @block.scalar
        def _(act):
            def read(b, banks, s):
                for m in range(mb):
                    ins = nc.scalar.activation(scr[:, s * mb + m, :], banks[m], ACT.Relu)
                ins.then_inc(relu, 1)
            core.round_parts(act, g, op, read)

        @block.vector
        def _(dve):
            core.rest_input(dve, op)

            def read(b, banks, s):
                dve.wait_ge(relu, b + 1)
                t = scr[:, s * mb:s * mb + mb, :]
                nc.vector.tensor_tensor(p[:, bass.ds(b * mb, mb), :], t, t, ALU.mult).then_inc(core.acc_free, 1)
            core.drain(dve, g, read)
    core.end_product(g, op)


def block2(core):
    norm_stage(core, ("norm_mix_g", 0), 1e-6, load_consts=2)
    project_stage(core, "b2_in")
    rnn_stage(core)
    sgu_stage(core)
    gated_stage(core, "branch_a", True, 36, Operand(core, RNNC, lambda m, k: m.p[:, k, :], lambda m, k: m.h[:, k, :] if k < DC else m.scr[:, k - DC, :]))
    gated_stage(core, "branch_b", False, 44, Operand(core, DC, lambda m, k: m.p[:, 20 + k, :], lambda m, k: m.h[:, k, :]))
    residual_stage(core, "b2_out", 1.0, Operand(core, DC, lambda m, k: m.p[:, 36 + k, :], lambda m, k: m.h[:, k, :]))
    norm_stage(core, ("norm_ffn_g", 0), 1e-6)
    relu2_stage(core, "mlp_up")
    part = lambda m, k: m.p[:, 32 + k, :] if k < 20 else m.h[:, k - 20, :] if k < 28 else m.scr[:, k - 28, :]
    residual_stage(core, "mlp_down", 1.0, Operand(core, 32, lambda m, k: m.p[:, k, :], part))


C3_DT = const_columns(3)[1]
C3_HEADS = C3_DT + DC * P
C3_SKIP = C3_HEADS + 2
C3_END = C3_SKIP + DC
Z, S5U, XS, SB, SC = 0, 16, 24, 32, 34


def ab_in_stage(core):
    nc, g, p, scr, acc = core.nc, core.gemms["ab_in"], core.p, core.scr, core.acc
    op = Operand(core, DC, lambda m, k: m.h[:, k, :], lambda m, k: m.scr[:, k, :])
    loaded, dt_done, dt_split = core.sem("dt_loaded"), core.sem("dt_done"), core.sem("dt_split")
    wdt, wdt_lo = (m.cst[:, C3_DT:C3_DT + DC * P].rearrange("p (k m) -> p k m", m=P) for m in (core, core.r))
    wdt_hi = lambda k: core.r.p[:, 36 + k // 4, (k % 4) * P:(k % 4 + 1) * P]
    mb = g.cols // P
    with nc.Block(no_gpsimd_drain=True) as block:
        @block.sync
        def _(sp):
            sp.dma_start(core.cst[:, C3_DT:C3_DT + DC * P], core.dram["w_dt"]).then_inc(loaded, 16)
            sp.dma_start(core.cst[:, C3_HEADS:C3_END], core.dram["ssd_small"]).then_inc(loaded, 16)
            core.stream(sp, g)

        @block.gpsimd
        def _(pool):
            core.rest_weights(pool, g)
            pool.wait_ge(loaded, 32)
            for k in range(DC):
                nc.gpsimd.tensor_copy(wdt_hi(k), wdt[:, k, :]).then_inc(dt_split, 1)
            for k in range(DC):
                pool.wait_ge(dt_split, k + 1)
                nc.gpsimd.tensor_tensor(wdt_lo[:, k, :], wdt[:, k, :], wdt_hi(k), ALU.subtract).then_inc(dt_split, 1)

        @block.vector
        def _(dve):
            core.rest_input(dve, op)

        @block.tensor
        def _(pe):
            core.product(pe, g, op)
            pe.wait_ge(dt_split, 2 * DC)
            pe.wait_ge(core.acc_free, core.blocks_read + g.blocks)
            for k in range(DC):
                for n, (w, x) in enumerate(((wdt_hi(k), op.hi), (wdt_hi(k), op.lo), (wdt_lo[:, k, :], op.hi))):
                    ins = pe.matmul(acc[:, 0, :], w, x(k), start=(k == 0 and n == 0), stop=(k == DC - 1 and n == 2))
            ins.then_inc(dt_done, 1)

        @block.scalar
        def _(act):
            def read(b, banks, s):
                for m in range(mb):
                    ins = nc.scalar.activation(p[:, b * mb + m, :], banks[m], ACT.Copy)
                ins.then_inc(core.acc_free, 1)
            core.round_parts(act, g, op, read)
            act.wait_ge(dt_done, 1)
            nc.scalar.activation(core.scr[:, 0, :], acc[:, 0, :], ACT.Copy)
    core.end_product(g, op)


def ssd_prepare_stage(core):
    nc, p, scr, h, acc, small = core.nc, core.p, core.scr, core.h, core.acc, core.small
    names = ("step", "conv", "silu", "sp_dve", "sp_act", "a", "turned", "sums", "last", "exps", "zeroed")
    q = {s: core.sem(f"sd_{s}") for s in names}
    R = slice(0, SSD_H)
    dt_raw, acs, tok = scr[:, 0, :], scr[:, 1, :], scr[:, 2, :]
    m, e, t, d = (scr[R, 3 + n, :] for n in range(4))
    dtf = scr[:, 3, :]
    heads = lambda n: core.cst[R, C3_HEADS + n:C3_HEADS + n + 1]
    a_col = small[R, 0:1]
    conv = lambda c: h[:, c % 4, :]
    NX = 12
    col = lambda n: tok[:, 64 * n:64 * n + 64]
    with nc.Block(no_gpsimd_drain=True) as block:
        @block.gpsimd
        def _(pool):
            nc.gpsimd.memset(scr[:, 1, :], 0.0)
            nc.gpsimd.memset(scr[:, 3, :], 0.0).then_inc(q["zeroed"], 1)

        @block.vector
        def _(dve):
            v = nc.vector
            mine = Steps(dve, q["step"])
            dve.wait_ge(q["zeroed"], 1)
            mine.then(v.tensor_scalar(dt_raw[R], dt_raw[R], heads(0), None, ALU.add))
            softplus_steps(nc, mine, dt_raw[R], m, e, t, d, q["sp_act"], q["sp_dve"], 0)
            dve.wait_ge(q["a"], 1)
            mine.then(v.tensor_scalar(t, m, a_col, -1.0, ALU.mult, ALU.mult))
            v.tensor_tensor_scan(acs[R], core.const(3, "dt_resets", R), t, 0.0, ALU.mult, ALU.add).then_inc(q["sums"], 1)
            wcol = lambda k, c: core.vcol("ssd_conv_w", k * NX + c)
            for c0 in range(0, NX, 4):
                group = range(c0, c0 + 4)
                if c0:
                    dve.wait_ge(q["silu"], c0)
                for c in group:
                    ins = v.tensor_scalar(conv(c), p[:, XS + c, :], wcol(SSD_K - 1, c), None, ALU.mult)
                mine.then(ins)
                for k in range(SSD_K - 2, -1, -1):
                    back = SSD_K - 1 - k
                    for c in group:
                        ins = v.scalar_tensor_tensor(out=conv(c)[:, back:T], in0=p[:, XS + c, 0:T - back], scalar=wcol(k, c),
                                                     in1=conv(c)[:, back:T], op0=ALU.mult, op1=ALU.add)
                    if k:
                        mine.then(ins)
                ins.then_inc(q["conv"], 1)
            dve.wait_ge(q["turned"], 1)
            for n in range(NCH):
                v.tensor_copy(col(0)[:, n * SSD_H:(n + 1) * SSD_H], acc[:, 0, n * P:n * P + SSD_H])
                ins = v.tensor_copy(col(1)[:, n * SSD_H:(n + 1) * SSD_H], acc[:, 1, n * P:n * P + SSD_H])
            mine.then(ins)
            dve.wait_ge(q["last"], 1)
            mine.then(v.tensor_tensor(col(2), acc[:, 2, 0:64], col(1), ALU.subtract))

        @block.scalar
        def _(act):
            s = nc.scalar
            s.activation(a_col, heads(1), ACT.Exp).then_inc(q["a"], 1)
            softplus_act(nc, act, e, t, q["sp_dve"], q["sp_act"], 0)
            for c in range(NX):
                act.wait_ge(q["conv"], c // 4 + 1)
                s.activation(p[:, XS + c, :], conv(c), ACT.Silu, bias=core.vcol("ssd_conv_b", c)).then_inc(q["silu"], 1)
            act.wait_ge(q["step"], SSD_PREP_STEPS)
            s.activation(col(2), col(2), ACT.Exp)
            s.activation(col(3), col(1), ACT.Exp)
            s.activation(col(4), acc[:, 2, 0:64], ACT.Exp)

        @block.tensor
        def _(pe):
            pe.wait_ge(q["sums"], 1)
            for n in range(NCH):
                pe.transpose(acc[:, 0, n * P:(n + 1) * P], dtf[:, n * P:(n + 1) * P], core.eye[:, :])
                ins = pe.transpose(acc[:, 1, n * P:(n + 1) * P], acs[:, n * P:(n + 1) * P], core.eye[:, :])
            ins.then_inc(q["turned"], 1)
            pe.wait_ge(q["step"], SSD_PREP_STEPS - 1)
            pe.matmul(acc[:, 2, 0:64], core.const(3, "last_row"), col(1), start=True, stop=True).then_inc(q["last"], 1)


SSD_K = 4
SSD_PREP_STEPS = 1 + SOFTPLUS_STEPS + 1 + 3 * 3 + 2


def ssd_stage(core):
    nc, p, scr, h, acc, small = core.nc, core.p, core.scr, core.h, core.acc, core.small
    names = ("step", "staged", "xs_t", "xdt", "b_read", "cb", "cb_read", "bc", "seg", "exp", "m", "yd", "off", "y", "state", "yt", "st", "xds", "zero")
    q = {s: core.sem(f"ssd_{s}") for s in names}
    tok, acs = scr[:, 2, :], scr[:, 1, :]
    col = lambda k, n: tok[:, bass.ds(64 * k + n * SSD_H, SSD_H)]
    free = p[:, 36:52, :]
    stg = p[:, 36:39, :].rearrange("p a t -> p (a t)").rearrange("p (c t) -> p c t", t=P)
    xdt = p[:, 39:41, :].rearrange("p a (h d) -> p (a h) d", d=64)
    xds = p[:, 41:43, :].rearrange("p a (h d) -> p (a h) d", d=64)
    mt = p[:, 43:47, :].rearrange("p a (h l) -> p (a h) l", l=P)
    prev = p[:, 47:49, :]
    y = p[:, 49:51, :]
    btok = p[:, 51, 0:2 * P].rearrange("p (g n) -> p g n", n=P)
    cbs = p[:, 51, 2 * P:4 * P].rearrange("p (g n) -> p g n", n=P)
    h4 = lambda a: a.rearrange("p (h l) -> p h l", l=P)
    h8 = lambda a: a.rearrange("p (h d) -> p h d", d=64)
    b8 = lambda c, g: c[:, 8 * g:8 * g + 8].unsqueeze(2).to_broadcast([P, 8, 64])
    causal = core.const(3, "causal").unsqueeze(1).to_broadcast([P, 4, P])
    rows = core.const(3, "head_rows").rearrange("p (h l) -> p h l", l=P)
    with nc.Block(no_gpsimd_drain=True) as block:
        @block.gpsimd
        def _(pool):
            nc.gpsimd.memset(prev, 0.0).then_inc(q["zero"], 1)
            with pool.Fori(0, NCH) as n:
                pool.wait_ge(q["zero"], 1)
                with_n = bass.ds(n * CH, CH)
                pool.wait_ge(q["step"], n * SSD_STEPS + 1)
                nc.gpsimd.tensor_copy(stg[:, 0:12, :], p[:, XS:XS + 12, with_n]).then_inc(q["staged"], 1)

        @block.vector
        def _(dve):
            v = nc.vector
            mine = Steps(dve, q["step"])
            dve.wait_ge(q["zero"], 1)
            with dve.Fori(0, NCH) as n:
                mine.loop(n, SSD_STEPS)
                ce = small[:, 32:48]
                mine.then(v.tensor_copy(ce, col(3, n)))
                cs, cdt, cds, cdec = col(1, n), col(0, n), col(2, n), col(4, n)
                v.tensor_copy(small[:, 48:64], cdec)
                v.tensor_copy(small[:, 64:80], cdt)
                v.tensor_copy(small[:, 80:96], cds)
                mine.then(v.tensor_copy(small[:, 96:112], cs))
                ldec, ldt, lds, lcs = (small[:, 48 + 16 * k:64 + 16 * k] for k in range(4))
                dve.wait_ge(q["xs_t"], n + 1)
                for g in range(2):
                    v.tensor_tensor(xdt[:, 8 * g:8 * g + 8, :], h8(acc[:, g, :]), b8(ldt, g), ALU.mult)
                v.tensor_copy(btok, acc[:, 2, 0:2 * P].rearrange("p (g n) -> p g n", n=P))
                v.tensor_copy(cbs, acc[:, 2, 2 * P:4 * P].rearrange("p (g n) -> p g n", n=P)).then_inc(q["xdt"], 1)
                dve.wait_ge(q["xdt"], 2 * n + 1)
                for g in range(2):
                    ins = v.tensor_tensor(xds[:, 8 * g:8 * g + 8, :], xdt[:, 8 * g:8 * g + 8, :], b8(lds, g), ALU.mult)
                ins.then_inc(q["xdt"], 1)
                dve.wait_ge(q["bc"], n + 1)
                for b in range(4):
                    ins = v.tensor_tensor(mt[:, 4 * b:4 * b + 4, :], h4(acc[:, 4 + b, :]),
                                          lcs[:, 4 * b:4 * b + 4].unsqueeze(2).to_broadcast([P, 4, P]), ALU.subtract)
                mine.then(ins)
                for b in range(4):
                    v.tensor_tensor(mt[:, 4 * b:4 * b + 4, :], mt[:, 4 * b:4 * b + 4, :], causal, ALU.add).then_inc(q["seg"], 1)
                for b in range(4):
                    dve.wait_ge(q["exp"], 4 * n + b + 1)
                    v.tensor_tensor(mt[:, 4 * b:4 * b + 4, :], mt[:, 4 * b:4 * b + 4, :],
                                    cbs[:, b // 2, :].unsqueeze(1).to_broadcast([P, 4, P]), ALU.mult).then_inc(q["m"], 1)
                dve.wait_ge(q["off"], n + 1)
                for g in range(2):
                    ins = v.tensor_tensor(h8(y[:, g, :]), h8(acc[:, 4 + g, :]), b8(ce, g), ALU.mult)
                mine.then(ins)
                dve.wait_ge(q["yd"], n + 1)
                for g in range(2):
                    ins = v.tensor_tensor(y[:, g, :], y[:, g, :], acc[:, g, :], ALU.add)
                ins.then_inc(q["y"], 1)
                for g in range(2):
                    ins = v.tensor_tensor(h8(prev[:, g, :]), h8(prev[:, g, :]), b8(ldec, g), ALU.mult)
                mine.then(ins)
                for g in range(2):
                    ins = v.tensor_tensor(prev[:, g, :], prev[:, g, :], acc[:, 6 + g, :], ALU.add)
                mine.then(ins)
                dve.wait_ge(q["yt"], n + 1)
                for c in range(8):
                    xs = p[:, XS + c, bass.ds(n * CH, CH)]
                    ins = v.scalar_tensor_tensor(out=xs, in0=xs, scalar=core.cst[:, C3_SKIP + c:C3_SKIP + c + 1],
                                                 in1=h4(acc[:, 2 + c // 4, :])[:, c % 4, :], op0=ALU.mult, op1=ALU.add)
                mine.then(ins)
            mine.end(NCH)

        @block.scalar
        def _(act):
            with act.Fori(0, NCH) as n:
                for b in range(4):
                    act.wait_ge(q["seg"], 4 * n + b + 1)
                    nc.scalar.activation(mt[:, 4 * b:4 * b + 4, :], mt[:, 4 * b:4 * b + 4, :], ACT.Exp).then_inc(q["exp"], 1)

        @block.tensor
        def _(pe):
            mm = pe.matmul
            pe.wait_ge(q["zero"], 1)
            with pe.Fori(0, NCH) as n:
                pe.wait_ge(q["staged"], n + 1)
                for c in range(8):
                    pe.transpose(acc[:, c // 4, (c % 4) * P:(c % 4 + 1) * P], stg[:, c, :], core.eye[:, :])
                for g in range(2):
                    pe.transpose(acc[:, 2, g * P:(g + 1) * P], stg[:, 8 + g, :], core.eye[:, :])
                for g in range(2):
                    ins = mm(acc[:, 2, (2 + g) * P:(3 + g) * P], stg[:, 8 + g, :], stg[:, 10 + g, :], start=True, stop=True)
                ins.then_inc(q["xs_t"], 1)
                for hd in range(SSD_H):
                    ins = mm(acc[:, 4 + hd // 4, (hd % 4) * P:(hd % 4 + 1) * P], rows[:, hd, :], acs[:, bass.ds(n * CH, CH)], start=True, stop=True)
                ins.then_inc(q["bc"], 1)
                pe.wait_ge(q["seg"], 4 * n + 4)
                for g in range(2):
                    ins = mm(acc[:, 4 + g, :], stg[:, 10 + g, :], prev[:, g, :], start=True, stop=True)
                ins.then_inc(q["off"], 1)
                pe.wait_ge(q["xdt"], 2 * n + 2)
                for g in range(2):
                    mm(acc[:, 6 + g, :], btok[:, g, :], xds[:, 8 * g:8 * g + 8, :], start=True, stop=True)
                for hd in range(SSD_H):
                    if hd % 4 == 0:
                        pe.wait_ge(q["m"], 4 * n + hd // 4 + 1)
                    ins = mm(acc[:, hd // 8, (hd % 8) * 64:(hd % 8 + 1) * 64], mt[:, hd, :], xdt[:, hd, :], start=True, stop=True)
                ins.then_inc(q["yd"], 1)
                pe.wait_ge(q["y"], n + 1)
                for c in range(8):
                    ins = pe.transpose(acc[:, 2 + c // 4, (c % 4) * P:(c % 4 + 1) * P], y[:, c // 4, (c % 4) * P:(c % 4 + 1) * P], core.eye[:, :])
                ins.then_inc(q["yt"], 1)


SSD_STEPS = 7


def ssd_gate_stage(core):
    nc, p, scr, h, acc = core.nc, core.p, core.scr, core.h, core.acc
    names = ("step", "gate", "sq", "sum", "inv", "rstd")
    q = {s: core.sem(f"sg_{s}") for s in names}
    rs = scr[:, 0:2, :]
    with nc.Block(no_gpsimd_drain=True) as block:
        @block.scalar
        def _(act):
            s = nc.scalar
            for c in range(8):
                s.activation(h[:, c, :], p[:, Z + 8 + c, :], ACT.Silu).then_inc(q["gate"], 1)
            for c in range(8):
                act.wait_ge(q["step"], c + 1)
                s.activation(h[:, c, :], p[:, XS + c, :], ACT.Square).then_inc(q["sq"], 1)
            act.wait_ge(q["inv"], 1)
            s.activation(rs, rs, ACT.Sqrt).then_inc(q["rstd"], 1)

        @block.tensor
        def _(pe):
            for c in range(8):
                pe.wait_ge(q["sq"], c + 1)
                ins = pe.matmul(acc[:, c // 4, :], core.ones[:, :], h[:, c, :], start=(c % 4 == 0), stop=(c % 4 == 3))
            ins.then_inc(q["sum"], 1)

        @block.vector
        def _(dve):
            v = nc.vector
            mine = Steps(dve, q["step"])
            for c in range(8):
                dve.wait_ge(q["gate"], c + 1)
                mine.then(v.tensor_tensor(p[:, XS + c, :], p[:, XS + c, :], h[:, c, :], ALU.mult))
            dve.wait_ge(q["sum"], 1)
            mine.then(v.tensor_scalar(rs, acc[:, 0:2, :], 2.0 / D, 1e-6, ALU.mult, ALU.add))
            v.reciprocal(rs, rs).then_inc(q["inv"], 1)
            dve.wait_ge(q["rstd"], 1)
            for c in range(8):
                v.scalar_tensor_tensor(out=p[:, XS + c, :], in0=p[:, XS + c, :], scalar=core.vcol("ssd_norm_w", c), in1=rs[:, c // 4, :],
                                       op0=ALU.mult, op1=ALU.mult)


S5_TAB = const_columns(3)[0]["head_rows"][0]
S5_REV = S5_TAB + 2 * 9 * S5_G
S5_COEF = S5_REV + 2 * 8 * S5_G
TWO_PI_1 = 6.28125
TWO_PI_2 = float(np.float32(np.round((2 * np.pi - TWO_PI_1) * 2 ** 22) / 2 ** 22))
TWO_PI_3 = float(np.float32(2 * np.pi - TWO_PI_1 - TWO_PI_2))
TO_INT = 1.5 * 2.0 ** 23
PI_BELOW = 3.1415925


def s5_discretize_stage(core):
    nc, p, scr, cst = core.nc, core.p, core.scr, core.cst
    names = ("loaded", "step", "exp", "half", "tanh", "angle", "sin", "lifted", "stored", "back")
    q = {s: core.sem(f"s5_{s}") for s in names}
    tile = lambda n: scr[:, 6 + n // 8, (n % 8) * 64:(n % 8 + 1) * 64]
    lre, li, dt, th, em, ang, kf, r, sn, hs, cm, cos, rec, t0 = (tile(n) for n in range(14))
    tab = cst[:, S5_TAB:S5_REV].rearrange("p (r m g) -> p r m g", r=2, g=S5_G)
    rev = cst[:, S5_REV:S5_COEF].rearrange("p (r m g) -> p r m g", r=2, g=S5_G)
    y1, y2 = p[:, 32:34, :], p[:, 34:36, :]
    b_, b2 = scr[:, 0:2, :], scr[:, 2:4, :]
    g3 = lambda a: a.rearrange("p a (g i) -> p (a g) i", i=S5_IN)
    bc = lambda c: c.unsqueeze(2).to_broadcast([P, S5_G, S5_IN])
    spread = p[:, 44:52, :]
    big = g3(scr[:, 4:6, :])
    with nc.Block(no_gpsimd_drain=True) as block:
        @block.sync
        def _(sp):
            sp.dma_start(lre, core.dram["lam_re"]).then_inc(q["loaded"], 16)
            sp.dma_start(li, core.dram["lam_im"]).then_inc(q["loaded"], 16)
            sp.dma_start(dt, core.dram["log_dt"].partition_broadcast(P)).then_inc(q["loaded"], 16)
            sp.dma_start(p[:, 32:36, :], core.dram["s5_b"]).then_inc(q["loaded"], 16)
            sp.wait_ge(q["lifted"], DC)
            sp.dma_start(core.dram["lift"].rearrange("(c p) t -> p c t", p=P), spread).then_inc(q["stored"], 16)
            sp.wait_ge(q["stored"], 16)
            by_place = core.dram["lift"].rearrange("(g i) (l n) -> l i g n", i=S5_IN, l=S5_L)
            for l in range(S5_L):
                sp.dma_start(p[l * S5_IN:(l + 1) * S5_IN, 36:44, :].rearrange("p a (g n) -> p (a g) n", n=S5_N), by_place[l]).then_inc(q["back"], 16)
            sp.wait_ge(q["back"], 16 * S5_L)

        @block.gpsimd
        def _(pool):
            for c in range(DC):
                nc.gpsimd.tensor_copy(spread[:, c, :].rearrange("p (l n) -> p l n", l=S5_L),
                                      p[:, S5U + c, :].rearrange("p (n l) -> p l n", l=S5_L)).then_inc(q["lifted"], 1)

        @block.scalar
        def _(act):
            s = nc.scalar
            act.wait_ge(q["loaded"], 64)
            s.activation(dt, dt, ACT.Exp).then_inc(q["exp"], 1)
            act.wait_ge(q["half"], 1)
            s.activation(th, th, ACT.Tanh).then_inc(q["tanh"], 1)
            act.wait_ge(q["angle"], 1)
            s.activation(sn, r, ACT.Sin)
            s.activation(hs, r, ACT.Sin, scale=0.5).then_inc(q["sin"], 1)

        @block.vector
        def _(dve):
            v = nc.vector
            mine = Steps(dve, q["step"])
            then = mine.then
            mul = lambda o, a, b: v.tensor_tensor(o, a, b, ALU.mult)
            dve.wait_ge(q["exp"], 1)
            then(v.tensor_scalar(lre, lre, -1e-4, None, ALU.min))
            v.scalar_tensor_tensor(out=th, in0=lre, scalar=0.5, in1=dt, op0=ALU.mult, op1=ALU.mult).then_inc(q["half"], 1)
            then(mul(ang, li, dt))
            then(v.tensor_scalar(kf, ang, 1 / (2 * np.pi), TO_INT, ALU.mult, ALU.add))
            then(v.tensor_scalar(kf, kf, -TO_INT, None, ALU.add))
            for src, part in ((ang, TWO_PI_1), (r, TWO_PI_2), (r, TWO_PI_3)):
                then(v.scalar_tensor_tensor(out=r, in0=kf, scalar=-part, in1=src, op0=ALU.mult, op1=ALU.add))
            v.tensor_scalar(r, r, PI_BELOW, -PI_BELOW, ALU.min, ALU.max).then_inc(q["angle"], 1)
            dve.wait_ge(q["tanh"], 1)
            then(v.tensor_scalar(em, th, -1.0, 1.0, ALU.mult, ALU.add))
            then(v.reciprocal(em, em))
            then(v.scalar_tensor_tensor(out=em, in0=th, scalar=2.0, in1=em, op0=ALU.mult, op1=ALU.mult))
            then(v.tensor_scalar(t0, em, 1.0, None, ALU.add))
            dve.wait_ge(q["sin"], 1)
            then(v.scalar_tensor_tensor(out=cm, in0=hs, scalar=-2.0, in1=hs, op0=ALU.mult, op1=ALU.mult))
            then(v.tensor_scalar(cos, cm, 1.0, None, ALU.add))
            are, aim = tab[:, 0, 1, :], tab[:, 1, 1, :]
            mul(are, t0, cos)
            then(mul(aim, t0, sn))
            nr = em
            then(mul(nr, em, cos))
            then(v.tensor_tensor(nr, nr, cm, ALU.add))
            mul(rec, lre, lre)
            then(mul(t0, li, li))
            then(v.tensor_tensor(rec, rec, t0, ALU.add))
            then(v.reciprocal(rec, rec))
            mul(ang, nr, lre)
            mul(kf, aim, li)
            mul(r, aim, lre)
            then(mul(t0, nr, li))
            cre, cim = ang, r
            v.tensor_tensor(cre, ang, kf, ALU.add)
            then(v.tensor_tensor(cim, r, t0, ALU.subtract))
            mul(cre, cre, rec)
            then(mul(cim, cim, rec))
            then(v.tensor_scalar(y2, y2, core.const(3, "sign"), -1.0, ALU.mult, ALU.mult))
            mul(g3(b_), g3(y1), bc(cre))
            mul(g3(b2), g3(y2), bc(cre))
            then(mul(big, g3(y2), bc(cim)))
            then(v.tensor_tensor(g3(b_), g3(b_), big, ALU.add))
            then(mul(big, g3(y1), bc(cim)))
            then(v.tensor_tensor(g3(b2), g3(b2), big, ALU.subtract))
            v.memset(tab[:, 0, 0, :], 1.0)
            then(v.memset(tab[:, 1, 0, :], 0.0))
            for m in range(2, S5_L + 1):
                xr, xi = tab[:, 0, m - 1, :], tab[:, 1, m - 1, :]
                mul(th, xr, are)
                mul(em, xi, aim)
                mul(kf, xr, aim)
                then(mul(t0, xi, are))
                v.tensor_tensor(tab[:, 0, m, :], th, em, ALU.subtract)
                then(v.tensor_tensor(tab[:, 1, m, :], kf, t0, ALU.add))
            for s_ in range(S5_L):
                v.tensor_copy(rev[:, :, s_, :], tab[:, :, S5_L - 1 - s_, :])


S5_NB = 8
S5_ROUNDS = S5_G // S5_NB


def past(c, n):
    return not isinstance(c, int) or c >= n


def before(b, i):
    return (2 * i, 0, i) if b else (2 * i - 1, 1, i - 1)


def s5_rounds(eng, step, mine=None, per=0):
    for c in range(4):
        step(c, c % 2, c // 2)
    with eng.Fori(2, S5_ROUNDS // 2) as i:
        if mine is not None:
            mine.loop(i - 2, per)
        step(2 * i, 0, i)
        step(2 * i + 1, 1, i)
    if mine is not None:
        mine.end(S5_ROUNDS // 2 - 2)


S5_LAST = (S5_ROUNDS - 1, 1, S5_ROUNDS // 2 - 1)


def s5_state_stage(core):
    nc, p, scr, h, acc, cst = core.nc, core.p, core.scr, core.h, core.acc, core.cst
    names = ("step", "r", "rt", "rt_read", "v", "v_read", "swap", "ready")
    q = {s: core.sem(f"sh_{s}") for s in names}
    rev = cst[:, S5_REV:S5_COEF].rearrange("p (r m g) -> p r g m", r=2, g=S5_G)
    tab = cst[:, S5_TAB:S5_REV].rearrange("p (r m g) -> p r m g", r=2, g=S5_G)
    g3 = lambda a: a.rearrange("p a (g i) -> p (a g) i", i=S5_IN)
    b_, b2 = g3(scr[:, 0:2, :]), g3(scr[:, 2:4, :])
    NB = S5_NB
    rows = lambda a: a.rearrange("p a (g s i) -> p (a g) s i", g=4, i=S5_IN)
    cols = lambda a: a.rearrange("p a (g c) -> p (a g) c", g=4)
    r, rt, tmp = (p[:, 44:46, :], p[:, 50:52, :]), (p[:, 46:48, :], p[:, 32:34, :]), p[:, 48:50, :]
    ul = p[:, 36:44, :].rearrange("p a (g n) -> p (a g) n", n=S5_N)
    hp = h[:, :, :].rearrange("p a (n g) -> p (a n) g", g=S5_G)
    RUNS = 8
    col = lambda k: h[:, :, k * S5_G:(k + 1) * S5_G]
    by_run = lambda a: a.rearrange("p (a g) -> p a g", g=S5_G)
    carry, d = by_run(p[:, 32, :]), [by_run(p[:, 33 + n, :]) for n in range(2)]
    m1, m2 = by_run(p[:, 35, :]), by_run(core.rstd[:, :])
    sq = [core.small[:, n * 64:(n + 1) * 64] for n in range(4)]
    a8 = [tab[:, n, S5_L, :] for n in range(2)]
    N_PRODUCTS = 3 * (RUNS - 1)
    with nc.Block(no_gpsimd_drain=True) as block:
        @block.vector
        def _(dve):
            v = nc.vector
            mine = Steps(dve, q["step"])
            v.memset(hp[:, 0, :], 0.0)

            def read_v(c, b, i):
                dve.wait_ge(q["v"], c + 1)
                v.tensor_copy(hp[:, 1:S5_N, bass.ds(c * NB, NB)].rearrange("p n g -> p g n"),
                              acc[:, 4 * b + 2, :].rearrange("p (g n) -> p g n", n=S5_N)[:, :, 0:S5_N - 1]).then_inc(q["v_read"], 1)

            def step(c, b, i):
                gs = bass.ds(c * NB, NB)
                wide = lambda a: a[:, gs, :].unsqueeze(2).to_broadcast([P, NB, S5_L, S5_IN])
                power = lambda k: rev[:, k, gs, :].unsqueeze(3).to_broadcast([P, NB, S5_L, S5_IN])
                if past(c, 2):
                    dve.wait_ge(q["rt"], c - 1)
                v.tensor_tensor(rows(r[b]), wide(b_), power(0), ALU.mult)
                mine.then(v.tensor_tensor(rows(tmp), wide(b2), power(1), ALU.mult))
                v.tensor_tensor(r[b], r[b], tmp, ALU.add).then_inc(q["r"], 1)
                if past(c, 1):
                    read_v(*before(b, i))
                dve.wait_ge(q["r"], c + 1)

            s5_rounds(dve, step, mine, 2)
            read_v(*S5_LAST)
            re, im = a8
            for n in range(3):
                mine.then(v.tensor_tensor(sq[2], re, im, ALU.mult))
                v.tensor_tensor(sq[3], im, im, ALU.mult)
                mine.then(v.tensor_tensor(sq[0], re, re, ALU.mult))
                v.tensor_scalar(sq[1], sq[2], 2.0, None, ALU.mult)
                mine.then(v.tensor_tensor(sq[0], sq[0], sq[3], ALU.subtract))
                re, im = sq[0], sq[1]
            dve.wait_ge(q["v_read"], S5_ROUNDS)
            done = 0

            def product(a, x, target, add, runs):
                nonlocal done
                of = lambda t: t[:, 0:runs, :]
                wide = lambda t: t.unsqueeze(1).to_broadcast([P, runs, S5_G])
                if add:
                    mine.then(v.tensor_tensor(of(m1), wide(a[0]), x, ALU.mult))
                    mine.then(v.tensor_tensor(target, target, of(m1), ALU.add))
                else:
                    mine.then(v.tensor_tensor(target, wide(a[0]), x, ALU.mult))
                dve.wait_ge(q["swap"], done + 1)
                swapped = by_run(acc[:, done % 2, :])[:, 0:runs, :]
                mine.then(v.tensor_tensor(of(m2), wide(a[1]), swapped, ALU.mult))
                v.tensor_tensor(target, target, of(m2), ALU.add).then_inc(q["ready"], 1)
                done += 1
                dve.wait_ge(q["ready"], done)

            for k in range(1, RUNS):
                product(a8, col(k - 1), col(k), True, RUNS)
            product(a8, col(RUNS - 1), carry, False, RUNS)
            for a in range(1, RUNS - 1):
                product(sq, carry[:, a - 1:a, :], carry[:, a:a + 1, :], True, 1)
            later = lambda k: col(k)[:, 1:RUNS, :]
            x = carry[:, 0:RUNS - 1, :]
            v.tensor_tensor(later(0), later(0), x, ALU.add)
            for k in range(1, RUNS):
                y = d[k % 2][:, 0:RUNS - 1, :]
                product(a8, x, y, False, RUNS - 1)
                ins = v.tensor_tensor(later(k), later(k), y, ALU.add)
                x = y
            mine.then(ins)

        @block.scalar
        def _(act):
            def step(c, b, i):
                act.wait_ge(q["rt"], c + 1)
                if past(c, 2):
                    act.wait_ge(q["v"], c - 1)
                nc.scalar.activation(cols(rt[b]), acc[:, 4 * b:4 * b + 2, :].rearrange("p a (g c) -> p (a g) c", g=4), ACT.Copy).then_inc(q["rt_read"], 1)

            s5_rounds(act, step)

        @block.tensor
        def _(pe):
            def multiply(c, b, i):
                pe.wait_ge(q["rt_read"], c + 1)
                if past(c, 2):
                    pe.wait_ge(q["v_read"], c - 1)
                for g in range(NB):
                    ins = pe.matmul(acc[:, 4 * b + 2, g * S5_N:(g + 1) * S5_N], cols(rt[b])[:, g, :], ul[:, c * NB + g, :], start=True, stop=True)
                ins.then_inc(q["v"], 1)

            def step(c, b, i):
                pe.wait_ge(q["r"], c + 1)
                if past(c, 2):
                    pe.wait_ge(q["rt_read"], c - 1)
                for g in range(NB):
                    ins = pe.transpose(acc[:, 4 * b + g // 4, (g % 4) * P:(g % 4 + 1) * P], cols(r[b])[:, g, :], core.eye[:, :])
                ins.then_inc(q["rt"], 1)
                if past(c, 1):
                    multiply(*before(b, i))

            s5_rounds(pe, step)
            multiply(*S5_LAST)
            operands = [col(k) for k in range(RUNS)] + [carry[:, a:a + 1, :] for a in range(RUNS - 2)]
            operands += [carry[:, 0:RUNS - 1, :]] + [d[k % 2][:, 0:RUNS - 1, :] for k in range(1, RUNS - 1)]
            assert len(operands) == N_PRODUCTS
            for n, x in enumerate(operands):
                if n == 0:
                    pe.wait_ge(q["v_read"], S5_ROUNDS)
                else:
                    pe.wait_ge(q["ready"], n)
                out = by_run(acc[:, n % 2, :])[:, 0:x.shape[1], :]
                pe.matmul(out, core.const(3, "swap"), x, start=True, stop=True).then_inc(q["swap"], 1)


def s5_output_stage(core):
    nc, p, scr, h, acc, cst, small = core.nc, core.p, core.scr, core.h, core.acc, core.cst, core.small
    names = ("step", "loaded", "zeroed", "powers", "row", "row_read", "y", "y_read", "back")
    q = {s: core.sem(f"so_{s}") for s in names}
    stored, laid = ([core.sem(f"so_{s}{b}") for b in range(2)] for s in ("stored", "laid"))
    tab = cst[:, S5_TAB:S5_REV].rearrange("p (r m g) -> p r g m", r=2, g=S5_G)
    NB = S5_NB
    g3 = lambda a: a.rearrange("p a (g i) -> p (a g) i", i=S5_IN)
    x1, x2, b_ = g3(p[:, 32:34, :]), g3(p[:, 34:36, :]), g3(scr[:, 0:2, :])
    NP = S5_L + 1
    flat = p[:, 44:49, :].rearrange("p a t -> p (a t)")
    powers = [flat[:, b * 1280:b * 1280 + NB * NP * S5_IN].rearrange("p (g m o) -> p g m o", g=NB, o=S5_IN) for b in range(2)]
    rows_of = lambda b, g, m: flat[:, b * 1280 + g * NP * S5_IN + m * S5_IN:][:, 0:P]
    tmp = scr[:, 2:4, :].rearrange("p a (g m o) -> p (a g) m o", g=4, o=S5_IN)
    last = small[:, 0:NB * S5_IN].rearrange("p (g o) -> p g o", o=S5_IN)
    b_now = small[:, P:2 * P].rearrange("p (g i) -> p g i", i=S5_IN)
    row = p[0:S5_IN, 49:51, :].rearrange("p a (g c) -> p (a g) c", c=P)
    kt = [scr[:, 4 + 2 * b:6 + 2 * b, :].rearrange("p a (g c) -> p (a g) c", c=P) for b in range(2)]
    yl = [a.rearrange("p (g n) -> p g n", n=S5_N) for a in (p[:, 51, :], core.rstd[:, :])]
    ul = p[:, 36:44, :].rearrange("p a (g n) -> p (a g) n", n=S5_N)
    hp = h[:, :, :].rearrange("p a (n g) -> p (a n) g", g=S5_G)
    lift = core.dram["lift"].rearrange("(g o) (l n) -> l o g n", o=S5_IN, l=S5_L)
    ALL = 16 * S5_L

    with nc.Block(no_gpsimd_drain=True) as block:
        @block.sync
        def _(sp):
            sp.dma_start(p[:, 32:36, :], core.dram["s5_c"]).then_inc(q["loaded"], 16)

            def step(c, b, i):
                sp.wait_ge(q["row_read"], c + 1)
                for s_ in range(S5_L):
                    sp.dma_start(kt[b][s_ * S5_IN:(s_ + 1) * S5_IN, :, s_ * S5_IN:P], row[:, :, 0:P - s_ * S5_IN]).then_inc(laid[b], 16)

            sp.wait_ge(q["zeroed"], 1)
            s5_rounds(sp, step)
            for b in range(2):
                sp.wait_ge(stored[b], ALL * (S5_ROUNDS // 2))
            sp.dma_start(p[:, 36:44, :], core.dram["lift"].rearrange("(c p) t -> p c t", p=P)).then_inc(q["back"], 16)
            sp.wait_ge(q["back"], 16)

        @block.gpsimd
        def _(pool):
            nc.gpsimd.memset(scr[:, 4:8, :], 0.0).then_inc(q["zeroed"], 1)

        @block.vector
        def _(dve):
            v = nc.vector
            mine = Steps(dve, q["step"])
            dve.wait_ge(q["loaded"], 16)
            v.tensor_scalar(p[:, 32:34, :], p[:, 32:34, :], core.const(3, "sign"), None, ALU.mult)
            mine.then(v.tensor_scalar(p[:, 34:36, :], p[:, 34:36, :], -1.0, None, ALU.mult))

            def step(c, b, i):
                gs = bass.ds(c * NB, NB)
                wide = lambda a, m: a[:, gs, :].unsqueeze(2).to_broadcast([P, NB, m, S5_IN])
                power = lambda k, m0, m1: tab[:, k, gs, m0:m1].unsqueeze(3).to_broadcast([P, NB, m1 - m0, S5_IN])
                if past(c, 2):
                    dve.wait_ge(q["y"], c - 1)
                v.tensor_tensor(tmp, wide(x2, 8), power(1, 0, 8), ALU.mult)
                v.tensor_tensor(last.unsqueeze(2), wide(x2, 1), power(1, 8, 9), ALU.mult)
                mine.then(v.tensor_tensor(powers[b], wide(x1, 9), power(0, 0, 9), ALU.mult))
                v.tensor_tensor(powers[b][:, :, 0:8, :], powers[b][:, :, 0:8, :], tmp, ALU.add)
                mine.then(v.tensor_tensor(powers[b][:, :, 8:9, :], powers[b][:, :, 8:9, :], last.unsqueeze(2), ALU.add))
                if past(c, 1):
                    dve.wait_ge(q["row"], c)
                v.tensor_copy(b_now, b_[:, gs, :]).then_inc(q["powers"], 1)

            s5_rounds(dve, step, mine, 4)

        @block.scalar
        def _(act):
            def read_y(c, b, i):
                act.wait_ge(q["y"], c + 1)
                if past(c, 2):
                    act.wait_ge(stored[b], i * ALL)
                nc.scalar.activation(yl[b], acc[:, 2 + b, :].rearrange("p (g n) -> p g n", n=S5_N), ACT.Copy).then_inc(q["y_read"], 1)
                act.wait_ge(q["y_read"], c + 1)
                for l in range(S5_L):
                    act.dma_start(lift[l][:, bass.ds(c * NB, NB), :], yl[b][l * S5_IN:(l + 1) * S5_IN]).then_inc(stored[b], 16)

            def step(c, b, i):
                act.wait_ge(q["row"], c + 1)
                if past(c, 1):
                    act.wait_ge(laid[1 - b], (before(b, i)[2] + 1) * ALL)
                nc.scalar.activation(row, acc[0:S5_IN, 0:2, :].rearrange("p a (g c) -> p (a g) c", c=P), ACT.Copy).then_inc(q["row_read"], 1)
                if past(c, 1):
                    read_y(*before(b, i))

            s5_rounds(act, step)
            read_y(*S5_LAST)

        @block.tensor
        def _(pe):
            def multiply(c, b, i):
                pe.wait_ge(laid[b], (i + 1) * ALL)
                if past(c, 2):
                    pe.wait_ge(q["y_read"], c - 1)
                for g in range(NB):
                    out = acc[:, 2 + b, g * S5_N:(g + 1) * S5_N]
                    pe.matmul(out, kt[b][:, g, :], ul[:, c * NB + g, :], start=True, stop=False)
                    ins = pe.matmul(out, rows_of(b, g, 1), hp[:, :, c * NB + g], start=False, stop=True)
                ins.then_inc(q["y"], 1)

            def step(c, b, i):
                pe.wait_ge(q["powers"], c + 1)
                if past(c, 1):
                    pe.wait_ge(q["row_read"], c)
                for g in range(NB):
                    ins = pe.matmul(acc[0:S5_IN, g // 4, (g % 4) * P:(g % 4 + 1) * P], b_now[:, g, :], rows_of(b, g, 0), start=True, stop=True)
                ins.then_inc(q["row"], 1)
                if past(c, 1):
                    multiply(*before(b, i))

            s5_rounds(pe, step)
            multiply(*S5_LAST)


def s5_skip_stage(core):
    nc, p = core.nc, core.p
    step = core.sem("s5_skipped")
    with nc.Block(no_gpsimd_drain=True) as block:
        @block.vector
        def _(dve):
            for c in range(DC):
                by_token = lambda a: a.rearrange("p (n l) -> p n l", l=S5_L)
                u = by_token(p[:, S5U + c, :])
                nc.vector.scalar_tensor_tensor(out=u, in0=u, scalar=core.vcol("s5_d", c), in1=p[:, 36 + c, :].rearrange("p (l n) -> p n l", l=S5_L),
                                               op0=ALU.mult, op1=ALU.add).then_inc(step, 1)

        @block.scalar
        def _(act):
            nc.scalar.activation(p[:, Z:Z + DC, :], p[:, Z:Z + DC, :], ACT.Silu)
            for c in range(DC):
                act.wait_ge(step, c + 1)
                nc.scalar.activation(p[:, S5U + c, :], p[:, S5U + c, :], ACT.Gelu_apprx_tanh)


def s5_glu_stage(core):
    nc, g, p, scr = core.nc, core.gemms["s5_glu"], core.p, core.scr
    op = Operand(core, DC, lambda m, k: m.p[:, S5U + k, :], lambda m, k: m.h[:, k, :], lambda m, k: m.p[:, 44 + k, :])
    gate, step = core.sem("glu_gate"), core.sem("glu_step")
    mb = g.cols // P
    with nc.Block(no_gpsimd_drain=True) as block:
        @block.sync
        def _(sp):
            core.stream(sp, g)

        @block.gpsimd
        def _(pool):
            core.rest_weights(pool, g)

        @block.tensor
        def _(pe):
            core.product(pe, g, op)

        @block.scalar
        def _(act):
            def read(b, banks, s):
                for m in range(mb):
                    ins = nc.scalar.activation(scr[:, s * mb + m, :], banks[m], ACT.Sigmoid, bias=core.vcol("s5_glu_b", b * mb + m))
                ins.then_inc(gate, 1)
            core.round_parts(act, g, op, read)

        @block.vector
        def _(dve):
            core.rest_input(dve, op)

            def read(b, banks, s):
                dve.wait_ge(gate, b + 1)
                t = scr[:, s * mb:s * mb + mb, :]
                nc.vector.tensor_tensor(t, t, p[:, bass.ds(S5U + b * mb, mb), :], ALU.mult).then_inc(step, 1)
                dve.wait_ge(step, b + 1)
                nc.vector.tensor_tensor(p[:, bass.ds(36 + b * mb, mb), :], t, p[:, bass.ds(Z + b * mb, mb), :], ALU.mult).then_inc(core.acc_free, 1)
            core.drain(dve, g, read)
    core.end_product(g, op)


def block3_first(core):
    norm_stage(core, ("layer_norm", 0), 1e-6, load_consts=3)
    ab_in_stage(core)
    ssd_prepare_stage(core)
    ssd_stage(core)
    ssd_gate_stage(core)
    s5_discretize_stage(core)
    s5_state_stage(core)
    s5_output_stage(core)
    s5_skip_stage(core)
    s5_glu_stage(core)
    residual_stage(core, "ab_out", 1.0, Operand(core, 2 * DC, lambda m, k: m.p[:, 36 + k, :] if k < DC else m.p[:, XS + k - DC, :],
                                                 lambda m, k: m.h[:, k, :] if k < DC else m.scr[:, k - DC, :]))


RQ, RK, RV, RG, RO = 0, DC, 2 * DC, 4 * DC, 6 * DC
RET_C = RET_V // P


def ret_rotate_stage(core):
    nc, p, scr, acc = core.nc, core.p, core.scr, core.acc
    names = ("rot", "sin", "cos", "turned")
    q = {s: core.sem(f"rr_{s}") for s in names}
    table = lambda name, c: core.const(4, f"{name}{c % 2}")
    with nc.Block(no_gpsimd_drain=True) as block:
        @block.tensor
        def _(pe):
            for c in range(2 * DC):
                if c >= BANKS:
                    pe.wait_ge(q["sin"], c - BANKS + 1)
                pe.matmul(acc[:, c % BANKS, :], core.const(4, "rotate"), p[:, RQ + c, :], start=True, stop=True).then_inc(q["rot"], 1)

        @block.gpsimd
        def _(pool):
            for c in range(2 * DC):
                pool.wait_ge(q["rot"], c + 1)
                nc.gpsimd.tensor_tensor(p[:, RQ + c, :], p[:, RQ + c, :], table("cos", c), ALU.mult).then_inc(q["cos"], 1)

        @block.vector
        def _(dve):
            for c in range(2 * DC):
                t = scr[:, c % 8, :]
                dve.wait_ge(q["rot"], c + 1)
                if c >= 8:
                    dve.wait_ge(q["turned"], c - 7)
                nc.vector.tensor_tensor(t, acc[:, c % BANKS, :], table("sin", c), ALU.mult).then_inc(q["sin"], 1)
                dve.wait_ge(q["sin"], c + 1)
                dve.wait_ge(q["cos"], c + 1)
                nc.vector.tensor_tensor(p[:, RQ + c, :], p[:, RQ + c, :], t, ALU.add).then_inc(q["turned"], 1)


def retention_stage(core):
    nc, p, scr, h, acc, small = core.nc, core.p, core.scr, core.h, core.acc, core.small
    names = ("step", "staged", "qd", "scores", "st", "kd", "o", "su", "state", "var", "std", "normed", "ot", "gained", "gated")
    q = {s: core.sem(f"rt_{s}") for s in names}
    wide = lambda a, b: scr[:, a:b, :].rearrange("p a (c t) -> p (a c) t", t=CH)
    k_now, q_now, s_t, k_dec = wide(0, 2), wide(2, 4), wide(4, 5), wide(5, 7)
    gains = [scr[:, 7, :], core.rstd[:, :]]
    o_n = p[:, RO:RO + RET_H, :]
    state = lambda hd: h[:, 2 * hd:2 * hd + 2, :]
    value = lambda hd, n: p[:, RV + 4 * hd:RV + 4 * hd + 4, :].rearrange("p (j a) t -> p j (a t)", j=2)[:, :, bass.ds(n * 256, 256)]
    stats, mv, rs = small[:, 0:24], small[:, 24:32], small[:, 32:36]
    tables = lambda name: core.cst[:, const_columns(4)[0][name + "0"][0]:][:, 0:RET_H * P].rearrange("p (h t) -> p h t", t=P)
    with nc.Block(no_gpsimd_drain=True) as block:
        @block.gpsimd
        def _(pool):

            def chunk(n, first=False, last=False):
                if not first:
                    pool.wait_ge(q["o"], n * RET_H)
                nc.gpsimd.tensor_tensor(q_now.rearrange("p (h c) t -> p h c t", c=2),
                                        p[:, RQ:RQ + DC, bass.ds(n * CH, CH)].rearrange("p (h c) t -> p h c t", c=2),
                                        tables("q_decay").unsqueeze(2).to_broadcast([P, RET_H, 2, CH]), ALU.mult).then_inc(q["qd"], 1)

            chunk(0, first=True)
            with pool.Fori(1, NCH - 1) as n:
                chunk(n)
            chunk(NCH - 1, last=True)

        @block.scalar
        def _(act):
            s = nc.scalar

            def chunk(n, first=False, last=False):
                if not first:
                    act.wait_ge(q["scores"], n)
                s.activation(k_now, p[:, RK:RK + DC, bass.ds(n * CH, CH)], ACT.Copy, scale=float(RET_QK ** -0.5)).then_inc(q["staged"], 1)
                act.wait_ge(q["scores"], n + 1)
                if not first:
                    act.wait_ge(q["su"], n * RET_H)
                for hd in range(0 if last else RET_H):
                    ins = s.activation(k_dec[:, 2 * hd:2 * hd + 2, :], acc[:, 1 + hd // 2, (hd % 2) * 256:(hd % 2 + 1) * 256].rearrange("p (c t) -> p c t", t=P),
                                       ACT.Copy, scale=core.const(4, "k_decay")[:, hd:hd + 1])
                if not last:
                    ins.then_inc(q["kd"], 1)
                act.wait_ge(q["var"], n + 1)
                s.activation(rs, rs, ACT.Sqrt).then_inc(q["std"], 1)
                for hd in range(RET_H):
                    act.wait_ge(q["ot"], n * RET_H + hd + 1)
                    if hd >= 2 or not first:
                        act.wait_ge(q["gated"], n * RET_H + hd - 1)
                    for j in range(RET_C):
                        c = RET_C * hd + j
                        ins = s.activation(gains[hd % 2][:, j * P:(j + 1) * P], acc[:, 4 + hd, j * P:(j + 1) * P], ACT.Identity,
                                           scale=core.vcol("ret_gn_w", c), bias=core.vcol("ret_gn_b", c))
                    ins.then_inc(q["gained"], 1)

            chunk(0, first=True)
            with act.Fori(1, NCH - 1) as n:
                chunk(n)
            chunk(NCH - 1, last=True)

        @block.vector
        def _(dve):
            v = nc.vector
            mine = Steps(dve, q["step"])

            def chunk(n, first=False, last=False):
                if not (first or last):
                    mine.loop(n - 1, 3)
                dve.wait_ge(q["scores"], n + 1)
                v.tensor_tensor(s_t, acc[:, 0, :].rearrange("p (h t) -> p h t", t=P), tables("intra"), ALU.mult).then_inc(q["st"], 1)
                for hd in range(RET_H):
                    if hd == RET_H - 1:
                        dve.wait_ge(q["o"], n * RET_H + RET_H)
                        for o in range(RET_H):
                            ins = v.bn_stats(stats[:, 6 * o:6 * o + 6], acc[:, 4 + o, :])
                        mine.then(ins)
                    if last:
                        continue
                    dve.wait_ge(q["su"], n * RET_H + hd + 1)
                    added = acc[:, 2 * (hd % 2):2 * (hd % 2) + 2, :]
                    if first:
                        v.tensor_copy(state(hd), added).then_inc(q["state"], 1)
                    else:
                        v.scalar_tensor_tensor(out=state(hd), in0=state(hd), scalar=core.const(4, "chunk_decay")[:, hd:hd + 1], in1=added,
                                               op0=ALU.mult, op1=ALU.add).then_inc(q["state"], 1)
                for hd in range(RET_H):
                    ins = v.bn_aggr(mv[:, 2 * hd:2 * hd + 2], stats[:, 6 * hd:6 * hd + 6])
                mine.then(ins)
                mine.then(v.tensor_scalar(rs, mv.rearrange("p (h k) -> p h k", k=2)[:, :, 1:2].rearrange("p h k -> p (h k)"), 1e-6, None, ALU.add))
                v.reciprocal(rs, rs).then_inc(q["var"], 1)
                dve.wait_ge(q["std"], n + 1)
                if not first:
                    dve.wait_ge(q["ot"], n * RET_H)
                for hd in range(RET_H):
                    v.tensor_scalar(o_n[:, hd, :], acc[:, 4 + hd, :], mv[:, 2 * hd:2 * hd + 1], rs[:, hd:hd + 1], ALU.subtract, ALU.mult).then_inc(q["normed"], 1)
                for hd in range(RET_H):
                    dve.wait_ge(q["gained"], n * RET_H + hd + 1)
                    y = p[:, RG + 4 * hd:RG + 4 * hd + 4, bass.ds(n * CH, CH)]
                    v.tensor_tensor(y, y, gains[hd % 2].rearrange("p (c t) -> p c t", t=P), ALU.mult).then_inc(q["gated"], 1)

            chunk(0, first=True)
            with dve.Fori(1, NCH - 1) as n:
                chunk(n)
            mine.end(NCH - 2)
            chunk(NCH - 1, last=True)

        @block.tensor
        def _(pe):
            mm = pe.matmul

            def chunk(n, first=False, last=False):
                pe.wait_ge(q["staged"], n + 1)
                if not first:
                    pe.wait_ge(q["state"], n * RET_H)
                for hd in range(RET_H):
                    for j in range(2):
                        ins = mm(acc[:, 0, hd * P:(hd + 1) * P], k_now[:, 2 * hd + j, :], p[:, RQ + 2 * hd + j, bass.ds(n * CH, CH)], start=(j == 0), stop=(j == 1))
                for c in range(0 if last else 2 * RET_H):
                    ins = pe.transpose(acc[:, 1 + c // 4, (c % 4) * P:(c % 4 + 1) * P], k_now[:, c, :], core.eye[:, :])
                ins.then_inc(q["scores"], 1)
                pe.wait_ge(q["qd"], n + 1)
                if not first:
                    pe.wait_ge(q["gained"], n * RET_H)
                pe.wait_ge(q["st"], n + 1)
                if not last:
                    pe.wait_ge(q["kd"], n + 1)
                for pair in range(0, RET_H, 2):
                    for hd in (pair, pair + 1):
                        for j in range(0 if first else 2):
                            mm(acc[:, 4 + hd, :], q_now[:, 2 * hd + j, :], state(hd)[:, j, :], start=(j == 0), stop=False)
                        mm(acc[:, 4 + hd, :], s_t[:, hd, :], value(hd, n), start=first, stop=True).then_inc(q["o"], 1)
                    if last:
                        continue
                    if pair:
                        pe.wait_ge(q["state"], n * RET_H + 2)
                    for hd in (pair, pair + 1):
                        for j in range(2):
                            ins = mm(acc[:, 2 * (hd % 2) + j, :], k_dec[:, 2 * hd + j, :], value(hd, n), start=True, stop=True)
                        ins.then_inc(q["su"], 1)
                for hd in range(RET_H):
                    pe.wait_ge(q["normed"], n * RET_H + hd + 1)
                    for j in range(RET_C):
                        ins = pe.transpose(acc[:, 4 + hd, j * P:(j + 1) * P], o_n[:, hd, j * P:(j + 1) * P], core.eye[:, :])
                    ins.then_inc(q["ot"], 1)

            chunk(0, first=True)
            with pe.Fori(1, NCH - 1) as n:
                chunk(n)
            chunk(NCH - 1, last=True)


def block3_second(core):
    norm_stage(core, ("layer_norm", DC), 1e-6, load_consts=4)
    project_stage(core, "ret_qk")
    project_stage(core, "ret_v", at=RV, fresh=False)
    project_stage(core, "ret_g", at=RG, func=ACT.Silu, fresh=False)
    ret_rotate_stage(core)
    retention_stage(core)
    residual_stage(core, "ret_out", 1.0, Operand(core, 2 * DC, lambda m, k: m.p[:, RG + k, :], lambda m, k: m.p[:, k, :]))


def lay_weights(which, inputs):
    gemms, n = lay_stream(which)
    out = np.zeros((n, P, SLOT), np.float32)

    def fill(name, *mats):
        g = gemms.get(name)
        if g is None:
            return
        cols = g.cols // len(mats)
        for b in range(g.blocks):
            for sub in range(g.q):
                slot = out[g.first + b * g.q + sub, :, 0:g.width].reshape(P, g.kc, g.cols)
                for j, w in enumerate(mats):
                    part = w[sub * g.kc * P:(sub + 1) * g.kc * P, b * cols:(b + 1) * cols]
                    slot[:, :, j * cols:(j + 1) * cols] = part.reshape(g.kc, P, cols).transpose(1, 0, 2)

    a = {k: np.asarray(v) for k, v in inputs.items()}
    for f in ("ffn1", "ffn2"):
        fill(f"{f}_up", a[f"{f}_gate"][0], a[f"{f}_up"][0])
        fill(f"{f}_down", a[f"{f}_down"][0])
    fill("mix_in", a["w_in"][0])
    fill("mix_out", a["w_out"][0])
    fill("b2_in", a["w_in_2"][0])
    fill("branch_a", a["w_branch_a_2"][0])
    fill("branch_b", a["w_branch_b_2"][0])
    fill("b2_out", a["w_out_2"][0])
    fill("mlp_up", a["w_up_2"][0])
    fill("mlp_down", a["w_down_2"][0])
    fill("ab_in", a["ab_w_in_3"][0][:, 0:18 * 2 * P])
    fill("s5_glu", a["s5_glu_w_3"][0])
    fill("ab_out", a["ab_w_out_3"][0])
    qk = 2 * RET_H * RET_QK
    fill("ret_qk", a["ret_w_in_3"][0][:, 0:qk])
    fill("ret_v", a["ret_w_in_3"][0][:, qk:qk + RET_H * RET_V])
    fill("ret_g", a["ret_w_in_3"][0][:, qk + RET_H * RET_V:])
    fill("ret_out", a["ret_w_out_3"][0])
    return out


def lay_vectors(inputs):
    a = {k: np.asarray(v) for k, v in inputs.items()}
    src = {"norm_ffn1": "norm_ffn1", "norm_mix": "norm_mix", "b_in_attn": "b_in_attn", "shift_mix": "rwkv_shift_mix",
           "w0": "rwkv_w0", "a0": "rwkv_a0", "k_k": "rwkv_k_k", "k_a": "rwkv_k_a", "r_k": "rwkv_r_k", "ln_w": "rwkv_ln_w",
           "ln_b": "rwkv_ln_b", "norm_ffn2": "norm_ffn2", "norm_final": "norm_final", "norm_mix_g": "norm_mix_g_2",
           "conv_w": "conv_w_2", "conv_b": "conv_b_2", "lru_b_a": "lru_b_a_2", "lru_b_x": "lru_b_x_2",
           "lru_lambda": "lru_lambda_2", "sgu_ln_g": "sgu_ln_g_2", "sgu_ln_b": "sgu_ln_b_2", "norm_ffn_g": "norm_ffn_g_2",
           "final_norm_g": "final_norm_g_2", "layer_norm": "layer_norm_w_3", "s5_d": "s5_d_3", "s5_glu_b": "s5_glu_b_3",
           "ssd_conv_w": "ssd_conv_w_3", "ssd_conv_b": "ssd_conv_b_3", "ssd_norm_w": "ssd_norm_w_3", "ret_gn_w": "ret_gn_w_3", "ret_gn_b": "ret_gn_b_3",
           "final_norm_w": "final_norm_w_3"}
    cols = [a[src[name]].reshape(k, P) for name, k in VECTORS]
    return np.ascontiguousarray(np.concatenate(cols, 0).T)


def lay_small(inputs):
    a = {k: np.asarray(v) for k, v in inputs.items()}
    out = {}
    lora = np.zeros((P, 3, T), np.float32)
    lora[0:64, 0], lora[64:128, 1], lora[:, 2] = a["rwkv_w2"][0], a["rwkv_a2"][0], a["rwkv_g2"][0]
    out["lora"] = lora
    out["sinks"] = a["attn_sinks"].reshape(Q_HEADS)
    bd = np.zeros((P, RNNC, 2, P), np.float32)
    for g, w in enumerate((a["lru_w_a_2"][0], a["lru_w_x_2"][0])):
        for c in range(RNNC):
            for j in range(2):
                bd[j * 64:j * 64 + 64, c, g, j * 64:j * 64 + 64] = w[2 * c + j]
    out["lru_w"] = bd.reshape(P, -1)
    out["sgu_w"] = np.ascontiguousarray(a["sgu_w_s_2"][0].transpose(2, 0, 1))
    out["sgu_b"] = a["sgu_b_s_2"].reshape(-1)
    wdt = np.zeros((DC, P, P), np.float32)
    wdt[:, :, 0:SSD_H] = a["ab_w_in_3"][0][:, 18 * 2 * P:].reshape(DC, P, SSD_H)
    out["w_dt"] = np.ascontiguousarray(wdt.transpose(1, 0, 2)).reshape(P, -1)
    heads = np.zeros((P, 2 + DC), np.float32)
    heads[0:SSD_H, 0], heads[0:SSD_H, 1] = a["ssd_dt_bias_3"][0], a["ssd_a_log_3"][0]
    heads[:, 2:] = np.repeat(a["ssd_d_3"][0], 64).reshape(DC, P).T
    out["ssd_small"] = heads
    twice = lambda m: np.ascontiguousarray(np.concatenate([m, m], 0))
    out["lam_re"], out["lam_im"] = twice(a["s5_lam_re_3"][0].T), twice(a["s5_lam_im_3"][0].T)
    out["log_dt"] = a["s5_log_dt_3"].reshape(-1)
    by_state = lambda re, im: np.concatenate([re, im], 0).reshape(P, -1)
    br, bi = (a[f"s5_b_{k}_3"][0].transpose(1, 0, 2) for k in ("re", "im"))
    cr, ci = (a[f"s5_c_{k}_3"][0].transpose(2, 0, 1) for k in ("re", "im"))
    out["s5_b"] = np.concatenate([by_state(br, bi), by_state(bi, br)], 1).reshape(P, 4, T)
    out["s5_c"] = np.concatenate([by_state(cr, ci), by_state(ci, cr)], 1).reshape(P, 4, T)
    return out


def lay_out(which, inputs):
    x = np.asarray(inputs["x"])[0]
    arrays = {"x": np.ascontiguousarray(x.reshape(T, DC, P).transpose(2, 1, 0)), "weights": lay_weights(which, inputs),
              "vectors": lay_vectors(inputs)}
    arrays.update(lay_small(inputs))
    for n, make in CONSTS.items():
        arrays[f"consts{n}"] = np.concatenate([part for _, part in make()], axis=1)
    return arrays


def build(nc, dram, out, run, which=None):
    dram = dict(dram, lift=nc.dram_tensor("lift", (D, T), F32, kind="Internal").ap())
    with ExitStack() as ctx:
        core = Core(nc, ctx, dram, which)
        run(core, out)


def whole(core, out):
    start_stage(core, 1)
    block1(core)
    norm_stage(core, ("norm_final", 0), 1e-5, dst=core.x)
    core.clear_sems()
    block2(core)
    norm_stage(core, ("final_norm_g", 0), 1e-6, dst=core.x)
    core.clear_sems()
    block3_first(core)
    block3_second(core)
    norm_stage(core, ("final_norm_w", 0), 1e-6, dst=core.x)
    finish_stage(core, out)


def finish_stage(core, out):
    nc = core.nc
    stored = core.sem("stored")
    with nc.Block(no_gpsimd_drain=True) as block:
        @block.sync
        def _(sp):
            sp.dma_start(out, core.x[:, :, :]).then_inc(stored, 16)
            sp.wait_ge(stored, 16)


def kernel(**inputs):
    import concourse.bacc as bacc
    from concourse.bass_utils import run_bass_kernel_spmd

    nc = bacc.Bacc("TRN2", target_bir_lowering=False, num_devices=1)
    arrays = lay_out(None, inputs)
    dram = {n: nc.dram_tensor(f"in_{n}", a.shape, F32, kind="ExternalInput").ap() for n, a in arrays.items()}
    out = nc.dram_tensor("out", (P, DC, T), F32, kind="ExternalOutput").ap()
    build(nc, dram, out, whole)
    r = run_bass_kernel_spmd(nc, [{f"in_{n}": a for n, a in arrays.items()}], core_ids=[0])
    got = r.results[0]["out"]
    return np.ascontiguousarray(got.transpose(2, 1, 0)).reshape(1, T, D)
```

```python
from contextlib import ExitStack

import numpy as np

import concourse.bass as bass
from concourse import mybir

F32 = mybir.dt.float32
F32R = mybir.dt.float32r
ALU = mybir.AluOpType
ACT = mybir.ActivationFunctionType
AX = mybir.AxisListType

P = 128
T = 512
D = 1024
DC = D // P
SLOT = 1408
RING = 4
AHEAD = 2
BANKS = 8

FF = 2816
FFC = FF // P
HEAD = 64
RW_HEADS = 8
PAIRS = RW_HEADS // 2
LC = 64
NLC = T // LC
LORA_W, LORA_G = 12, 13
ATT_Q, ATT_K, ATT_V = 14, 18, 19
AB = 128
NAB = T // AB
Q_HEADS = 8
MASKED = -1.0e30
DECAY_RATE = float(np.exp(-0.5))
RNNC = 1280 // P
CONV = 4
SGU_G = 8
S5_G, S5_IN, S5_P = 64, 16, 64
S5_L = P // S5_IN
S5_N = T // S5_L
SSD_H, SSD_REP = 16, 8
CH = 128
NCH = T // CH
RET_H, RET_QK, RET_V = 4, 256, 512


class Gemm:

    def __init__(self, first, blocks, q, kc, cols, by_token):
        self.by_token = by_token
        self.first, self.blocks, self.q, self.kc, self.cols = first, blocks, q, kc, cols
        self.n = blocks * q
        self.width = kc * cols
        self.body = max(8, 2 * q)
        self.per = self.body // q
        self.mb = T // P if by_token else cols // P
        self.sets = min(self.per, BANKS // self.mb)


class Operand:

    def __init__(self, core, n, x, hi, lo=None, source=None):
        self.n, self.source = n, source
        self.x = lambda k: x(core, k)
        self.hi = lambda k: hi(core.r, k)
        self.lo = lambda k: (lo or x)(core.r, k)


class Norm:

    def __init__(self, core, gain, eps, dst=None, after_residual=False):
        self.after_residual = after_residual
        self.core, self.gain, self.eps, self.dst, self.nth = core, gain, eps, core.h if dst is None else dst, core.norms
        core.norms += 1
        self.squares_before = core.chunks_squared
        core.chunks_squared += 0 if after_residual else DC
        self.squared, self.summed, self.var_ready, self.inv_ready, self.rstd_ready, self.made = core.norm.values()

    def act_first(self, act):
        if self.after_residual:
            return
        for c in range(DC):
            self.core.nc.scalar.activation(self.core.p[:, c, :], self.core.x[:, c, :], ACT.Square).then_inc(self.squared, 1)

    def act_then(self, act):
        rstd = self.core.rstd[:, :]
        act.wait_ge(self.inv_ready, self.nth + 1)
        self.core.nc.scalar.activation(rstd, rstd, ACT.Sqrt).then_inc(self.rstd_ready, 1)

    def pe_share(self, pe):
        core = self.core
        if self.after_residual:
            mm = pe.matmul(core.acc[:, BANKS - 1, :], core.ones[:, :], core.rstd[:, :], start=True, stop=True)
        else:
            for c in range(DC):
                pe.wait_ge(self.squared, self.squares_before + c + 1)
                mm = pe.matmul(core.acc[:, BANKS - 1, :], core.ones[:, :], core.p[:, c, :], start=(c == 0), stop=(c == DC - 1))
        mm.then_inc(self.summed, 1)

    def dve_share(self, dve):
        v, rstd = self.core.nc.vector, self.core.rstd[:, :]
        dve.wait_ge(self.summed, self.nth + 1)
        v.tensor_scalar(rstd, self.core.acc[:, BANKS - 1, :], 1.0 / D, self.eps, ALU.mult, ALU.add).then_inc(self.var_ready, 1)
        dve.wait_ge(self.var_ready, self.nth + 1)
        v.reciprocal(rstd, rstd).then_inc(self.inv_ready, 1)
        dve.wait_ge(self.rstd_ready, self.nth + 1)

    def chunk(self, dve, c):
        self.core.nc.vector.scalar_tensor_tensor(
            out=self.dst[:, c, :], in0=self.core.x[:, c, :], scalar=self.core.vcol(self.gain[0], self.gain[1] + c),
            in1=self.core.rstd[:, :], op0=ALU.mult, op1=ALU.mult).then_inc(self.made, 1)

    def ready(self, act, c):
        act.wait_ge(self.made, DC * self.nth + c + 1)


class Rounded:
    pass


class Chunks:

    def __init__(self, chunks):
        self.chunks = chunks

    def __getitem__(self, at):
        partitions, chunk, tokens = at
        return self.chunks[chunk][partitions, tokens]


STREAM = [
    ("ffn1_up", FF // P, 2, 4, 2 * P), ("ffn1_down", DC, 2, FFC // 2, P),
    ("mix_in", 10, 2, 4, 2 * P), ("mix_out", 4, 2, 4, 2 * P),
    ("ffn2_up", FF // P, 2, 4, 2 * P), ("ffn2_down", DC, 2, FFC // 2, P),
    ("b2_rnn", 5, 2, 4, 2 * P), ("b2_gelu", 13, 2, 4, 2 * P), ("b2_gate", 8, 2, 4, 2 * P),
    ("branch_a", 4, 2, RNNC // 2, 2 * P), ("branch_b", 4, 2, 4, 2 * P),
    ("b2_out", 4, 2, 4, 2 * P), ("mlp_up", 16, 2, 4, 2 * P), ("mlp_down", 4, 8, 4, 2 * P),
    ("ab_in", 18, 2, 4, 2 * P), ("s5_glu", 4, 2, 4, 2 * P), ("ab_out", 4, 4, 4, 2 * P),
    ("ret_qk", 8, 2, 4, 2 * P), ("ret_v", 8, 2, 4, 2 * P), ("ret_g", 8, 2, 4, 2 * P), ("ret_out", 4, 4, 4, 2 * P),
]
BY_TOKEN = ("ret_v",)


def lay_stream(which):
    gemms, at = {}, 0
    for name, blocks, q, kc, cols in STREAM:
        if which is None or name in which:
            gemms[name] = Gemm(at, blocks, q, kc, cols, name in BY_TOKEN)
            at += blocks * q
    return gemms, at


VECTORS = [
    ("norm_ffn1", 8), ("norm_mix", 8), ("b_in_attn", 6), ("shift_mix", 14), ("w0", 4), ("a0", 4),
    ("k_k", 4), ("k_a", 4), ("r_k", 4), ("ln_w", 4), ("ln_b", 4), ("norm_ffn2", 8), ("norm_final", 8),
    ("norm_mix_g", 8), ("conv_w", 40), ("conv_b", 10), ("lru_b_a", 10), ("lru_b_x", 10), ("lru_lambda", 10),
    ("sgu_ln_g", 8), ("sgu_ln_b", 8), ("norm_ffn_g", 8), ("final_norm_g", 8),
    ("layer_norm", 16), ("s5_d", 8), ("s5_glu_b", 8), ("ssd_conv_w", 48), ("ssd_conv_b", 12),
    ("ssd_norm_w", 8), ("ret_gn_w", 16), ("ret_gn_b", 16), ("final_norm_w", 8),
]
VEC_AT = {}
_n = 0
for _name, _k in VECTORS:
    VEC_AT[_name] = _n
    _n += _k
N_VEC = _n


def pair_masks():
    i = np.arange(P)
    same = (i[:, None] // LC) == (i[None, :] // LC)
    r, c = i[:, None] % LC, i[None, :] % LC
    f = lambda m: (m & same).astype(np.float32)
    out = {"strict": f(r < c), "upto": f(r <= c)}
    for n in (1, 2, 4, 8, 16, 32):
        m = (r // (2 * n) == c // (2 * n)) & (r // n % 2 == 0) & (c // n % 2 == 1)
        out[f"level{n}"] = f(m)
    m = (c // 2 == r // 2) & (c % 2 == 0) & (r % 2 == 1)
    out["level1_ts"] = f(m)
    return out


def block1_consts():
    i = np.arange(P)
    m = pair_masks()
    parts = [("head_ones", ((i[:, None] // HEAD) == (i[None, :] // HEAD)).astype(np.float32)),
             ("stacked_eye", np.concatenate([np.eye(HEAD), np.eye(HEAD)]).astype(np.float32)),
             ("resets", np.tile((np.arange(T) % LC != 0).astype(np.float32), (P, 1)))]
    parts += list(m.items())
    qi, kj = np.arange(AB)[:, None], np.arange(2 * AB)[None, :]
    dist = qi + AB - kj
    band = (dist >= 0) & (dist < AB)
    for n in range(NAB):
        ok = band if n else band & (kj >= AB)
        parts.append((f"band{n}", np.where(ok, 0.0, MASKED).astype(np.float32)))
    for g in range(2):
        dup = np.zeros((P, P), np.float32)
        for j in range(2):
            dup[g * HEAD + np.arange(HEAD), j * HEAD + np.arange(HEAD)] = 1
        parts.append((f"dup{g}", dup))
    return parts


def block2_consts():
    chunk = np.arange(P) // 64
    return [("sgu_mask", (chunk[None, :] >= chunk[:, None]).astype(np.float32))]


def s5_swap():
    swap = np.zeros((P, P), np.float32)
    p = np.arange(S5_P)
    swap[S5_P + p, p] = -1.0
    swap[p, S5_P + p] = 1.0
    return swap


def block3_consts():
    i = np.arange(P)
    sign = np.where(i < S5_P, 1.0, -1.0).astype(np.float32)[:, None]
    sel = np.zeros((P, SSD_H, P), np.float32)
    for h in range(SSD_H):
        sel[h, h, :] = 1.0
    last = np.zeros((P, P), np.float32)
    last[P - 1, :] = 1.0
    return [("swap", s5_swap()), ("sign", sign), ("causal", np.where(i[:, None] <= i[None, :], 0.0, MASKED).astype(np.float32)),
            ("last_row", last), ("head_rows", sel.reshape(P, -1)),
            ("dt_resets", np.tile((np.arange(T) % CH != 0).astype(np.float32), (P, 1)))]


def block4_consts():
    f = np.float32
    i = np.arange(P)
    rot = np.zeros((P, P), f)
    rot[np.arange(1, P, 2), np.arange(0, P, 2)] = -1.0
    rot[np.arange(0, P, 2), np.arange(1, P, 2)] = 1.0
    angle = np.repeat(f(1.0) / (f(10000.0) ** np.linspace(0.0, 1.0, RET_QK // 2, dtype=f)), 2).astype(f)
    theta = angle[:, None] * np.arange(T, dtype=f)[None, :]
    cos, sin = np.cos(theta).astype(f), np.sin(theta).astype(f)
    parts = [("rotate", rot)]
    for h in range(2):
        parts += [(f"cos{h}", cos[h * P:(h + 1) * P]), (f"sin{h}", sin[h * P:(h + 1) * P])]
    lg = np.log(1.0 - 2.0 ** (-5.0 - np.arange(RET_H)))
    rel = i[None, :] - i[:, None]
    for h in range(RET_H):
        parts.append((f"intra{h}", np.where(rel >= 0, np.exp(lg[h] * np.maximum(rel, 0)), 0.0).astype(f)))
    for h in range(RET_H):
        parts.append((f"q_decay{h}", np.tile(np.exp(lg[h] * (i + 1.0)), (P, 1)).astype(f)))
    parts.append(("k_decay", np.exp(lg[None, :] * (CH - 1.0 - i)[:, None]).astype(f)))
    parts.append(("chunk_decay", np.tile(np.exp(lg * CH)[None, :], (P, 1)).astype(f)))
    return parts


CONSTS = {1: block1_consts, 2: block2_consts, 3: block3_consts, 4: block4_consts}


def const_columns(which):
    at, out = 0, {}
    for name, a in CONSTS[which]():
        out[name] = (at, a.shape[1])
        at += a.shape[1]
    return out, at


class Steps:

    def __init__(self, eng, sem):
        self.eng, self.sem, self.base, self.n, self.i, self.per = eng, sem, 0, 0, None, 0

    def loop(self, i, per):
        self.base, self.i, self.per, self.n = self.base + self.n, i, per, 0

    def end(self, times):
        assert self.n == self.per, (self.n, self.per)
        self.base, self.i, self.n = self.base + times * self.per, None, 0

    def value(self):
        return self.base + self.n + (0 if self.i is None else self.i * self.per)

    def then(self, ins):
        ins.then_inc(self.sem, 1)
        self.n += 1
        self.eng.wait_ge(self.sem, self.value())


class Core:

    def __init__(self, nc, ctx, dram, which):
        self.nc, self.ctx, self.dram = nc, ctx, dram
        self.block_sems = []
        self.gemms, self.n_slots = lay_stream(which)
        shapes = dict(
            x=[P, DC, T],
            h=[P, DC, T],
            p=[P, 52, T],
            weight_ring=[P, RING, SLOT],
            weight_hi=[P, AHEAD, SLOT],
            vec=[P, N_VEC],
            cst=[P, 3980],
            eye=[P, P], ones=[P, P], rstd=[P, T], scr=[P, 8, T], small=[P, 256])
        self.r, at = Rounded(), -(-nc.sbuf_base // 32) * 32
        place, alias = {}, {}
        for name, shape in shapes.items():
            place[name] = nc.alloc_sbuf_tensor_at(name, shape, F32, offset=at)
            if name in ("weight_ring", "weight_hi", "cst"):
                alias[name] = nc.alloc_sbuf_tensor_at(f"{name}_r", shape, F32R, offset=at)
            elif name in ("h", "p", "scr"):
                alias[name] = Chunks([nc.alloc_sbuf_tensor_at(f"{name}_r{c}", [P, T], F32R, offset=at + 4 * T * c) for c in range(shape[1])])
            at += -(-4 * int(np.prod(shape[1:])) // 32) * 32
        self.x, self.h, self.p, self.weight_ring, self.weight_hi, self.vec, self.cst, self.eye, self.ones, self.rstd, self.scr, self.small = place.values()
        self.r.h, self.r.p, self.r.weight_ring, self.r.weight_hi, self.r.cst, self.r.scr = (
            alias[n] for n in ("h", "p", "weight_ring", "weight_hi", "cst", "scr"))
        self.acc = ctx.enter_context(nc.psum_tensor("acc", [P, BANKS, T], F32))
        self.slot_loaded = [self.sem(f"slot{r}_loaded") for r in range(RING)]
        self.weights_rounded, self.weights_split = self.sem("weights_rounded"), self.sem("weights_split")
        self.input_rounded, self.input_split = self.sem("input_rounded"), self.sem("input_split")
        self.inputs = 0
        self.products_done = self.sem("products_done")
        self.acc_free = self.sem("acc_free")
        self.blocks_read = 0
        self.norm = {n: self.sem(f"norm_{n}") for n in ("squared", "summed", "var", "inv", "rstd", "made")}
        self.consts_in, self.const_loads = self.sem("consts_in"), 0
        self.lifted = self.sem("lifted")
        self.norms = 0
        self.chunks_squared = 0
        self.block_sems = []

    def sem(self, name):
        s = self.nc.alloc_semaphore(name)
        self.block_sems.append(s)
        return s

    def clear_sems(self):
        self.nc.clear_and_free_semaphores(self.block_sems)
        self.nc.all_engine_barrier()
        self.block_sems = []

    def vcol(self, name, c):
        return self.vec[:, bass.ds(VEC_AT[name] + c, 1)]

    def const(self, which, name, part=slice(None)):
        at, n = const_columns(which)[0][name]
        return self.cst[part, at:at + n]

    def const_load(self, eng, which, signal):
        source = self.dram[f"consts{which}"]
        eng.dma_start(self.cst[:, 0:source.shape[1]], source).then_inc(signal, 16)

    def next_consts(self, sp, which):
        self.const_load(sp, which, self.consts_in)
        self.const_loads += 16

    def width_of(self, s):
        for g in self.gemms.values():
            if g.first <= s < g.first + g.n:
                return g.width
        raise ValueError(s)

    def one_load(self, sp, s, r, width, wait):
        if wait is not None:
            sp.wait_ge(self.products_done, wait)
        sp.dma_start(self.weight_ring[:, r, 0:width], self.dram["weights"][s, :, 0:width])\
            .then_inc(self.slot_loaded[r], 16)

    def first_loads(self, sp):
        for s in range(min(RING, self.n_slots)):
            self.one_load(sp, s, s % RING, self.width_of(s), None)

    def stream(self, sp, g):
        lo, hi = g.first + RING, g.first + g.n
        rounds = max(0, hi - lo) // RING
        if rounds > 0:
            with sp.Fori(0, rounds) as i:
                for j in range(RING):
                    self.one_load(sp, lo + i * RING + j, (lo + j) % RING, g.width, g.first + 1 + i * RING + j)
        for s in range(lo + rounds * RING, min(hi + RING, self.n_slots)):
            self.one_load(sp, s, s % RING, self.width_of(s), s - RING + 1)

    def round_slot(self, act, s, r, ahead, width, turn, used=None):
        act.wait_ge(self.slot_loaded[r], turn)
        if used is not None:
            act.wait_ge(self.products_done, used)
        self.nc.scalar.activation(self.r.weight_hi[:, ahead, 0:width], self.weight_ring[:, r, 0:width], ACT.Copy)\
            .then_inc(self.weights_rounded, 1)

    def rest_slot(self, pool, s, r, ahead, width):
        raw, rest, hi = (m[:, n, 0:width] for m, n in ((self.weight_ring, r), (self.r.weight_ring, r), (self.r.weight_hi, ahead)))
        pool.wait_ge(self.weights_rounded, s + 1)
        self.nc.gpsimd.tensor_tensor(rest, raw, hi, ALU.subtract).then_inc(self.weights_split, 1)

    def round_parts(self, act, g, op, read=None):
        mb, per, sets, body = g.mb, g.per, g.sets, g.body
        turn = lambda s: 16 * (s // RING + 1)

        def inputs(sub):
            for k in range(sub * g.kc, (sub + 1) * g.kc):
                if op.source is not None:
                    op.source.ready(act, k)
                self.nc.scalar.activation(op.hi(k), op.x(k), ACT.Copy).then_inc(self.input_rounded, 1)

        def round_of(i, at, n):
            for b in range(n):
                for sub in range(g.q):
                    done = g.first + (at + b) * g.q + sub + 1
                    s = done + 1
                    if i is None and s < min(g.first + g.n + 1, self.n_slots):
                        self.round_slot(act, s, s % RING, s % AHEAD, self.width_of(s), turn(s), done)
                    elif i is not None:
                        self.round_slot(act, s + i * body, s % RING, s % AHEAD, g.width, turn(s) + i * (16 * body // RING), done + i * body)
                    if op is not None and i is None and at + b == 0 and sub + 2 < g.q:
                        inputs(sub + 2)
                if read is not None:
                    block_ = at + b if i is None else at + b + i * per
                    act.wait_ge(self.products_done, g.first + (block_ + 1) * g.q)
                    set_ = b % sets
                    read(block_, [self.acc[:, set_ * mb + m, :] for m in range(mb)], set_)

        second = g.first + 1
        second_slot = lambda: self.round_slot(act, second, second % RING, second % AHEAD, g.width, turn(second), second - 1 if second > 1 else None)
        if op is not None and op.source is not None:
            op.source.act_first(act)
            second_slot()
            op.source.act_then(act)
            inputs(0)
            inputs(1)
        else:
            if op is not None:
                inputs(0)
            second_slot()
            if op is not None:
                inputs(1)
        rounds = -(-g.blocks // per)
        round_of(None, 0, min(per, g.blocks))
        if rounds > 2:
            with act.Fori(0, rounds - 2) as i:
                round_of(i, per, per)
        if rounds > 1:
            round_of(None, (rounds - 1) * per, g.blocks - (rounds - 1) * per)

    def rest_weights(self, pool, g):
        lo, hi = g.first + 1, g.first + g.n
        rounds = (hi - lo) // RING
        if rounds > 0:
            with pool.Fori(0, rounds) as i:
                for s in range(lo, lo + RING):
                    self.rest_slot(pool, i * RING + s, s % RING, s % AHEAD, g.width)
        for s in range(lo + rounds * RING, min(hi + 1, self.n_slots)):
            self.rest_slot(pool, s, s % RING, s % AHEAD, self.width_of(s))

    def rest_input(self, dve, op):
        lead = 0
        if op.source is not None:
            op.source.dve_share(dve)
            lead = 2
            for k in range(lead):
                op.source.chunk(dve, k)
        for k in range(op.n):
            if op.source is not None and k + lead < op.n:
                op.source.chunk(dve, k + lead)
            dve.wait_ge(self.input_rounded, self.inputs + k + 1)
            self.nc.vector.tensor_tensor(op.lo(k), op.x(k), op.hi(k), ALU.subtract).then_inc(self.input_split, 1)

    def end_product(self, g, op, fresh=True):
        self.blocks_read += g.blocks
        self.inputs += op.n if fresh else 0

    def product(self, pe, g, op, fresh=True):
        mb, body, sets, by_token = g.mb, g.body, g.sets, g.by_token

        def parts(out, w, x, start, stop):
            for n, (wp, xp) in enumerate(((w[0], x[0]), (w[0], x[1]), (w[1], x[0]))):
                a, b = (xp, wp) if by_token else (wp, xp)
                mm = pe.matmul(out, a, b, start=start and n == 0, stop=stop and n == 2)
            return mm

        def round_of(i, at, n):
            for j in range(n):
                s, b, sub = at + j, (at + j) // g.q if i is None else None, j % g.q
                local = j // g.q
                r, ahead = (g.first + s) % RING, (g.first + s) % AHEAD
                ready = g.first + s + 1
                pe.wait_ge(self.weights_split, ready if i is None else ready + i * body)
                if sub == 0 and (i is not None or b >= sets):
                    freed = self.blocks_read + s // g.q - sets + 1
                    pe.wait_ge(self.acc_free, freed if i is None else freed + i * g.per)
                bank0 = (local % sets) * mb
                for m in range(mb):
                    for k in range(g.kc):
                        kx = sub * g.kc + k
                        if fresh and b == 0 and m == 0:
                            pe.wait_ge(self.input_split, self.inputs + kx + 1)
                        first, last = kx == 0, sub == g.q - 1 and k == g.kc - 1
                        if by_token:
                            w_at, x_at = slice(k * g.cols, (k + 1) * g.cols), slice(m * P, (m + 1) * P)
                        else:
                            w_at, x_at = slice(k * g.cols + m * P, k * g.cols + m * P + P), slice(0, T)
                        out = self.acc[:, bank0 + m, 0:g.cols if by_token else T]
                        mm = parts(out, (self.r.weight_hi[:, ahead, w_at], self.r.weight_ring[:, r, w_at]),
                                   (op.hi(kx)[:, x_at], op.lo(kx)[:, x_at]), first, last)
                mm.then_inc(self.products_done, 1)

        if fresh and op.source is not None:
            op.source.pe_share(pe)
        rounds = g.n // body
        round_of(None, 0, min(body, g.n))
        if rounds > 1:
            with pe.Fori(0, rounds - 1) as i:
                round_of(i, body, body)
        if g.n > body and g.n % body:
            round_of(None, rounds * body, g.n % body)

    def drain(self, eng, g, read):
        mb, per, sets = g.mb, g.per, g.sets

        def round_of(i, at, n):
            for l in range(n):
                b = at + l if i is None else at + l + i * per
                eng.wait_ge(self.products_done, g.first + (b + 1) * g.q)
                set_ = l % sets
                read(b, [self.acc[:, set_ * mb + m, :] for m in range(mb)], set_)

        rounds = g.blocks // per
        if rounds > 0:
            with eng.Fori(0, rounds) as i:
                round_of(i, 0, per)
        if g.blocks % per:
            round_of(None, rounds * per, g.blocks % per)


def start_stage(core, block0):
    nc = core.nc
    loaded, eye_zero = core.sem("inputs_loaded"), core.sem("eye_zeroed")
    with nc.Block(no_gpsimd_drain=True) as block:
        @block.sync
        def _(sp):
            sp.dma_start(core.x[:, :, :], core.dram["x"]).then_inc(loaded, 16)
            sp.dma_start(core.vec[:, :], core.dram["vectors"]).then_inc(loaded, 16)
            core.first_loads(sp)
            core.const_load(sp, block0, loaded)
            sp.wait_ge(loaded, 48)

        @block.gpsimd
        def _(pool):
            nc.gpsimd.memset(core.ones[:, :], 1.0)
            nc.gpsimd.memset(core.eye[:, :], 0.0).then_inc(eye_zero, 1)
            pool.wait_ge(eye_zero, 1)
            nc.gpsimd.affine_select(out=core.eye[:, :], in_=core.eye[:, :], compare_op=ALU.not_equal, fill=1.0,
                                    base=0, pattern=[[-1, P]], channel_multiplier=1).then_inc(eye_zero, 1)
            core.rest_slot(pool, 0, 0, 0, core.width_of(0))
            pool.wait_ge(eye_zero, 2)

        @block.scalar
        def _(act):
            core.round_slot(act, 0, 0, 0, core.width_of(0), 16)


def norm_stage(core, gain, eps):
    norm = Norm(core, gain, eps, core.x, after_residual=True)
    with core.nc.Block(no_gpsimd_drain=True) as block:
        @block.scalar
        def _(act):
            norm.act_first(act)
            norm.act_then(act)

        @block.tensor
        def _(pe):
            norm.pe_share(pe)

        @block.vector
        def _(dve):
            norm.dve_share(dve)
            for c in range(DC):
                norm.chunk(dve, c)


def swiglu_up_stage(core, name, norm):
    nc, g = core.nc, core.gemms[name]
    op = Operand(core, DC, lambda m, k: m.h[:, k, :], lambda m, k: m.p[:, 44 + k, :], source=norm)
    silu_ready = core.sem(f"{name}_silu")
    with nc.Block(no_gpsimd_drain=True) as block:
        @block.sync
        def _(sp):
            core.stream(sp, g)

        @block.gpsimd
        def _(pool):
            core.rest_weights(pool, g)

        @block.tensor
        def _(pe):
            core.product(pe, g, op)

        @block.scalar
        def _(act):
            def read(b, banks, s):
                nc.scalar.activation(core.scr[:, s, :], banks[0], ACT.Silu).then_inc(silu_ready, 1)
            core.round_parts(act, g, op, read)

        @block.vector
        def _(dve):
            core.rest_input(dve, op)

            def read(b, banks, s):
                dve.wait_ge(silu_ready, b + 1)
                nc.vector.tensor_tensor(core.p[:, b, :], core.scr[:, s, :], banks[1], ALU.mult).then_inc(core.acc_free, 1)
            core.drain(dve, g, read)
    core.end_product(g, op)


def residual_stage(core, name, scale, op, squares=lambda core: core.p[:, 50:52, :]):
    nc, g = core.nc, core.gemms[name]
    mb = g.cols // P
    total, square = core.rstd[:, :], squares(core)
    added = core.sem(f"{name}_added")
    per = 1 + mb
    with nc.Block(no_gpsimd_drain=True) as block:
        @block.sync
        def _(sp):
            core.stream(sp, g)

        @block.gpsimd
        def _(pool):
            core.rest_weights(pool, g)

        @block.tensor
        def _(pe):
            core.product(pe, g, op)

        @block.scalar
        def _(act):
            core.round_parts(act, g, op)

        @block.vector
        def _(dve):
            nc.vector.memset(total, 0.0).then_inc(added, 1)
            core.rest_input(dve, op)

            def read(b, banks, s):
                for m in range(mb):
                    xc = core.x[:, b * mb + m, :]
                    ins = nc.vector.scalar_tensor_tensor(out=xc, in0=banks[m], scalar=scale, in1=xc, op0=ALU.mult, op1=ALU.add)
                ins.then_inc(core.acc_free, 1)
                dve.wait_ge(core.acc_free, core.blocks_read + b + 1)
                for m in range(mb):
                    xc = core.x[:, b * mb + m, :]
                    ins = nc.vector.tensor_tensor(square[:, m, :], xc, xc, ALU.mult)
                ins.then_inc(added, 1)
                for m in range(mb):
                    dve.wait_ge(added, per * b + m + 2)
                    nc.vector.tensor_tensor(total, total, square[:, m, :], ALU.add).then_inc(added, 1)
            core.drain(dve, g, read)
    core.end_product(g, op)


def project_stage(core, name, at=0, func=ACT.Copy, norm=None, meanwhile=None, consts=None):
    nc, g = core.nc, core.gemms[name]
    fresh = norm is not None
    op = Operand(core, DC, lambda m, k: m.h[:, k, :], lambda m, k: m.scr[:, k, :], source=norm)
    mb = g.cols // P
    with nc.Block(no_gpsimd_drain=True) as block:
        @block.sync
        def _(sp):
            if consts is not None:
                core.next_consts(sp, consts)
            core.stream(sp, g)
            if consts is not None:
                sp.wait_ge(core.consts_in, core.const_loads)

        @block.gpsimd
        def _(pool):
            core.rest_weights(pool, g)

        @block.tensor
        def _(pe):
            core.product(pe, g, op, fresh)

        @block.vector
        def _(dve):
            if fresh:
                core.rest_input(dve, op)
            if meanwhile is not None:
                meanwhile(dve)

        @block.scalar
        def _(act):
            def read(b, banks, s):
                if g.by_token:
                    to = core.p[:, bass.ds(at + b * mb, mb), :].rearrange("p a (n c) -> p (a n) c", c=g.cols)
                    nc.scalar.activation(to, core.acc[:, s * g.mb:(s + 1) * g.mb, 0:g.cols], func).then_inc(core.acc_free, 1)
                    return
                for m in range(mb):
                    ins = nc.scalar.activation(core.p[:, at + b * mb + m, :], banks[m], func)
                ins.then_inc(core.acc_free, 1)
            core.round_parts(act, g, op if fresh else None, read)
    core.end_product(g, op, fresh)


def token_shift(core, dve):
    nc, p = core.nc, core.p
    mine = Steps(dve, core.sem("shift_step"))
    diff = [p[:, 50 + j, :] for j in range(2)]
    drained = core.blocks_read
    with dve.Fori(0, 7) as b:
        mine.loop(b, 2)
        dve.wait_ge(core.acc_free, b + drained + 1)
        for j in range(2):
            c = 2 * b + j
            nc.vector.tensor_scalar(diff[j][:, 0:1], p[:, c, 0:1], -1.0, None, ALU.mult)
            ins = nc.vector.tensor_tensor(diff[j][:, 1:T], p[:, c, 0:T - 1], p[:, c, 1:T], ALU.subtract)
        mine.then(ins)
        for j in range(2):
            c = 2 * b + j
            ins = nc.vector.scalar_tensor_tensor(out=p[:, c, :], in0=diff[j], scalar=core.vcol("shift_mix", c),
                                                 in1=p[:, c, :], op0=ALU.mult, op1=ALU.add)
        mine.then(ins)
    mine.end(7)


def rwkv_lora_stage(core):
    nc, p, scr, h, acc = core.nc, core.p, core.scr, core.h, core.acc
    act_in, done, read, lora_loaded, zeroed = (core.sem(f"rw_{s}") for s in (
        "lora_act", "lora_mm", "lora_read", "lora_loaded", "zeroed"))
    lora = p[:, 40:43, :]
    bd_zero = p[:, RW_BD:RW_BD + 12, :]
    with nc.Block(no_gpsimd_drain=True) as block:
        @block.sync
        def _(sp):
            sp.dma_start(lora, core.dram["lora"]).then_inc(lora_loaded, 16)

        @block.gpsimd
        def _(pool):
            nc.gpsimd.memset(bd_zero, 0.0).then_inc(zeroed, 1)
            pool.wait_ge(zeroed, 1)

        @block.scalar
        def _(act):
            nc.scalar.activation(scr[:, 6, :], p[:, LORA_W, :], ACT.Tanh)
            nc.scalar.activation(scr[:, 7, :], p[:, LORA_G, :], ACT.Sigmoid).then_inc(act_in, 1)
            act.wait_ge(done, 1)
            for c in range(PAIRS):
                nc.scalar.activation(scr[:, c, :], acc[:, c, :], ACT.Sigmoid, bias=core.vcol("w0", c)).then_inc(read, 1)
            for c in range(PAIRS):
                nc.scalar.activation(h[:, 4 + c, :], acc[:, 4 + c, :], ACT.Sigmoid, bias=core.vcol("a0", c))
            act.wait_ge(done, 2)
            for c in range(PAIRS):
                nc.scalar.activation(h[:, c, :], acc[:, c, :], ACT.Copy)

        @block.tensor
        def _(pe):
            pe.wait_ge(lora_loaded, 16)
            pe.wait_ge(act_in, 1)
            for c in range(PAIRS):
                pe.matmul(acc[:, c, :], lora[:, 0, c * P:(c + 1) * P], scr[:, 6, :], start=True, stop=True)
            for c in range(PAIRS):
                mm = pe.matmul(acc[:, 4 + c, :], lora[:, 1, c * P:(c + 1) * P], p[:, LORA_W, :], start=True, stop=True)
            mm.then_inc(done, 1)
            for c in range(PAIRS):
                pe.wait_ge(read, c + 1)
                mm = pe.matmul(acc[:, c, :], lora[:, 2, c * P:(c + 1) * P], scr[:, 7, :], start=True, stop=True)
            mm.then_inc(done, 1)


RW_BD = 20
RW_STEPS = 15


def rwkv_stage(core):
    nc, p, scr, h, acc = core.nc, core.p, core.scr, core.h, core.acc
    names = ("step", "cs", "exps", "sq", "sqsum", "inv", "root", "rates", "bd_pool", "bd_act", "bd", "bonus_in", "bonus_sum", "bonus_read", "unit1", "unit2",
             "a_read", "u1_read", "u2_read", "atn", "y", "y_read", "z", "z_read", "gt_read", "vst", "vst_read",
             "w", "w_neg", "sa", "sa_read", "s", "s_new", "o", "var", "std", "obd", "ot")
    q = {s: core.sem(f"rw_{s}") for s in names}
    C = lambda n: core.const(1, n)
    two = lambda a: p[:, a:a + 2, :].rearrange("p a (b c) -> p (a b) c", c=P)
    bdb, bdkk, bdk, bdr, bdv, obd = (two(RW_BD + 2 * n) for n in range(6))
    et, gt, ft, at, tm, tt, btok, ktok = (two(RW_BD + 12 + 2 * n) for n in range(8))
    ym, atn = bdb, bdk
    vst = p[:, RW_BD + 28, :].rearrange("p (c v) -> p c v", v=HEAD)
    t8, t9, tq = (p[:, RW_BD + 29 + n, :] for n in range(3))
    e1, e2, e3 = (p[:, RW_BD + 18 + n, :] for n in range(3))
    t4, t5, t6, t7 = (scr[:, n, :] for n in range(4, 8))
    chunks = lambda a: a.rearrange("p (c t) -> p c t", t=LC)
    small = core.small
    pend, wneg, sas = small[:, 0:8], small[:, 128:192], small[:, 192:256]
    state, decayed = (small[:, 64:128], core.rstd[:, 0:HEAD]), core.rstd[:, HEAD:2 * HEAD]
    s1, s2 = small[:, 16:24], small[:, 24:32]
    bank2 = lambda b: acc[:, b:b + 2, :].rearrange("p a (b c) -> p (a b) c", c=P)
    half = lambda m, k: m[:, 4 * k:4 * k + 4, :]
    rep = lambda m: m.unsqueeze(1).to_broadcast([P, 4, P])
    heads = [slice(j * HEAD, (j + 1) * HEAD) for j in range(2)]
    block_of = lambda m, j: m[heads[j], :, j * LC:(j + 1) * LC]
    LEVELS = (2, 4, 8, 16, 32)
    NL = len(LEVELS)
    eye = core.eye[:, :]
    LAST = PAIRS - 1

    def over_pairs(eng, body, mine=None, per=0):
        body(0, True, False)
        with eng.Fori(1, LAST) as i:
            if mine is not None:
                mine.loop(i - 1, per)
            body(i, False, False)
        if mine is not None:
            mine.end(LAST - 1)
        body(LAST, False, True)

    with nc.Block(no_gpsimd_drain=True) as block:
        @block.vector
        def _(dve):
            v = nc.vector
            mine = Steps(dve, q["step"])

            def prepare(i):
                r, k, a, sig = p[:, i, :], p[:, 4 + i, :], h[:, 4 + i, :], scr[:, i, :]

                def norms_and_sums():
                    v.tensor_scalar(t6, k, core.vcol("k_k", i), None, ALU.mult).then_inc(q["sq"], 1)
                    mine.then(v.tensor_tensor_scan(t4, C("resets"), sig, 0.0, ALU.mult, ALU.add))

                def sums_before():
                    v.tensor_tensor(t5, t4, sig, ALU.subtract).then_inc(q["cs"], 1)
                    mine.then(v.tensor_scalar(t8, a, -1.0, core.vcol("k_a", i), ALU.add, ALU.mult))

                def keys():
                    v.tensor_scalar(t9, r, core.vcol("r_k", i), None, ALU.mult)
                    mine.then(v.scalar_tensor_tensor(out=t8, in0=t8, scalar=1.0, in1=k, op0=ALU.add, op1=ALU.mult))

                def bonus():
                    v.tensor_tensor(t9, t9, t8, ALU.mult).then_inc(q["bonus_in"], 1)
                    dve.wait_ge(q["sqsum"], i + 1)
                    mine.then(v.tensor_scalar(tq, acc[:, 6, :], 1e-24, None, ALU.max))

                def inverse():
                    v.reciprocal(tq, tq).then_inc(q["inv"], 1)

                def unit_keys():
                    dve.wait_ge(q["root"], i + 1)
                    dve.wait_ge(q["exps"], i + 1)
                    mine.then(v.tensor_tensor(t6, t6, tq, ALU.mult))

                def rates():
                    v.tensor_tensor(t5, t6, a, ALU.mult).then_inc(q["rates"], 1)

                return norms_and_sums, sums_before, keys, bonus, inverse, unit_keys, rates

            def operands(i):
                r = p[:, i, :]
                dve.wait_ge(q["exps"], i + 1)
                v.tensor_copy(pend, chunks(e1)[:, :, LC - 1:LC].rearrange("p c o -> p (c o)"))
                for j in range(2):
                    v.tensor_tensor(block_of(bdkk, j), chunks(t6)[heads[j]], chunks(e3)[heads[j]], ALU.mult)
                    ins = v.tensor_tensor(block_of(bdr, j), chunks(r)[heads[j]], chunks(e1)[heads[j]], ALU.mult)
                ins.then_inc(q["bd"], 1)

            def normalise(i):
                ob = chunks(acc[:, 7, :])
                col = lambda x: x.unsqueeze(2).to_broadcast([P, NLC, HEAD])
                dve.wait_ge(q["o"], i + 1)
                mine.then(v.tensor_reduce(s1, ob, AX.X, ALU.add))
                mine.then(v.tensor_scalar(s1, s1, 1.0 / HEAD, None, ALU.mult))
                mine.then(v.tensor_tensor(chunks(t5), ob, col(s1), ALU.subtract))
                mine.then(v.tensor_tensor(t6, t5, t5, ALU.mult))
                mine.then(v.tensor_reduce(s2, chunks(t6), AX.X, ALU.add))
                mine.then(v.tensor_scalar(s2, s2, 1.0 / HEAD, 64e-5, ALU.mult, ALU.add))
                v.reciprocal(s2, s2).then_inc(q["var"], 1)
                dve.wait_ge(q["std"], i + 1)
                for j in range(2):
                    ins = v.tensor_tensor(block_of(obd, j), chunks(t5)[heads[j]], col(s2)[heads[j]], ALU.mult)
                ins.then_inc(q["obd"], 1)

            def gate(i):
                dve.wait_ge(q["ot"], i + 1)
                mine.then(v.tensor_scalar(t4, acc[:, 5, :], core.vcol("ln_w", i), core.vcol("ln_b", i), ALU.mult, ALU.add))
                mine.then(v.tensor_tensor(t4, t4, t7, ALU.add))
                mine.then(v.tensor_tensor(h[:, i, :], t4, h[:, i, :], ALU.mult))

            def pair(i, first, last):
                if not first:
                    dve.wait_ge(q["bd_pool"], i + 1)
                    normalise(i - 1)
                dve.wait_ge(q["unit1"], i + 1)
                for k2 in range(2):
                    v.tensor_copy(half(at, k2), half(bank2(0), k2))
                    v.scalar_tensor_tensor(out=half(tm, k2), in0=half(bank2(2), k2), scalar=-1.0, in1=rep(C("level1_ts")), op0=ALU.mult, op1=ALU.mult)
                    ins = v.tensor_tensor(half(et, k2), half(bank2(4), k2), rep(C("upto")), ALU.mult)
                ins.then_inc(q["u1_read"], 1)
                dve.wait_ge(q["u1_read"], 2 * i + 1)
                for k2 in range(2):
                    v.scalar_tensor_tensor(out=half(tt, k2), in0=half(at, k2), scalar=-1.0, in1=rep(C("level1")), op0=ALU.mult, op1=ALU.mult)
                    ins = v.tensor_tensor(half(tm, k2), half(tm, k2), rep(eye), ALU.add)
                mine.then(ins)
                for k2 in range(2):
                    ins = v.tensor_tensor(half(tt, k2), half(tt, k2), rep(eye), ALU.add)
                ins.then_inc(q["u1_read"], 1)
                if not first:
                    gate(i - 1)
                dve.wait_ge(q["bonus_sum"], i + 1)
                v.tensor_tensor(t7, acc[:, 6, :], p[:, 8 + i, :], ALU.mult).then_inc(q["bonus_read"], 1)
                dve.wait_ge(q["unit2"], i + 1)
                for k2 in range(2):
                    v.tensor_tensor(half(gt, k2), half(bank2(2), k2), rep(C("strict")), ALU.mult)
                    ins = v.tensor_tensor(half(ft, k2), half(bank2(0), k2), rep(C("upto")), ALU.mult)
                ins.then_inc(q["gt_read"], 1)
                for n in range(NL):
                    for k2 in range(2):
                        dve.wait_ge(q["z"], i * (2 * NL) + 2 * n + k2 + 1)
                        if n < NL - 1:
                            v.tensor_tensor(half(tm, k2), half(tm, k2), half(bank2(2), k2), ALU.subtract)
                        ins = v.tensor_tensor(half(tt, k2), half(tt, k2), half(bank2(4), k2), ALU.subtract)
                        ins.then_inc(q["z_read"], 1)
                parts = () if last else prepare(i + 1)
                dve.wait_ge(q["z_read"], (i + 1) * (2 * NL))
                for c in range(NLC):
                    dve.wait_ge(q["w"], i * NLC + c + 1)
                    v.tensor_scalar(wneg, acc[:, 2, 0:HEAD], -1.0, None, ALU.mult).then_inc(q["w_neg"], 1)
                    if 0 < c < NLC - 1:
                        v.tensor_scalar(decayed, state[c % 2], pend[:, c:c + 1], None, ALU.mult)
                    dve.wait_ge(q["sa"], i * NLC + c + 1)
                    v.tensor_copy(sas, acc[:, 3, 0:HEAD]).then_inc(q["sa_read"], 1)
                    if c < NLC - 1:
                        dve.wait_ge(q["sa_read"], i * NLC + c + 1)
                        dve.wait_ge(q["s"], i * (NLC - 1) + c + 1)
                        if c:
                            v.scalar_tensor_tensor(out=state[(c + 1) % 2], in0=acc[:, 4, 0:HEAD], scalar=pend[:, c:c + 1], in1=decayed,
                                                   op0=ALU.mult, op1=ALU.add).then_inc(q["s_new"], 1)
                        else:
                            v.tensor_scalar(state[1], acc[:, 4, 0:HEAD], pend[:, 0:1], None, ALU.mult).then_inc(q["s_new"], 1)
                        dve.wait_ge(q["s_new"], i * (NLC - 1) + c + 1)
                    if c < len(parts):
                        parts[c]()
                if not last:
                    operands(i + 1)

            for part in prepare(0):
                part()
            operands(0)
            over_pairs(dve, pair, mine, RW_STEPS)
            normalise(LAST)
            gate(LAST)

        @block.scalar
        def _(act):
            s = nc.scalar

            def prepare(i):
                act.wait_ge(q["sq"], i + 1)
                s.activation(tq, t6, ACT.Square).then_inc(q["a_read"], 1)
                act.wait_ge(q["cs"], i + 1)
                s.activation(e1, t4, ACT.Exp, scale=-DECAY_RATE)
                s.activation(e2, t4, ACT.Exp, scale=DECAY_RATE)
                s.activation(e3, t5, ACT.Exp, scale=-DECAY_RATE).then_inc(q["exps"], 1)
                for j in range(2):
                    ins = s.activation(block_of(bdv, j), chunks(p[:, 8 + i, :])[heads[j]], ACT.Copy)
                ins.then_inc(q["bd_act"], 1)
                act.wait_ge(q["inv"], i + 1)
                s.activation(tq, tq, ACT.Sqrt).then_inc(q["root"], 1)

            def deviations(i):
                act.wait_ge(q["var"], i + 1)
                s.activation(s2, s2, ACT.Sqrt).then_inc(q["std"], 1)

            def pair(i, first, last):
                if not first:
                    deviations(i - 1)
                act.wait_ge(q["unit2"], i + 1)
                for k2 in range(2):
                    s.activation(half(btok, k2), half(bank2(6), k2), ACT.Copy)
                    s.activation(half(ktok, k2), half(bank2(4), k2), ACT.Copy).then_inc(q["u2_read"], 1)
                act.wait_ge(q["vst"], i + 1)
                s.activation(vst, acc[:, 7, :].rearrange("p (c v) -> p c v", v=HEAD), ACT.Copy).then_inc(q["vst_read"], 1)
                for n in range(NL):
                    for k2 in range(2):
                        act.wait_ge(q["y"], i * (2 * NL) + 2 * n + k2 + 1)
                        s.activation(half(ym, k2), half(bank2(0), k2), ACT.Copy).then_inc(q["y_read"], 1)
                if not last:
                    act.wait_ge(q["z"], (i + 1) * (2 * NL))
                    prepare(i + 1)

            prepare(0)
            over_pairs(act, pair)
            deviations(LAST)

        @block.gpsimd
        def _(pool):
            def prepare(i):
                pool.wait_ge(q["rates"], i + 1)
                pool.wait_ge(q["exps"], i + 1)
                for j in range(2):
                    nc.gpsimd.tensor_tensor(block_of(bdb, j), chunks(t5)[heads[j]], chunks(e2)[heads[j]], ALU.mult)
                    ins = nc.gpsimd.tensor_tensor(block_of(bdk, j), chunks(t8)[heads[j]], chunks(e2)[heads[j]], ALU.mult)
                ins.then_inc(q["bd_pool"], 1)

            def pair(i, first, last):
                pool.wait_ge(q["u1_read"], 2 * i + 1)
                pool.wait_ge(q["unit2"], i + 1)
                for n, level in enumerate(LEVELS):
                    for k2 in range(2):
                        if n:
                            pool.wait_ge(q["y"], i * (2 * NL) + 2 * (n - 1) + k2 + 1)
                        nc.gpsimd.tensor_tensor(half(atn, k2), half(at, k2), rep(C(f"level{level}")), ALU.mult).then_inc(q["atn"], 1)
                if not last:
                    pool.wait_ge(q["z"], (i + 1) * (2 * NL))
                    prepare(i + 1)

            prepare(0)
            over_pairs(pool, pair)

        @block.tensor
        def _(pe):
            mm = pe.matmul

            def square_sums(i):
                pe.wait_ge(q["a_read"], i + 1)
                mm(acc[:, 6, :], C("head_ones"), tq, start=True, stop=True).then_inc(q["sqsum"], 1)

            def bonus_sums(i):
                pe.wait_ge(q["bonus_in"], i + 1)
                pe.wait_ge(q["inv"], i + 1)
                mm(acc[:, 6, :], C("head_ones"), t9, start=True, stop=True).then_inc(q["bonus_sum"], 1)

            def turn_back(i):
                pe.wait_ge(q["obd"], i + 1)
                for c in range(NLC):
                    ins = mm(acc[:, 5, c * LC:(c + 1) * LC], obd[:, c, :], C("stacked_eye"), start=True, stop=True)
                ins.then_inc(q["ot"], 1)

            def pair(i, first, last):
                pe.wait_ge(q["bd"], i + 1)
                pe.wait_ge(q["bd_pool"], i + 1)
                for c in range(NLC):
                    mm(bank2(0)[:, c, :], bdb[:, c, :], bdkk[:, c, :], start=True, stop=True)
                    mm(bank2(2)[:, c, :], bdkk[:, c, :], bdb[:, c, :], start=True, stop=True)
                    ins = mm(bank2(4)[:, c, :], bdb[:, c, :], bdr[:, c, :], start=True, stop=True)
                ins.then_inc(q["unit1"], 1)
                pe.wait_ge(q["u1_read"], 2 * i + 1)
                if not first:
                    turn_back(i - 1)
                for c in range(NLC):
                    mm(bank2(2)[:, c, :], bdk[:, c, :], bdkk[:, c, :], start=True, stop=True)
                    ins = mm(bank2(0)[:, c, :], bdk[:, c, :], bdr[:, c, :], start=True, stop=True)
                pe.wait_ge(q["bonus_read"], i + 1)
                for c in range(NLC):
                    pe.transpose(bank2(6)[:, c, :], bdb[:, c, :], eye)
                    ins = pe.transpose(bank2(4)[:, c, :], bdk[:, c, :], eye)
                ins.then_inc(q["unit2"], 1)
                pe.wait_ge(q["gt_read"], i + 1)
                pe.wait_ge(q["u2_read"], 2 * i + 2)
                pe.wait_ge(q["bd_act"], i + 1)
                for c in range(NLC):
                    ins = mm(acc[:, 7, c * HEAD:(c + 1) * HEAD], bdv[:, c, :], C("stacked_eye"), start=True, stop=True)
                ins.then_inc(q["vst"], 1)
                pe.wait_ge(q["u1_read"], 2 * i + 2)
                for n in range(NL):
                    for k2 in range(2):
                        at_ = i * (2 * NL) + 2 * n + k2
                        pe.wait_ge(q["atn"], at_ + 1)
                        if n:
                            pe.wait_ge(q["z_read"], i * (2 * NL) + 2 * (n - 1) + k2 + 1)
                        for c in range(4 * k2, 4 * k2 + 4):
                            ins = mm(bank2(0)[:, c, :], atn[:, c, :], tm[:, c, :], start=True, stop=True)
                        ins.then_inc(q["y"], 1)
                    for k2 in range(2):
                        pe.wait_ge(q["y_read"], i * (2 * NL) + 2 * n + k2 + 1)
                        for c in range(4 * k2, 4 * k2 + 4):
                            if n < NL - 1:
                                mm(bank2(2)[:, c, :], tt[:, c, :], ym[:, c, :], start=True, stop=True)
                            ins = mm(bank2(4)[:, c, :], ym[:, c, :], tt[:, c, :], start=True, stop=True)
                        ins.then_inc(q["z"], 1)
                pe.wait_ge(q["z_read"], (i + 1) * (2 * NL))
                pe.wait_ge(q["vst_read"], i + 1)
                mm(acc[:, 2, 0:HEAD], gt[:, 0, :], vst[:, 0, :], start=True, stop=True).then_inc(q["w"], 1)
                for c in range(NLC):
                    s_now, o = state[c % 2], acc[:, 7, c * HEAD:(c + 1) * HEAD]
                    if c:
                        pe.wait_ge(q["s_new"], i * (NLC - 1) + c)
                        mm(acc[:, 2, 0:HEAD], bdkk[:, c, :], s_now, start=False, stop=True).then_inc(q["w"], 1)
                        mm(o, bdr[:, c, :], s_now, start=True, stop=False)
                    mm(o, ft[:, c, :], vst[:, c, :], start=(c == 0), stop=False)
                    if c < NLC - 1:
                        mm(acc[:, 4, 0:HEAD], ktok[:, c, :], vst[:, c, :], start=True, stop=False)
                    pe.wait_ge(q["w_neg"], i * NLC + c + 1)
                    mm(acc[:, 3, 0:HEAD], tt[:, c, :], wneg, start=True, stop=True).then_inc(q["sa"], 1)
                    if c < NLC - 1:
                        mm(acc[:, 2, 0:HEAD], gt[:, c + 1, :], vst[:, c + 1, :], start=True, stop=False)
                    pe.wait_ge(q["sa_read"], i * NLC + c + 1)
                    if c < NLC - 1:
                        mm(acc[:, 4, 0:HEAD], btok[:, c, :], sas, start=False, stop=True).then_inc(q["s"], 1)
                    ins = mm(o, et[:, c, :], sas, start=False, stop=True)
                    if not last and c == 2:
                        square_sums(i + 1)
                ins.then_inc(q["o"], 1)
                if not last:
                    bonus_sums(i + 1)

            square_sums(0)
            bonus_sums(0)
            over_pairs(pe, pair)
            turn_back(LAST)


def attention_stage(core):
    nc, p, h, acc, small = core.nc, core.p, core.h, core.acc, core.small
    names = ("step", "biased", "mm0", "kd_read", "q_ready", "scores", "masked", "max", "exp", "pt", "pt_read", "o",
             "o_ready", "ot", "ot_read")
    q = {s: core.sem(f"at_{s}") for s in names}
    C = lambda n: core.const(1, n)
    kdup = p[:, 20:23, :].rearrange("p a t -> p (a t)")[:, 0:2 * (AB + T)].rearrange("p (g t) -> p g t", g=2)
    vtok = p[:, 23:25, :].rearrange("p a t -> p (a t)")[:, 0:5 * AB].rearrange("p (n d) -> p n d", d=AB)
    qz = p[:, 26:28, :].rearrange("p a (h t) -> p (a h) t", t=AB)
    scs = [p[:, a:a + 4, :].rearrange("p a (h t) -> p (a h) t", t=2 * AB) for a in (28, 37)]
    pt = p[:, 32:36, :].rearrange("p a (h t) -> p (a h) t", t=AB)
    otok = p[:, 36, :]
    sinks = small[:, 0:8]
    mxs, nmxs, rss, ess = ([small[:, 16 * n + 8 * b:16 * n + 8 * b + 8] for b in range(2)] for n in range(1, 5))
    pairs2 = lambda b: acc[:, b, :].rearrange("p (h t) -> p h t", t=2 * AB)
    with nc.Block(no_gpsimd_drain=True) as block:
        sinks_in = core.sem("at_sinks")

        @block.sync
        def _(sp):
            sp.dma_start(sinks, core.dram["sinks"].partition_broadcast(P)).then_inc(sinks_in, 16)
            sp.wait_ge(sinks_in, 16)

        @block.gpsimd
        def _(pool):
            nc.gpsimd.memset(kdup[:, :, 0:AB], 0.0)
            nc.gpsimd.memset(vtok[:, 0, :], 0.0)
            nc.gpsimd.memset(qz, 0.0).then_inc(q["biased"], 1)
            pool.wait_ge(q["biased"], 1)
            pool.wait_ge(q["step"], 1)
            for n in range(NAB):
                if n:
                    pool.wait_ge(q["scores"], n)
                for hd in range(Q_HEADS):
                    rows = slice(hd % 2 * HEAD, hd % 2 * HEAD + HEAD)
                    ins = nc.gpsimd.tensor_copy(qz[rows, hd, :], p[rows, ATT_Q + hd // 2, n * AB:(n + 1) * AB])
                ins.then_inc(q["q_ready"], 1)

        @block.vector
        def _(dve):
            v = nc.vector
            mine = Steps(dve, q["step"])
            for c in range(4):
                v.tensor_scalar(p[:, ATT_Q + c, :], p[:, ATT_Q + c, :], core.vcol("b_in_attn", c), HEAD ** -0.5, ALU.add, ALU.mult)
            for c in (4, 5):
                ins = v.tensor_scalar(p[:, ATT_Q + c, :], p[:, ATT_Q + c, :], core.vcol("b_in_attn", c), None, ALU.add)
            mine.then(ins)
            dve.wait_ge(q["mm0"], 1)
            for g in range(2):
                v.tensor_copy(kdup[:, g, AB:AB + T], acc[:, g, :])
            v.tensor_copy(vtok[:, 1:5, :], acc[:, 2, :].rearrange("p (n d) -> p n d", d=AB)).then_inc(q["kd_read"], 1)
            dve.wait_ge(sinks_in, 16)
            def front(n):
                sc, mx, nmx, es = scs[n % 2], mxs[n % 2], nmxs[n % 2], ess[n % 2]
                dve.wait_ge(q["scores"], n + 1)
                band = C(f"band{n}").unsqueeze(1).to_broadcast([P, 2, 2 * AB])
                for b in range(4):
                    ins = v.tensor_tensor(sc[:, 2 * b:2 * b + 2, :], pairs2(b), band, ALU.add)
                ins.then_inc(q["masked"], 1)
                dve.wait_ge(q["masked"], n + 1)
                mine.then(v.tensor_reduce(mx, sc, AX.X, ALU.max))
                mine.then(v.tensor_tensor(mx, mx, sinks, ALU.max))
                mine.then(v.tensor_tensor(es, sinks, mx, ALU.subtract))
                v.tensor_scalar(nmx, mx, -1.0, None, ALU.mult).then_inc(q["max"], 1)

            def back(n):
                rs, es = rss[n % 2], ess[n % 2]
                dve.wait_ge(q["exp"], n + 1)
                mine.then(v.tensor_tensor(rs, rs, es, ALU.add))
                mine.then(v.reciprocal(rs, rs))
                dve.wait_ge(q["o"], n + 1)
                v.tensor_tensor(otok.rearrange("p (a d) -> p a d", d=HEAD), acc[:, 4, :].rearrange("p (a d) -> p a d", d=HEAD),
                                rs.unsqueeze(2).to_broadcast([P, Q_HEADS, HEAD]), ALU.mult).then_inc(q["o_ready"], 1)
                dve.wait_ge(q["ot"], n + 1)
                v.tensor_copy(h[:, 4:8, n * AB:(n + 1) * AB], acc[:, 5, :].rearrange("p (c t) -> p c t", t=AB)).then_inc(q["ot_read"], 1)

            front(0)
            for n in range(NAB):
                if n + 1 < NAB:
                    front(n + 1)
                back(n)
            dve.wait_ge(q["ot_read"], NAB)

        @block.scalar
        def _(act):
            def turned(n):
                act.wait_ge(q["pt"], n + 1)
                for b in range(4):
                    ins = nc.scalar.activation(pt[:, 4 * b:4 * b + 4, :], acc[:, 4 + b, :].rearrange("p (a t) -> p a t", t=AB), ACT.Copy)
                ins.then_inc(q["pt_read"], 1)

            for n in range(NAB):
                sc, nmx, rs, es = scs[n % 2], nmxs[n % 2], rss[n % 2], ess[n % 2]
                if n:
                    turned(n - 1)
                act.wait_ge(q["max"], n + 1)
                for hd in range(Q_HEADS):
                    nc.scalar.activation(sc[:, hd, :], sc[:, hd, :], ACT.Exp, bias=nmx[:, hd:hd + 1], accum_out=rs[:, hd:hd + 1])
                nc.scalar.activation(es, es, ACT.Exp).then_inc(q["exp"], 1)
            turned(NAB - 1)

        @block.tensor
        def _(pe):
            pe.wait_ge(q["step"], 1)
            for g in range(2):
                pe.matmul(acc[:, g, :], C(f"dup{g}"), p[:, ATT_K, :], start=True, stop=True)
            for n in range(NAB):
                ins = pe.transpose(acc[:, 2, n * AB:(n + 1) * AB], p[:, ATT_V, n * AB:(n + 1) * AB], core.eye[:, :])
            ins.then_inc(q["mm0"], 1)
            pe.wait_ge(q["kd_read"], 1)

            def front(n):
                pe.wait_ge(q["q_ready"], n + 1)
                if n:
                    pe.wait_ge(q["masked"], n)
                for hd in range(Q_HEADS):
                    keys = kdup[:, hd // 4, n * AB:(n + 2) * AB]
                    ins = pe.matmul(pairs2(hd // 2)[:, hd % 2, :], qz[:, hd, :], keys, start=True, stop=True)
                ins.then_inc(q["scores"], 1)

            def back(n):
                pe.wait_ge(q["exp"], n + 1)
                if n:
                    pe.wait_ge(q["ot_read"], n)
                for hd in range(Q_HEADS):
                    for k in range(2):
                        m = 2 * hd + k
                        ins = pe.transpose(acc[:, 4 + m // 4, m % 4 * AB:(m % 4 + 1) * AB], scs[n % 2][:, hd, k * AB:(k + 1) * AB], core.eye[:, :])
                ins.then_inc(q["pt"], 1)
                pe.wait_ge(q["pt_read"], n + 1)
                for hd in range(Q_HEADS):
                    g = hd // 4
                    for k in range(2):
                        ins = pe.matmul(acc[:, 4, hd * HEAD:(hd + 1) * HEAD], pt[:, 2 * hd + k, :],
                                        vtok[:, n + k, g * HEAD:(g + 1) * HEAD], start=(k == 0), stop=(k == 1))
                ins.then_inc(q["o"], 1)
                pe.wait_ge(q["o_ready"], n + 1)
                for c in range(4):
                    ins = pe.transpose(acc[:, 5, c * AB:(c + 1) * AB], otok[:, c * AB:(c + 1) * AB], core.eye[:, :])
                ins.then_inc(q["ot"], 1)

            front(0)
            for n in range(NAB):
                if n + 1 < NAB:
                    front(n + 1)
                back(n)




def block1(core):
    swiglu_up_stage(core, "ffn1_up", Norm(core, ("norm_ffn1", 0), 1e-5))
    residual_stage(core, "ffn1_down", 0.5, Operand(core, FFC, lambda m, k: m.p[:, k, :], lambda m, k: m.p[:, FFC + k, :]))
    project_stage(core, "mix_in", norm=Norm(core, ("norm_mix", 0), 1e-5, after_residual=True), meanwhile=lambda dve: token_shift(core, dve))
    rwkv_lora_stage(core)
    rwkv_stage(core)
    attention_stage(core)
    residual_stage(core, "mix_out", 1.0, Operand(core, DC, lambda m, k: m.h[:, k, :], lambda m, k: m.scr[:, k, :]))
    swiglu_up_stage(core, "ffn2_up", Norm(core, ("norm_ffn2", 0), 1e-5, after_residual=True))
    residual_stage(core, "ffn2_down", 0.5, Operand(core, FFC, lambda m, k: m.p[:, k, :], lambda m, k: m.p[:, FFC + k, :]))


def softplus_steps(nc, mine, x, m, e, t, d, act_wait, act_signal, n):
    v = nc.vector
    mine.then(v.tensor_scalar(m, x, 0.0, None, ALU.max))
    mine.then(v.tensor_scalar(e, x, 0.0, None, ALU.min))
    ins = v.tensor_tensor(e, e, m, ALU.subtract)
    ins.then_inc(act_signal, 1)
    mine.eng.wait_ge(act_wait, 2 * n + 1)
    mine.then(v.tensor_scalar(t, e, 1.0, None, ALU.add))
    v.tensor_scalar(d, t, -1.0, None, ALU.add).then_inc(act_signal, 1)
    mine.eng.wait_ge(act_wait, 2 * n + 2)
    mine.then(v.scalar_tensor_tensor(out=t, in0=d, scalar=0.0, in1=t, op0=ALU.is_equal, op1=ALU.add))
    mine.then(v.scalar_tensor_tensor(out=d, in0=d, scalar=0.0, in1=d, op0=ALU.is_equal, op1=ALU.add))
    mine.then(v.reciprocal(d, d))
    mine.then(v.tensor_tensor(t, t, d, ALU.mult))
    mine.then(v.tensor_tensor(t, t, e, ALU.mult))
    mine.then(v.tensor_tensor(m, m, t, ALU.add))


SOFTPLUS_STEPS = 9


def softplus_act(nc, act, e, t, from_dve, to_dve, n):
    act.wait_ge(from_dve, 2 * n + 1)
    nc.scalar.activation(e, e, ACT.Exp).then_inc(to_dve, 1)
    act.wait_ge(from_dve, 2 * n + 2)
    nc.scalar.activation(t, t, ACT.Ln).then_inc(to_dve, 1)


HC = RNNC // 2


def rnn_convolution(core, dve):
    nc, p = core.nc, core.p
    v = nc.vector
    mine = Steps(dve, core.sem("rnn_conv"))
    out = [p[:, 50 + j, :] for j in range(2)]
    with dve.Fori(0, RNNC // 2) as i:
        mine.loop(i, CONV + 1)
        chunk = [2 * i + j for j in range(2)]
        wcol = lambda k, c: core.vcol("conv_w", k * RNNC + c)
        for o, c in zip(out, chunk):
            ins = v.tensor_scalar(o, p[:, c, :], wcol(CONV - 1, c), core.vcol("conv_b", c), ALU.mult, ALU.add)
        mine.then(ins)
        for k in range(CONV - 2, -1, -1):
            back = CONV - 1 - k
            for o, c in zip(out, chunk):
                ins = v.scalar_tensor_tensor(out=o[:, back:T], in0=p[:, c, 0:T - back], scalar=wcol(k, c),
                                             in1=o[:, back:T], op0=ALU.mult, op1=ALU.add)
            mine.then(ins)
        for o, c in zip(out, chunk):
            ins = v.tensor_scalar(p[:, c, :], o, 1.0, None, ALU.mult)
        mine.then(ins)
    mine.end(RNNC // 2)


def rnn_stage(core):
    nc, p, scr, h, acc, small = core.nc, core.p, core.scr, core.h, core.acc, core.small
    names = ("step", "sp_dve", "sp_act", "gates", "r", "i", "exped", "decay", "half", "root", "done")
    q = {s: core.sem(f"rnn_{s}") for s in names}
    at = const_columns(2)[1]
    lruw = core.cst[:, at:at + 2 * RNNC * P].rearrange("p (c g j) -> p c g j", g=2, j=P)
    x0 = small[:, 0:10]
    m, e, t, d = (small[:, 16 * n:16 * n + RNNC] for n in range(1, 5))
    coef = m
    ncoef = small[:, 80:90]
    xr = lambda i, c: p[:, i * HC + c, :]
    ix = lambda c: scr[:, c, :]
    decays = [h[:, 5, :], h[:, 6, :], h[:, 7, :], scr[:, 5, :], scr[:, 6, :]]
    with nc.Block(no_gpsimd_drain=True) as block:
        @block.vector
        def _(dve):
            v = nc.vector
            mine = Steps(dve, q["step"])
            mine.then(v.tensor_scalar(x0, core.vec[:, VEC_AT["lru_lambda"]:VEC_AT["lru_lambda"] + RNNC], -1.0, None, ALU.mult))
            softplus_steps(nc, mine, x0, m, e, t, d, q["sp_act"], q["sp_dve"], 0)
            v.tensor_scalar(ncoef, m, 8.0, None, ALU.mult)
            mine.then(v.tensor_scalar(coef, m, -8.0, None, ALU.mult))
            for i in range(2):
                for c in range(HC):
                    dve.wait_ge(q["i"], i * HC + c + 1)
                    mine.then(v.tensor_tensor(ix(c), ix(c), xr(i, c), ALU.mult))
                tanh5 = h[:, 0:HC, :]
                den5 = p[:, i * HC:(i + 1) * HC, :]
                for c in range(HC):
                    dve.wait_ge(q["decay"], i * HC + c + 1)
                    mine.then(v.tensor_scalar(den5[:, c, :], tanh5[:, c, :], 1.0, None, ALU.add))
                    ins = v.reciprocal(den5[:, c, :], den5[:, c, :])
                mine.then(ins)
                mine.then(v.tensor_tensor(den5, den5, tanh5, ALU.mult))
                v.tensor_scalar(den5, den5, 1e-34, None, ALU.max).then_inc(q["half"], 1)
                dve.wait_ge(q["root"], i + 1)
                for c in range(HC):
                    ins = v.tensor_tensor(ix(c), ix(c), den5[:, c, :], ALU.mult)
                mine.then(ins)
                for c in range(HC):
                    mine.then(v.tensor_tensor_scan(ix(c), decays[c], ix(c), 0.0, ALU.mult, ALU.add))
                ins = v.tensor_tensor(den5, scr[:, 0:HC, :], p[:, RNNC + i * HC:RNNC + (i + 1) * HC, :], ALU.mult)
                ins.then_inc(q["done"], 1)

        @block.scalar
        def _(act):
            s = nc.scalar
            softplus_act(nc, act, e, t, q["sp_dve"], q["sp_act"], 0)
            for i in range(2):
                if i:
                    act.wait_ge(q["done"], i)
                for c in range(HC):
                    act.wait_ge(q["gates"], i * HC + c + 1)
                    s.activation(h[:, c, :], acc[:, 2 * c % 8, :], ACT.Sigmoid, bias=core.vcol("lru_b_a", i * HC + c)).then_inc(q["r"], 1)
                    s.activation(ix(c), acc[:, (2 * c + 1) % 8, :], ACT.Sigmoid, bias=core.vcol("lru_b_x", i * HC + c)).then_inc(q["i"], 1)
                act.wait_ge(q["r"], i * HC + HC)
                if i == 0:
                    act.wait_ge(q["step"], SOFTPLUS_STEPS + 2)
                for c in range(HC):
                    ins = s.activation(decays[c], h[:, c, :], ACT.Exp, scale=coef_at(core, 16, i * HC + c))
                ins.then_inc(q["exped"], 1)
                act.wait_ge(q["exped"], i + 1)
                for c in range(HC):
                    s.activation(h[:, c, :], h[:, c, :], ACT.Tanh, scale=coef_at(core, 80, i * HC + c)).then_inc(q["decay"], 1)
                act.wait_ge(q["half"], i + 1)
                s.activation(p[:, i * HC:(i + 1) * HC, :], p[:, i * HC:(i + 1) * HC, :], ACT.Sqrt, scale=2.0).then_inc(q["root"], 1)

        @block.tensor
        def _(pe):
            for i in range(2):
                if i:
                    pe.wait_ge(q["i"], HC)
                for c in range(HC):
                    w = lruw[:, i * HC + c]
                    if c == HC - 1:
                        pe.wait_ge(q["i"], i * HC + 1)
                    pe.matmul(acc[:, 2 * c % 8, :], w[:, 0, :], xr(i, c), start=True, stop=True)
                    pe.matmul(acc[:, (2 * c + 1) % 8, :], w[:, 1, :], xr(i, c), start=True, stop=True).then_inc(q["gates"], 1)


def coef_at(core, at, c):
    return core.small[:, bass.ds(at + c, 1)]


def sgu_stage(core):
    nc, p, scr, h, acc = core.nc, core.p, core.scr, core.h, core.acc
    names = ("step", "loaded", "sum", "sq", "sum2", "inv", "rstd", "gained", "normed", "turned", "turned_read", "mixed", "mixed_read", "masked")
    q = {s: core.sem(f"sgu_{s}") for s in names}
    V, U = 28, 20
    wt = core.cst[:, 2688:2688 + SGU_G * P].rearrange("p (g t) -> p g t", t=P)
    bias = scr[:, 0:2, :].rearrange("p a (g t) -> p (a g) t", t=P)
    mean = scr[:, 2, :]
    vt = h[:, :, :].rearrange("p (n a) t -> p n (a t)", n=4)
    blocks = lambda a: a.rearrange("p (n t) -> p n t", t=P)
    with nc.Block(no_gpsimd_drain=True) as block:
        @block.sync
        def _(sp):
            sp.dma_start(wt, core.dram["sgu_w"]).then_inc(q["loaded"], 16)
            sp.dma_start(scr[:, 0:2, :].rearrange("p a t -> p (a t)"), core.dram["sgu_b"].partition_broadcast(P)).then_inc(q["loaded"], 16)

        @block.gpsimd
        def _(pool):
            pool.wait_ge(q["loaded"], 32)
            nc.gpsimd.tensor_tensor(wt, wt, core.const(2, "sgu_mask").unsqueeze(1).to_broadcast([P, SGU_G, P]), ALU.mult).then_inc(q["masked"], 1)

        @block.vector
        def _(dve):
            v = nc.vector
            mine = Steps(dve, q["step"])
            dve.wait_ge(q["sum"], 1)
            mine.then(v.tensor_scalar(mean, acc[:, 0, :], 1.0 / D, None, ALU.mult))
            for c in range(DC):
                v.tensor_tensor(p[:, V + c, :], p[:, V + c, :], mean, ALU.subtract).then_inc(q["gained"], 1)
            dve.wait_ge(q["sum2"], 1)
            mine.then(v.tensor_scalar(core.rstd[:, :], acc[:, 1, :], 1.0 / D, 1e-6, ALU.mult, ALU.add))
            v.reciprocal(core.rstd[:, :], core.rstd[:, :]).then_inc(q["inv"], 1)
            dve.wait_ge(q["rstd"], 1)
            for c in range(DC):
                v.scalar_tensor_tensor(out=p[:, V + c, :], in0=p[:, V + c, :], scalar=core.vcol("sgu_ln_g", c),
                                       in1=core.rstd[:, :], op0=ALU.mult, op1=ALU.mult).then_inc(q["gained"], 1)
            for g in range(SGU_G):
                dve.wait_ge(q["mixed"], g + 1)
                if g >= 2:
                    dve.wait_ge(q["step"], mine.base + mine.n)
                t = scr[:, 3 + g % 2, :]
                mine.then(v.tensor_tensor(blocks(t), blocks(acc[:, 4 + g % 4, :]), bias[:, g, :].unsqueeze(1).to_broadcast([P, 4, P]), ALU.add))
                v.tensor_tensor(p[:, U + g, :], p[:, U + g, :], t, ALU.mult).then_inc(q["mixed_read"], 1)

        @block.scalar
        def _(act):
            s = nc.scalar
            for c in range(DC):
                act.wait_ge(q["gained"], c + 1)
                s.activation(h[:, c, :], p[:, V + c, :], ACT.Square).then_inc(q["sq"], 1)
            act.wait_ge(q["inv"], 1)
            s.activation(core.rstd[:, :], core.rstd[:, :], ACT.Sqrt).then_inc(q["rstd"], 1)
            for c in range(DC):
                act.wait_ge(q["gained"], DC + c + 1)
                s.activation(p[:, V + c, :], p[:, V + c, :], ACT.Identity, bias=core.vcol("sgu_ln_b", c)).then_inc(q["normed"], 1)
            for g in range(SGU_G):
                act.wait_ge(q["turned"], g + 1)
                s.activation(vt[:, :, g * P:(g + 1) * P], blocks(acc[:, g % 4, :]), ACT.Copy).then_inc(q["turned_read"], 1)

        @block.tensor
        def _(pe):
            for c in range(DC):
                ins = pe.matmul(acc[:, 0, :], core.ones[:, :], p[:, V + c, :], start=(c == 0), stop=(c == DC - 1))
            ins.then_inc(q["sum"], 1)
            for c in range(DC):
                pe.wait_ge(q["sq"], c + 1)
                ins = pe.matmul(acc[:, 1, :], core.ones[:, :], h[:, c, :], start=(c == 0), stop=(c == DC - 1))
            ins.then_inc(q["sum2"], 1)
            for g in range(SGU_G):
                pe.wait_ge(q["normed"], g + 1)
                if g >= 4:
                    pe.wait_ge(q["turned_read"], g - 3)
                for n in range(4):
                    ins = pe.transpose(acc[:, g % 4, n * P:(n + 1) * P], p[:, V + g, n * P:(n + 1) * P], core.eye[:, :])
                ins.then_inc(q["turned"], 1)
            pe.wait_ge(q["masked"], 1)
            for g in range(SGU_G):
                pe.wait_ge(q["turned_read"], g + 1)
                if g >= 4:
                    pe.wait_ge(q["mixed_read"], g - 3)
                for n in range(4):
                    ins = pe.matmul(acc[:, 4 + g % 4, n * P:(n + 1) * P], vt[:, n, g * P:(g + 1) * P], wt[:, g, :], start=True, stop=True)
                ins.then_inc(q["mixed"], 1)


def gated_stage(core, name, first, gate, op):
    nc, g, p, scr = core.nc, core.gemms[name], core.p, core.scr
    mb = g.cols // P
    step = None if first else core.sem(f"{name}_step")
    with nc.Block(no_gpsimd_drain=True) as block:
        @block.sync
        def _(sp):
            core.stream(sp, g)

        @block.gpsimd
        def _(pool):
            core.rest_weights(pool, g)

        @block.tensor
        def _(pe):
            core.product(pe, g, op)

        @block.scalar
        def _(act):
            core.round_parts(act, g, op)

        @block.vector
        def _(dve):
            core.rest_input(dve, op)
            mine = None if first else Steps(dve, step)

            def read(b, banks, s):
                for m in range(mb):
                    c = b * mb + m
                    if first:
                        ins = nc.vector.tensor_tensor(p[:, 36 + c, :], banks[m], p[:, gate + c, :], ALU.mult)
                    else:
                        t = scr[:, s * mb + m, :]
                        ins = nc.vector.tensor_tensor(t, banks[m], p[:, gate + c, :], ALU.mult)
                ins.then_inc(core.acc_free, 1)
                if not first:
                    dve.wait_ge(core.acc_free, core.blocks_read + b + 1)
                    for m in range(mb):
                        c = b * mb + m
                        nc.vector.tensor_tensor(p[:, 36 + c, :], p[:, 36 + c, :], scr[:, s * mb + m, :], ALU.add)
            core.drain(dve, g, read)
    core.end_product(g, op)


def relu2_stage(core, name, norm):
    nc, g, p, scr = core.nc, core.gemms[name], core.p, core.scr
    mb = g.cols // P
    op = Operand(core, DC, lambda m, k: m.h[:, k, :], lambda m, k: m.p[:, 44 + k, :], source=norm)
    relu = core.sem(f"{name}_relu")
    with nc.Block(no_gpsimd_drain=True) as block:
        @block.sync
        def _(sp):
            core.stream(sp, g)

        @block.gpsimd
        def _(pool):
            core.rest_weights(pool, g)

        @block.tensor
        def _(pe):
            core.product(pe, g, op)

        @block.scalar
        def _(act):
            def read(b, banks, s):
                for m in range(mb):
                    ins = nc.scalar.activation(scr[:, s * mb + m, :], banks[m], ACT.Relu)
                ins.then_inc(relu, 1)
            core.round_parts(act, g, op, read)

        @block.vector
        def _(dve):
            core.rest_input(dve, op)

            def read(b, banks, s):
                dve.wait_ge(relu, b + 1)
                t = scr[:, s * mb:s * mb + mb, :]
                nc.vector.tensor_tensor(p[:, bass.ds(b * mb, mb), :], t, t, ALU.mult).then_inc(core.acc_free, 1)
            core.drain(dve, g, read)
    core.end_product(g, op)


def block2(core):
    project_stage(core, "b2_rnn", norm=Norm(core, ("norm_mix_g", 0), 1e-6), consts=2)
    project_stage(core, "b2_gelu", at=RNNC, func=ACT.Gelu_apprx_tanh, meanwhile=lambda dve: rnn_convolution(core, dve))
    project_stage(core, "b2_gate", at=36, func=ACT.Sigmoid)
    rnn_stage(core)
    sgu_stage(core)
    gated_stage(core, "branch_a", True, 36, Operand(core, RNNC, lambda m, k: m.p[:, k, :], lambda m, k: m.h[:, k, :] if k < DC else m.scr[:, k - DC, :]))
    gated_stage(core, "branch_b", False, 44, Operand(core, DC, lambda m, k: m.p[:, 20 + k, :], lambda m, k: m.h[:, k, :]))
    residual_stage(core, "b2_out", 1.0, Operand(core, DC, lambda m, k: m.p[:, 36 + k, :], lambda m, k: m.h[:, k, :]))
    relu2_stage(core, "mlp_up", Norm(core, ("norm_ffn_g", 0), 1e-6, after_residual=True))
    part = lambda m, k: m.p[:, 32 + k, :] if k < 20 else m.h[:, k - 20, :] if k < 28 else m.scr[:, k - 28, :]
    residual_stage(core, "mlp_down", 1.0, Operand(core, 32, lambda m, k: m.p[:, k, :], part), squares=lambda core: core.scr[:, 4:6, :])


C3_DT = const_columns(3)[1]
C3_HEADS = C3_DT + DC * P
C3_SKIP = C3_HEADS + 2
C3_END = C3_SKIP + DC
XS, SB, SC, Z, S5U = 0, 8, 10, 12, 28


def ssd_convolution(core, dve):
    nc, p = core.nc, core.p
    v = nc.vector
    mine = Steps(dve, core.sem("ssd_conv"))
    drained = core.blocks_read
    wcol = lambda k, c: core.vcol("ssd_conv_w", k * 12 + c)
    with dve.Fori(0, 6) as b:
        mine.loop(b, SSD_K)
        dve.wait_ge(core.acc_free, b + drained + 1)
        chunk = [2 * b + j for j in range(2)]
        conv = lambda c: p[:, SSD_CONV + c, :]
        for c in chunk:
            ins = v.tensor_scalar(conv(c), p[:, XS + c, :], wcol(SSD_K - 1, c), None, ALU.mult)
        mine.then(ins)
        for k in range(SSD_K - 2, -1, -1):
            back = SSD_K - 1 - k
            for c in chunk:
                ins = v.scalar_tensor_tensor(out=conv(c)[:, back:T], in0=p[:, XS + c, 0:T - back], scalar=wcol(k, c),
                                             in1=conv(c)[:, back:T], op0=ALU.mult, op1=ALU.add)
            mine.then(ins)
    mine.end(6)


def ab_in_stage(core):
    nc, g, p, acc = core.nc, core.gemms["ab_in"], core.p, core.acc
    op = Operand(core, DC, lambda m, k: m.h[:, k, :], lambda m, k: m.scr[:, k, :], source=Norm(core, ("layer_norm", 0), 1e-6))
    loaded, dt_done, dt_split = core.sem("dt_loaded"), core.sem("dt_done"), core.sem("dt_split")
    wdt, wdt_lo = (m.cst[:, C3_DT:C3_DT + DC * P].rearrange("p (k m) -> p k m", m=P) for m in (core, core.r))
    wdt_hi = lambda k: core.r.p[:, 36 + k // 4, (k % 4) * P:(k % 4 + 1) * P]
    mb = g.cols // P
    with nc.Block(no_gpsimd_drain=True) as block:
        @block.sync
        def _(sp):
            core.next_consts(sp, 3)
            sp.dma_start(core.cst[:, C3_DT:C3_DT + DC * P], core.dram["w_dt"]).then_inc(loaded, 16)
            sp.dma_start(core.cst[:, C3_HEADS:C3_END], core.dram["ssd_small"]).then_inc(loaded, 16)
            core.stream(sp, g)
            sp.wait_ge(core.consts_in, core.const_loads)

        @block.gpsimd
        def _(pool):
            core.rest_weights(pool, g)
            pool.wait_ge(loaded, 32)
            for k in range(DC):
                nc.gpsimd.tensor_copy(wdt_hi(k), wdt[:, k, :]).then_inc(dt_split, 1)
            for k in range(DC):
                pool.wait_ge(dt_split, k + 1)
                nc.gpsimd.tensor_tensor(wdt_lo[:, k, :], wdt[:, k, :], wdt_hi(k), ALU.subtract).then_inc(dt_split, 1)

        @block.vector
        def _(dve):
            core.rest_input(dve, op)
            ssd_convolution(core, dve)

        @block.tensor
        def _(pe):
            core.product(pe, g, op)
            pe.wait_ge(dt_split, 2 * DC)
            pe.wait_ge(core.acc_free, core.blocks_read + g.blocks)
            for k in range(DC):
                for n, (w, x) in enumerate(((wdt_hi(k), op.hi), (wdt_hi(k), op.lo), (wdt_lo[:, k, :], op.hi))):
                    ins = pe.matmul(acc[:, 0, :], w, x(k), start=(k == 0 and n == 0), stop=(k == DC - 1 and n == 2))
            ins.then_inc(dt_done, 1)

        @block.scalar
        def _(act):
            def read(b, banks, s):
                for m in range(mb):
                    ins = nc.scalar.activation(p[:, b * mb + m, :], banks[m], ACT.Copy)
                ins.then_inc(core.acc_free, 1)
            core.round_parts(act, g, op, read)
            act.wait_ge(dt_done, 1)
            nc.scalar.activation(core.scr[:, 0, :], acc[:, 0, :], ACT.Copy)
    core.end_product(g, op)


def ssd_prepare_stage(core):
    nc, p, scr, h, acc, small = core.nc, core.p, core.scr, core.h, core.acc, core.small
    names = ("step", "sp_dve", "sp_act", "a", "turned", "sums", "last", "zeroed", "lifted")
    q = {s: core.sem(f"sd_{s}") for s in names}
    R = slice(0, SSD_H)
    dt_raw, acs, tok = scr[:, 0, :], scr[:, 1, :], scr[:, 2, :]
    m, e, t, d = (scr[R, 3 + n, :] for n in range(4))
    dtf = scr[:, 3, :]
    heads = lambda n: core.cst[R, C3_HEADS + n:C3_HEADS + n + 1]
    a_col = small[R, 0:1]
    conv = lambda c: p[:, SSD_CONV + c, :]
    NX = 12
    col = lambda n: tok[:, 64 * n:64 * n + 64]
    with nc.Block(no_gpsimd_drain=True) as block:
        @block.gpsimd
        def _(pool):
            nc.gpsimd.memset(scr[:, 1, :], 0.0)
            nc.gpsimd.memset(scr[:, 3, :], 0.0).then_inc(q["zeroed"], 1)
            for c in range(DC):
                nc.gpsimd.tensor_copy(h[:, c, :].rearrange("p (l n) -> p l n", l=S5_L),
                                      p[:, S5U + c, :].rearrange("p (n l) -> p l n", l=S5_L)).then_inc(q["lifted"], 1)
            pool.wait_ge(q["lifted"], DC)

        @block.vector
        def _(dve):
            v = nc.vector
            mine = Steps(dve, q["step"])
            dve.wait_ge(q["zeroed"], 1)
            mine.then(v.tensor_scalar(dt_raw[R], dt_raw[R], heads(0), None, ALU.add))
            softplus_steps(nc, mine, dt_raw[R], m, e, t, d, q["sp_act"], q["sp_dve"], 0)
            dve.wait_ge(q["a"], 1)
            mine.then(v.tensor_scalar(t, m, a_col, -1.0, ALU.mult, ALU.mult))
            v.tensor_tensor_scan(acs[R], core.const(3, "dt_resets", R), t, 0.0, ALU.mult, ALU.add).then_inc(q["sums"], 1)
            dve.wait_ge(q["turned"], 1)
            for n in range(NCH):
                v.tensor_copy(col(0)[:, n * SSD_H:(n + 1) * SSD_H], acc[:, 0, n * P:n * P + SSD_H])
                ins = v.tensor_copy(col(1)[:, n * SSD_H:(n + 1) * SSD_H], acc[:, 1, n * P:n * P + SSD_H])
            mine.then(ins)
            dve.wait_ge(q["last"], 1)
            mine.then(v.tensor_tensor(col(2), acc[:, 2, 0:64], col(1), ALU.subtract))

        @block.scalar
        def _(act):
            s = nc.scalar
            s.activation(a_col, heads(1), ACT.Exp).then_inc(q["a"], 1)
            softplus_act(nc, act, e, t, q["sp_dve"], q["sp_act"], 0)
            for c in range(NX):
                s.activation(p[:, XS + c, :], conv(c), ACT.Silu, bias=core.vcol("ssd_conv_b", c))
            act.wait_ge(q["step"], SSD_PREP_STEPS)
            s.activation(col(2), col(2), ACT.Exp)
            s.activation(col(3), col(1), ACT.Exp)
            s.activation(col(4), acc[:, 2, 0:64], ACT.Exp)

        @block.tensor
        def _(pe):
            pe.wait_ge(q["sums"], 1)
            for n in range(NCH):
                pe.transpose(acc[:, 0, n * P:(n + 1) * P], dtf[:, n * P:(n + 1) * P], core.eye[:, :])
                ins = pe.transpose(acc[:, 1, n * P:(n + 1) * P], acs[:, n * P:(n + 1) * P], core.eye[:, :])
            ins.then_inc(q["turned"], 1)
            pe.wait_ge(q["step"], SSD_PREP_STEPS - 1)
            pe.matmul(acc[:, 2, 0:64], core.const(3, "last_row"), col(1), start=True, stop=True).then_inc(q["last"], 1)


SSD_K = 4
SSD_PREP_STEPS = 1 + SOFTPLUS_STEPS + 1 + 2
SSD_CONV = 40


def ssd_stage(core):
    nc, p, scr, h, acc, small = core.nc, core.p, core.scr, core.h, core.acc, core.small
    names = ("step", "staged", "xs_t", "xdt", "bc", "seg", "exp", "m", "yd", "off", "y", "yt", "zero")
    q = {s: core.sem(f"ssd_{s}") for s in names}
    tok, acs = scr[:, 2, :], scr[:, 1, :]
    col = lambda k, n: tok[:, bass.ds(64 * k + n * SSD_H, SSD_H)]
    stg = p[:, 36:39, :].rearrange("p a t -> p (a t)").rearrange("p (c t) -> p c t", t=P)
    xdt = p[:, 39:41, :].rearrange("p a (h d) -> p (a h) d", d=64)
    xds = p[:, 41:43, :].rearrange("p a (h d) -> p (a h) d", d=64)
    mt = p[:, 43:47, :].rearrange("p a (h l) -> p (a h) l", l=P)
    prev = p[:, 47:49, :]
    y = p[:, 49:51, :]
    btok = p[:, 51, 0:2 * P].rearrange("p (g n) -> p g n", n=P)
    cbs = p[:, 51, 2 * P:4 * P].rearrange("p (g n) -> p g n", n=P)
    h4 = lambda a: a.rearrange("p (h l) -> p h l", l=P)
    h8 = lambda a: a.rearrange("p (h d) -> p h d", d=64)
    b8 = lambda c, g: c[:, 8 * g:8 * g + 8].unsqueeze(2).to_broadcast([P, 8, 64])
    causal = core.const(3, "causal").unsqueeze(1).to_broadcast([P, 4, P])
    rows = core.const(3, "head_rows").rearrange("p (h l) -> p h l", l=P)
    with nc.Block(no_gpsimd_drain=True) as block:
        @block.gpsimd
        def _(pool):
            nc.gpsimd.memset(prev, 0.0).then_inc(q["zero"], 1)

        @block.sync
        def _(sp):
            sp.dma_start(core.dram["lift"].rearrange("(c p) t -> p c t", p=P), h[:, :, :]).then_inc(core.lifted, 16)
            sp.wait_ge(core.lifted, 16)

        @block.vector
        def _(dve):
            v = nc.vector
            mine = Steps(dve, q["step"])
            dve.wait_ge(q["zero"], 1)
            with dve.Fori(0, NCH) as n:
                mine.loop(n, SSD_STEPS)
                ce = small[:, 32:48]
                mine.then(v.tensor_copy(ce, col(3, n)))
                cs, cdt, cds, cdec = col(1, n), col(0, n), col(2, n), col(4, n)
                v.tensor_copy(small[:, 48:64], cdec)
                v.tensor_copy(small[:, 64:80], cdt)
                v.tensor_copy(small[:, 80:96], cds)
                mine.then(v.tensor_copy(small[:, 96:112], cs))
                ldec, ldt, lds, lcs = (small[:, 48 + 16 * k:64 + 16 * k] for k in range(4))
                dve.wait_ge(q["xs_t"], n + 1)
                for g in range(2):
                    v.tensor_tensor(xdt[:, 8 * g:8 * g + 8, :], h8(acc[:, g, :]), b8(ldt, g), ALU.mult)
                v.tensor_copy(btok, acc[:, 2, 0:2 * P].rearrange("p (g n) -> p g n", n=P))
                v.tensor_copy(cbs, acc[:, 2, 2 * P:4 * P].rearrange("p (g n) -> p g n", n=P)).then_inc(q["xdt"], 1)
                dve.wait_ge(q["xdt"], 2 * n + 1)
                for g in range(2):
                    ins = v.tensor_tensor(xds[:, 8 * g:8 * g + 8, :], xdt[:, 8 * g:8 * g + 8, :], b8(lds, g), ALU.mult)
                ins.then_inc(q["xdt"], 1)
                dve.wait_ge(q["bc"], n + 1)
                for b in range(4):
                    ins = v.tensor_tensor(mt[:, 4 * b:4 * b + 4, :], h4(acc[:, 4 + b, :]),
                                          lcs[:, 4 * b:4 * b + 4].unsqueeze(2).to_broadcast([P, 4, P]), ALU.subtract)
                mine.then(ins)
                for b in range(4):
                    v.tensor_tensor(mt[:, 4 * b:4 * b + 4, :], mt[:, 4 * b:4 * b + 4, :], causal, ALU.add).then_inc(q["seg"], 1)
                for b in range(4):
                    dve.wait_ge(q["exp"], 4 * n + b + 1)
                    v.tensor_tensor(mt[:, 4 * b:4 * b + 4, :], mt[:, 4 * b:4 * b + 4, :],
                                    cbs[:, b // 2, :].unsqueeze(1).to_broadcast([P, 4, P]), ALU.mult).then_inc(q["m"], 1)
                dve.wait_ge(q["off"], n + 1)
                for g in range(2):
                    ins = v.tensor_tensor(h8(y[:, g, :]), h8(acc[:, 4 + g, :]), b8(ce, g), ALU.mult)
                mine.then(ins)
                dve.wait_ge(q["yd"], n + 1)
                for g in range(2):
                    ins = v.tensor_tensor(y[:, g, :], y[:, g, :], acc[:, g, :], ALU.add)
                ins.then_inc(q["y"], 1)
                for g in range(2):
                    ins = v.tensor_tensor(h8(prev[:, g, :]), h8(prev[:, g, :]), b8(ldec, g), ALU.mult)
                mine.then(ins)
                for g in range(2):
                    ins = v.tensor_tensor(prev[:, g, :], prev[:, g, :], acc[:, 6 + g, :], ALU.add)
                mine.then(ins)
                dve.wait_ge(q["yt"], n + 1)
                for c in range(8):
                    xs = p[:, XS + c, bass.ds(n * CH, CH)]
                    ins = v.scalar_tensor_tensor(out=xs, in0=xs, scalar=core.cst[:, C3_SKIP + c:C3_SKIP + c + 1],
                                                 in1=h4(acc[:, 2 + c // 4, :])[:, c % 4, :], op0=ALU.mult, op1=ALU.add)
                mine.then(ins)
            mine.end(NCH)

        @block.scalar
        def _(act):
            def stage(n):
                nc.scalar.activation(stg[:, 0:12, :], p[:, XS:XS + 12, bass.ds(n * CH, CH)], ACT.Copy).then_inc(q["staged"], 1)

            def decays(n):
                for b in range(4):
                    act.wait_ge(q["seg"], 4 * n + b + 1)
                    nc.scalar.activation(mt[:, 4 * b:4 * b + 4, :], mt[:, 4 * b:4 * b + 4, :], ACT.Exp).then_inc(q["exp"], 1)

            stage(0)
            with act.Fori(0, NCH - 1) as n:
                decays(n)
                act.wait_ge(q["off"], n + 1)
                stage(n + 1)
            decays(NCH - 1)

        @block.tensor
        def _(pe):
            mm = pe.matmul
            pe.wait_ge(q["zero"], 1)
            with pe.Fori(0, NCH) as n:
                pe.wait_ge(q["staged"], n + 1)
                for c in range(8):
                    pe.transpose(acc[:, c // 4, (c % 4) * P:(c % 4 + 1) * P], stg[:, c, :], core.eye[:, :])
                pe.wait_ge(q["step"], SSD_STEPS * n + 1)
                for g in range(2):
                    pe.transpose(acc[:, 2, g * P:(g + 1) * P], stg[:, 8 + g, :], core.eye[:, :])
                for g in range(2):
                    ins = mm(acc[:, 2, (2 + g) * P:(3 + g) * P], stg[:, 8 + g, :], stg[:, 10 + g, :], start=True, stop=True)
                ins.then_inc(q["xs_t"], 1)
                for hd in range(SSD_H):
                    ins = mm(acc[:, 4 + hd // 4, (hd % 4) * P:(hd % 4 + 1) * P], rows[:, hd, :], acs[:, bass.ds(n * CH, CH)], start=True, stop=True)
                ins.then_inc(q["bc"], 1)
                pe.wait_ge(q["seg"], 4 * n + 4)
                for g in range(2):
                    ins = mm(acc[:, 4 + g, :], stg[:, 10 + g, :], prev[:, g, :], start=True, stop=True)
                ins.then_inc(q["off"], 1)
                pe.wait_ge(q["xdt"], 2 * n + 2)
                for g in range(2):
                    mm(acc[:, 6 + g, :], btok[:, g, :], xds[:, 8 * g:8 * g + 8, :], start=True, stop=True)
                for hd in range(SSD_H):
                    if hd % 4 == 0:
                        pe.wait_ge(q["m"], 4 * n + hd // 4 + 1)
                    ins = mm(acc[:, hd // 8, (hd % 8) * 64:(hd % 8 + 1) * 64], mt[:, hd, :], xdt[:, hd, :], start=True, stop=True)
                ins.then_inc(q["yd"], 1)
                pe.wait_ge(q["y"], n + 1)
                for c in range(8):
                    ins = pe.transpose(acc[:, 2 + c // 4, (c % 4) * P:(c % 4 + 1) * P], y[:, c // 4, (c % 4) * P:(c % 4 + 1) * P], core.eye[:, :])
                ins.then_inc(q["yt"], 1)


SSD_STEPS = 7


def ssd_gate_stage(core):
    nc, p, scr, h, acc = core.nc, core.p, core.scr, core.h, core.acc
    names = ("step", "gate", "sq", "sum", "inv", "rstd")
    q = {s: core.sem(f"sg_{s}") for s in names}
    rs = scr[:, 0:2, :]
    with nc.Block(no_gpsimd_drain=True) as block:
        @block.sync
        def _(sp):
            by_place = core.dram["lift"].rearrange("(g i) (l n) -> l i g n", i=S5_IN, l=S5_L)
            for l in range(S5_L):
                sp.dma_start(p[l * S5_IN:(l + 1) * S5_IN, 36:44, :].rearrange("p a (g n) -> p (a g) n", n=S5_N), by_place[l]).then_inc(core.lifted, 16)
            sp.wait_ge(core.lifted, 16 * (S5_L + 1))

        @block.scalar
        def _(act):
            s = nc.scalar
            for c in range(8):
                s.activation(h[:, c, :], p[:, Z + 8 + c, :], ACT.Silu).then_inc(q["gate"], 1)
            s.activation(p[:, Z:Z + DC, :], p[:, Z:Z + DC, :], ACT.Silu)
            for c in range(8):
                act.wait_ge(q["step"], c + 1)
                s.activation(h[:, c, :], p[:, XS + c, :], ACT.Square).then_inc(q["sq"], 1)
            act.wait_ge(q["inv"], 1)
            s.activation(rs, rs, ACT.Sqrt).then_inc(q["rstd"], 1)

        @block.tensor
        def _(pe):
            for c in range(8):
                pe.wait_ge(q["sq"], c + 1)
                ins = pe.matmul(acc[:, c // 4, :], core.ones[:, :], h[:, c, :], start=(c % 4 == 0), stop=(c % 4 == 3))
            ins.then_inc(q["sum"], 1)

        @block.vector
        def _(dve):
            v = nc.vector
            mine = Steps(dve, q["step"])
            for c in range(8):
                dve.wait_ge(q["gate"], c + 1)
                mine.then(v.tensor_tensor(p[:, XS + c, :], p[:, XS + c, :], h[:, c, :], ALU.mult))
            dve.wait_ge(q["sum"], 1)
            mine.then(v.tensor_scalar(rs, acc[:, 0:2, :], 2.0 / D, 1e-6, ALU.mult, ALU.add))
            v.reciprocal(rs, rs).then_inc(q["inv"], 1)
            dve.wait_ge(q["rstd"], 1)
            for c in range(8):
                v.scalar_tensor_tensor(out=p[:, XS + c, :], in0=p[:, XS + c, :], scalar=core.vcol("ssd_norm_w", c), in1=rs[:, c // 4, :],
                                       op0=ALU.mult, op1=ALU.mult)


S5_TAB = const_columns(3)[0]["head_rows"][0]
S5_REV = S5_TAB + 2 * 9 * S5_G
S5_COEF = S5_REV + 2 * 8 * S5_G
TWO_PI_1 = 6.28125
TWO_PI_2 = float(np.float32(np.round((2 * np.pi - TWO_PI_1) * 2 ** 22) / 2 ** 22))
TWO_PI_3 = float(np.float32(2 * np.pi - TWO_PI_1 - TWO_PI_2))
TO_INT = 1.5 * 2.0 ** 23
PI_BELOW = 3.1415925


def s5_discretize_stage(core):
    nc, p, scr, cst = core.nc, core.p, core.scr, core.cst
    names = ("loaded", "step", "exp", "half", "tanh", "angle", "sin")
    q = {s: core.sem(f"s5_{s}") for s in names}
    tile = lambda n: scr[:, 6 + n // 8, (n % 8) * 64:(n % 8 + 1) * 64]
    lre, li, dt, th, em, ang, kf, r, sn, hs, cm, cos, rec, t0 = (tile(n) for n in range(14))
    tab = cst[:, S5_TAB:S5_REV].rearrange("p (r m g) -> p r m g", r=2, g=S5_G)
    rev = cst[:, S5_REV:S5_COEF].rearrange("p (r m g) -> p r m g", r=2, g=S5_G)
    y1, y2 = p[:, SB:SB + 2, :], p[:, SB + 2:SB + 4, :]
    b_, b2 = scr[:, 0:2, :], scr[:, 2:4, :]
    g3 = lambda a: a.rearrange("p a (g i) -> p (a g) i", i=S5_IN)
    bc = lambda c: c.unsqueeze(2).to_broadcast([P, S5_G, S5_IN])
    big = g3(scr[:, 4:6, :])
    with nc.Block(no_gpsimd_drain=True) as block:
        @block.sync
        def _(sp):
            sp.dma_start(lre, core.dram["lam_re"]).then_inc(q["loaded"], 16)
            sp.dma_start(li, core.dram["lam_im"]).then_inc(q["loaded"], 16)
            sp.dma_start(dt, core.dram["log_dt"].partition_broadcast(P)).then_inc(q["loaded"], 16)
            sp.dma_start(p[:, SB:SB + 4, :], core.dram["s5_b"]).then_inc(q["loaded"], 16)
            sp.wait_ge(q["loaded"], 64)

        @block.scalar
        def _(act):
            s = nc.scalar
            act.wait_ge(q["loaded"], 64)
            s.activation(dt, dt, ACT.Exp).then_inc(q["exp"], 1)
            act.wait_ge(q["half"], 1)
            s.activation(th, th, ACT.Tanh).then_inc(q["tanh"], 1)
            act.wait_ge(q["angle"], 1)
            s.activation(sn, r, ACT.Sin)
            s.activation(hs, r, ACT.Sin, scale=0.5).then_inc(q["sin"], 1)

        @block.vector
        def _(dve):
            v = nc.vector
            mine = Steps(dve, q["step"])
            then = mine.then
            mul = lambda o, a, b: v.tensor_tensor(o, a, b, ALU.mult)
            dve.wait_ge(q["exp"], 1)
            then(v.tensor_scalar(lre, lre, -1e-4, None, ALU.min))
            v.scalar_tensor_tensor(out=th, in0=lre, scalar=0.5, in1=dt, op0=ALU.mult, op1=ALU.mult).then_inc(q["half"], 1)
            then(mul(ang, li, dt))
            then(v.tensor_scalar(kf, ang, 1 / (2 * np.pi), TO_INT, ALU.mult, ALU.add))
            then(v.tensor_scalar(kf, kf, -TO_INT, None, ALU.add))
            for src, part in ((ang, TWO_PI_1), (r, TWO_PI_2), (r, TWO_PI_3)):
                then(v.scalar_tensor_tensor(out=r, in0=kf, scalar=-part, in1=src, op0=ALU.mult, op1=ALU.add))
            v.tensor_scalar(r, r, PI_BELOW, -PI_BELOW, ALU.min, ALU.max).then_inc(q["angle"], 1)
            dve.wait_ge(q["tanh"], 1)
            then(v.tensor_scalar(em, th, -1.0, 1.0, ALU.mult, ALU.add))
            then(v.reciprocal(em, em))
            then(v.scalar_tensor_tensor(out=em, in0=th, scalar=2.0, in1=em, op0=ALU.mult, op1=ALU.mult))
            then(v.tensor_scalar(t0, em, 1.0, None, ALU.add))
            dve.wait_ge(q["sin"], 1)
            then(v.scalar_tensor_tensor(out=cm, in0=hs, scalar=-2.0, in1=hs, op0=ALU.mult, op1=ALU.mult))
            then(v.tensor_scalar(cos, cm, 1.0, None, ALU.add))
            are, aim = tab[:, 0, 1, :], tab[:, 1, 1, :]
            mul(are, t0, cos)
            then(mul(aim, t0, sn))
            nr = em
            then(mul(nr, em, cos))
            then(v.tensor_tensor(nr, nr, cm, ALU.add))
            mul(rec, lre, lre)
            then(mul(t0, li, li))
            then(v.tensor_tensor(rec, rec, t0, ALU.add))
            then(v.reciprocal(rec, rec))
            mul(ang, nr, lre)
            mul(kf, aim, li)
            mul(r, aim, lre)
            then(mul(t0, nr, li))
            cre, cim = ang, r
            v.tensor_tensor(cre, ang, kf, ALU.add)
            then(v.tensor_tensor(cim, r, t0, ALU.subtract))
            mul(cre, cre, rec)
            then(mul(cim, cim, rec))
            then(v.tensor_scalar(y2, y2, core.const(3, "sign"), -1.0, ALU.mult, ALU.mult))
            mul(g3(b_), g3(y1), bc(cre))
            mul(g3(b2), g3(y2), bc(cre))
            then(mul(big, g3(y2), bc(cim)))
            then(v.tensor_tensor(g3(b_), g3(b_), big, ALU.add))
            then(mul(big, g3(y1), bc(cim)))
            then(v.tensor_tensor(g3(b2), g3(b2), big, ALU.subtract))
            v.memset(tab[:, 0, 0, :], 1.0)
            then(v.memset(tab[:, 1, 0, :], 0.0))
            for m in range(2, S5_L + 1):
                xr, xi = tab[:, 0, m - 1, :], tab[:, 1, m - 1, :]
                mul(th, xr, are)
                mul(em, xi, aim)
                mul(kf, xr, aim)
                then(mul(t0, xi, are))
                v.tensor_tensor(tab[:, 0, m, :], th, em, ALU.subtract)
                then(v.tensor_tensor(tab[:, 1, m, :], kf, t0, ALU.add))
            for s_ in range(S5_L):
                v.tensor_copy(rev[:, :, s_, :], tab[:, :, S5_L - 1 - s_, :])


S5_NB = 8
S5_ROUNDS = S5_G // S5_NB


def past(c, n):
    return not isinstance(c, int) or c >= n


def before(b, i):
    return (2 * i, 0, i) if b else (2 * i - 1, 1, i - 1)


def s5_rounds(eng, step, mine=None, per=0):
    for c in range(4):
        step(c, c % 2, c // 2)
    with eng.Fori(2, S5_ROUNDS // 2) as i:
        if mine is not None:
            mine.loop(i - 2, per)
        step(2 * i, 0, i)
        step(2 * i + 1, 1, i)
    if mine is not None:
        mine.end(S5_ROUNDS // 2 - 2)


S5_LAST = (S5_ROUNDS - 1, 1, S5_ROUNDS // 2 - 1)


def s5_state_stage(core):
    nc, p, scr, h, acc, cst = core.nc, core.p, core.scr, core.h, core.acc, core.cst
    names = ("step", "r", "rt", "rt_read", "v", "v_read", "swap", "ready")
    q = {s: core.sem(f"sh_{s}") for s in names}
    rev = cst[:, S5_REV:S5_COEF].rearrange("p (r m g) -> p r g m", r=2, g=S5_G)
    tab = cst[:, S5_TAB:S5_REV].rearrange("p (r m g) -> p r m g", r=2, g=S5_G)
    g3 = lambda a: a.rearrange("p a (g i) -> p (a g) i", i=S5_IN)
    b_, b2 = g3(scr[:, 0:2, :]), g3(scr[:, 2:4, :])
    NB = S5_NB
    rows = lambda a: a.rearrange("p a (g s i) -> p (a g) s i", g=4, i=S5_IN)
    cols = lambda a: a.rearrange("p a (g c) -> p (a g) c", g=4)
    r, rt, tmp = (p[:, 44:46, :], p[:, 50:52, :]), (p[:, 46:48, :], p[:, SB:SB + 2, :]), p[:, 48:50, :]
    ul = p[:, 36:44, :].rearrange("p a (g n) -> p (a g) n", n=S5_N)
    hp = h[:, :, :].rearrange("p a (n g) -> p (a n) g", g=S5_G)
    RUNS = 8
    col = lambda k: h[:, :, k * S5_G:(k + 1) * S5_G]
    by_run = lambda a: a.rearrange("p (a g) -> p a g", g=S5_G)
    carry, d = by_run(p[:, SB, :]), [by_run(p[:, SB + 1 + n, :]) for n in range(2)]
    m1, m2 = by_run(p[:, SB + 3, :]), by_run(core.rstd[:, :])
    sq = [core.small[:, n * 64:(n + 1) * 64] for n in range(4)]
    a8 = [tab[:, n, S5_L, :] for n in range(2)]
    N_PRODUCTS = 3 * (RUNS - 1)
    with nc.Block(no_gpsimd_drain=True) as block:
        @block.vector
        def _(dve):
            v = nc.vector
            mine = Steps(dve, q["step"])
            v.memset(hp[:, 0, :], 0.0)

            def step(c, b, i):
                gs = bass.ds(c * NB, NB)
                wide = lambda a: a[:, gs, :].unsqueeze(2).to_broadcast([P, NB, S5_L, S5_IN])
                power = lambda k: rev[:, k, gs, :].unsqueeze(3).to_broadcast([P, NB, S5_L, S5_IN])
                if past(c, 2):
                    dve.wait_ge(q["rt"], c - 1)
                v.tensor_tensor(rows(r[b]), wide(b_), power(0), ALU.mult)
                mine.then(v.tensor_tensor(rows(tmp), wide(b2), power(1), ALU.mult))
                v.tensor_tensor(r[b], r[b], tmp, ALU.add).then_inc(q["r"], 1)
                dve.wait_ge(q["r"], c + 1)

            s5_rounds(dve, step, mine, 2)
            re, im = a8
            for n in range(3):
                mine.then(v.tensor_tensor(sq[2], re, im, ALU.mult))
                v.tensor_tensor(sq[3], im, im, ALU.mult)
                mine.then(v.tensor_tensor(sq[0], re, re, ALU.mult))
                v.tensor_scalar(sq[1], sq[2], 2.0, None, ALU.mult)
                mine.then(v.tensor_tensor(sq[0], sq[0], sq[3], ALU.subtract))
                re, im = sq[0], sq[1]
            dve.wait_ge(q["v_read"], S5_ROUNDS)
            done = 0

            def product(a, x, target, add, runs):
                nonlocal done
                of = lambda t: t[:, 0:runs, :]
                wide = lambda t: t.unsqueeze(1).to_broadcast([P, runs, S5_G])
                if add:
                    mine.then(v.tensor_tensor(of(m1), wide(a[0]), x, ALU.mult))
                    mine.then(v.tensor_tensor(target, target, of(m1), ALU.add))
                else:
                    mine.then(v.tensor_tensor(target, wide(a[0]), x, ALU.mult))
                dve.wait_ge(q["swap"], done + 1)
                swapped = by_run(acc[:, done % 2, :])[:, 0:runs, :]
                mine.then(v.tensor_tensor(of(m2), wide(a[1]), swapped, ALU.mult))
                v.tensor_tensor(target, target, of(m2), ALU.add).then_inc(q["ready"], 1)
                done += 1
                dve.wait_ge(q["ready"], done)

            for k in range(1, RUNS):
                product(a8, col(k - 1), col(k), True, RUNS)
            product(a8, col(RUNS - 1), carry, False, RUNS)
            for a in range(1, RUNS - 1):
                product(sq, carry[:, a - 1:a, :], carry[:, a:a + 1, :], True, 1)
            later = lambda k: col(k)[:, 1:RUNS, :]
            x = carry[:, 0:RUNS - 1, :]
            v.tensor_tensor(later(0), later(0), x, ALU.add)
            for k in range(1, RUNS):
                y = d[k % 2][:, 0:RUNS - 1, :]
                product(a8, x, y, False, RUNS - 1)
                ins = v.tensor_tensor(later(k), later(k), y, ALU.add)
                x = y
            mine.then(ins)

        @block.scalar
        def _(act):
            def step(c, b, i):
                act.wait_ge(q["rt"], c + 1)
                if past(c, 2):
                    act.wait_ge(q["v"], c - 1)
                nc.scalar.activation(cols(rt[b]), acc[:, 4 * b:4 * b + 2, :].rearrange("p a (g c) -> p (a g) c", g=4), ACT.Copy).then_inc(q["rt_read"], 1)
                if past(c, 1):
                    read_v(*before(b, i))

            def read_v(c, b, i):
                act.wait_ge(q["v"], c + 1)
                nc.scalar.activation(hp[:, 1:S5_N, bass.ds(c * NB, NB)].rearrange("p n g -> p g n"),
                                     acc[:, 4 * b + 2, :].rearrange("p (g n) -> p g n", n=S5_N)[:, :, 0:S5_N - 1], ACT.Copy).then_inc(q["v_read"], 1)

            s5_rounds(act, step)
            read_v(*S5_LAST)

        @block.tensor
        def _(pe):
            def multiply(c, b, i):
                pe.wait_ge(q["rt_read"], c + 1)
                if past(c, 2):
                    pe.wait_ge(q["v_read"], c - 1)
                for g in range(NB):
                    ins = pe.matmul(acc[:, 4 * b + 2, g * S5_N:(g + 1) * S5_N], cols(rt[b])[:, g, :], ul[:, c * NB + g, :], start=True, stop=True)
                ins.then_inc(q["v"], 1)

            def step(c, b, i):
                pe.wait_ge(q["r"], c + 1)
                if past(c, 2):
                    pe.wait_ge(q["rt_read"], c - 1)
                for g in range(NB):
                    ins = pe.transpose(acc[:, 4 * b + g // 4, (g % 4) * P:(g % 4 + 1) * P], cols(r[b])[:, g, :], core.eye[:, :])
                ins.then_inc(q["rt"], 1)
                if past(c, 1):
                    multiply(*before(b, i))

            s5_rounds(pe, step)
            multiply(*S5_LAST)
            operands = [col(k) for k in range(RUNS)] + [carry[:, a:a + 1, :] for a in range(RUNS - 2)]
            operands += [carry[:, 0:RUNS - 1, :]] + [d[k % 2][:, 0:RUNS - 1, :] for k in range(1, RUNS - 1)]
            assert len(operands) == N_PRODUCTS
            for n, x in enumerate(operands):
                if n == 0:
                    pe.wait_ge(q["v_read"], S5_ROUNDS)
                else:
                    pe.wait_ge(q["ready"], n)
                out = by_run(acc[:, n % 2, :])[:, 0:x.shape[1], :]
                pe.matmul(out, core.const(3, "swap"), x, start=True, stop=True).then_inc(q["swap"], 1)


def s5_output_stage(core):
    nc, p, scr, h, acc, cst, small = core.nc, core.p, core.scr, core.h, core.acc, core.cst, core.small
    names = ("step", "loaded", "zeroed", "powers", "row", "row_read", "y", "y_read", "back")
    q = {s: core.sem(f"so_{s}") for s in names}
    stored, laid = ([core.sem(f"so_{s}{b}") for b in range(2)] for s in ("stored", "laid"))
    tab = cst[:, S5_TAB:S5_REV].rearrange("p (r m g) -> p r g m", r=2, g=S5_G)
    NB = S5_NB
    g3 = lambda a: a.rearrange("p a (g i) -> p (a g) i", i=S5_IN)
    x1, x2, b_ = g3(p[:, SB:SB + 2, :]), g3(p[:, SB + 2:SB + 4, :]), g3(scr[:, 0:2, :])
    NP = S5_L + 1
    flat = p[:, 44:49, :].rearrange("p a t -> p (a t)")
    powers = [flat[:, b * 1280:b * 1280 + NB * NP * S5_IN].rearrange("p (g m o) -> p g m o", g=NB, o=S5_IN) for b in range(2)]
    rows_of = lambda b, g, m: flat[:, b * 1280 + g * NP * S5_IN + m * S5_IN:][:, 0:P]
    tmp = scr[:, 2:4, :].rearrange("p a (g m o) -> p (a g) m o", g=4, o=S5_IN)
    last = small[:, 0:NB * S5_IN].rearrange("p (g o) -> p g o", o=S5_IN)
    b_now = small[:, P:2 * P].rearrange("p (g i) -> p g i", i=S5_IN)
    row = p[0:S5_IN, 49:51, :].rearrange("p a (g c) -> p (a g) c", c=P)
    kt = [scr[:, 4 + 2 * b:6 + 2 * b, :].rearrange("p a (g c) -> p (a g) c", c=P) for b in range(2)]
    yl = [a.rearrange("p (g n) -> p g n", n=S5_N) for a in (p[:, 51, :], core.rstd[:, :])]
    ul = p[:, 36:44, :].rearrange("p a (g n) -> p (a g) n", n=S5_N)
    hp = h[:, :, :].rearrange("p a (n g) -> p (a n) g", g=S5_G)
    lift = core.dram["lift"].rearrange("(g o) (l n) -> l o g n", o=S5_IN, l=S5_L)
    ALL = 16 * S5_L

    with nc.Block(no_gpsimd_drain=True) as block:
        @block.sync
        def _(sp):
            sp.dma_start(p[:, SB:SB + 4, :], core.dram["s5_c"]).then_inc(q["loaded"], 16)

            def step(c, b, i):
                sp.wait_ge(q["row_read"], c + 1)
                for s_ in range(S5_L):
                    sp.dma_start(kt[b][s_ * S5_IN:(s_ + 1) * S5_IN, :, s_ * S5_IN:P], row[:, :, 0:P - s_ * S5_IN]).then_inc(laid[b], 16)

            sp.wait_ge(q["zeroed"], 1)
            s5_rounds(sp, step)
            for b in range(2):
                sp.wait_ge(stored[b], ALL * (S5_ROUNDS // 2))
            sp.dma_start(p[:, 36:44, :], core.dram["lift"].rearrange("(c p) t -> p c t", p=P)).then_inc(q["back"], 16)
            sp.wait_ge(q["back"], 16)

        @block.gpsimd
        def _(pool):
            nc.gpsimd.memset(scr[:, 4:8, :], 0.0).then_inc(q["zeroed"], 1)

        @block.vector
        def _(dve):
            v = nc.vector
            mine = Steps(dve, q["step"])
            dve.wait_ge(q["loaded"], 16)
            v.tensor_scalar(p[:, SB:SB + 2, :], p[:, SB:SB + 2, :], core.const(3, "sign"), None, ALU.mult)
            mine.then(v.tensor_scalar(p[:, SB + 2:SB + 4, :], p[:, SB + 2:SB + 4, :], -1.0, None, ALU.mult))

            def step(c, b, i):
                gs = bass.ds(c * NB, NB)
                wide = lambda a, m: a[:, gs, :].unsqueeze(2).to_broadcast([P, NB, m, S5_IN])
                power = lambda k, m0, m1: tab[:, k, gs, m0:m1].unsqueeze(3).to_broadcast([P, NB, m1 - m0, S5_IN])
                if past(c, 2):
                    dve.wait_ge(q["y"], c - 1)
                v.tensor_tensor(tmp, wide(x2, 8), power(1, 0, 8), ALU.mult)
                v.tensor_tensor(last.unsqueeze(2), wide(x2, 1), power(1, 8, 9), ALU.mult)
                mine.then(v.tensor_tensor(powers[b], wide(x1, 9), power(0, 0, 9), ALU.mult))
                v.tensor_tensor(powers[b][:, :, 0:8, :], powers[b][:, :, 0:8, :], tmp, ALU.add)
                mine.then(v.tensor_tensor(powers[b][:, :, 8:9, :], powers[b][:, :, 8:9, :], last.unsqueeze(2), ALU.add))
                if past(c, 1):
                    dve.wait_ge(q["row"], c)
                v.tensor_copy(b_now, b_[:, gs, :]).then_inc(q["powers"], 1)

            s5_rounds(dve, step, mine, 4)

        @block.scalar
        def _(act):
            def read_y(c, b, i):
                act.wait_ge(q["y"], c + 1)
                if past(c, 2):
                    act.wait_ge(stored[b], i * ALL)
                nc.scalar.activation(yl[b], acc[:, 2 + b, :].rearrange("p (g n) -> p g n", n=S5_N), ACT.Copy).then_inc(q["y_read"], 1)
                act.wait_ge(q["y_read"], c + 1)
                for l in range(S5_L):
                    act.dma_start(lift[l][:, bass.ds(c * NB, NB), :], yl[b][l * S5_IN:(l + 1) * S5_IN]).then_inc(stored[b], 16)

            def step(c, b, i):
                act.wait_ge(q["row"], c + 1)
                if past(c, 1):
                    act.wait_ge(laid[1 - b], (before(b, i)[2] + 1) * ALL)
                nc.scalar.activation(row, acc[0:S5_IN, 0:2, :].rearrange("p a (g c) -> p (a g) c", c=P), ACT.Copy).then_inc(q["row_read"], 1)
                if past(c, 1):
                    read_y(*before(b, i))

            s5_rounds(act, step)
            read_y(*S5_LAST)

        @block.tensor
        def _(pe):
            def multiply(c, b, i):
                pe.wait_ge(laid[b], (i + 1) * ALL)
                if past(c, 2):
                    pe.wait_ge(q["y_read"], c - 1)
                for g in range(NB):
                    out = acc[:, 2 + b, g * S5_N:(g + 1) * S5_N]
                    pe.matmul(out, kt[b][:, g, :], ul[:, c * NB + g, :], start=True, stop=False)
                    ins = pe.matmul(out, rows_of(b, g, 1), hp[:, :, c * NB + g], start=False, stop=True)
                ins.then_inc(q["y"], 1)

            def step(c, b, i):
                pe.wait_ge(q["powers"], c + 1)
                if past(c, 1):
                    pe.wait_ge(q["row_read"], c)
                for g in range(NB):
                    ins = pe.matmul(acc[0:S5_IN, g // 4, (g % 4) * P:(g % 4 + 1) * P], b_now[:, g, :], rows_of(b, g, 0), start=True, stop=True)
                ins.then_inc(q["row"], 1)
                if past(c, 1):
                    multiply(*before(b, i))

            s5_rounds(pe, step)
            multiply(*S5_LAST)


class SkipGelu:

    def __init__(self, core):
        self.core, self.skipped, self.made = core, core.sem("s5_skipped"), core.sem("s5_gelu")

    def chunk(self, dve, c):
        core, p = self.core, self.core.p
        u = p[:, S5U + c, :].rearrange("p (n l) -> p n l", l=S5_L)
        core.nc.vector.scalar_tensor_tensor(out=u, in0=u, scalar=core.vcol("s5_d", c), in1=p[:, 36 + c, :].rearrange("p (l n) -> p n l", l=S5_L),
                                            op0=ALU.mult, op1=ALU.add).then_inc(self.skipped, 1)

    def ready(self, act, c):
        u = self.core.p[:, S5U + c, :]
        act.wait_ge(self.skipped, c + 1)
        self.core.nc.scalar.activation(u, u, ACT.Gelu_apprx_tanh).then_inc(self.made, 1)
        act.wait_ge(self.made, c + 1)

    def act_first(self, act):
        pass

    def act_then(self, act):
        pass

    def dve_share(self, dve):
        pass

    def pe_share(self, pe):
        pass


def s5_glu_stage(core):
    nc, g, p, scr = core.nc, core.gemms["s5_glu"], core.p, core.scr
    op = Operand(core, DC, lambda m, k: m.p[:, S5U + k, :], lambda m, k: m.h[:, k, :], lambda m, k: m.p[:, 44 + k, :],
                 source=SkipGelu(core))
    gate, step = core.sem("glu_gate"), core.sem("glu_step")
    mb = g.cols // P
    with nc.Block(no_gpsimd_drain=True) as block:
        @block.sync
        def _(sp):
            core.stream(sp, g)

        @block.gpsimd
        def _(pool):
            core.rest_weights(pool, g)

        @block.tensor
        def _(pe):
            core.product(pe, g, op)

        @block.scalar
        def _(act):
            def read(b, banks, s):
                for m in range(mb):
                    ins = nc.scalar.activation(scr[:, s * mb + m, :], banks[m], ACT.Sigmoid, bias=core.vcol("s5_glu_b", b * mb + m))
                ins.then_inc(gate, 1)
            core.round_parts(act, g, op, read)

        @block.vector
        def _(dve):
            core.rest_input(dve, op)

            def read(b, banks, s):
                dve.wait_ge(gate, b + 1)
                t = scr[:, s * mb:s * mb + mb, :]
                nc.vector.tensor_tensor(t, t, p[:, bass.ds(S5U + b * mb, mb), :], ALU.mult).then_inc(step, 1)
                dve.wait_ge(step, b + 1)
                nc.vector.tensor_tensor(p[:, bass.ds(36 + b * mb, mb), :], t, p[:, bass.ds(Z + b * mb, mb), :], ALU.mult).then_inc(core.acc_free, 1)
            core.drain(dve, g, read)
    core.end_product(g, op)


def block3_first(core):
    ab_in_stage(core)
    ssd_prepare_stage(core)
    ssd_stage(core)
    ssd_gate_stage(core)
    s5_discretize_stage(core)
    s5_state_stage(core)
    s5_output_stage(core)
    s5_glu_stage(core)
    residual_stage(core, "ab_out", 1.0, Operand(core, 2 * DC, lambda m, k: m.p[:, 36 + k, :] if k < DC else m.p[:, XS + k - DC, :],
                                                 lambda m, k: m.h[:, k, :] if k < DC else m.scr[:, k - DC, :]))


RQ, RK, RV, RG, RO = 0, DC, 2 * DC, 4 * DC, 6 * DC
RET_C = RET_V // P


def ret_rotate_stage(core):
    nc, p, scr, acc = core.nc, core.p, core.scr, core.acc
    names = ("rot", "sin", "cos", "turned")
    q = {s: core.sem(f"rr_{s}") for s in names}
    table = lambda name, c: core.const(4, f"{name}{c % 2}")
    with nc.Block(no_gpsimd_drain=True) as block:
        @block.tensor
        def _(pe):
            for c in range(2 * DC):
                if c >= BANKS:
                    pe.wait_ge(q["sin"], c - BANKS + 1)
                pe.matmul(acc[:, c % BANKS, :], core.const(4, "rotate"), p[:, RQ + c, :], start=True, stop=True).then_inc(q["rot"], 1)

        @block.gpsimd
        def _(pool):
            for c in range(2 * DC):
                pool.wait_ge(q["rot"], c + 1)
                nc.gpsimd.tensor_tensor(p[:, RQ + c, :], p[:, RQ + c, :], table("cos", c), ALU.mult).then_inc(q["cos"], 1)

        @block.vector
        def _(dve):
            for c in range(2 * DC):
                t = scr[:, c % 8, :]
                dve.wait_ge(q["rot"], c + 1)
                if c >= 8:
                    dve.wait_ge(q["turned"], c - 7)
                nc.vector.tensor_tensor(t, acc[:, c % BANKS, :], table("sin", c), ALU.mult).then_inc(q["sin"], 1)
                dve.wait_ge(q["sin"], c + 1)
                dve.wait_ge(q["cos"], c + 1)
                nc.vector.tensor_tensor(p[:, RQ + c, :], p[:, RQ + c, :], t, ALU.add).then_inc(q["turned"], 1)


def retention_stage(core):
    nc, p, scr, h, acc, small = core.nc, core.p, core.scr, core.h, core.acc, core.small
    names = ("step", "staged", "qd", "scores", "st", "kd", "o", "su", "state", "var", "std", "normed", "ot", "gained", "gated")
    q = {s: core.sem(f"rt_{s}") for s in names}
    wide = lambda a, b: scr[:, a:b, :].rearrange("p a (c t) -> p (a c) t", t=CH)
    k_now, q_now, s_t, k_dec = wide(0, 2), wide(2, 4), wide(4, 5), wide(5, 7)
    gains = [scr[:, 7, :], core.rstd[:, :]]
    o_n = p[:, RO:RO + RET_H, :]
    state = lambda hd: h[:, 2 * hd:2 * hd + 2, :]
    value = lambda hd, n: p[:, RV + 4 * hd:RV + 4 * hd + 4, :].rearrange("p (j a) t -> p j (a t)", j=2)[:, :, bass.ds(n * 256, 256)]
    stats, mv, rs = small[:, 0:24], small[:, 24:32], small[:, 32:36]
    tables = lambda name: core.cst[:, const_columns(4)[0][name + "0"][0]:][:, 0:RET_H * P].rearrange("p (h t) -> p h t", t=P)
    with nc.Block(no_gpsimd_drain=True) as block:
        @block.gpsimd
        def _(pool):

            def chunk(n, first=False, last=False):
                if not first:
                    pool.wait_ge(q["o"], n * RET_H)
                nc.gpsimd.tensor_tensor(q_now.rearrange("p (h c) t -> p h c t", c=2),
                                        p[:, RQ:RQ + DC, bass.ds(n * CH, CH)].rearrange("p (h c) t -> p h c t", c=2),
                                        tables("q_decay").unsqueeze(2).to_broadcast([P, RET_H, 2, CH]), ALU.mult).then_inc(q["qd"], 1)

            chunk(0, first=True)
            with pool.Fori(1, NCH - 1) as n:
                chunk(n)
            chunk(NCH - 1, last=True)

        @block.scalar
        def _(act):
            s = nc.scalar

            def chunk(n, first=False, last=False):
                if not first:
                    act.wait_ge(q["scores"], n)
                s.activation(k_now, p[:, RK:RK + DC, bass.ds(n * CH, CH)], ACT.Copy, scale=float(RET_QK ** -0.5)).then_inc(q["staged"], 1)
                act.wait_ge(q["scores"], n + 1)
                if not first:
                    act.wait_ge(q["su"], n * RET_H)
                for hd in range(0 if last else RET_H):
                    ins = s.activation(k_dec[:, 2 * hd:2 * hd + 2, :], acc[:, 1 + hd // 2, (hd % 2) * 256:(hd % 2 + 1) * 256].rearrange("p (c t) -> p c t", t=P),
                                       ACT.Copy, scale=core.const(4, "k_decay")[:, hd:hd + 1])
                if not last:
                    ins.then_inc(q["kd"], 1)
                act.wait_ge(q["var"], n + 1)
                s.activation(rs, rs, ACT.Sqrt).then_inc(q["std"], 1)
                for hd in range(RET_H):
                    act.wait_ge(q["ot"], n * RET_H + hd + 1)
                    if hd >= 2 or not first:
                        act.wait_ge(q["gated"], n * RET_H + hd - 1)
                    for j in range(RET_C):
                        c = RET_C * hd + j
                        ins = s.activation(gains[hd % 2][:, j * P:(j + 1) * P], acc[:, 4 + hd, j * P:(j + 1) * P], ACT.Identity,
                                           scale=core.vcol("ret_gn_w", c), bias=core.vcol("ret_gn_b", c))
                    ins.then_inc(q["gained"], 1)

            chunk(0, first=True)
            with act.Fori(1, NCH - 1) as n:
                chunk(n)
            chunk(NCH - 1, last=True)

        @block.vector
        def _(dve):
            v = nc.vector
            mine = Steps(dve, q["step"])

            def chunk(n, first=False, last=False):
                if not (first or last):
                    mine.loop(n - 1, 3)
                dve.wait_ge(q["scores"], n + 1)
                v.tensor_tensor(s_t, acc[:, 0, :].rearrange("p (h t) -> p h t", t=P), tables("intra"), ALU.mult).then_inc(q["st"], 1)
                for hd in range(RET_H):
                    if hd == RET_H - 1:
                        dve.wait_ge(q["o"], n * RET_H + RET_H)
                        for o in range(RET_H):
                            ins = v.bn_stats(stats[:, 6 * o:6 * o + 6], acc[:, 4 + o, :])
                        mine.then(ins)
                    if last:
                        continue
                    dve.wait_ge(q["su"], n * RET_H + hd + 1)
                    added = acc[:, 2 * (hd % 2):2 * (hd % 2) + 2, :]
                    if first:
                        v.tensor_copy(state(hd), added).then_inc(q["state"], 1)
                    else:
                        v.scalar_tensor_tensor(out=state(hd), in0=state(hd), scalar=core.const(4, "chunk_decay")[:, hd:hd + 1], in1=added,
                                               op0=ALU.mult, op1=ALU.add).then_inc(q["state"], 1)
                for hd in range(RET_H):
                    ins = v.bn_aggr(mv[:, 2 * hd:2 * hd + 2], stats[:, 6 * hd:6 * hd + 6])
                mine.then(ins)
                mine.then(v.tensor_scalar(rs, mv.rearrange("p (h k) -> p h k", k=2)[:, :, 1:2].rearrange("p h k -> p (h k)"), 1e-6, None, ALU.add))
                v.reciprocal(rs, rs).then_inc(q["var"], 1)
                dve.wait_ge(q["std"], n + 1)
                if not first:
                    dve.wait_ge(q["ot"], n * RET_H)
                for hd in range(RET_H):
                    v.tensor_scalar(o_n[:, hd, :], acc[:, 4 + hd, :], mv[:, 2 * hd:2 * hd + 1], rs[:, hd:hd + 1], ALU.subtract, ALU.mult).then_inc(q["normed"], 1)
                for hd in range(RET_H):
                    dve.wait_ge(q["gained"], n * RET_H + hd + 1)
                    y = p[:, RG + 4 * hd:RG + 4 * hd + 4, bass.ds(n * CH, CH)]
                    v.tensor_tensor(y, y, gains[hd % 2].rearrange("p (c t) -> p c t", t=P), ALU.mult).then_inc(q["gated"], 1)

            chunk(0, first=True)
            with dve.Fori(1, NCH - 1) as n:
                chunk(n)
            mine.end(NCH - 2)
            chunk(NCH - 1, last=True)

        @block.tensor
        def _(pe):
            mm = pe.matmul

            def chunk(n, first=False, last=False):
                pe.wait_ge(q["staged"], n + 1)
                if not first:
                    pe.wait_ge(q["state"], n * RET_H)
                for hd in range(RET_H):
                    for j in range(2):
                        ins = mm(acc[:, 0, hd * P:(hd + 1) * P], k_now[:, 2 * hd + j, :], p[:, RQ + 2 * hd + j, bass.ds(n * CH, CH)], start=(j == 0), stop=(j == 1))
                for c in range(0 if last else 2 * RET_H):
                    ins = pe.transpose(acc[:, 1 + c // 4, (c % 4) * P:(c % 4 + 1) * P], k_now[:, c, :], core.eye[:, :])
                ins.then_inc(q["scores"], 1)
                pe.wait_ge(q["qd"], n + 1)
                if not first:
                    pe.wait_ge(q["gained"], n * RET_H)
                pe.wait_ge(q["st"], n + 1)
                if not last:
                    pe.wait_ge(q["kd"], n + 1)
                for pair in range(0, RET_H, 2):
                    for hd in (pair, pair + 1):
                        for j in range(0 if first else 2):
                            mm(acc[:, 4 + hd, :], q_now[:, 2 * hd + j, :], state(hd)[:, j, :], start=(j == 0), stop=False)
                        mm(acc[:, 4 + hd, :], s_t[:, hd, :], value(hd, n), start=first, stop=True).then_inc(q["o"], 1)
                    if last:
                        continue
                    if pair:
                        pe.wait_ge(q["state"], n * RET_H + 2)
                    for hd in (pair, pair + 1):
                        for j in range(2):
                            ins = mm(acc[:, 2 * (hd % 2) + j, :], k_dec[:, 2 * hd + j, :], value(hd, n), start=True, stop=True)
                        ins.then_inc(q["su"], 1)
                for hd in range(RET_H):
                    pe.wait_ge(q["normed"], n * RET_H + hd + 1)
                    for j in range(RET_C):
                        ins = pe.transpose(acc[:, 4 + hd, j * P:(j + 1) * P], o_n[:, hd, j * P:(j + 1) * P], core.eye[:, :])
                    ins.then_inc(q["ot"], 1)

            chunk(0, first=True)
            with pe.Fori(1, NCH - 1) as n:
                chunk(n)
            chunk(NCH - 1, last=True)


def block3_second(core):
    project_stage(core, "ret_qk", norm=Norm(core, ("layer_norm", DC), 1e-6, after_residual=True), consts=4)
    project_stage(core, "ret_v", at=RV)
    project_stage(core, "ret_g", at=RG, func=ACT.Silu)
    ret_rotate_stage(core)
    retention_stage(core)
    residual_stage(core, "ret_out", 1.0, Operand(core, 2 * DC, lambda m, k: m.p[:, RG + k, :], lambda m, k: m.p[:, k, :]))


def lay_weights(which, inputs):
    gemms, n = lay_stream(which)
    out = np.zeros((n, P, SLOT), np.float32)

    def fill(name, *mats):
        g = gemms.get(name)
        if g is None:
            return
        cols = g.cols // len(mats)
        for b in range(g.blocks):
            for sub in range(g.q):
                slot = out[g.first + b * g.q + sub, :, 0:g.width].reshape(P, g.kc, g.cols)
                for j, w in enumerate(mats):
                    part = w[sub * g.kc * P:(sub + 1) * g.kc * P, b * cols:(b + 1) * cols]
                    slot[:, :, j * cols:(j + 1) * cols] = part.reshape(g.kc, P, cols).transpose(1, 0, 2)

    a = {k: np.asarray(v) for k, v in inputs.items()}
    for f in ("ffn1", "ffn2"):
        fill(f"{f}_up", a[f"{f}_gate"][0], a[f"{f}_up"][0])
        fill(f"{f}_down", a[f"{f}_down"][0])
    fill("mix_in", a["w_in"][0])
    fill("mix_out", a["w_out"][0])
    rnn, gate = 2 * P * 5, 2 * P * 18
    fill("b2_rnn", a["w_in_2"][0][:, 0:rnn])
    fill("b2_gelu", a["w_in_2"][0][:, rnn:gate])
    fill("b2_gate", a["w_in_2"][0][:, gate:])
    fill("branch_a", a["w_branch_a_2"][0])
    fill("branch_b", a["w_branch_b_2"][0])
    fill("b2_out", a["w_out_2"][0])
    fill("mlp_up", a["w_up_2"][0])
    fill("mlp_down", a["w_down_2"][0])
    w = a["ab_w_in_3"][0]
    fill("ab_in", np.concatenate([w[:, 24 * P:36 * P], w[:, 0:24 * P]], 1))
    fill("s5_glu", a["s5_glu_w_3"][0])
    fill("ab_out", a["ab_w_out_3"][0])
    qk = 2 * RET_H * RET_QK
    fill("ret_qk", a["ret_w_in_3"][0][:, 0:qk])
    fill("ret_v", a["ret_w_in_3"][0][:, qk:qk + RET_H * RET_V])
    fill("ret_g", a["ret_w_in_3"][0][:, qk + RET_H * RET_V:])
    fill("ret_out", a["ret_w_out_3"][0])
    return out


def lay_vectors(inputs):
    a = {k: np.asarray(v) for k, v in inputs.items()}
    src = {"norm_ffn1": "norm_ffn1", "norm_mix": "norm_mix", "b_in_attn": "b_in_attn", "shift_mix": "rwkv_shift_mix",
           "w0": "rwkv_w0", "a0": "rwkv_a0", "k_k": "rwkv_k_k", "k_a": "rwkv_k_a", "r_k": "rwkv_r_k", "ln_w": "rwkv_ln_w",
           "ln_b": "rwkv_ln_b", "norm_ffn2": "norm_ffn2", "norm_final": "norm_final", "norm_mix_g": "norm_mix_g_2",
           "conv_w": "conv_w_2", "conv_b": "conv_b_2", "lru_b_a": "lru_b_a_2", "lru_b_x": "lru_b_x_2",
           "lru_lambda": "lru_lambda_2", "sgu_ln_g": "sgu_ln_g_2", "sgu_ln_b": "sgu_ln_b_2", "norm_ffn_g": "norm_ffn_g_2",
           "final_norm_g": "final_norm_g_2", "layer_norm": "layer_norm_w_3", "s5_d": "s5_d_3", "s5_glu_b": "s5_glu_b_3",
           "ssd_conv_w": "ssd_conv_w_3", "ssd_conv_b": "ssd_conv_b_3", "ssd_norm_w": "ssd_norm_w_3", "ret_gn_w": "ret_gn_w_3", "ret_gn_b": "ret_gn_b_3",
           "final_norm_w": "final_norm_w_3"}
    cols = [a[src[name]].reshape(k, P) for name, k in VECTORS]
    return np.ascontiguousarray(np.concatenate(cols, 0).T)


def lay_small(inputs):
    a = {k: np.asarray(v) for k, v in inputs.items()}
    out = {}
    lora = np.zeros((P, 3, T), np.float32)
    lora[0:64, 0], lora[64:128, 1], lora[:, 2] = a["rwkv_w2"][0], a["rwkv_a2"][0], a["rwkv_g2"][0]
    out["lora"] = lora
    out["sinks"] = a["attn_sinks"].reshape(Q_HEADS)
    bd = np.zeros((P, RNNC, 2, P), np.float32)
    for g, w in enumerate((a["lru_w_a_2"][0], a["lru_w_x_2"][0])):
        for c in range(RNNC):
            for j in range(2):
                bd[j * 64:j * 64 + 64, c, g, j * 64:j * 64 + 64] = w[2 * c + j]
    out["lru_w"] = bd.reshape(P, -1)
    out["sgu_w"] = np.ascontiguousarray(a["sgu_w_s_2"][0].transpose(2, 0, 1))
    out["sgu_b"] = a["sgu_b_s_2"].reshape(-1)
    wdt = np.zeros((DC, P, P), np.float32)
    wdt[:, :, 0:SSD_H] = a["ab_w_in_3"][0][:, 18 * 2 * P:].reshape(DC, P, SSD_H)
    out["w_dt"] = np.ascontiguousarray(wdt.transpose(1, 0, 2)).reshape(P, -1)
    heads = np.zeros((P, 2 + DC), np.float32)
    heads[0:SSD_H, 0], heads[0:SSD_H, 1] = a["ssd_dt_bias_3"][0], a["ssd_a_log_3"][0]
    heads[:, 2:] = np.repeat(a["ssd_d_3"][0], 64).reshape(DC, P).T
    out["ssd_small"] = heads
    twice = lambda m: np.ascontiguousarray(np.concatenate([m, m], 0))
    out["lam_re"], out["lam_im"] = twice(a["s5_lam_re_3"][0].T), twice(a["s5_lam_im_3"][0].T)
    out["log_dt"] = a["s5_log_dt_3"].reshape(-1)
    by_state = lambda re, im: np.concatenate([re, im], 0).reshape(P, -1)
    br, bi = (a[f"s5_b_{k}_3"][0].transpose(1, 0, 2) for k in ("re", "im"))
    cr, ci = (a[f"s5_c_{k}_3"][0].transpose(2, 0, 1) for k in ("re", "im"))
    out["s5_b"] = np.concatenate([by_state(br, bi), by_state(bi, br)], 1).reshape(P, 4, T)
    out["s5_c"] = np.concatenate([by_state(cr, ci), by_state(ci, cr)], 1).reshape(P, 4, T)
    return out


def lay_out(which, inputs):
    x = np.asarray(inputs["x"])[0]
    arrays = {"x": np.ascontiguousarray(x.reshape(T, DC, P).transpose(2, 1, 0)), "weights": lay_weights(which, inputs),
              "vectors": lay_vectors(inputs)}
    arrays.update(lay_small(inputs))
    for n, make in CONSTS.items():
        arrays[f"consts{n}"] = np.concatenate([part for _, part in make()], axis=1)
    arrays["consts2"] = np.concatenate([arrays["consts2"], arrays.pop("lru_w")], axis=1)
    return arrays


def build(nc, dram, out, run, which=None):
    dram = dict(dram, lift=nc.dram_tensor("lift", (D, T), F32, kind="Internal").ap())
    with ExitStack() as ctx:
        core = Core(nc, ctx, dram, which)
        run(core, out)


def whole(core, out):
    start_stage(core, 1)
    block1(core)
    norm_stage(core, ("norm_final", 0), 1e-5)
    core.clear_sems()
    block2(core)
    norm_stage(core, ("final_norm_g", 0), 1e-6)
    core.clear_sems()
    block3_first(core)
    block3_second(core)
    norm_stage(core, ("final_norm_w", 0), 1e-6)
    finish_stage(core, out)


def finish_stage(core, out):
    nc = core.nc
    stored = core.sem("stored")
    with nc.Block(no_gpsimd_drain=True) as block:
        @block.sync
        def _(sp):
            sp.dma_start(out, core.x[:, :, :]).then_inc(stored, 16)
            sp.wait_ge(stored, 16)


def kernel(**inputs):
    import concourse.bacc as bacc
    from concourse.bass_utils import run_bass_kernel_spmd

    nc = bacc.Bacc("TRN2", target_bir_lowering=False, num_devices=1)
    arrays = lay_out(None, inputs)
    dram = {n: nc.dram_tensor(f"in_{n}", a.shape, F32, kind="ExternalInput").ap() for n, a in arrays.items()}
    out = nc.dram_tensor("out", (P, DC, T), F32, kind="ExternalOutput").ap()
    build(nc, dram, out, whole)
    r = run_bass_kernel_spmd(nc, [{f"in_{n}": a for n, a in arrays.items()}], core_ids=[0])
    got = r.results[0]["out"]
    return np.ascontiguousarray(got.transpose(2, 1, 0)).reshape(1, T, D)
```
